# Optimizing a Trainium2 kernel written in Bass

```python
import math
import jax, jax.numpy as jnp
from jax import lax
import numpy as np
import jax
import jax.numpy as jnp

D_MODEL = 1024
BATCH = 1
SEQ = 512
DEPTH = 2

CHUNK = 64
Q_BLOCK = 128
N_MIXERS = 4
HEAD_DIM = 64
GW = D_MODEL // N_MIXERS
HG = GW // HEAD_DIM
CG = GW // HG
DQ = HEAD_DIM // 2
RW_DECAY_RANK = 32
RW_A_RANK = 32
RW_GATE_RANK = 64
RW_GN_EPS = 64e-5
SG_CHUNK = 128
D_FF = 2816
FFN_CONV = 3
ROPE_THETA = 10000.0
EPS = 1e-6
NEG_INF = -1e30

A_SIZES = [GW, GW, GW, RW_DECAY_RANK, RW_A_RANK, RW_GATE_RANK]
B_SIZES = [GW, GW, GW]
C_SIZES = [GW, GW]
D_SIZES = [GW, GW, GW, HG]
GROUP_COLS = [sum(A_SIZES), sum(B_SIZES), sum(C_SIZES), sum(D_SIZES)]
N_IN = sum(GROUP_COLS)


def _split(t, sizes):
    idx = [int(i) for i in np.cumsum(sizes)[:-1]]
    return jnp.split(t, idx, axis=-1)

def _rms_norm(x, g):
    xf = x.astype(jnp.float32)
    y = xf * lax.rsqrt(jnp.mean(xf * xf, axis=-1, keepdims=True) + EPS)
    return (y * g).astype(x.dtype)

def _layer_norm(x, g, b):
    xf = x.astype(jnp.float32)
    mu = jnp.mean(xf, axis=-1, keepdims=True)
    xc = xf - mu
    var = jnp.mean(xc * xc, axis=-1, keepdims=True)
    return (xc * lax.rsqrt(var + EPS) * g + b).astype(x.dtype)

def _rope_tables(seq, dim):
    inv = 1.0 / (ROPE_THETA ** (jnp.arange(0, dim, 2, dtype=jnp.float32) / dim))
    ang = jnp.arange(seq, dtype=jnp.float32)[:, None] * inv[None, :]
    return jnp.cos(ang), jnp.sin(ang)

def _apply_rope(x, cos, sin):
    x1, x2 = jnp.split(x, 2, axis=-1)
    c = cos.astype(x.dtype)
    s = sin.astype(x.dtype)
    return jnp.concatenate([x1 * c - x2 * s, x2 * c + x1 * s], axis=-1)

def _causal_dwconv(x, w, b):
    K, C = w.shape
    y = lax.conv_general_dilated(x, w[:, None, :].astype(x.dtype), window_strides=(1,),
                                 padding=[(K - 1, 0)],
                                 dimension_numbers=('NWC', 'WIO', 'NWC'),
                                 feature_group_count=C)
    return y + b

def _rwkv7_scan(r, w, k, v, kk, b):
    Bn, S, H, N = r.shape

    def step(state, inp):
        r_t, w_t, k_t, v_t, kk_t, b_t = inp
        sa = jnp.einsum('bhvk,bhk->bhv', state, -kk_t)
        state = (state * w_t[:, :, None, :]
                 + sa[..., None] * b_t[:, :, None, :]
                 + v_t[..., None] * k_t[:, :, None, :])
        return state, jnp.einsum('bhvk,bhk->bhv', state, r_t)

    xs = tuple(jnp.swapaxes(t, 0, 1) for t in (r, w, k, v, kk, b))
    state0 = jnp.zeros((Bn, H, N, N), jnp.float32)
    _, ys = lax.scan(step, state0, xs)
    return jnp.swapaxes(ys, 0, 1)

def _rwkv7_mixer(p, mu, w0, w_up, a0, a_up, g_up, k_k, k_a, r_k, ln_g, ln_b):
    Bn, S, _ = p.shape
    f32 = jnp.float32
    p_prev = jnp.pad(p, ((0, 0), (1, 0), (0, 0)))[:, :-1]
    p = p + (p_prev - p) * mu
    r, k, v, wd, ad, gd = _split(p, A_SIZES)
    w_log = -jax.nn.softplus(-(w0 + jnp.tanh(wd) @ w_up).astype(f32)) - 0.5
    decay = jnp.exp(-jnp.exp(w_log))
    a = jax.nn.sigmoid((a0 + ad @ a_up).astype(f32))
    g = jax.nn.sigmoid(gd) @ g_up
    heads = lambda t: t.reshape(Bn, S, HG, HEAD_DIM)
    k = k.astype(f32)
    kk = heads(k * k_k)
    kk = kk / jnp.maximum(jnp.sqrt(jnp.sum(kk * kk, axis=-1, keepdims=True)), 1e-12)
    k = heads(k * (1.0 + (a - 1.0) * k_a))
    r = heads(r.astype(f32))
    v = heads(v.astype(f32))
    ah = heads(a)
    y = _rwkv7_scan(r, heads(decay), k, v, kk, kk * ah)
    mean = jnp.mean(y, axis=-1, keepdims=True)
    yc = y - mean
    y = yc * lax.rsqrt(jnp.mean(yc * yc, axis=-1, keepdims=True) + RW_GN_EPS)
    y = y.reshape(Bn, S, GW) * ln_g + ln_b
    bonus = jnp.sum(r * k * r_k, axis=-1, keepdims=True) * v
    return (y + bonus.reshape(Bn, S, GW)) * g

def _diff_attention(q1, q2, k1, k2, v, lam):
    Bn, H, S, dq = q1.shape
    scale = dq ** -0.5
    key_chunk = jnp.arange(S) // CHUNK

    def block(i):
        start = i * Q_BLOCK
        q1b = lax.dynamic_slice_in_dim(q1, start, Q_BLOCK, axis=2)
        q2b = lax.dynamic_slice_in_dim(q2, start, Q_BLOCK, axis=2)
        q_chunk = (start + jnp.arange(Q_BLOCK)) // CHUNK
        mask = key_chunk[None, :] <= q_chunk[:, None]
        s1 = jnp.einsum('bhqd,bhkd->bhqk', q1b, k1).astype(jnp.float32) * scale
        s2 = jnp.einsum('bhqd,bhkd->bhqk', q2b, k2).astype(jnp.float32) * scale
        p1 = jax.nn.softmax(jnp.where(mask, s1, NEG_INF), axis=-1)
        p2 = jax.nn.softmax(jnp.where(mask, s2, NEG_INF), axis=-1)
        return jnp.einsum('bhqk,bhkd->bhqd', (p1 - lam * p2).astype(v.dtype), v)

    out = lax.map(block, jnp.arange(S // Q_BLOCK))
    return jnp.moveaxis(out, 0, 2).reshape(Bn, H, S, v.shape[-1])

def _diff_attn_mixer(p, lam_q1, lam_k1, lam_q2, lam_k2, q_g, k_g, sub_g, cos, sin, lambda_init):
    Bn, S, _ = p.shape
    q, k, v = _split(p, B_SIZES)
    q = _rms_norm(q.reshape(Bn, S, HG, 2, DQ), q_g).transpose(0, 3, 2, 1, 4)
    k = _rms_norm(k.reshape(Bn, S, HG, 2, DQ), k_g).transpose(0, 3, 2, 1, 4)
    q = _apply_rope(q, cos, sin)
    k = _apply_rope(k, cos, sin)
    v = v.reshape(Bn, S, HG, HEAD_DIM).transpose(0, 2, 1, 3)
    f32 = jnp.float32
    lam = (jnp.exp(jnp.sum(lam_q1.astype(f32) * lam_k1.astype(f32)))
           - jnp.exp(jnp.sum(lam_q2.astype(f32) * lam_k2.astype(f32))) + lambda_init)
    o = _diff_attention(q[:, 0], q[:, 1], k[:, 0], k[:, 1], v, lam)
    o = _rms_norm(o, sub_g) * (1.0 - lambda_init)
    return o.transpose(0, 2, 1, 3).reshape(Bn, S, GW)

def _spatial_gating_mixer(p, sg_w, sg_b, ln_g, ln_b):
    Bn, S, _ = p.shape
    u, v = _split(jax.nn.gelu(p, approximate=False), C_SIZES)
    v = _layer_norm(v, ln_g, ln_b)
    v = v.reshape(Bn, S // SG_CHUNK, SG_CHUNK, HG, CG)
    w = sg_w * jnp.tril(jnp.ones((SG_CHUNK, SG_CHUNK), sg_w.dtype))
    sv = jnp.einsum('gij,bnjgc->bnigc', w, v) + sg_b.T[None, None, :, :, None]
    return u * sv.reshape(Bn, S, GW)

def _forgetting_attention(q, k, v, log_f):
    Bn, H, S, d = q.shape
    scale = d ** -0.5
    F = lax.cumsum(log_f, axis=2)
    key_pos = jnp.arange(S)

    def block(i):
        start = i * Q_BLOCK
        qb = lax.dynamic_slice_in_dim(q, start, Q_BLOCK, axis=2)
        Fq = lax.dynamic_slice_in_dim(F, start, Q_BLOCK, axis=2)
        q_pos = start + jnp.arange(Q_BLOCK)
        mask = key_pos[None, :] <= q_pos[:, None]
        s = (jnp.einsum('bhqd,bhkd->bhqk', qb, k).astype(jnp.float32) * scale
             + (Fq[..., :, None] - F[..., None, :]))
        pr = jax.nn.softmax(jnp.where(mask, s, NEG_INF), axis=-1)
        return jnp.einsum('bhqk,bhkd->bhqd', pr.astype(v.dtype), v)

    out = lax.map(block, jnp.arange(S // Q_BLOCK))
    return jnp.moveaxis(out, 0, 2).reshape(Bn, H, S, d)

def _forgetting_attn_mixer(p, q_g, k_g, f_b):
    Bn, S, _ = p.shape
    q, k, v, fl = _split(p, D_SIZES)
    q = _rms_norm(q.reshape(Bn, S, HG, HEAD_DIM), q_g).transpose(0, 2, 1, 3)
    k = _rms_norm(k.reshape(Bn, S, HG, HEAD_DIM), k_g).transpose(0, 2, 1, 3)
    v = v.reshape(Bn, S, HG, HEAD_DIM).transpose(0, 2, 1, 3)
    log_f = jax.nn.log_sigmoid((fl + f_b).astype(jnp.float32)).transpose(0, 2, 1)
    o = _forgetting_attention(q, k, v, log_f)
    return o.transpose(0, 2, 1, 3).reshape(Bn, S, GW)

def _conv_glu_ffn(h, w_up, w_conv, b_conv, w_down):
    u = _causal_dwconv(h @ w_up, w_conv, b_conv)
    a, g = jnp.split(u, 2, axis=-1)
    return (a * jax.nn.silu(g)) @ w_down

def first_inputs(seed: int = 0) -> dict:
    key = jax.random.key(seed)
    ks = iter(list(jax.random.split(key, 48)))
    L, D = DEPTH, D_MODEL
    f32 = jnp.float32

    def nrm(shape, scale):
        return jax.random.normal(next(ks), shape, f32) * scale

    def gain(shape):
        return 1.0 + 0.05 * jax.random.normal(next(ks), shape, f32)

    return {
        'x': nrm((BATCH, SEQ, D), 1.0),
        'c': nrm((BATCH, D), 1.0),
        'ada_w': nrm((L, D, 6 * D), 0.5 * D ** -0.5),
        'ada_b': nrm((L, 6 * D), 0.02),
        'norm1_g': gain((L, D)),
        'norm2_g': gain((L, D)),
        'w_in': nrm((L, D, N_IN), D ** -0.5),
        'w_out': nrm((L, D, D), D ** -0.5),
        'rw_mu': jax.random.uniform(next(ks), (L, GROUP_COLS[0]), f32),
        'rw_w0': nrm((L, GW), 0.5),
        'rw_w_up': nrm((L, RW_DECAY_RANK, GW), RW_DECAY_RANK ** -0.5),
        'rw_a0': nrm((L, GW), 0.1),
        'rw_a_up': nrm((L, RW_A_RANK, GW), RW_A_RANK ** -0.5),
        'rw_g_up': nrm((L, RW_GATE_RANK, GW), RW_GATE_RANK ** -0.5),
        'rw_k_k': 0.85 + 0.05 * jax.random.normal(next(ks), (L, GW), f32),
        'rw_k_a': gain((L, GW)),
        'rw_r_k': nrm((L, HG, HEAD_DIM), 0.1),
        'rw_ln_g': gain((L, GW)),
        'rw_ln_b': nrm((L, GW), 0.02),
        'df_lam_q1': nrm((L, DQ), 0.1),
        'df_lam_k1': nrm((L, DQ), 0.1),
        'df_lam_q2': nrm((L, DQ), 0.1),
        'df_lam_k2': nrm((L, DQ), 0.1),
        'df_q_g': gain((L, DQ)),
        'df_k_g': gain((L, DQ)),
        'df_sub_g': gain((L, HEAD_DIM)),
        'sg_w': nrm((L, HG, SG_CHUNK, SG_CHUNK), SG_CHUNK ** -0.5),
        'sg_b': gain((L, HG, SG_CHUNK)),
        'sg_ln_g': gain((L, GW)),
        'sg_ln_b': nrm((L, GW), 0.02),
        'fx_q_g': gain((L, HEAD_DIM)),
        'fx_k_g': gain((L, HEAD_DIM)),
        'fx_f_b': 2.0 + 0.5 * jax.random.normal(next(ks), (L, HG), f32),
        'ffn_up': nrm((L, D, 2 * D_FF), D ** -0.5),
        'ffn_conv': nrm((L, FFN_CONV, 2 * D_FF), FFN_CONV ** -0.5),
        'ffn_conv_b': nrm((L, 2 * D_FF), 0.02),
        'ffn_down': nrm((L, D_FF, D), D_FF ** -0.5),
    }

def first_block(x, c, ada_w, ada_b, norm1_g, norm2_g, w_in, w_out,
              rw_mu, rw_w0, rw_w_up, rw_a0, rw_a_up, rw_g_up, rw_k_k, rw_k_a, rw_r_k,
              rw_ln_g, rw_ln_b,
              df_lam_q1, df_lam_k1, df_lam_q2, df_lam_k2, df_q_g, df_k_g, df_sub_g,
              sg_w, sg_b, sg_ln_g, sg_ln_b,
              fx_q_g, fx_k_g, fx_f_b,
              ffn_up, ffn_conv, ffn_conv_b, ffn_down):
    Bn, S, D = x.shape
    dt = x.dtype
    cos, sin = _rope_tables(S, DQ)
    cond = jax.nn.silu(c)
    for l in range(DEPTH):
        lambda_init = 0.8 - 0.6 * math.exp(-0.3 * l)
        mod = cond @ ada_w[l] + ada_b[l]
        sh1, sc1, g1, sh2, sc2, g2 = [m[:, None, :] for m in jnp.split(mod, 6, axis=-1)]
        h = _rms_norm(x, norm1_g[l]) * (1.0 + sc1) + sh1
        pa, pb, pc, pd = _split(h @ w_in[l], GROUP_COLS)
        ya = _rwkv7_mixer(pa, rw_mu[l], rw_w0[l], rw_w_up[l], rw_a0[l], rw_a_up[l], rw_g_up[l],
                          rw_k_k[l], rw_k_a[l], rw_r_k[l], rw_ln_g[l], rw_ln_b[l])
        yb = _diff_attn_mixer(pb, df_lam_q1[l], df_lam_k1[l], df_lam_q2[l], df_lam_k2[l],
                              df_q_g[l], df_k_g[l], df_sub_g[l], cos, sin, lambda_init)
        yc = _spatial_gating_mixer(pc, sg_w[l], sg_b[l], sg_ln_g[l], sg_ln_b[l])
        yd = _forgetting_attn_mixer(pd, fx_q_g[l], fx_k_g[l], fx_f_b[l])
        y = jnp.concatenate([ya.astype(dt), yb.astype(dt), yc.astype(dt), yd.astype(dt)], axis=-1)
        x = x + g1 * (y @ w_out[l])
        h = _rms_norm(x, norm2_g[l]) * (1.0 + sc2) + sh2
        x = x + g2 * _conv_glu_ffn(h, ffn_up[l], ffn_conv[l], ffn_conv_b[l], ffn_down[l])
    return x


DEPTH_2 = 1

GRID_W = 64
CTX_LEN = 256
N_MIXERS_2 = 2

GLA_HEADS = 4
GLA_KDIM = D_MODEL // 2
GLA_VDIM = D_MODEL
GLA_KHEAD = GLA_KDIM // GLA_HEADS
GLA_VHEAD = GLA_VDIM // GLA_HEADS
GLA_GATE_RANK = 16
GLA_GATE_NORM = 16.0
GLA_CHUNK = 64

POOL_WINDOWS = (2, 4, 8, 16)
POOL_GROUP = D_MODEL // len(POOL_WINDOWS)

N_EXPERTS = 16
N_EXPERT_GROUPS = 4
EXPERTS_PER_GROUP = N_EXPERTS // N_EXPERT_GROUPS
TOP_K = 2
D_EXPERT = D_MODEL // 2


def _rmsnorm(x, g):
    xf = x.astype(jnp.float32)
    y = xf * lax.rsqrt(jnp.mean(xf * xf, axis=-1, keepdims=True) + EPS)
    return (y * g.astype(jnp.float32)).astype(x.dtype)

def _modulate(h, shift, scale):
    return h * (1 + scale) + shift

def _gla_scan(q, k, v, g, s0, with_outputs):
    bsz, nh, t, _ = q.shape
    dv = v.shape[-1]
    n = t // GLA_CHUNK

    def chunks(a):
        a = a.astype(jnp.float32).reshape(bsz, nh, n, GLA_CHUNK, a.shape[-1])
        return jnp.moveaxis(a, 2, 0)

    lower = jnp.tril(jnp.ones((GLA_CHUNK, GLA_CHUNK), dtype=bool))[:, :, None]

    def step(s, inp):
        qc, kc, vc, gc = inp
        cum = jnp.cumsum(gc, axis=2)
        last = cum[:, :, -1:, :]
        s_new = jnp.exp(last[:, :, 0, :])[..., None] * s + jnp.einsum(
            'bhjd,bhje->bhde', kc * jnp.exp(last - cum), vc)
        if not with_outputs:
            return s_new, None
        diff = cum[:, :, :, None, :] - cum[:, :, None, :, :]
        decay = jnp.exp(jnp.where(lower, diff, -jnp.inf))
        scores = jnp.einsum('bhid,bhjd,bhijd->bhij', qc, kc, decay)
        o = jnp.einsum('bhid,bhde->bhie', qc * jnp.exp(cum), s) + jnp.einsum(
            'bhij,bhje->bhie', scores, vc)
        return s_new, o

    s_fin, o = lax.scan(step, s0, (chunks(q), chunks(k), chunks(v), chunks(g)))
    if not with_outputs:
        return None, s_fin
    o = jnp.moveaxis(o, 0, 2).reshape(bsz, nh, t, dv)
    return o, s_fin

def _gla_project(h, w_in, w_ga, w_gb, b_g):
    bsz, t, _ = h.shape
    proj = h @ w_in
    q, k, v, r = jnp.split(proj, [GLA_KDIM, 2 * GLA_KDIM, 2 * GLA_KDIM + GLA_VDIM], axis=-1)

    def heads(a, d):
        return a.reshape(bsz, t, GLA_HEADS, d).transpose(0, 2, 1, 3)

    q = heads(q, GLA_KHEAD) * (GLA_KHEAD ** -0.5)
    k = heads(k, GLA_KHEAD)
    v = heads(v, GLA_VHEAD)
    low = jnp.einsum('btd,zdr->zbtr', h, w_ga)
    z = jnp.einsum('zbtr,zrk->zbtk', low, w_gb) + b_g[:, None, None, :]
    logdecay = jax.nn.log_sigmoid(z.astype(jnp.float32)) / GLA_GATE_NORM
    logdecay = logdecay.reshape(2, bsz, t, GLA_HEADS, GLA_KHEAD).transpose(0, 1, 3, 2, 4)
    return q, k, v, r, logdecay

def _gla_readout(o, r, norm_g, w_out):
    bsz, _, t, _ = o.shape
    o = o * lax.rsqrt(jnp.mean(o * o, axis=-1, keepdims=True) + EPS) * norm_g.astype(jnp.float32)
    o = o.transpose(0, 2, 1, 3).reshape(bsz, t, GLA_VDIM).astype(r.dtype)
    return (o * jax.nn.silu(r)) @ w_out

def _gla_mixer(h_lat, h_ctx, w_in, w_ga, w_gb, b_g, norm_g, w_out, ctx_out):
    ql, kl, vl, rl, gl = _gla_project(h_lat, w_in, w_ga, w_gb, b_g)
    qc, kc, vc, rc, gc = _gla_project(h_ctx, w_in, w_ga, w_gb, b_g)

    def flip(a):
        return jnp.flip(a, axis=2)

    s0 = jnp.zeros((h_lat.shape[0], GLA_HEADS, GLA_KHEAD, GLA_VHEAD), jnp.float32)
    oc_f, sc_f = _gla_scan(qc, kc, vc, gc[0], s0, ctx_out)
    oc_b, sc_b = _gla_scan(flip(qc), flip(kc), flip(vc), flip(gc[1]), s0, ctx_out)
    ol_f, _ = _gla_scan(ql, kl, vl, gl[0], sc_f, True)
    ol_b, _ = _gla_scan(flip(ql), flip(kl), flip(vl), flip(gl[1]), sc_b, True)
    y_lat = _gla_readout(ol_f + flip(ol_b), rl, norm_g, w_out)
    y_ctx = _gla_readout(oc_f + flip(oc_b), rc, norm_g, w_out) if ctx_out else None
    return y_lat, y_ctx

def _pool_mixer(h, w_pool, b_pool, scale):
    s, l, _ = h.shape
    hf = h.astype(jnp.float32).reshape(s, l, len(POOL_WINDOWS), POOL_GROUP)
    csum = jnp.concatenate([jnp.zeros_like(hf[:, :1]), jnp.cumsum(hf, axis=1)], axis=1)
    pos = np.arange(l)
    outs = []
    for gi, w in enumerate(POOL_WINDOWS):
        lo = np.clip(pos - w // 2, 0, l)
        hi = np.clip(pos - w // 2 + w, 0, l)
        cnt = (hi - lo).astype(np.float32)
        mean = (csum[:, hi, gi] - csum[:, lo, gi]) / cnt[None, :, None]
        outs.append(mean - hf[:, :, gi])
    pooled = jnp.stack(outs, axis=2).astype(h.dtype)
    y = jnp.einsum('slgc,gce->slge', pooled, w_pool) + b_pool
    return y.reshape(s, l, D_MODEL) * scale

def _moe(h, w_router, b_router, w1, w3, w2):
    n = h.shape[0]
    scores = jax.nn.sigmoid((h @ w_router).astype(jnp.float32))
    sel = scores + b_router.astype(jnp.float32)
    grp = sel.reshape(n, N_EXPERT_GROUPS, EXPERTS_PER_GROUP)
    grp_score = jnp.sum(lax.top_k(grp, TOP_K)[0], axis=-1)
    best = jnp.argmax(grp_score, axis=-1)
    in_group = (jnp.arange(N_EXPERTS) // EXPERTS_PER_GROUP)[None, :] == best[:, None]
    _, idx = lax.top_k(jnp.where(in_group, sel, -jnp.inf), TOP_K)
    wts = jnp.take_along_axis(scores, idx, axis=-1)
    wts = wts / jnp.sum(wts, axis=-1, keepdims=True)
    gates = jnp.sum(jax.nn.one_hot(idx, N_EXPERTS, dtype=jnp.float32) * wts[..., None], axis=1)
    gates = gates.astype(h.dtype)
    out = jnp.zeros_like(h)
    for e in range(N_EXPERTS):
        he = jax.nn.silu(h @ w1[e]) * (h @ w3[e])
        out = out + gates[:, e:e + 1] * (he @ w2[e])
    return out

def second_inputs(seed: int = 0) -> dict:
    key = jax.random.key(seed)
    ks = jax.random.split(key, 24)
    n_gla = len(range(0, DEPTH_2, N_MIXERS_2))
    n_pool = len(range(1, DEPTH_2, N_MIXERS_2))
    f32 = jnp.float32

    def nrm(k, shape, fan):
        return jax.random.normal(k, shape, f32) * (fan ** -0.5)

    def rnd(k, shape, s):
        return jax.random.normal(k, shape, f32) * s

    return {
        'x': rnd(ks[0], (BATCH, SEQ, D_MODEL), 1.0),
        'c': rnd(ks[1], (BATCH, D_MODEL), 1.0),
        'ctx': rnd(ks[2], (BATCH, CTX_LEN, D_MODEL), 1.0),
        'c_ctx': rnd(ks[3], (D_MODEL,), 1.0),
        'norm1_g': 1.0 + rnd(ks[4], (DEPTH_2, D_MODEL), 0.02),
        'norm2_g': 1.0 + rnd(ks[5], (DEPTH_2, D_MODEL), 0.02),
        'w_mod': 0.5 * nrm(ks[6], (DEPTH_2, D_MODEL, 6 * D_MODEL), D_MODEL),
        'b_mod': rnd(ks[7], (DEPTH_2, 6 * D_MODEL), 0.02),
        'gla_w_in': nrm(ks[8], (n_gla, D_MODEL, 2 * GLA_KDIM + 2 * GLA_VDIM), D_MODEL),
        'gla_w_gate_a': nrm(ks[9], (n_gla, 2, D_MODEL, GLA_GATE_RANK), D_MODEL),
        'gla_w_gate_b': nrm(ks[10], (n_gla, 2, GLA_GATE_RANK, GLA_KDIM), GLA_GATE_RANK),
        'gla_b_gate': rnd(ks[11], (n_gla, 2, GLA_KDIM), 0.1),
        'gla_norm_g': 1.0 + rnd(ks[12], (n_gla, GLA_VHEAD), 0.02),
        'gla_w_out': nrm(ks[13], (n_gla, GLA_VDIM, D_MODEL), GLA_VDIM),
        'pool_w': nrm(ks[14], (n_pool, len(POOL_WINDOWS), POOL_GROUP, POOL_GROUP), POOL_GROUP),
        'pool_b': rnd(ks[15], (n_pool, len(POOL_WINDOWS), POOL_GROUP), 0.02),
        'pool_scale': 1.0 + rnd(ks[16], (n_pool, D_MODEL), 0.1),
        'w_router': nrm(ks[17], (D_MODEL, N_EXPERTS), D_MODEL),
        'b_router': rnd(ks[18], (N_EXPERTS,), 0.01),
        'w_gate_e': nrm(ks[19], (DEPTH_2, N_EXPERTS, D_MODEL, D_EXPERT), D_MODEL),
        'w_up_e': nrm(ks[20], (DEPTH_2, N_EXPERTS, D_MODEL, D_EXPERT), D_MODEL),
        'w_down_e': nrm(ks[21], (DEPTH_2, N_EXPERTS, D_EXPERT, D_MODEL), D_EXPERT),
        'final_g': 1.0 + rnd(ks[22], (D_MODEL,), 0.02),
    }

def second_block(x, c, ctx, c_ctx, norm1_g, norm2_g, w_mod, b_mod, gla_w_in, gla_w_gate_a,
              gla_w_gate_b, gla_b_gate, gla_norm_g, gla_w_out, pool_w, pool_b, pool_scale,
              w_router, b_router, w_gate_e, w_up_e, w_down_e, final_g):
    bsz, t, _ = x.shape
    rows = t // GRID_W
    n_lat = bsz * t
    for i in range(DEPTH_2):
        mixer = i % N_MIXERS_2
        slot = i // N_MIXERS_2
        ctx_next = any(j % N_MIXERS_2 == 0 for j in range(i + 1, DEPTH_2))
        use_ctx = mixer == 0 or ctx_next

        mod = jax.nn.silu(c) @ w_mod[i] + b_mod[i]
        sh1, sc1, g1, sh2, sc2, g2 = jnp.split(mod[:, None, :], 6, axis=-1)
        h = _modulate(_rmsnorm(x, norm1_g[i]), sh1, sc1)
        if use_ctx:
            mod_c = jax.nn.silu(c_ctx) @ w_mod[i] + b_mod[i]
            csh1, csc1, cg1, csh2, csc2, cg2 = jnp.split(mod_c, 6, axis=-1)
            hc = _modulate(_rmsnorm(ctx, norm1_g[i]), csh1, csc1)

        if mixer == 0:
            y, yc = _gla_mixer(h, hc, gla_w_in[slot], gla_w_gate_a[slot], gla_w_gate_b[slot],
                               gla_b_gate[slot], gla_norm_g[slot], gla_w_out[slot], ctx_next)
        else:
            y = _pool_mixer(h.reshape(bsz * rows, GRID_W, D_MODEL), pool_w[slot], pool_b[slot],
                            pool_scale[slot]).reshape(bsz, t, D_MODEL)
            yc = _pool_mixer(hc, pool_w[slot], pool_b[slot], pool_scale[slot]) if ctx_next else None

        x = x + g1 * y
        h2 = _modulate(_rmsnorm(x, norm2_g[i]), sh2, sc2).reshape(n_lat, D_MODEL)
        if ctx_next:
            ctx = ctx + cg1 * yc
            h2c = _modulate(_rmsnorm(ctx, norm2_g[i]), csh2, csc2).reshape(-1, D_MODEL)
            f = _moe(jnp.concatenate([h2, h2c], axis=0), w_router, b_router,
                     w_gate_e[i], w_up_e[i], w_down_e[i])
            x = x + g2 * f[:n_lat].reshape(bsz, t, D_MODEL)
            ctx = ctx + cg2 * f[n_lat:].reshape(ctx.shape)
        else:
            f = _moe(h2, w_router, b_router, w_gate_e[i], w_up_e[i], w_down_e[i])
            x = x + g2 * f.reshape(bsz, t, D_MODEL)
    return _rmsnorm(x, final_g)


def setup_inputs(seed=0):
    out = dict(first_inputs(seed))
    for name, value in second_inputs(seed + 1).items():
        if name != "x":
            out[name + "_2"] = value
    return out


def reference(
    x, c, ada_w, ada_b, norm1_g, norm2_g, w_in, w_out, rw_mu, rw_w0, rw_w_up, rw_a0, rw_a_up,
    rw_g_up, rw_k_k, rw_k_a, rw_r_k, rw_ln_g, rw_ln_b, df_lam_q1, df_lam_k1, df_lam_q2,
    df_lam_k2, df_q_g, df_k_g, df_sub_g, sg_w, sg_b, sg_ln_g, sg_ln_b, fx_q_g, fx_k_g, fx_f_b,
    ffn_up, ffn_conv, ffn_conv_b, ffn_down, c_2, ctx_2, c_ctx_2, norm1_g_2, norm2_g_2, w_mod_2,
    b_mod_2, gla_w_in_2, gla_w_gate_a_2, gla_w_gate_b_2, gla_b_gate_2, gla_norm_g_2,
    gla_w_out_2, pool_w_2, pool_b_2, pool_scale_2, w_router_2, b_router_2, w_gate_e_2, w_up_e_2,
    w_down_e_2, final_g_2,
):
    x = first_block(
        x, c, ada_w, ada_b, norm1_g, norm2_g, w_in, w_out, rw_mu, rw_w0, rw_w_up, rw_a0,
        rw_a_up, rw_g_up, rw_k_k, rw_k_a, rw_r_k, rw_ln_g, rw_ln_b, df_lam_q1, df_lam_k1,
        df_lam_q2, df_lam_k2, df_q_g, df_k_g, df_sub_g, sg_w, sg_b, sg_ln_g, sg_ln_b, fx_q_g,
        fx_k_g, fx_f_b, ffn_up, ffn_conv, ffn_conv_b, ffn_down,
    )
    return second_block(
        x, c_2, ctx_2, c_ctx_2, norm1_g_2, norm2_g_2, w_mod_2, b_mod_2, gla_w_in_2,
        gla_w_gate_a_2, gla_w_gate_b_2, gla_b_gate_2, gla_norm_g_2, gla_w_out_2, pool_w_2,
        pool_b_2, pool_scale_2, w_router_2, b_router_2, w_gate_e_2, w_up_e_2, w_down_e_2,
        final_g_2,
    )


_drawn_inputs = setup_inputs


def setup_inputs(seed=0):
    import zlib

    import numpy as np

    out = dict(_drawn_inputs(seed))
    spreads = {}
    factors = {'rw_a0': 4.173,
     'rw_k_k': 22.183,
     'rw_k_a': 3.582,
     'rw_ln_g': 4.36,
     'rw_ln_b': 8.0,
     'df_lam_q1': 8.0,
     'df_lam_k1': 7.702,
     'df_lam_q2': 3.647,
     'df_lam_k2': 2.998,
     'df_q_g': 8.0,
     'df_k_g': 5.031,
     'df_sub_g': 2.764,
     'sg_b': 3.221,
     'sg_ln_g': 4.397,
     'sg_ln_b': 7.712,
     'fx_q_g': 5.176,
     'fx_k_g': 8.0,
     'ffn_conv_b': 3.388,
     'c_ctx_2': 3.059,
     'norm1_g_2': 3.927,
     'gla_b_gate_2': 2.702,
     'gla_norm_g_2': 16.006,
     'final_g_2': 8.61,
     'norm2_g_2': 8.0,
     'b_router_2': 6.357}
    for name, (base, spread) in spreads.items():
        noise = np.random.default_rng([zlib.crc32(name.encode()), seed]).standard_normal(out[name].shape)
        drawn = base * np.exp(spread * noise) if base else spread * noise
        out[name] = jnp.asarray(drawn.astype(out[name].dtype))
    for name, factor in factors.items():
        out[name] = (out[name] * factor).astype(out[name].dtype)
    return out
```

```python
import math
from contextlib import ExitStack, contextmanager

import numpy as np
import concourse.bass as bass
from concourse import mybir

F32 = mybir.dt.float32
ACT = mybir.ActivationFunctionType
ALU = mybir.AluOpType
AXX = mybir.AxisListType.X

P = 128
D = 1024
KT = D // P
S = 512
L = 2
NMOD = 6 * KT
FF = 2816
FT = FF // P
IN_T = 24
RING = 4
CH = 64
NCH = S // CH
E_N = 16
DE = 512
ET = DE // P
CTX = 256
LNC = CTX // CH
EPS = 1e-6
GN_EPS = 64e-5
NEG = -1e30

COLS = [("norm1_g", 8), ("norm2_g", 8), ("rw_mu", 7), ("rw_w0", 2), ("rw_a0", 2), ("rw_k_k", 2), ("rw_k_a", 2),
        ("rw_r_k", 2), ("rw_ln_g", 2), ("rw_ln_b", 2), ("df_q_g", 1), ("df_k_g", 1), ("df_sub_g", 1),
        ("sg_ln_g", 2), ("sg_ln_b", 2), ("fx_q_g", 1), ("fx_k_g", 1), ("fx_f_b", 1), ("lam_init", 1),
        ("lam_vec", 128), ("ffn_tap", 176), ("ffn_bias", 44)]
COLS2 = [("norm1_g", 8), ("norm2_g", 8), ("final_g", 8), ("b_gate", 8), ("gla_norm_g", 2), ("b_router", 16)]
CONST = [("ident", 128), ("ones", 128), ("bo64", 128), ("bo32", 128), ("perm", 128), ("cos", 512), ("sin", 512),
         ("mask_causal", 128), ("mask_chunk", 128), ("scan", 512), ("m_ld", 512), ("m_ldT", 512), ("m_loT", 512),
         ("m_kaT", 512), ("m_r", 512), ("ident4", 512), ("gla_f", 256), ("gla_b", 256), ("eps", 1), ("gn_eps", 1),
         ("kk_shift", 1)]
KK_SCALE = 2.0 ** 40


def offsets(table):
    at, n = {}, 0
    for name, width in table:
        at[name] = n
        n += width
    return at, n


C_AT, C_N = offsets(COLS)
C2_AT, C2_N = offsets(COLS2)
K_AT, K_N = offsets(CONST)


class Core:

    def __init__(self, nc, ctx, dram):
        self.nc, self.ctx, self.dram = nc, ctx, dram
        self.groups = []

        def sb(name, *shape):
            return ctx.enter_context(nc.sbuf_tensor(name, [P, *shape], F32))

        self.x = sb("x", KT, S)
        self.h = sb("h", KT, S)
        self.p = sb("p", IN_T, S)
        self.y = sb("y", KT, S)
        self.ring = sb("ring", 4 * FT * P)
        self.vt = sb("vt", 4, 1024)
        self.k = sb("k", K_N)
        self.cols = sb("cols", C_N)
        self.mod = sb("mod", NMOD)
        self.w2b = sb("w2b", 4, 1024)
        self.cols2 = sb("cols2", C2_N)
        self.cond = sb("cond", KT)
        self.ctxmod = sb("ctxmod", 2 * KT)
        self.small = sb("small", 128)
        self.small2 = sb("small2", 256)
        self.acc = [self.y[:, 2 * i:2 * i + 2, :].rearrange("p a n -> p (a n)") for i in range(4)]
        self.acc += [self.vt[:, i, :] for i in range(2)]
        self.piece = [self.vt[:, 2 + i, :] for i in range(2)]
        self.ps = ctx.enter_context(nc.psum_tensor("ps", [P, 8, 512], F32))

    def sem(self, name):
        stack, sems = self.groups[-1]
        s = stack.enter_context(self.nc.semaphore(name))
        sems.append(s)
        return s

    @contextmanager
    def stages(self):
        with ExitStack() as stack:
            self.groups.append((stack, []))
            yield
            _, sems = self.groups.pop()
            self.clear(sems)

    def const(self, name, width=None):
        at = K_AT[name]
        return self.k[:, at:at + (width or dict(CONST)[name])]

    def col(self, name, i=0, n=1):
        at = C_AT[name] + i
        return self.cols[:, at:at + n]

    def slot(self, s, size=D):
        return self.ring[:, s * size:(s + 1) * size]

    def clear(self, sems):
        nc = self.nc
        with nc.Block() as block:
            @block.gpsimd
            def _(pool):
                for s in sems:
                    nc.gpsimd.sem_clear(s)


class Chain:

    def __init__(self, eng, sem):
        self.eng, self.sem, self.n = eng, sem, 0

    def __call__(self, ins):
        self.n += 1
        ins.then_inc(self.sem, 1)
        self.eng.wait_ge(self.sem, self.n)


def load_constants(c):
    nc, dram = c.nc, c.dram
    loaded = c.sem("const_loaded")
    with nc.Block() as block:
        @block.sync
        def _(sp):
            sp.dma_start(c.k[:, :], dram["const"]).then_inc(loaded, 16)
            for t in range(KT):
                sp.dma_start(c.x[:, t, :], dram["xT"][t, :, :]).then_inc(loaded, 16)
            sp.wait_ge(loaded, 16 * (KT + 1))


class AdaLN:

    def __init__(self, c, name, which, width=6 * D):
        self.c, self.which, self.per_row = c, which, width // D
        self.pieces = KT * self.per_row
        self.loaded = [c.sem(f"{name}_piece_loaded{i}") for i in range(2)]
        self.used = c.sem(f"{name}_piece_used")

    def load(self, queue):
        for n in range(self.pieces):
            kt, j = divmod(n, self.per_row)
            if n >= 2:
                queue.wait_ge(self.used, n - 1)
            src = self.c.dram["ada"][bass.ds(self.which, 1), :, kt, j * D:(j + 1) * D]
            queue.dma_start(self.c.piece[n % 2], src.rearrange("a p n -> p (a n)")).then_inc(self.loaded[n % 2], 16)

    def add(self, dve, first, last):
        c, nc = self.c, self.c.nc
        for n in range(first, last):
            kt, j = divmod(n, self.per_row)
            dve.wait_ge(self.loaded[n % 2], 16 * (n // 2 + 1))
            out, cond = c.acc[j], c.cond[:, kt:kt + 1]
            if kt == 0:
                ins = nc.vector.tensor_scalar(out, c.piece[n % 2], cond, None, ALU.mult)
            else:
                dve.wait_ge(self.used, n - self.per_row + 1)
                ins = nc.vector.scalar_tensor_tensor(out, c.piece[n % 2], cond, out, ALU.mult, ALU.add)
            ins.then_inc(self.used, 1)


def load_cond(c, name, which):
    nc, dram = c.nc, c.dram
    loaded, ready = c.sem(f"{name}_cond_loaded"), c.sem(f"{name}_cond_ready")

    def scalar(act):
        act.dma_start(c.small[:, 0:KT], dram["cond"][bass.ds(which, 1), :, :].rearrange("a p n -> p (a n)")
                      ).then_inc(loaded, 16)
        act.wait_ge(loaded, 16)
        nc.scalar.activation(c.cond[:, :], c.small[:, 0:KT], ACT.Silu).then_inc(ready, 1)

    return scalar, ready


def adaln_finish(c, name, which, dst, width=6 * D):
    nc, dram = c.nc, c.dram
    summed, biased, loaded = c.sem(f"{name}_summed"), c.sem(f"{name}_biased"), c.sem(f"{name}_bias_loaded")
    n = width // P
    with nc.Block() as block:
        @block.sync
        def _(sp):
            sp.dma_start(dst, dram["ada_b"][bass.ds(which, 1), :, 0:n].rearrange("a p n -> p (a n)")
                         ).then_inc(loaded, 16)

        @block.tensor
        def _(pe):
            for t in range(n):
                last = nc.tensor.matmul(c.ps[:, 0, t:t + 1], c.acc[t // KT][:, t % KT * P:(t % KT + 1) * P], c.const("ones", 1),
                                        start=True, stop=True)
            last.then_inc(summed, 1)

        @block.vector
        def _(dve):
            dve.wait_ge(loaded, 16)
            dve.wait_ge(summed, 1)
            nc.vector.tensor_tensor(dst, c.ps[:, 0, 0:n], dst, ALU.add).then_inc(biased, 1)
            dve.wait_ge(biased, 1)


def norm_modulate(c, name, x, h, gain, scale, shift, n_tok=S, extra_act=None, extra_sp=None, tmp=None):
    nc = c.nc
    squared, summed, rs_ready = c.sem(f"{name}_squared"), c.sem(f"{name}_summed"), c.sem(f"{name}_rs")
    a_ready, scaled, done = c.sem(f"{name}_a"), c.sem(f"{name}_scaled"), c.sem(f"{name}_done")
    rs = tmp[:, 0:n_tok]
    a = c.small[:, 16:24]
    with nc.Block() as block:
        if extra_sp is not None:
            @block.sync
            def _(sp):
                extra_sp(sp)

        @block.tensor
        def _(pe):
            for t in range(KT):
                pe.wait_ge(squared, t + 1)
                last = nc.tensor.matmul(c.ps[:, 0, 0:n_tok], c.const("ones"), h[:, t, :], start=(t == 0),
                                        stop=(t == KT - 1))
            last.then_inc(summed, 1)

        @block.scalar
        def _(act):
            for t in range(KT):
                nc.scalar.activation(h[:, t, :], x[:, t, :], ACT.Square).then_inc(squared, 1)
            act.wait_ge(summed, 1)
            nc.scalar.activation(rs, c.ps[:, 0, 0:n_tok], ACT.Ln, bias=c.const("eps"), scale=1.0 / D
                                 ).then_inc(rs_ready, 1)
            act.wait_ge(rs_ready, 1)
            nc.scalar.activation(rs, rs, ACT.Exp, scale=-0.5).then_inc(rs_ready, 1)
            for t in range(KT):
                if shift is not None:
                    act.wait_ge(scaled, t + 1)
                    nc.scalar.activation(h[:, t, :], h[:, t, :], ACT.Identity, bias=shift[:, t:t + 1]
                                         ).then_inc(done, 1)
            if extra_act is not None:
                extra_act(act)

        @block.vector
        def _(dve):
            if scale is not None:
                nc.vector.tensor_scalar(a, scale, 1.0, None, ALU.add).then_inc(a_ready, 1)
                dve.wait_ge(a_ready, 1)
                nc.vector.tensor_tensor(a, a, gain, ALU.mult).then_inc(a_ready, 1)
                dve.wait_ge(a_ready, 2)
            g = a if scale is not None else gain
            dve.wait_ge(rs_ready, 2)
            for t in range(KT):
                nc.vector.scalar_tensor_tensor(h[:, t, :], x[:, t, :], g[:, t:t + 1], rs, ALU.mult, ALU.mult
                                               ).then_inc(scaled, 1)


class Linear:

    def __init__(self, c, name, n_tiles, weights, k_tiles=KT, size=D):
        self.c, self.n, self.weights, self.kt, self.size = c, n_tiles, weights, k_tiles, size
        assert n_tiles % RING == 0
        self.loaded = [c.sem(f"{name}_w_loaded{s}") for s in range(RING)]
        self.multiplied = c.sem(f"{name}_multiplied")
        self.emptied = c.sem(f"{name}_bank_emptied")

    def prefetch(self, sp):
        for s in range(RING):
            sp.dma_start(self.c.slot(s, self.size), self.weights(s)).then_inc(self.loaded[s], 16)

    def load(self, sp):
        with sp.Fori(1, self.n // RING) as g:
            for s in range(RING):
                sp.wait_ge(self.multiplied, (g - 1) * RING + s + 1)
                sp.dma_start(self.c.slot(s, self.size), self.weights(g * RING + s)).then_inc(self.loaded[s], 16)

    def multiply(self, pe, rhs):
        nc, c = self.c.nc, self.c

        def tile(s, g):
            pe.wait_ge(self.loaded[s], 16 * (g + 1))
            w = c.slot(s, self.size)
            for kt in range(self.kt):
                last = nc.tensor.matmul(c.ps[:, s, :], w[:, kt * P:(kt + 1) * P], rhs(kt), start=(kt == 0),
                                        stop=(kt == self.kt - 1))
            last.then_inc(self.multiplied, 1)

        for s in range(RING):
            tile(s, 0)
        with pe.Fori(1, self.n // RING) as g:
            for s in range(RING):
                pe.wait_ge(self.emptied, (g - 1) * RING + s + 1)
                tile(s, g)


def copy_out_tiles(c, lin, act, dst):
    nc = c.nc
    with act.Fori(0, lin.n // RING) as g:
        for s in range(RING):
            act.wait_ge(lin.multiplied, g * RING + s + 1)
            out = dst[:, bass.ds(g * RING + s, 1), :].rearrange("p a n -> p (a n)")
            nc.scalar.activation(out, c.ps[:, s, :], ACT.Copy).then_inc(lin.emptied, 1)


def residual_tiles(c, lin, dve, gate, first=0, last=KT):
    nc = c.nc
    for t in range(first, last):
        dve.wait_ge(lin.multiplied, t + 1)
        nc.vector.scalar_tensor_tensor(c.x[:, t, :], c.ps[:, t % RING, :], gate[:, t:t + 1], c.x[:, t, :], ALU.mult,
                                       ALU.add).then_inc(lin.emptied, 1)


def after(steps, n):
    return sum(s <= n for s in steps)


T_A, T_B, T_C, T_D = 0, 7, 13, 17
V_B, V_D, V_C = 0, 256, 512
Y_A, Y_B, Y_C, Y_D = 0, 2, 4, 6


def scratch(c, i, n=1):
    at = RING * D + i * S
    return c.ring[:, at:at + n * S]


def prepare_attentions(c, name, prefetch):
    nc = c.nc
    blocks, blocks_out = c.sem(f"{name}_v_transposed"), c.sem(f"{name}_v_copied")
    squared, summed = c.sem(f"{name}_squared"), c.sem(f"{name}_summed")
    rs_step, rs_ready, normed = c.sem(f"{name}_rs_step"), c.sem(f"{name}_rs_ready"), c.sem(f"{name}_normed")
    gains = c.sem(f"{name}_gains")
    rotated, roped = c.sem(f"{name}_rotated"), c.sem(f"{name}_roped")
    f_in, f_exp, f_dve, f_ready, f_moved = (c.sem(f"{name}_f_{n}") for n in ("in", "exp", "dve", "ready", "moved"))
    f_one = c.sem(f"{name}_f_one")

    qb, qd = c.small[:, 24:25], c.small[:, 25:26]
    jobs = [(T_B + 0, "bo32", 32, qb), (T_B + 1, "bo32", 32, qb), (T_B + 2, "bo32", 32, c.col("df_k_g")),
            (T_B + 3, "bo32", 32, c.col("df_k_g")), (T_D + 0, "bo64", 64, qd), (T_D + 1, "bo64", 64, qd),
            (T_D + 2, "bo64", 64, c.col("fx_k_g")), (T_D + 3, "bo64", 64, c.col("fx_k_g"))]
    values = [(T_B + 4, V_B), (T_B + 5, V_B + P), (T_D + 4, V_D), (T_D + 5, V_D + P)]
    sq = [scratch(c, i) for i in range(2)]
    rs = [scratch(c, 2 + i) for i in range(2)]
    turn = scratch(c, 4)
    f_gate, f_abs = scratch(c, 5)[0:4, :], scratch(c, 6)[0:4, :]
    f_neg = scratch(c, 7)[0:4, :]

    with nc.Block() as block:
        @block.sync
        def _(sp):
            prefetch(sp)
            sp.wait_ge(f_ready, 2)
            sp.wait_ge(f_one, 2)
            for h in range(4):
                sp.dma_start(c.h[1:2, h, :], f_gate[h:h + 1, :]).then_inc(f_moved, 16)
                sp.dma_start(c.h[0:1, 4 + h, :], f_neg[h:h + 1, :]).then_inc(f_moved, 16)
            sp.wait_ge(f_moved, 16 * 8)

        @block.gpsimd
        def _(pool):
            nc.gpsimd.memset(c.h[0:2, 0:4, :], 1.0).then_inc(f_one, 1)
            nc.gpsimd.memset(c.h[0:2, 4:8, :], 1.0).then_inc(f_one, 1)

        @block.tensor
        def _(pe):
            for j, (tile, _) in enumerate(values):
                for b in range(4):
                    last = nc.tensor.transpose(c.ps[:, 4 + j, b * P:(b + 1) * P], c.p[:, tile, b * P:(b + 1) * P],
                                               c.const("ident"))
                last.then_inc(blocks, 1)
            for j, (_, ones, _, _) in enumerate(jobs):
                pe.wait_ge(squared, j + 1)
                if j >= 2:
                    pe.wait_ge(rs_step, j - 1)
                nc.tensor.matmul(c.ps[:, j % 2, :], c.const(ones), sq[j % 2], start=True, stop=True
                                 ).then_inc(summed, 1)
            for j in range(4):
                pe.wait_ge(normed, j + 1)
                if j >= 2:
                    pe.wait_ge(roped, 3 * (j - 2) + 1)
                nc.tensor.matmul(c.ps[:, 2 + j % 2, :], c.const("perm"), c.p[:, T_B + j, :], start=True, stop=True
                                 ).then_inc(rotated, 1)

        @block.scalar
        def _(act):
            nc.scalar.activation(f_gate, c.p[0:4, IN_T - 1, :], ACT.Identity, bias=c.col("fx_f_b")[0:4, :]
                                 ).then_inc(f_in, 1)
            act.wait_ge(f_in, 1)
            nc.scalar.activation(f_abs, f_gate, ACT.Abs).then_inc(f_in, 1)
            act.wait_ge(f_in, 2)
            nc.scalar.activation(f_abs, f_abs, ACT.Exp, scale=-1.0).then_inc(f_in, 1)
            act.wait_ge(f_in, 3)
            nc.scalar.activation(f_abs, f_abs, ACT.Ln, bias=1.0).then_inc(f_exp, 1)
            for j, (_, off) in enumerate(values):
                act.wait_ge(blocks, j + 1)
                nc.scalar.activation(c.vt[:, :, off:off + P], c.ps[:, 4 + j, :].rearrange("p (b n) -> p b n", b=4),
                                     ACT.Copy).then_inc(blocks_out, 1)

            def square(j):
                if j >= 2:
                    act.wait_ge(summed, j - 1)
                nc.scalar.activation(sq[j % 2], c.p[:, jobs[j][0], :], ACT.Square).then_inc(squared, 1)

            square(0)
            for j, (_, _, n, _) in enumerate(jobs):
                if j + 1 < len(jobs):
                    square(j + 1)
                act.wait_ge(summed, j + 1)
                if j >= 2:
                    act.wait_ge(normed, j - 1)
                nc.scalar.activation(rs[j % 2], c.ps[:, j % 2, :], ACT.Ln, bias=c.const("eps"), scale=1.0 / n
                                     ).then_inc(rs_step, 1)
                act.wait_ge(rs_step, j + 1)
                nc.scalar.activation(rs[j % 2], rs[j % 2], ACT.Exp, scale=-0.5).then_inc(rs_ready, 1)
            act.wait_ge(blocks_out, 4)

        @block.vector
        def _(dve):
            nc.vector.tensor_scalar(qb, c.col("df_q_g"), 32 ** -0.5, None, ALU.mult).then_inc(gains, 1)
            nc.vector.tensor_scalar(qd, c.col("fx_q_g"), 64 ** -0.5, None, ALU.mult).then_inc(gains, 1)
            dve.wait_ge(f_exp, 1)
            nc.vector.scalar_tensor_tensor(f_gate, f_gate, 0.0, f_abs, ALU.min, ALU.subtract).then_inc(f_dve, 1)
            dve.wait_ge(f_dve, 1)
            nc.vector.tensor_tensor_scan(f_abs, c.const("ones", 1)[0:4, :].to_broadcast([4, S]), f_gate, 0.0, ALU.mult,
                                         ALU.add).then_inc(f_dve, 1)
            dve.wait_ge(f_dve, 2)
            nc.vector.tensor_copy(f_gate, f_abs).then_inc(f_ready, 1)
            nc.vector.tensor_scalar(f_neg, f_abs, -1.0, None, ALU.mult).then_inc(f_ready, 1)
            dve.wait_ge(gains, 2)
            for j, (tile, _, _, gain) in enumerate(jobs):
                dve.wait_ge(rs_ready, j + 1)
                nc.vector.scalar_tensor_tensor(c.p[:, tile, :], c.p[:, tile, :], gain, rs[j % 2], ALU.mult, ALU.mult
                                               ).then_inc(normed, 1)
            for j in range(4):
                q = c.p[:, T_B + j, :]
                dve.wait_ge(rotated, j + 1)
                if j >= 1:
                    dve.wait_ge(roped, 3 * j)
                nc.vector.tensor_tensor(turn, c.ps[:, 2 + j % 2, :], c.const("sin"), ALU.mult).then_inc(roped, 1)
                nc.vector.tensor_tensor(q, q, c.const("cos"), ALU.mult).then_inc(roped, 1)
                dve.wait_ge(roped, 3 * j + 2)
                nc.vector.tensor_tensor(q, q, turn, ALU.add).then_inc(roped, 1)
            dve.wait_ge(roped, 12)


def attention_forget(c, name):
    nc = c.nc
    scored, masked, maxed = c.sem(f"{name}_scored"), c.sem(f"{name}_masked"), c.sem(f"{name}_maxed")
    exped, inv, scaled = c.sem(f"{name}_exped"), c.sem(f"{name}_inv"), c.sem(f"{name}_scaled")
    turned, copied, summed = c.sem(f"{name}_turned"), c.sem(f"{name}_copied"), c.sem(f"{name}_summed")
    out = c.sem(f"{name}_out")
    units = [(h, i) for h in range(4) for i in range(4)]
    NU = len(units)
    prob = [scratch(c, i) for i in range(3)]
    prob_t = [scratch(c, 3 + i) for i in range(2)]
    nmax, rsum = c.small[:, 32:48], c.small[:, 48:64]

    def rows(h):
        return slice(64 * (h % 2), 64 * (h % 2) + 64)

    with nc.Block() as block:
        @block.tensor
        def _(pe):
            def score(u):
                h, i = units[u]
                nk = (i + 1) * P
                if u >= 2:
                    pe.wait_ge(exped, u - 1)
                bank = c.ps[:, u % 2, 0:nk]
                nc.tensor.matmul(bank, c.p[rows(h), T_D + h // 2, i * P:(i + 1) * P],
                                 c.p[rows(h), T_D + 2 + h // 2, 0:nk], start=True, stop=False)
                nc.tensor.matmul(bank, c.h[0:2, h, i * P:(i + 1) * P], c.h[0:2, 4 + h, 0:nk], start=False, stop=True
                                 ).then_inc(scored, 1)

            def turn(u):
                _, i = units[u]
                pe.wait_ge(scaled, u + 1)
                if u >= 2:
                    pe.wait_ge(copied, u - 1)
                for b in range(i + 1):
                    last = nc.tensor.transpose(c.ps[:, 2 + u % 2, b * P:(b + 1) * P],
                                               prob[u % 3][:, b * P:(b + 1) * P], c.const("ident"))
                last.then_inc(turned, 1)

            def sum_values(u):
                h, i = units[u]
                pe.wait_ge(copied, u + 1)
                for b in range(i + 1):
                    v = c.vt[:, b, V_D + 64 * h:V_D + 64 * h + 64]
                    last = nc.tensor.matmul(c.ps[rows(h), 4 + h // 2, i * P:(i + 1) * P], v,
                                            prob_t[u % 2][:, b * P:(b + 1) * P], start=(b == 0), stop=(b == i))
                last.then_inc(summed, 1)

            score(0)
            score(1)
            for u in range(NU):
                turn(u)
                if u + 2 < NU:
                    score(u + 2)
                if u >= 1:
                    sum_values(u - 1)
            sum_values(NU - 1)

        @block.scalar
        def _(act):
            def exp(u):
                nk = (units[u][1] + 1) * P
                act.wait_ge(maxed, u + 1)
                if u >= 3:
                    act.wait_ge(turned, u - 2)
                nc.scalar.activation(prob[u % 3][:, 0:nk], c.ps[:, u % 2, 0:nk], ACT.Exp, bias=nmax[:, u:u + 1],
                                     accum_out=rsum[:, u:u + 1]).then_inc(exped, 1)

            def copy(u):
                nk = (units[u][1] + 1) * P
                act.wait_ge(turned, u + 1)
                if u >= 2:
                    act.wait_ge(summed, u - 1)
                nc.scalar.activation(prob_t[u % 2][:, 0:nk], c.ps[:, 2 + u % 2, 0:nk], ACT.Copy).then_inc(copied, 1)

            exp(0)
            for u in range(NU):
                if u + 1 < NU:
                    exp(u + 1)
                copy(u)
            for t in range(2):
                act.wait_ge(summed, 8 * (t + 1))
                nc.scalar.activation(c.y[:, Y_D + t, :], c.ps[:, 4 + t, :], ACT.Copy).then_inc(out, 1)

        @block.vector
        def _(dve):
            def maximum(u):
                i = units[u][1]
                dve.wait_ge(scored, u + 1)
                diagonal = c.ps[:, u % 2, i * P:(i + 1) * P]
                nc.vector.tensor_tensor(diagonal, diagonal, c.const("mask_causal"), ALU.add).then_inc(masked, 1)
                dve.wait_ge(masked, u + 1)
                nc.vector.tensor_reduce(nmax[:, u:u + 1], c.ps[:, u % 2, 0:(i + 1) * P], AXX, ALU.max, negate=True
                                        ).then_inc(maxed, 1)

            def normalise(u):
                nk = (units[u][1] + 1) * P
                dve.wait_ge(exped, u + 1)
                nc.vector.reciprocal(rsum[:, u:u + 1], rsum[:, u:u + 1]).then_inc(inv, 1)
                dve.wait_ge(inv, u + 1)
                nc.vector.tensor_scalar(prob[u % 3][:, 0:nk], prob[u % 3][:, 0:nk], rsum[:, u:u + 1], None, ALU.mult
                                        ).then_inc(scaled, 1)

            maximum(0)
            for u in range(NU):
                if u + 1 < NU:
                    maximum(u + 1)
                normalise(u)


def attention_diff(c, name):
    nc = c.nc
    lam_dve, lam_exp, lam_ready = c.sem(f"{name}_lam_dve"), c.sem(f"{name}_lam_exp"), c.sem(f"{name}_lam_ready")
    scored, masked, maxed = c.sem(f"{name}_scored"), c.sem(f"{name}_masked"), c.sem(f"{name}_maxed")
    exped, inv, mixed = c.sem(f"{name}_exped"), c.sem(f"{name}_inv"), c.sem(f"{name}_mixed")
    turned, copied, summed = c.sem(f"{name}_turned"), c.sem(f"{name}_copied"), c.sem(f"{name}_summed")
    squared, ms, rs_ready, out = (c.sem(f"{name}_{n}") for n in ("squared", "ms", "rs_ready", "out"))
    units = [(h, i) for h in range(4) for i in range(4)]
    NU = len(units)
    prob = [[scratch(c, 2 * i + m) for m in range(2)] for i in range(2)]
    prob_t = [scratch(c, 4 + i) for i in range(2)]
    o, sq, rs = [scratch(c, 6), scratch(c, 7)], [scratch(c, 8), scratch(c, 9)], [scratch(c, 0), scratch(c, 1)]
    nmax, rsum = c.small[:, 32:64], c.small[:, 64:96]
    lam_prod = c.cols[:, C_AT["lam_vec"]:C_AT["lam_vec"] + 64].rearrange("p (m n) -> p m n", m=2)
    lam_other = c.cols[:, C_AT["lam_vec"] + 64:C_AT["lam_vec"] + 128].rearrange("p (m n) -> p m n", m=2)
    lam2, nlam, sub_gain = c.small[:, 26:28], c.small[:, 28:29], c.small[:, 29:30]

    with nc.Block() as block:
        @block.tensor
        def _(pe):
            def score(u):
                h, i = units[u]
                nk = (i + 1) * P
                for m in range(2):
                    lane = 32 * ((2 * h + m) % 4)
                    if u >= 2:
                        pe.wait_ge(exped, 2 * (u - 2) + m + 1)
                    nc.tensor.matmul(c.ps[:, 2 * (u % 2) + m, 0:nk], c.p[lane:lane + 32, T_B + h // 2, i * P:(i + 1) * P],
                                     c.p[lane:lane + 32, T_B + 2 + h // 2, 0:nk], start=True, stop=True,
                                     tile_position=(lane, 0)).then_inc(scored, 1)

            def turn(u):
                _, i = units[u]
                pe.wait_ge(mixed, u + 1)
                if u >= 2:
                    pe.wait_ge(copied, u - 1)
                for b in range(i + 1):
                    last = nc.tensor.transpose(c.ps[:, 4 + u % 2, b * P:(b + 1) * P],
                                               prob[u % 2][0][:, b * P:(b + 1) * P], c.const("ident"))
                last.then_inc(turned, 1)

            def sum_values(u):
                h, i = units[u]
                r = slice(64 * (h % 2), 64 * (h % 2) + 64)
                pe.wait_ge(copied, u + 1)
                for b in range(i + 1):
                    v = c.vt[:, b, V_B + 64 * h:V_B + 64 * h + 64]
                    last = nc.tensor.matmul(c.ps[r, 6 + h // 2, i * P:(i + 1) * P], v,
                                            prob_t[u % 2][:, b * P:(b + 1) * P], start=(b == 0), stop=(b == i))
                last.then_inc(summed, 1)

            score(0)
            score(1)
            for u in range(NU):
                turn(u)
                if u + 2 < NU:
                    score(u + 2)
                if u >= 1:
                    sum_values(u - 1)
            sum_values(NU - 1)
            for t in range(2):
                pe.wait_ge(squared, 2 * t + 2)
                nc.tensor.matmul(c.ps[:, t, :], c.const("bo64"), sq[t], start=True, stop=True).then_inc(ms, 1)

        @block.scalar
        def _(act):
            def exp(u):
                nk = (units[u][1] + 1) * P
                for m in range(2):
                    n = 2 * u + m
                    act.wait_ge(maxed, n + 1)
                    if u >= 2:
                        act.wait_ge(turned, u - 1)
                    nc.scalar.activation(prob[u % 2][m][:, 0:nk], c.ps[:, 2 * (u % 2) + m, 0:nk], ACT.Exp,
                                         bias=nmax[:, n:n + 1], accum_out=rsum[:, n:n + 1]).then_inc(exped, 1)

            def copy(u):
                nk = (units[u][1] + 1) * P
                act.wait_ge(turned, u + 1)
                if u >= 2:
                    act.wait_ge(summed, u - 1)
                nc.scalar.activation(prob_t[u % 2][:, 0:nk], c.ps[:, 4 + u % 2, 0:nk], ACT.Copy).then_inc(copied, 1)

            act.wait_ge(lam_dve, 2)
            nc.scalar.activation(lam2, lam2, ACT.Exp).then_inc(lam_exp, 1)
            exp(0)
            for u in range(NU):
                if u + 1 < NU:
                    exp(u + 1)
                copy(u)
            for t in range(2):
                act.wait_ge(summed, 8 * (t + 1))
                nc.scalar.activation(o[t], c.ps[:, 6 + t, :], ACT.Copy).then_inc(squared, 1)
                nc.scalar.activation(sq[t], c.ps[:, 6 + t, :], ACT.Square).then_inc(squared, 1)
            for t in range(2):
                act.wait_ge(ms, t + 1)
                nc.scalar.activation(rs[t], c.ps[:, t, :], ACT.Ln, bias=c.const("eps"), scale=1.0 / 64
                                     ).then_inc(rs_ready, 1)
                act.wait_ge(rs_ready, 2 * t + 1)
                nc.scalar.activation(rs[t], rs[t], ACT.Exp, scale=-0.5).then_inc(rs_ready, 1)

        @block.vector
        def _(dve):
            nc.vector.tensor_tensor(lam_prod, lam_prod, lam_other, ALU.mult).then_inc(lam_dve, 1)
            dve.wait_ge(lam_dve, 1)
            nc.vector.tensor_reduce(lam2, lam_prod, AXX, ALU.add).then_inc(lam_dve, 1)
            dve.wait_ge(lam_exp, 1)
            nc.vector.tensor_tensor(nlam, lam2[:, 1:2], lam2[:, 0:1], ALU.subtract).then_inc(lam_ready, 1)
            dve.wait_ge(lam_ready, 1)
            nc.vector.tensor_tensor(nlam, nlam, c.col("lam_init"), ALU.subtract).then_inc(lam_ready, 1)
            nc.vector.tensor_scalar(sub_gain, c.col("lam_init"), -1.0, 1.0, ALU.mult, ALU.add).then_inc(lam_ready, 1)
            dve.wait_ge(lam_ready, 3)
            nc.vector.tensor_tensor(sub_gain, sub_gain, c.col("df_sub_g"), ALU.mult).then_inc(lam_ready, 1)
            dve.wait_ge(lam_ready, 4)

            def maximum(u):
                i = units[u][1]
                for m in range(2):
                    n = 2 * u + m
                    bank = 2 * (u % 2) + m
                    dve.wait_ge(scored, n + 1)
                    diagonal = c.ps[:, bank, i * P:(i + 1) * P]
                    nc.vector.tensor_tensor(diagonal, diagonal, c.const("mask_chunk"), ALU.add).then_inc(masked, 1)
                    dve.wait_ge(masked, n + 1)
                    nc.vector.tensor_reduce(nmax[:, n:n + 1], c.ps[:, bank, 0:(i + 1) * P], AXX, ALU.max, negate=True
                                            ).then_inc(maxed, 1)

            def mix(u):
                nk = (units[u][1] + 1) * P
                dve.wait_ge(exped, 2 * u + 2)
                r = rsum[:, 2 * u:2 * u + 2]
                nc.vector.reciprocal(r, r).then_inc(inv, 1)
                dve.wait_ge(inv, 3 * u + 1)
                nc.vector.tensor_tensor(r[:, 1:2], r[:, 1:2], nlam, ALU.mult).then_inc(inv, 1)
                dve.wait_ge(inv, 3 * u + 2)
                p1, p2 = prob[u % 2][0][:, 0:nk], prob[u % 2][1][:, 0:nk]
                nc.vector.tensor_scalar(p2, p2, r[:, 1:2], None, ALU.mult).then_inc(inv, 1)
                dve.wait_ge(inv, 3 * u + 3)
                nc.vector.scalar_tensor_tensor(p1, p1, r[:, 0:1], p2, ALU.mult, ALU.add).then_inc(mixed, 1)

            maximum(0)
            for u in range(NU):
                if u + 1 < NU:
                    maximum(u + 1)
                mix(u)
            for t in range(2):
                dve.wait_ge(rs_ready, 2 * t + 2)
                nc.vector.scalar_tensor_tensor(c.y[:, Y_B + t, :], o[t], sub_gain, rs[t], ALU.mult, ALU.mult
                                               ).then_inc(out, 1)
            dve.wait_ge(out, 2)


def spatial_gating(c, name):
    nc = c.nc
    gelu, loaded, mean_of, centred = (c.sem(f"{name}_{n}") for n in ("gelu", "w_loaded", "mean", "centred"))
    squared, var, rs_ready, normed = (c.sem(f"{name}_{n}") for n in ("squared", "var", "rs_ready", "normed"))
    turned, copied, mixed, out = (c.sem(f"{name}_{n}") for n in ("turned", "copied", "mixed", "out"))
    sq, rs = [scratch(c, 0), scratch(c, 1)], scratch(c, 2)
    w = scratch(c, 3)
    bias, pick = c.h[0:4, 0, 0:P], c.h[0:4, 1, 0:2 * P]
    masked = c.sem(f"{name}_w_masked")
    u, v = [c.p[:, T_C + t, :] for t in range(2)], [c.p[:, T_C + 2 + t, :] for t in range(2)]
    layer = c.layer
    with nc.Block() as block:
        @block.sync
        def _(sp):
            sp.dma_start(w, c.dram["sg_wT"][bass.ds(layer, 1), :, :].rearrange("a p n -> p (a n)")).then_inc(loaded, 16)
            sp.dma_start(bias, c.dram["sg_b"][bass.ds(layer, 1), :, :].rearrange("a p n -> p (a n)")
                         ).then_inc(loaded, 16)
            sp.dma_start(pick, c.dram["sg_pick"]).then_inc(loaded, 16)
            sp.wait_ge(loaded, 48)

        @block.gpsimd
        def _(pool):
            pool.wait_ge(loaded, 48)
            w3 = w.rearrange("p (g i) -> p g i", g=4)
            nc.gpsimd.affine_select(out=w3, in_=w3, compare_op=ALU.is_ge, fill=0.0, base=0, pattern=[[0, 4], [1, P]],
                                    channel_multiplier=-1).then_inc(masked, 1)

        @block.tensor
        def _(pe):
            for t in range(2):
                pe.wait_ge(gelu, 3 + t)
                last = nc.tensor.matmul(c.ps[:, 0, :], c.const("ones"), v[t], start=(t == 0), stop=(t == 1))
            last.then_inc(mean_of, 1)
            for t in range(2):
                pe.wait_ge(squared, t + 1)
                last = nc.tensor.matmul(c.ps[:, 1, :], c.const("ones"), sq[t], start=(t == 0), stop=(t == 1))
            last.then_inc(var, 1)
            for t in range(2):
                pe.wait_ge(normed, 2 * t + 2)
                for b in range(4):
                    last = nc.tensor.transpose(c.ps[:, 2 + t, b * P:(b + 1) * P], v[t][:, b * P:(b + 1) * P],
                                               c.const("ident"))
                last.then_inc(turned, 1)
            pe.wait_ge(copied, 2)
            pe.wait_ge(masked, 1)
            for t in range(2):
                for n in range(4):
                    nc.tensor.matmul(c.ps[:, 4 + t, n * P:(n + 1) * P], pick[:, t * P:(t + 1) * P], bias,
                                     start=(n == 0), stop=False, skip_group_check=True)
                for g in (2 * t, 2 * t + 1):
                    r = slice(64 * (g % 2), 64 * (g % 2) + 64)
                    for n in range(4):
                        last = nc.tensor.matmul(c.ps[r, 4 + t, n * P:(n + 1) * P],
                                                c.vt[:, n, V_C + 64 * g:V_C + 64 * g + 64], w[:, g * P:(g + 1) * P],
                                                start=False, stop=(n == 3), skip_group_check=True)
                last.then_inc(mixed, 1)

        @block.scalar
        def _(act):
            for tile in (*u, *v):
                nc.scalar.activation(tile, tile, ACT.Gelu).then_inc(gelu, 1)
            for t in range(2):
                act.wait_ge(centred, t + 1)
                nc.scalar.activation(sq[t], v[t], ACT.Square).then_inc(squared, 1)
            act.wait_ge(var, 1)
            nc.scalar.activation(rs, c.ps[:, 1, :], ACT.Ln, bias=c.const("eps"), scale=1.0 / 256).then_inc(rs_ready, 1)
            act.wait_ge(rs_ready, 1)
            nc.scalar.activation(rs, rs, ACT.Exp, scale=-0.5).then_inc(rs_ready, 1)
            for t in range(2):
                act.wait_ge(turned, t + 1)
                nc.scalar.activation(c.vt[:, :, V_C + t * P:V_C + (t + 1) * P],
                                     c.ps[:, 2 + t, :].rearrange("p (b n) -> p b n", b=4), ACT.Copy
                                     ).then_inc(copied, 1)

        @block.vector
        def _(dve):
            dve.wait_ge(mean_of, 1)
            for t in range(2):
                nc.vector.scalar_tensor_tensor(v[t], c.ps[:, 0, :], -1.0 / 256, v[t], ALU.mult, ALU.add
                                               ).then_inc(centred, 1)
            dve.wait_ge(rs_ready, 2)
            dve.wait_ge(centred, 2)
            dve.wait_ge(squared, 2)
            for t in range(2):
                nc.vector.scalar_tensor_tensor(v[t], v[t], c.col("sg_ln_g", t), rs, ALU.mult, ALU.mult
                                               ).then_inc(normed, 1)
                dve.wait_ge(normed, 2 * t + 1)
                nc.vector.tensor_scalar(v[t], v[t], c.col("sg_ln_b", t), None, ALU.add).then_inc(normed, 1)
            for t in range(2):
                dve.wait_ge(mixed, t + 1)
                nc.vector.tensor_tensor(c.y[:, Y_C + t, :], c.ps[:, 4 + t, :], u[t], ALU.mult).then_inc(out, 1)
            dve.wait_ge(out, 2)


class Rwkv:

    def __init__(self, c):
        self.c, self.used = c, 0
        self.keep = [dict(ax=self.tiles(2), xT=self.tiles(2), kaT=self.tiles(2), rT=self.tiles(2), b_tok=self.tiles(2),
                          k_tok=self.tiles(2), v_tok=self.tiles(1), r=self.tiles(1), gate=self.tiles(1),
                          bonus=self.tiles(1)) for _ in range(2)]
        self.bx, self.kx = self.tiles(2), self.tiles(2)
        at = self.used
        self.temp = [self.tiles(1) for _ in range(9)]
        self.used = at
        self.group = [[self.tiles(1) for _ in range(5)] for _ in range(2)]
        self.lora = self.c.y[:, 0, :]
        self.pt = [self.c.y[:, 1, :], self.c.p[:, IN_T - 1, :]]
        self.last_decay = c.small[:, 96:112]

    def tiles(self, n):
        c, i = self.c, self.used
        if n == 2 and i % 2:
            i += 1
        self.used = i + n
        if i < 8:
            return c.h[:, i:i + n, :].rearrange("p a n -> p (a n)")
        if i < 24:
            return c.p[:, T_B + i - 8:T_B + i - 8 + n, :].rearrange("p a n -> p (a n)")
        if i < 38:
            return scratch(c, i - 24, n)
        flat = c.vt[:, :, :].rearrange("p b n -> p (b n)")
        assert i + n <= 46
        return flat[:, (i - 38) * S:(i - 38 + n) * S]


def by_chunk(ap, width):
    return ap.rearrange("p (c n) -> p c n", n=width)


def rwkv_shift(c, name, w):
    nc = c.nc
    done, act_done = c.sem(f"{name}_dve"), c.sem(f"{name}_act")
    diff = [w.temp[0], w.temp[1]]
    lora = w.lora
    with nc.Block() as block:
        @block.vector
        def _(dve):
            for j in range(7):
                x, d = c.p[:, T_A + j, :], diff[j % 2]
                if j >= 2:
                    dve.wait_ge(done, 3 * (j - 1))
                nc.vector.tensor_tensor(d[:, 1:S], x[:, 0:S - 1], x[:, 1:S], ALU.subtract).then_inc(done, 1)
                nc.vector.tensor_scalar(d[:, 0:1], x[:, 0:1], -1.0, None, ALU.mult).then_inc(done, 1)
                dve.wait_ge(done, 3 * j + 2)
                nc.vector.scalar_tensor_tensor(x, d, c.col("rw_mu", j), x, ALU.mult, ALU.add).then_inc(done, 1)
            dve.wait_ge(done, 21)

        @block.scalar
        def _(act):
            act.wait_ge(done, 21)
            m = c.p[:, T_A + 6, :]
            nc.scalar.activation(lora[0:32, :], m[0:32, :], ACT.Tanh).then_inc(act_done, 1)
            nc.scalar.activation(lora[32:64, :], m[32:64, :], ACT.Copy).then_inc(act_done, 1)
            nc.scalar.activation(lora[64:128, :], m[64:128, :], ACT.Sigmoid).then_inc(act_done, 1)
            act.wait_ge(act_done, 3)


def rwkv_prepare(c, name, w, pair):
    nc = c.nc
    keep = w.keep[pair]
    r, k, v = (c.p[:, T_A + 2 * i + pair, :] for i in range(3))
    logw, a, cum, cum_ex, e_neg, kk, ss, key, e_pos = w.temp
    lora_w = c.small2[:, :]
    loaded, zeroed = c.sem(f"{name}_lora_loaded"), c.sem(f"{name}_zeroed")
    lora, sig, dec, exps = (c.sem(f"{name}_{n}") for n in ("lora", "sig", "decay", "exps"))
    kk_raw, kk_sq, kk_ss, kk_cl, kk_rs = (c.sem(f"{name}_{n}") for n in ("kk_raw", "kk_sq", "kk_ss", "kk_cl", "kk_rs"))
    vx_s, v_turn, v_tok, bon_in, bon = (c.sem(f"{name}_{n}") for n in ("vx", "v_turn", "v_tok", "bon_in", "bon"))
    gate_s, chain_s, act_chain = c.sem(f"{name}_gate"), c.sem(f"{name}_dve"), c.sem(f"{name}_act")
    cs = slice(pair * P, (pair + 1) * P)
    vx = [keep["kaT"][:, 0:S], keep["kaT"][:, S:2 * S]]
    halves = [(slice(0, 64), 0), (slice(64, 128), 1)]

    def half(x, hh, rows):
        return x.rearrange("p (c h n) -> p c h n", h=2, n=64)[rows, :, hh, :]

    def chunks(x, rows):
        return x.rearrange("p (c n) -> p c n", n=64)[rows, :, :]

    def vhalf(i, hh, rows):
        return vx[i].rearrange("p (c h n) -> p c h n", h=2, n=64)[rows, :, hh, :]

    with nc.Block() as block:
        @block.sync
        def _(sp):
            sp.dma_start(lora_w, c.dram["rw_lora"][bass.ds(c.layer, 1), :, :].rearrange("a p n -> p (a n)")
                         ).then_inc(loaded, 16)
            sp.wait_ge(loaded, 16)

        @block.gpsimd
        def _(pool):
            for x in (vx[0], vx[1], keep["ax"], w.bx, w.kx):
                nc.gpsimd.memset(x, 0.0).then_inc(zeroed, 1)

        @block.tensor
        def _(pe):
            pe.wait_ge(loaded, 16)
            nc.tensor.matmul(c.ps[:, 0, :], lora_w[0:32, cs], w.lora[0:32, :], start=True, stop=True).then_inc(lora, 1)
            nc.tensor.matmul(c.ps[:, 1, :], lora_w[32:64, cs], w.lora[32:64, :], start=True, stop=True,
                             tile_position=(32, 0)).then_inc(lora, 1)
            nc.tensor.matmul(c.ps[:, 2, :], lora_w[64:128, cs], w.lora[64:128, :], start=True, stop=True
                             ).then_inc(lora, 1)
            for i in range(2):
                pe.wait_ge(vx_s, 2 * i + 2)
                for n in range(4):
                    last = nc.tensor.transpose(c.ps[:, 5 + i, n * P:(n + 1) * P], vx[i][:, n * P:(n + 1) * P],
                                               c.const("ident"))
                last.then_inc(v_turn, 1)
            pe.wait_ge(kk_sq, 1)
            nc.tensor.matmul(c.ps[:, 3, :], c.const("bo64"), ss, start=True, stop=True).then_inc(kk_ss, 1)
            pe.wait_ge(bon_in, 1)
            nc.tensor.matmul(c.ps[:, 4, :], c.const("bo64"), c.p[:, T_A + pair, :], start=True, stop=True
                             ).then_inc(bon, 1)

        @block.scalar
        def _(act):
            chain = Chain(act, act_chain)
            act.wait_ge(lora, 1)
            nc.scalar.activation(logw, c.ps[:, 0, :], ACT.Sigmoid, bias=c.col("rw_w0", pair)).then_inc(sig, 1)
            act.wait_ge(lora, 2)
            nc.scalar.activation(a, c.ps[:, 1, :], ACT.Sigmoid, bias=c.col("rw_a0", pair)).then_inc(sig, 1)
            act.wait_ge(lora, 3)
            nc.scalar.activation(keep["gate"], c.ps[:, 2, :], ACT.Copy).then_inc(gate_s, 1)
            act.wait_ge(zeroed, 2)
            for i in range(2):
                for rows, hh in halves:
                    nc.scalar.activation(vhalf(i, hh, rows), chunks(v, rows)[:, 4 * i:4 * i + 4, :], ACT.Copy
                                         ).then_inc(vx_s, 1)
            act.wait_ge(kk_raw, 1)
            nc.scalar.activation(ss, kk, ACT.Square).then_inc(kk_sq, 1)
            act.wait_ge(dec, 2)
            nc.scalar.activation(e_pos, cum, ACT.Exp).then_inc(exps, 1)
            nc.scalar.activation(cum_ex, cum_ex, ACT.Exp).then_inc(exps, 1)
            nc.scalar.activation(e_neg, cum, ACT.Exp, scale=-1.0).then_inc(exps, 1)
            act.wait_ge(kk_cl, 1)
            chain(nc.scalar.activation(ss, ss, ACT.Ln, scale=KK_SCALE))
            nc.scalar.activation(ss, ss, ACT.Exp, scale=-0.5, bias=c.const("kk_shift")).then_inc(kk_rs, 1)
            for i in range(2):
                act.wait_ge(v_turn, i + 1)
                for rows, hh in halves:
                    src = c.ps[:, 5 + i, :].rearrange("p (c h n) -> p c h n", h=2, n=64)[rows, :, hh, :]
                    nc.scalar.activation(chunks(keep["v_tok"], rows)[:, 4 * i:4 * i + 4, :], src, ACT.Copy
                                         ).then_inc(v_tok, 1)
            act.wait_ge(v_tok, 4)
            act.wait_ge(gate_s, 1)

        @block.vector
        def _(dve):
            chain = Chain(dve, chain_s)
            nc.vector.tensor_scalar(kk, k, c.col("rw_k_k", pair), None, ALU.mult).then_inc(kk_raw, 1)
            dve.wait_ge(sig, 1)
            chain(nc.vector.tensor_scalar(logw, logw, -math.exp(-0.5), None, ALU.mult))
            nc.vector.tensor_tensor_scan(cum, c.const("scan"), logw, 0.0, ALU.mult, ALU.add).then_inc(dec, 1)
            dve.wait_ge(dec, 1)
            nc.vector.tensor_tensor(cum_ex, cum, logw, ALU.subtract).then_inc(dec, 1)
            dve.wait_ge(sig, 2)
            chain(nc.vector.tensor_scalar(key, a, -1.0, c.col("rw_k_a", pair), ALU.add, ALU.mult))
            chain(nc.vector.scalar_tensor_tensor(key, key, 1.0, k, ALU.add, ALU.mult))
            dve.wait_ge(kk_ss, 1)
            nc.vector.tensor_scalar(ss, c.ps[:, 3, :], 1e-24, None, ALU.max).then_inc(kk_cl, 1)
            dve.wait_ge(exps, 3)
            chain(nc.vector.tensor_tensor(keep["r"], r, e_pos, ALU.mult))
            chain(nc.vector.scalar_tensor_tensor(r, r, c.col("rw_r_k", pair), key, ALU.mult, ALU.mult))
            nc.vector.tensor_copy(w.last_decay[:, 8 * pair:8 * pair + 8], by_chunk(e_pos, 64)[:, :, 63]
                                  ).then_inc(bon_in, 1)
            dve.wait_ge(zeroed, 5)
            for rows, hh in halves:
                chain(nc.vector.tensor_tensor(half(w.kx, hh, rows), chunks(key, rows), chunks(e_neg, rows), ALU.mult))
            dve.wait_ge(kk_rs, 1)
            chain(nc.vector.tensor_tensor(kk, kk, ss, ALU.mult))
            for rows, hh in halves:
                chain(nc.vector.scalar_tensor_tensor(half(keep["ax"], hh, rows), chunks(kk, rows), -1.0,
                                                     chunks(cum_ex, rows), ALU.mult, ALU.mult))
            chain(nc.vector.tensor_tensor(kk, kk, a, ALU.mult))
            for rows, hh in halves:
                chain(nc.vector.tensor_tensor(half(w.bx, hh, rows), chunks(kk, rows), chunks(e_neg, rows), ALU.mult))
            dve.wait_ge(bon, 1)
            chain(nc.vector.tensor_tensor(keep["bonus"], c.ps[:, 4, :], v, ALU.mult))


def rwkv_intra(c, name, w, pair):
    nc = c.nc
    keep = w.keep[pair]
    multiplied, on_dve, on_act, dve_chain = (c.sem(f"{name}_{n}") for n in ("multiplied", "on_dve", "on_act", "chain"))
    STEPS = 10
    DVE_AT, ACT_AT = [0, 1, 2, 3, 4, 6, 8, 9], [0, 1, 2, 3, 5, 6, 7]

    def buffers(g):
        A, B, LO, C2, E2 = w.group[g]
        return A, B, LO, C2, E2, w.pt[g]

    def unit(x, n):
        return x[:, n * P:(n + 1) * P]

    def seen(steps, s, g):
        return 2 * after(steps, s - 1) + (g + 1 if s in steps else 0)

    with nc.Block() as block:
        @block.tensor
        def _(pe):
            for s in range(STEPS):
                for g in range(2):
                    A, B, LO, C2, E2, PT = buffers(g)
                    bank = [c.ps[:, 4 * g + i, :] for i in range(4)]
                    if s >= 1:
                        n = seen(DVE_AT, s - 1, g)
                        pe.wait_ge(on_dve, n)
                        pe.wait_ge(on_act, seen(ACT_AT, s - 1, g))
                    last = None
                    for n in range(4):
                        u = 4 * g + n
                        ax, bx, kx = (x[:, u * P:(u + 1) * P] for x in (keep["ax"], w.bx, w.kx))
                        r = keep["r"][:, u * 64:(u + 1) * 64]

                        def mm(i, lhsT, rhs):
                            return nc.tensor.matmul(unit(bank[i], n), lhsT, rhs, start=True, stop=True)
                        if s == 0:
                            mm(0, ax, bx)
                            mm(1, bx, ax)
                            mm(2, kx, ax)
                            nc.tensor.matmul(bank[3][:, n * P:n * P + 64], bx, r, start=True, stop=True)
                            last = nc.tensor.matmul(bank[3][:, n * P + 64:(n + 1) * P], kx, r, start=True, stop=True)
                        elif s == 1:
                            mm(0, unit(B, n), unit(A, n))
                            last = mm(1, unit(A, n), unit(B, n))
                        elif s == 2:
                            mm(0, unit(E2, n), unit(C2, n))
                            mm(1, unit(C2, n), unit(E2, n))
                            last = mm(2, unit(C2, n), unit(PT, n))
                        elif s == 3:
                            mm(0, unit(B, n), unit(A, n))
                            last = mm(2, unit(A, n), unit(PT, n))
                        elif s == 4:
                            last = mm(1, unit(E2, n), unit(PT, n))
                        elif s == 5:
                            last = nc.tensor.transpose(unit(bank[0], n), unit(PT, n), c.const("ident"))
                        elif s == 6:
                            mm(1, unit(A, n), unit(LO, n))
                            last = mm(2, unit(LO, n), unit(A, n))
                        elif s == 7:
                            last = mm(0, unit(C2, n), unit(E2, n))
                        elif s == 8:
                            last = mm(1, unit(B, n), unit(PT, n))
                        else:
                            last = mm(2, unit(E2, n), unit(PT, n))
                    last.then_inc(multiplied, 1)
            for g in range(2):
                pe.wait_ge(on_dve, 2 * len(DVE_AT))
                pe.wait_ge(on_act, 2 * len(ACT_AT))
                for n in range(4):
                    u = 4 * g + n
                    nc.tensor.transpose(unit(c.ps[:, 4 * g, :], n), w.bx[:, u * P:(u + 1) * P], c.const("ident"))
                    last = nc.tensor.transpose(unit(c.ps[:, 4 * g + 1, :], n), w.kx[:, u * P:(u + 1) * P],
                                               c.const("ident"))
                last.then_inc(multiplied, 1)

        @block.scalar
        def _(act):
            for s in ACT_AT:
                for g in range(2):
                    A, B, LO, C2, E2, PT = buffers(g)
                    bank = [c.ps[:, 4 * g + i, :] for i in range(4)]
                    act.wait_ge(multiplied, 2 * s + g + 1)
                    out, i = {0: (None, None), 1: (C2, 0), 2: (A, 0), 3: (E2, 0), 5: (A, 0), 6: (C2, 1), 7: (B, 0)}[s]
                    if s == 0:
                        out, i = keep["rT"][:, g * S:(g + 1) * S], 3
                    nc.scalar.activation(out, bank[i], ACT.Copy).then_inc(on_act, 1)
            for g in range(2):
                act.wait_ge(multiplied, 2 * STEPS + g + 1)
                nc.scalar.activation(keep["b_tok"][:, g * S:(g + 1) * S], c.ps[:, 4 * g, :], ACT.Copy
                                     ).then_inc(on_act, 1)
            act.wait_ge(on_act, 2 * len(ACT_AT) + 2)

        @block.vector
        def _(dve):
            chain = Chain(dve, dve_chain)
            for s in DVE_AT:
                for g in range(2):
                    A, B, LO, C2, E2, PT = buffers(g)
                    bank = [c.ps[:, 4 * g + i, :] for i in range(4)]
                    cols = slice(g * S, (g + 1) * S)
                    dve.wait_ge(multiplied, 2 * s + g + 1)
                    if s == 0:
                        chain(nc.vector.tensor_tensor(A, bank[0], c.const("m_ld"), ALU.mult))
                        chain(nc.vector.tensor_tensor(B, bank[1], c.const("m_ldT"), ALU.mult))
                        chain(nc.vector.tensor_tensor(keep["kaT"][:, cols], bank[2], c.const("m_kaT"), ALU.mult))
                        chain(nc.vector.tensor_tensor(LO, bank[1], c.const("m_loT"), ALU.mult))
                        chain(nc.vector.tensor_tensor(PT, B, c.const("ident4"), ALU.add))
                        dve.wait_ge(on_act, g + 1)
                        rT = keep["rT"][:, cols]
                        last = nc.vector.tensor_tensor(rT, rT, c.const("m_r"), ALU.mult)
                    elif s == 1:
                        last = nc.vector.tensor_copy(E2, bank[1])
                    elif s == 2:
                        chain(nc.vector.tensor_copy(B, bank[1]))
                        last = nc.vector.tensor_tensor(PT, bank[2], PT, ALU.add)
                    elif s == 3:
                        last = nc.vector.tensor_tensor(PT, bank[2], PT, ALU.add)
                    elif s == 4:
                        last = nc.vector.tensor_tensor(PT, bank[1], PT, ALU.add)
                    elif s == 6:
                        last = nc.vector.tensor_copy(E2, bank[2])
                    elif s == 8:
                        last = nc.vector.tensor_tensor(PT, bank[1], PT, ALU.add)
                    else:
                        last = nc.vector.tensor_tensor(keep["xT"][:, cols], bank[2], PT, ALU.add)
                    last.then_inc(on_dve, 1)
            for g in range(2):
                dve.wait_ge(multiplied, 2 * STEPS + g + 1)
                chain(nc.vector.tensor_copy(keep["k_tok"][:, g * S:(g + 1) * S], c.ps[:, 4 * g + 1, :]))


def rwkv_scan(c, name, w):
    nc = c.nc
    names = ("zeroed", "rhs", "rhs_out", "sa", "sa_out", "state_mm", "state_add", "state", "y_mm", "y_out")
    zeroed, rhs, rhs_out, sa, sa_out, state_mm, state_add, state, y_mm, y_out = (c.sem(f"{name}_{n}") for n in names)
    mean, cent, sq, var, rs_s, chain_s = (c.sem(f"{name}_{n}") for n in ("mean", "cent", "sq", "var", "rs", "chain"))
    st = [[w.bx[:, (2 * q + i) * 64:(2 * q + i + 1) * 64] for i in range(2)] for q in range(2)]
    rh = [w.bx[:, 256 + q * 64:256 + (q + 1) * 64] for q in range(2)]
    sav = [w.bx[:, 384 + q * 64:384 + (q + 1) * 64] for q in range(2)]
    order = [(n, q) for n in range(NCH) for q in range(2)]
    y = [w.temp[0], w.temp[1]]
    sqt, rs = [w.temp[2], w.temp[3]], [w.temp[4], w.temp[5]]
    mmean = [w.temp[6], w.temp[7]]
    ONCE = len(order)

    with nc.Block() as block:
        @block.gpsimd
        def _(pool):
            for q in range(2):
                nc.gpsimd.memset(st[q][0], 0.0).then_inc(zeroed, 1)

        @block.tensor
        def _(pe):
            pe.wait_ge(zeroed, 2)

            def unit(x, n, width=P):
                return x[:, n * width:(n + 1) * width]

            def first(i):
                n, q = order[i]
                keep = w.keep[q]
                if n >= 1:
                    pe.wait_ge(state, i - 2 + 1)
                bank = c.ps[:, q, 0:64]
                nc.tensor.matmul(bank, unit(keep["ax"], n), st[q][n % 2], start=True, stop=False)
                nc.tensor.matmul(bank, unit(keep["kaT"], n), unit(keep["v_tok"], n, 64), start=False, stop=True
                                 ).then_inc(rhs, 1)

            def second(i):
                n, q = order[i]
                pe.wait_ge(rhs_out, i + 1)
                nc.tensor.matmul(c.ps[:, q, 64:128], unit(w.keep[q]["xT"], n), rh[q], start=True, stop=True
                                 ).then_inc(sa, 1)

            def third(i):
                n, q = order[i]
                keep = w.keep[q]
                pe.wait_ge(sa_out, i + 1)
                bank = c.ps[:, 2 + q, 0:64]
                nc.tensor.matmul(bank, unit(keep["b_tok"], n), sav[q], start=True, stop=False)
                nc.tensor.matmul(bank, unit(keep["k_tok"], n), unit(keep["v_tok"], n, 64), start=False, stop=True
                                 ).then_inc(state_mm, 1)
                for hh in range(2):
                    rows = slice(64 * hh, 64 * hh + 64)
                    out = c.ps[rows, 4 + q, n * 64:(n + 1) * 64]
                    rT = unit(keep["rT"], n)
                    nc.tensor.matmul(out, st[q][n % 2][rows, :], keep["r"][rows, n * 64:(n + 1) * 64], start=True,
                                     stop=False)
                    nc.tensor.matmul(out, sav[q][rows, :], rT[rows, 0:64], start=False, stop=False)
                    last = nc.tensor.matmul(out, unit(keep["v_tok"], n, 64)[rows, :], rT[rows, 64:128], start=False,
                                            stop=True)
                last.then_inc(y_mm, 1)

            for i in range(0, ONCE, 2):
                first(i)
                first(i + 1)
                second(i)
                second(i + 1)
                third(i)
                third(i + 1)
            for q in range(2):
                pe.wait_ge(y_out, q + 1)
                nc.tensor.matmul(c.ps[:, 6, :], c.const("bo64"), y[q], start=True, stop=True).then_inc(mean, 1)
                pe.wait_ge(sq, q + 1)
                nc.tensor.matmul(c.ps[:, 7, :], c.const("bo64"), sqt[q], start=True, stop=True).then_inc(var, 1)

        @block.scalar
        def _(act):
            for i, (n, q) in enumerate(order):
                act.wait_ge(rhs, i + 1)
                if i >= 2:
                    act.wait_ge(sa, i - 1)
                nc.scalar.activation(rh[q], c.ps[:, q, 0:64], ACT.Copy).then_inc(rhs_out, 1)
            for q in range(2):
                act.wait_ge(y_mm, ONCE - 1 + q)
                nc.scalar.activation(y[q], c.ps[:, 4 + q, :], ACT.Copy).then_inc(y_out, 1)
            for q in range(2):
                act.wait_ge(cent, q + 1)
                nc.scalar.activation(sqt[q], y[q], ACT.Square).then_inc(sq, 1)
                act.wait_ge(var, q + 1)
                nc.scalar.activation(rs[q], c.ps[:, 7, :], ACT.Ln, bias=c.const("gn_eps"), scale=1.0 / 64
                                     ).then_inc(rs_s, 1)
                act.wait_ge(rs_s, 2 * q + 1)
                nc.scalar.activation(rs[q], rs[q], ACT.Exp, scale=-0.5).then_inc(rs_s, 1)

        @block.vector
        def _(dve):
            for i, (n, q) in enumerate(order):
                if q == 0:
                    for j in (i, i + 1):
                        qq = order[j][1]
                        dve.wait_ge(sa, j + 1)
                        if j >= 2:
                            dve.wait_ge(y_mm, j - 1)
                        nc.vector.tensor_copy(sav[qq], c.ps[:, qq, 64:128]).then_inc(sa_out, 1)
                new = st[q][(n + 1) % 2]
                dve.wait_ge(state_mm, i + 1)
                if i >= 2:
                    dve.wait_ge(y_mm, i - 1)
                nc.vector.tensor_tensor(new, c.ps[:, 2 + q, 0:64], st[q][n % 2], ALU.add).then_inc(state_add, 1)
                dve.wait_ge(state_add, i + 1)
                nc.vector.tensor_scalar(new, new, w.last_decay[:, 8 * q + n:8 * q + n + 1], None, ALU.mult
                                        ).then_inc(state, 1)
            chain = Chain(dve, chain_s)
            for q in range(2):
                dve.wait_ge(mean, q + 1)
                nc.vector.scalar_tensor_tensor(y[q], c.ps[:, 6, :], -1.0 / 64, y[q], ALU.mult, ALU.add
                                               ).then_inc(cent, 1)
                dve.wait_ge(rs_s, 2 * q + 2)
                chain(nc.vector.scalar_tensor_tensor(y[q], y[q], c.col("rw_ln_g", q), rs[q], ALU.mult, ALU.mult))
                chain(nc.vector.scalar_tensor_tensor(y[q], y[q], c.col("rw_ln_b", q), w.keep[q]["bonus"], ALU.add,
                                                     ALU.add))
                chain(nc.vector.tensor_tensor(c.y[:, Y_A + q, :], y[q], w.keep[q]["gate"], ALU.mult))


def feed_forward_up(c, name, up):
    nc = c.nc
    tapped, act_g, conv = c.sem(f"{name}_tapped"), c.sem(f"{name}_silu"), c.sem(f"{name}_conv")
    hidden = c.sem(f"{name}_hidden")
    work = [c.y[:, s, :] for s in range(RING)]
    rounds = up.n // RING
    GATES = (1, 3)

    def tap(i, t):
        at = C_AT["ffn_tap"]
        return c.cols[:, bass.ds(t * 4 + (at + i), 1)]

    @contextmanager_block(nc)
    def _(block):
        @block.sync
        def _(sp):
            up.load(sp)

        @block.tensor
        def _(pe):
            up.multiply(pe, lambda kt: c.h[:, kt, :])

        @block.scalar
        def _(act):
            def tile(s, g):
                act.wait_ge(up.multiplied, g * RING + s + 1)
                nc.scalar.activation(work[s], c.ps[:, s, :], ACT.Identity, bias=tap(3, g * RING + s),
                                     scale=tap(2, g * RING + s)).then_inc(tapped, 1)

            def silu(i, g):
                s = GATES[i]
                act.wait_ge(conv, g * 2 * RING + 2 * s + 2)
                nc.scalar.activation(work[s], work[s], ACT.Silu).then_inc(act_g, 1)

            def round_of(g, first):
                for i in range(2):
                    for s in (2 * i, 2 * i + 1):
                        if not first:
                            act.wait_ge(hidden, 2 * (g - 1) + i + 1)
                        tile(s, g)
                    silu(i, g)

            round_of(0, True)
            with act.Fori(1, rounds) as g:
                round_of(g, False)

        @block.vector
        def _(dve):
            with dve.Fori(0, rounds) as g:
                for i in range(2):
                    for s in (2 * i, 2 * i + 1):
                        t = g * RING + s
                        dve.wait_ge(tapped, t + 1)
                        o, u = work[s], c.ps[:, s, :]
                        nc.vector.scalar_tensor_tensor(o[:, 1:S], u[:, 0:S - 1], tap(1, t), o[:, 1:S], ALU.mult,
                                                       ALU.add).then_inc(conv, 1)
                        dve.wait_ge(conv, t * 2 + 1)
                        nc.vector.scalar_tensor_tensor(o[:, 2:S], u[:, 0:S - 2], tap(0, t), o[:, 2:S], ALU.mult,
                                                       ALU.add).then_inc(conv, 1)
                        dve.wait_ge(conv, t * 2 + 2)
                        dve.sem_inc(up.emptied, 1)
                    dve.wait_ge(act_g, g * 2 + i + 1)
                    out = c.p[:, bass.ds(g * 2 + i, 1), :].rearrange("p a n -> p (a n)")
                    nc.vector.tensor_tensor(out, work[2 * i], work[2 * i + 1], ALU.mult).then_inc(hidden, 1)
            dve.wait_ge(hidden, up.n // 2)


class contextmanager_block:

    def __init__(self, nc):
        self.nc = nc

    def __call__(self, f):
        with self.nc.Block() as block:
            f(block)


def linear_stage(c, lin, rhs, out, prefetch=None, load=True):
    nc = c.nc
    engine, body = out
    with nc.Block() as block:
        @block.sync
        def _(sp):
            if load:
                lin.load(sp)
            if prefetch is not None:
                sp.wait_ge(lin.multiplied, lin.n)
                prefetch(sp)

        @block.tensor
        def _(pe):
            lin.multiply(pe, rhs)

        if engine == "scalar":
            @block.scalar
            def _(act):
                body(act)
        else:
            @block.vector
            def _(dve):
                body(dve)


def block_one_layer(c, layer, stop=None):
    nc, dram = c.nc, c.dram
    c.layer = layer

    def of_layer(name, tiles):
        return lambda t: dram[name][bass.ds(layer * tiles + t, 1), :, :].rearrange("a p n -> p (a n)")

    w_in = Linear(c, "w_in", IN_T, of_layer("w_in", IN_T))
    w_out = Linear(c, "w_out", KT, of_layer("w_out", KT))
    ffn_up = Linear(c, "ffn_up", 2 * FT, of_layer("ffn_up", 2 * FT))
    ffn_down = Linear(c, "ffn_down", KT, of_layer("ffn_down", KT), k_tiles=FT, size=FT * P)
    cols_loaded = c.sem("cols_loaded")
    mod = lambda i: c.mod[:, i * KT:(i + 1) * KT]
    tmp = c.ring[:, RING * D:]

    def start(sp):
        sp.dma_start(c.cols[:, :], dram["cols"][bass.ds(layer, 1), :, :].rearrange("a p n -> p (a n)")
                     ).then_inc(cols_loaded, 16)
        w_in.prefetch(sp)
        sp.wait_ge(cols_loaded, 16)

    with nc.Block() as block:
        @block.sync
        def _(sp):
            start(sp)
    next_cond, cond_ready = load_cond(c, "next_mod", layer + 1)
    norm_modulate(c, "norm1", c.x, c.h, c.col("norm1_g", 0, 8), mod(1), mod(0), tmp=tmp, extra_act=next_cond)
    linear_stage(c, w_in, lambda kt: c.h[:, kt, :], ("scalar", lambda act: copy_out_tiles(c, w_in, act, c.p)))
    if stop == "w_in":
        return
    with c.stages():
        prepare_attentions(c, "prep", w_out.prefetch)
        attention_forget(c, "fx")
        attention_diff(c, "df")
        spatial_gating(c, "sg")
    if stop == "attn":
        return
    w = Rwkv(c)
    with c.stages():
        rwkv_shift(c, "rw_shift", w)
        for q in range(2):
            rwkv_prepare(c, f"rw_prep{q}", w, q)
            rwkv_intra(c, f"rw_intra{q}", w, q)
        rwkv_scan(c, "rw_scan", w)
    if stop == "mix":
        return
    linear_stage(c, w_out, lambda kt: c.y[:, kt, :], ("vector", lambda dve: residual_tiles(c, w_out, dve, mod(2))),
                 prefetch=ffn_up.prefetch)
    next_sums = AdaLN(c, "next_mod", layer + 1)
    norm_modulate(c, "norm2", c.x, c.h, c.col("norm2_g", 0, 8), mod(4), mod(3), tmp=tmp)
    feed_forward_up(c, "ffn", ffn_up)
    with nc.Block() as block:
        @block.sync
        def _(sp):
            ffn_down.prefetch(sp)
            ffn_down.load(sp)

        @block.scalar
        def _(act):
            next_sums.load(act)

        @block.tensor
        def _(pe):
            ffn_down.multiply(pe, lambda kt: c.p[:, kt, :])

        @block.vector
        def _(dve):
            per_tile = next_sums.pieces // KT
            for t in range(KT):
                next_sums.add(dve, t * per_tile, (t + 1) * per_tile)
                residual_tiles(c, ffn_down, dve, mod(5), t, t + 1)
    adaln_finish(c, "next_mod", layer + 1, c.mod[:, :])


class Gla:

    LAT, SEG = S, S + CTX
    CHUNKS = 2 * (NCH + LNC)

    def __init__(self, c):
        self.c = c
        flat = lambda t: t.rearrange("p a n -> p (a n)")
        h, y, vt = flat(c.h[:, :, :]), flat(c.y[:, :, :]), flat(c.vt[:, :, :])
        self.ctx_x, self.ctx_h = (t.rearrange("p (a n) -> p a n", n=CTX) for t in (y[:, 0:4 * S], y[:, 4 * S:8 * S]))
        self.kc = vt[:, 0:4 * CTX].rearrange("p (a n) -> p a n", n=CTX)
        self.vc = vt[:, 4 * CTX:12 * CTX].rearrange("p (a n) -> p a n", n=CTX)
        self.low = vt[:, 12 * CTX:15 * CTX]
        self.q, self.r, self.k, self.v = 0, 4, 12, 16
        self.g, self.cum = h[:, 0:3 * S], h[:, 3 * S:6 * S]
        self.state = h[:, 6 * S:8 * S].rearrange("p (z i n) -> p z i n", z=2, i=2)
        self.e_pos, self.e_neg = scratch(c, 0, 2), scratch(c, 2, 3)
        self.k_tok = scratch(c, 5, 3)
        self.v_tok = scratch(c, 8, 3).rearrange("p (b n) -> p b n", n=2 * P)
        self.scores = scratch(c, 11, 2)
        self.gb = scratch(c, 13)
        self.tot, self.half, self.em, self.step = (c.small[:, 24 * i:24 * i + 24] for i in range(4))


def gla_project(c, w):
    nc = c.nc
    n1, n2 = 12, 12
    of = lambda first: lambda t: c.dram["gla_in"][bass.ds(first + t, 1), :, :].rearrange("a p n -> p (a n)")
    qr = Linear(c, "gla_qr", n1, of(0))
    kv = Linear(c, "gla_kv", n2, of(n1))
    ctx_multiplied, ctx_emptied = c.sem("gla_ctx_multiplied"), c.sem("gla_ctx_emptied")
    low_loaded, low_done, low_out = c.sem("gla_low_loaded"), c.sem("gla_low"), c.sem("gla_low_out")
    low_w = scratch(c, 0)
    ctx_kv = c.vt[:, :, :].rearrange("p b n -> p (b n)")

    with nc.Block() as block:
        @block.sync
        def _(sp):
            qr.prefetch(sp)
            sp.dma_start(low_w, c.dram["gla_low"]).then_inc(low_loaded, 16)
            sp.dma_start(w.gb, c.dram["gla_gb"]).then_inc(low_loaded, 16)
            qr.load(sp)
            for s in range(RING):
                sp.wait_ge(qr.multiplied, n1 - RING + s + 1)
                sp.dma_start(c.slot(s), kv.weights(s)).then_inc(kv.loaded[s], 16)

        @block.tensor
        def _(pe):
            qr.multiply(pe, lambda kt: c.h[:, kt, :])
            pe.wait_ge(low_loaded, 32)
            for half, (x, n) in enumerate(((c.h, S), (w.ctx_h, CTX))):
                for kt in range(KT):
                    last = nc.tensor.matmul(c.ps[0:64, 4 + half, 0:n], low_w[:, kt * 64:(kt + 1) * 64], x[:, kt, :],
                                            start=(kt == 0), stop=(kt == KT - 1))
                last.then_inc(low_done, 1)

        @block.scalar
        def _(act):
            copy_out_tiles(c, qr, act, c.p)
            act.wait_ge(low_done, 2)
            nc.scalar.activation(w.low[0:64, 0:S], c.ps[0:64, 4, :], ACT.Copy).then_inc(low_out, 1)
            nc.scalar.activation(w.low[0:64, S:S + CTX], c.ps[0:64, 5, 0:CTX], ACT.Copy).then_inc(low_out, 1)

    with nc.Block() as block:
        @block.sync
        def _(sp):
            kv.load(sp)

        @block.tensor
        def _(pe):
            def tile(s, g):
                pe.wait_ge(kv.loaded[s], 16 * (g + 1))
                wt = c.slot(s)
                for x, bank, n in ((c.h, s, S), (w.ctx_h, RING + s, CTX)):
                    for kt in range(KT):
                        last = nc.tensor.matmul(c.ps[:, bank, 0:n], wt[:, kt * P:(kt + 1) * P], x[:, kt, :],
                                                start=(kt == 0), stop=(kt == KT - 1))
                last.then_inc(kv.multiplied, 1)

            for s in range(RING):
                tile(s, 0)
            with pe.Fori(1, n2 // RING) as g:
                for s in range(RING):
                    pe.wait_ge(kv.emptied, (g - 1) * RING + s + 1)
                    pe.wait_ge(ctx_emptied, (g - 1) * RING + s + 1)
                    tile(s, g)

        @block.scalar
        def _(act):
            with act.Fori(0, n2 // RING) as g:
                for s in range(RING):
                    act.wait_ge(kv.multiplied, g * RING + s + 1)
                    out = c.p[:, bass.ds(g * RING + (n1 + s), 1), :].rearrange("p a n -> p (a n)")
                    nc.scalar.activation(out, c.ps[:, s, :], ACT.Copy).then_inc(kv.emptied, 1)

        @block.vector
        def _(dve):
            with dve.Fori(0, n2 // RING) as g:
                for s in range(RING):
                    dve.wait_ge(kv.multiplied, g * RING + s + 1)
                    out = ctx_kv[:, bass.ds(g * (RING * CTX) + s * CTX, CTX)]
                    nc.vector.tensor_copy(out, c.ps[:, RING + s, 0:CTX]).then_inc(ctx_emptied, 1)


def gla_prepare(c, name, w, head):
    nc = c.nc
    z, z_in, ln_in, soft, gate, scanned = (c.sem(f"{name}_{n}") for n in ("z", "z_in", "ln_in", "soft", "gate", "scan"))
    exps, q_done, k_done, chain_s = (c.sem(f"{name}_{n}") for n in ("exps", "q", "k", "chain"))
    v_turn, v_out, k_turn, k_out, act_chain = (c.sem(f"{name}_{n}") for n in ("v_turn", "v_out", "k_turn", "k_out", "act"))
    zeroed = c.sem(f"{name}_zeroed")
    cs = slice(head * P, (head + 1) * P)
    b = [c.cols2[:, C2_AT["b_gate"] + 4 * z_ + head:C2_AT["b_gate"] + 4 * z_ + head + 1] for z_ in range(2)]
    SEG = w.SEG
    parts = [(0, S, 0, 0, 0), (S, CTX, 2, 0, 0), (SEG, S, 1, 0, 1), (SEG + S, CTX, 6, 0, 1)]
    chunks = lambda t: t.rearrange("p (c n) -> p c n", n=CH)
    bc = lambda t, n: t.unsqueeze(2).to_broadcast([P, n, CH])
    with nc.Block() as block:
        @block.gpsimd
        def _(pool):
            nc.gpsimd.memset(w.scores, 0.0).then_inc(zeroed, 1)
            pool.wait_ge(zeroed, 1)

        @block.tensor
        def _(pe):
            for to, n, bank, frm, z_ in parts:
                lo = w.low[32 * z_:32 * z_ + 16, 0 if n == S else S:S if n == S else SEG]
                last = nc.tensor.matmul(c.ps[:, bank, frm:frm + n], w.gb[32 * z_:32 * z_ + 16, cs], lo, start=True,
                                        stop=True, tile_position=(32 * z_, 0))
            last.then_inc(z, 1)
            for j in range(2):
                for n in range(4):
                    nc.tensor.transpose(c.ps[:, 3 + j, n * P:(n + 1) * P],
                                        c.p[:, w.v + 2 * head + j, n * P:(n + 1) * P], c.const("ident"))
            for j in range(2):
                for n in range(2):
                    last = nc.tensor.transpose(c.ps[:, 5, (2 * j + n) * P:(2 * j + n + 1) * P],
                                               w.vc[:, 2 * head + j, n * P:(n + 1) * P], c.const("ident"))
            last.then_inc(v_turn, 1)
            pe.wait_ge(k_done, 4)
            pe.wait_ge(z_in, 8)
            for n in range(12):
                last = nc.tensor.transpose(c.ps[:, n // 4, n % 4 * P:(n % 4 + 1) * P], w.e_neg[:, n * P:(n + 1) * P],
                                           c.const("ident"))
                if n % 4 == 3:
                    last.then_inc(k_turn, 1)

        @block.scalar
        def _(act):
            chain = Chain(act, act_chain)
            act.wait_ge(z, 1)
            for to, n, bank, frm, z_ in parts:
                src = c.ps[:, bank, frm:frm + n]
                nc.scalar.activation(w.g[:, to:to + n], src, ACT.Identity, bias=b[z_]).then_inc(z_in, 1)
                nc.scalar.activation(w.cum[:, to:to + n], src, ACT.Abs, bias=b[z_]).then_inc(z_in, 1)
            act.wait_ge(z_in, 8)
            chain(nc.scalar.activation(w.cum, w.cum, ACT.Exp, scale=-1.0))
            nc.scalar.activation(w.cum, w.cum, ACT.Ln, bias=1.0).then_inc(soft, 1)
            act.wait_ge(v_turn, 1)
            for j in range(2):
                nc.scalar.activation(w.v_tok[:, 0:4, j * P:(j + 1) * P],
                                     c.ps[:, 3 + j, :].rearrange("p (b n) -> p b n", n=P), ACT.Copy).then_inc(v_out, 1)
                nc.scalar.activation(w.v_tok[:, 4:6, j * P:(j + 1) * P],
                                     c.ps[:, 5, 2 * j * P:2 * (j + 1) * P].rearrange("p (b n) -> p b n", n=P), ACT.Copy
                                     ).then_inc(v_out, 1)
            act.wait_ge(gate, 1)
            nc.scalar.activation(w.e_neg, w.cum, ACT.Exp, scale=-1.0 / 16).then_inc(exps, 1)
            nc.scalar.activation(w.e_pos[:, 0:S], w.cum[:, 0:S], ACT.Exp, scale=1.0 / 16).then_inc(exps, 1)
            nc.scalar.activation(w.e_pos[:, S:2 * S], w.cum[:, SEG:SEG + S], ACT.Exp, scale=1.0 / 16).then_inc(exps, 1)
            nc.scalar.activation(w.em, w.half, ACT.Exp, scale=1.0 / 16).then_inc(exps, 1)
            for i in range(3):
                act.wait_ge(k_turn, i + 1)
                nc.scalar.activation(w.k_tok[:, i * S:(i + 1) * S], c.ps[:, i, :], ACT.Copy).then_inc(k_out, 1)

        @block.vector
        def _(dve):
            chain = Chain(dve, chain_s)
            dve.wait_ge(soft, 1)
            chain(nc.vector.scalar_tensor_tensor(w.g, w.g, 0.0, w.cum, ALU.min, ALU.subtract))
            for i in range(3):
                chain(nc.vector.tensor_tensor_scan(w.cum[:, i * S:(i + 1) * S], c.const("scan"),
                                                   w.g[:, i * S:(i + 1) * S], 0.0, ALU.mult, ALU.add))
            chain(nc.vector.tensor_copy(w.tot, chunks(w.cum)[:, :, CH - 1]))
            chain(nc.vector.tensor_scalar(w.half, w.tot, 0.5, None, ALU.mult))
            f, r = w.cum[:, 0:SEG], w.cum[:, SEG:2 * SEG]
            chain(nc.vector.tensor_tensor(chunks(f), chunks(f), bc(w.half[:, 0:12], 12), ALU.subtract))
            chain(nc.vector.tensor_tensor(r, w.g[:, SEG:2 * SEG], r, ALU.subtract))
            chain(nc.vector.tensor_tensor(chunks(r), chunks(r), bc(w.half[:, 12:24], 12), ALU.add))
            nc.vector.tensor_scalar(w.cum, w.cum, 80.0 * 16, -80.0 * 16, ALU.min, ALU.max).then_inc(gate, 1)
            dve.wait_ge(exps, 1)
            k, kc = c.p[:, w.k + head, :], w.kc[:, head, :]
            for to, n, _, _, _ in parts:
                x = w.e_neg[:, to:to + n]
                nc.vector.tensor_tensor(x, x, k if n == S else kc, ALU.mult).then_inc(k_done, 1)
            dve.wait_ge(exps, 4)
            q = c.p[:, w.q + head, :]
            for z_ in range(2):
                x = w.e_pos[:, z_ * S:(z_ + 1) * S]
                nc.vector.scalar_tensor_tensor(x, q, P ** -0.5, x, ALU.mult, ALU.mult).then_inc(q_done, 1)
            em = w.em
            for lo, n in ((0, 7), (8, 3), (12, 7), (20, 3)):
                chain(nc.vector.tensor_tensor(w.step[:, lo:lo + n], em[:, lo:lo + n], em[:, lo + 1:lo + n + 1], ALU.mult))
            chain(nc.vector.tensor_tensor(w.step[:, 11:12], em[:, 11:12], em[:, 0:1], ALU.mult))
            chain(nc.vector.tensor_tensor(w.step[:, 23:24], em[:, 20:21], em[:, 19:20], ALU.mult))


def gla_scan(c, name, w, head):
    nc = c.nc
    scored, masked, update, added, state, summed = (c.sem(f"{name}_{n}") for n in
                                                    ("scored", "masked", "update", "added", "state", "summed"))
    squared, ms, rs_s, silu, chain_s = (c.sem(f"{name}_{n}") for n in ("squared", "ms", "rs", "silu", "chain"))
    STEPS = NCH + LNC
    seg = w.SEG

    def chunk(z, s):
        if s < LNC:
            return 12 * z + 8 + (s if z == 0 else LNC - 1 - s), None
        n = s - LNC if z == 0 else NCH - 1 - (s - LNC)
        return 12 * z + n, n

    def step_col(z, s):
        a, b = chunk(z, s)[0], chunk(z, s + 1)[0]
        return min(a, b) if abs(a - b) == 1 and s != LNC - 1 else 12 * z + 11

    sq = [w.g[:, 0:S], w.g[:, S:2 * S]]
    rs = w.g[:, 2 * S:3 * S]
    t1 = [w.cum[:, 0:S], w.cum[:, S:2 * S]]
    with nc.Block() as block:
        @block.tensor
        def _(pe):
            for z in range(2):
                for n in range(NCH):
                    rows = slice(64 * (n % 2), 64 * (n % 2) + 64)
                    last = nc.tensor.matmul(c.ps[rows, z, n * CH:(n + 1) * CH], w.e_neg[:, z * seg + n * CH:z * seg + (n + 1) * CH],
                                            w.e_pos[:, z * S + n * CH:z * S + (n + 1) * CH], start=True, stop=True)
            last.then_inc(scored, 1)

            def update_of(z, s):
                g, _ = chunk(z, s)
                rows = slice(64 * (g % 2), 64 * (g % 2) + 64)
                block_of = g % 12 // 2
                if s >= 2:
                    pe.wait_ge(added, 2 * (s - 2) + z + 1)
                nc.tensor.matmul(c.ps[:, 4 + 2 * z + s % 2, 0:2 * P], w.k_tok[rows, (g // 2) * P:(g // 2 + 1) * P],
                                 w.v_tok[rows, block_of, :], start=True, stop=True).then_inc(update, 1)

            for z in range(2):
                update_of(z, 0)
            pe.wait_ge(masked, 4)
            for z in range(2):
                for n in range(NCH // 2):
                    for j in range(2):
                        nc.tensor.matmul(c.ps[:, 2 + j, n * P:(n + 1) * P], w.v_tok[:, n, j * P:(j + 1) * P],
                                         w.scores[:, z * S + n * P:z * S + (n + 1) * P], start=(z == 0 and n == 0),
                                         stop=False, skip_group_check=True)
            for s in range(STEPS):
                for z in range(2):
                    if 1 <= s < STEPS - 1:
                        update_of(z, s)
                if s < LNC:
                    continue
                for z in range(2):
                    _, n = chunk(z, s)
                    pe.wait_ge(state, 2 * (s - 1) + z + 1)
                    for j in range(2):
                        last = nc.tensor.matmul(c.ps[:, 2 + j, n * CH:(n + 1) * CH],
                                                w.state[:, z, s % 2, j * P:(j + 1) * P],
                                                w.e_pos[:, z * S + n * CH:z * S + (n + 1) * CH], start=False,
                                                stop=(s == STEPS - 1 and z == 1), skip_group_check=True)
                    last.then_inc(summed, 1)
            for j in range(2):
                pe.wait_ge(squared, j + 1)
                last = nc.tensor.matmul(c.ps[:, 1, :], c.const("ones"), sq[j], start=(j == 0), stop=(j == 1))
            last.then_inc(ms, 1)

        @block.scalar
        def _(act):
            for j in range(2):
                r = c.p[:, w.r + 2 * head + j, :]
                nc.scalar.activation(r, r, ACT.Silu).then_inc(silu, 1)
            act.wait_ge(summed, 2 * NCH)
            for j in range(2):
                nc.scalar.activation(sq[j], c.ps[:, 2 + j, :], ACT.Square).then_inc(squared, 1)
            act.wait_ge(ms, 1)
            nc.scalar.activation(rs, c.ps[:, 1, :], ACT.Ln, bias=c.const("eps"), scale=1.0 / (2 * P)).then_inc(rs_s, 1)
            act.wait_ge(rs_s, 1)
            nc.scalar.activation(rs, rs, ACT.Exp, scale=-0.5).then_inc(rs_s, 1)

        @block.vector
        def _(dve):
            dve.wait_ge(scored, 1)
            pairs = lambda t, par: t.rearrange("p (n h i) -> p n h i", h=2, i=CH)[64 * par:64 * par + 64, :, par, :]
            for z, mask in enumerate(("gla_f", "gla_b")):
                for par in range(2):
                    m = c.const(mask).rearrange("p (n i) -> p n i", i=CH)[64 * par:64 * par + 64]
                    nc.vector.tensor_tensor(pairs(w.scores[:, z * S:(z + 1) * S], par), pairs(c.ps[:, z, :], par), m,
                                            ALU.mult).then_inc(masked, 1)
            for s in range(STEPS - 1):
                for z in range(2):
                    n = 2 * s + z
                    dve.wait_ge(update, n + 1)
                    new, old = w.state[:, z, (s + 1) % 2, :], w.state[:, z, s % 2, :]
                    u = c.ps[:, 4 + 2 * z + s % 2, 0:2 * P]
                    if s > LNC:
                        dve.wait_ge(summed, 2 * (s - 1 - LNC) + z + 1)
                    at = step_col(z, s)
                    decay = w.step[:, at:at + 1]
                    if s == 0:
                        nc.vector.tensor_copy(new, u).then_inc(added, 1)
                    else:
                        dve.wait_ge(state, n - 1)
                        nc.vector.tensor_tensor(new, u, old, ALU.add).then_inc(added, 1)
                    dve.wait_ge(added, n + 1)
                    nc.vector.tensor_scalar(new, new, decay, None, ALU.mult).then_inc(state, 1)
            chain = Chain(dve, chain_s)
            dve.wait_ge(rs_s, 2)
            dve.wait_ge(silu, 2)
            for j in range(2):
                gain = c.cols2[:, C2_AT["gla_norm_g"] + j:C2_AT["gla_norm_g"] + j + 1]
                chain(nc.vector.scalar_tensor_tensor(t1[j], c.ps[:, 2 + j, :], gain, rs, ALU.mult, ALU.mult))
                chain(nc.vector.tensor_tensor(c.y[:, 2 * head + j, :], t1[j], c.p[:, w.r + 2 * head + j, :], ALU.mult))


def route(c, name):
    nc = c.nc
    B = S // P
    loaded, logits, sig, gates, turned, turned_out, stored, chain_s = (
        c.sem(f"{name}_{n}") for n in ("loaded", "logits", "sig", "gates", "turned", "turned_out", "stored", "chain"))
    router_w = c.p[:, 0, 0:KT * E_N]
    cell = [c.p[:, 1 + i, 0:B * E_N] for i in range(9)]
    score, sel, rank, best_in, top, t0, t1, gs, chosen = cell
    four = lambda t: t.rearrange("p (g e) -> p g e", e=4)
    gT = c.p[0:E_N, 12, :]
    with nc.Block() as block:
        @block.sync
        def _(sp):
            sp.dma_start(router_w, c.dram["router"]).then_inc(loaded, 16)
            sp.wait_ge(turned_out, 1)
            sp.dma_start(c.dram["gates"], gT).then_inc(stored, 16)
            sp.wait_ge(stored, 16)

        @block.tensor
        def _(pe):
            pe.wait_ge(loaded, 16)
            for b in range(B):
                for kt in range(KT):
                    last = nc.tensor.matmul(c.ps[:, 0, b * E_N:(b + 1) * E_N], c.h[:, kt, b * P:(b + 1) * P],
                                            router_w[:, kt * E_N:(kt + 1) * E_N], start=(kt == 0), stop=(kt == KT - 1))
            last.then_inc(logits, 1)
            pe.wait_ge(gates, 1)
            for b in range(B):
                last = nc.tensor.transpose(c.ps[0:E_N, 1, b * P:(b + 1) * P], chosen[:, b * E_N:(b + 1) * E_N],
                                           c.const("ident"))
            last.then_inc(turned, 1)

        @block.scalar
        def _(act):
            act.wait_ge(logits, 1)
            nc.scalar.activation(score, c.ps[:, 0, 0:B * E_N], ACT.Sigmoid).then_inc(sig, 1)
            act.wait_ge(turned, 1)
            nc.scalar.activation(gT, c.ps[0:E_N, 1, :], ACT.Copy).then_inc(turned_out, 1)

        @block.vector
        def _(dve):
            chain = Chain(dve, chain_s)
            dve.wait_ge(sig, 1)
            bias = c.cols2[:, C2_AT["b_router"]:C2_AT["b_router"] + E_N]
            for b in range(B):
                chain(nc.vector.tensor_tensor(sel[:, b * E_N:(b + 1) * E_N], score[:, b * E_N:(b + 1) * E_N], bias,
                                              ALU.add))
            chain(nc.vector.memset(rank, 0.0))
            for i in range(4):
                for j in range(i + 1, 4):
                    si, sj = four(sel)[:, :, i], four(sel)[:, :, j]
                    ri, rj = four(rank)[:, :, i], four(rank)[:, :, j]
                    ge = t0[:, 0:16]
                    chain(nc.vector.tensor_tensor(ge, si, sj, ALU.is_ge))
                    chain(nc.vector.tensor_tensor(rj, rj, ge, ALU.add))
                    chain(nc.vector.tensor_tensor(ri, ri, ge, ALU.subtract))
                    chain(nc.vector.tensor_scalar(ri, ri, 1.0, None, ALU.add))
            chain(nc.vector.tensor_scalar(top, rank, 1.5, None, ALU.is_lt))
            chain(nc.vector.tensor_tensor(t0, top, sel, ALU.mult))
            chain(nc.vector.tensor_reduce(gs[:, 0:16], four(t0), AXX, ALU.add))
            groups = gs[:, 0:16].rearrange("p (b g) -> p b g", g=4)
            win = t1[:, 0:16]
            wins = win.rearrange("p (b g) -> p b g", g=4)
            ge = best_in[:, 0:4]
            chain(nc.vector.memset(win, 0.0))
            for i in range(4):
                for j in range(i + 1, 4):
                    chain(nc.vector.tensor_tensor(ge, groups[:, :, i], groups[:, :, j], ALU.is_ge))
                    chain(nc.vector.tensor_tensor(wins[:, :, i], wins[:, :, i], ge, ALU.add))
                    chain(nc.vector.tensor_tensor(wins[:, :, j], wins[:, :, j], ge, ALU.subtract))
                    chain(nc.vector.tensor_scalar(wins[:, :, j], wins[:, :, j], 1.0, None, ALU.add))
            chain(nc.vector.tensor_scalar(win, win, 2.5, None, ALU.is_gt))
            for e in range(4):
                chain(nc.vector.tensor_tensor(four(top)[:, :, e], four(top)[:, :, e], win, ALU.mult))
            chain(nc.vector.tensor_tensor(chosen, top, score, ALU.mult))
            total = t1[:, 16:16 + B]
            chain(nc.vector.tensor_reduce(total, chosen.rearrange("p (b e) -> p b e", e=E_N), AXX, ALU.add))
            chain(nc.vector.reciprocal(total, total))
            for b in range(B):
                ins = nc.vector.tensor_scalar(chosen[:, b * E_N:(b + 1) * E_N], chosen[:, b * E_N:(b + 1) * E_N],
                                              total[:, b:b + 1], None, ALU.mult)
                if b < B - 1:
                    chain(ins)
            ins.then_inc(gates, 1)


def experts(c, name, gain):
    nc = c.nc
    loaded = [[c.sem(f"{name}_{n}_loaded{i}") for n in ("w1", "w3", "w2", "gate")] for i in range(2)]
    up, up_used, silu, prod, gated, down, added = (c.sem(f"{name}_{n}") for n in
                                                   ("up", "up_used", "silu", "prod", "gated", "down", "added"))
    flat = lambda t: t.rearrange("p a n -> p (a n)")
    p = flat(c.p[:, :, :])
    big = ET * D
    w1 = [p[:, 0:big], c.ring[:, 0:big]]
    w3 = [p[:, big:2 * big], c.ring[:, big:2 * big]]
    w2 = [p[:, 2 * big:3 * big], flat(c.w2b[:, :, :])]
    gate = [c.vt[:, 0, 0:S], c.vt[:, 0, S:2 * S]]
    sil = [c.vt[:, 1, 0:S], c.vt[:, 1, S:2 * S]]
    he = [c.y[:, 0:4, :], c.y[:, 4:8, :]]
    DN = 4

    with nc.Block() as block:
        @block.sync
        def _(sp):
            def load(i, e, first):
                row = lambda t: c.dram[t][bass.ds(e, 1), :, :].rearrange("a p n -> p (a n)")
                if not first:
                    sp.wait_ge(up, (e - 2) * ET + ET)
                sp.dma_start(w1[i], row("moe_gate")).then_inc(loaded[i][0], 16)
                sp.dma_start(w3[i], row("moe_up")).then_inc(loaded[i][1], 16)
                if not first:
                    sp.wait_ge(gated, (e - 2) * ET + ET)
                sp.dma_start(gate[i], c.dram["gates"][bass.ds(e, 1), :].to_broadcast([P, S])).then_inc(loaded[i][3], 16)
                if not first:
                    sp.wait_ge(down, (e - 2) * KT + KT)
                sp.dma_start(w2[i], row("moe_down")).then_inc(loaded[i][2], 16)

            load(0, 0, True)
            load(1, 1, True)
            with sp.Fori(1, E_N // 2) as r:
                for i in range(2):
                    load(i, 2 * r + i, False)

        @block.tensor
        def _(pe):
            def ups(i, e, first):
                pe.wait_ge(loaded[i][0], 16 * (e_round(e, i) + 1))
                pe.wait_ge(loaded[i][1], 16 * (e_round(e, i) + 1))
                for f in range(ET):
                    if not (first and f < 2):
                        pe.wait_ge(prod, e * ET + f - 1)
                    for m, w in ((0, w1[i]), (1, w3[i])):
                        for kt in range(KT):
                            last = nc.tensor.matmul(c.ps[:, 2 * (f % 2) + m, :], w[:, f * D + kt * P:f * D + (kt + 1) * P],
                                                    c.h[:, kt, :], start=(kt == 0), stop=(kt == KT - 1))
                    last.then_inc(up, 1)

            def downs(i, e, first):
                pe.wait_ge(loaded[i][2], 16 * (e_round(e, i) + 1))
                pe.wait_ge(gated, e * ET + ET)
                for t in range(KT):
                    if not (first and t < DN):
                        pe.wait_ge(added, e * KT + t - DN + 1)
                    for f in range(ET):
                        last = nc.tensor.matmul(c.ps[:, 4 + t % DN, :], w2[i][:, t * DE + f * P:t * DE + (f + 1) * P],
                                                he[i][:, f, :], start=(f == 0), stop=(f == ET - 1))
                    last.then_inc(down, 1)

            def e_round(e, i):
                return (e - i) // 2 if isinstance(e, int) else pe_round[0]

            pe_round = [None]
            ups(0, 0, True)
            ups(1, 1, False)
            downs(0, 0, True)
            with pe.Fori(1, E_N // 2) as r:
                pe_round[0] = r
                ups(0, 2 * r, False)
                pe_round[0] = r - 1
                downs(1, 2 * r - 1, False)
                pe_round[0] = r
                ups(1, 2 * r + 1, False)
                downs(0, 2 * r, False)
            downs(1, E_N - 1, False)

        @block.scalar
        def _(act):
            def silus(e, first):
                for f in range(ET):
                    act.wait_ge(up, e * ET + f + 1)
                    if not (first and f < 2):
                        act.wait_ge(prod, e * ET + f - 1)
                    nc.scalar.activation(sil[f % 2], c.ps[:, 2 * (f % 2), :], ACT.Silu).then_inc(silu, 1)

            silus(0, True)
            silus(1, False)
            with act.Fori(1, E_N // 2) as r:
                silus(2 * r, False)
                silus(2 * r + 1, False)

        @block.vector
        def _(dve):
            def hidden(i, e, rnd, first):
                dve.wait_ge(loaded[i][3], 16 * (rnd + 1))
                if not first:
                    dve.wait_ge(down, (e - 2) * KT + KT)
                for f in range(ET):
                    dve.wait_ge(silu, e * ET + f + 1)
                    nc.vector.tensor_tensor(he[i][:, f, :], c.ps[:, 2 * (f % 2) + 1, :], sil[f % 2], ALU.mult
                                            ).then_inc(prod, 1)
                    dve.wait_ge(prod, e * ET + f + 1)
                    nc.vector.tensor_tensor(he[i][:, f, :], he[i][:, f, :], gate[i], ALU.mult).then_inc(gated, 1)

            def sums(e):
                for t in range(KT):
                    dve.wait_ge(down, e * KT + t + 1)
                    nc.vector.scalar_tensor_tensor(c.x[:, t, :], c.ps[:, 4 + t % DN, :], gain[:, t:t + 1], c.x[:, t, :],
                                                   ALU.mult, ALU.add).then_inc(added, 1)

            hidden(0, 0, 0, True)
            hidden(1, 1, 0, True)
            sums(0)
            with dve.Fori(1, E_N // 2) as r:
                hidden(0, 2 * r, r, False)
                sums(2 * r - 1)
                hidden(1, 2 * r + 1, r, False)
                sums(2 * r)
            sums(E_N - 1)
            dve.wait_ge(added, E_N * KT)


def block_two(c, stop=None):
    nc, dram = c.nc, c.dram
    mod = lambda i: c.mod[:, i * KT:(i + 1) * KT]
    col = lambda n, k=8: c.cols2[:, C2_AT[n]:C2_AT[n] + k]
    tmp = c.ring[:, RING * D:]
    w = Gla(c)
    with c.stages():
        ctx_loaded = c.sem("ctx_loaded")
        with nc.Block() as block:
            @block.sync
            def _(sp):
                sp.dma_start(c.cols2[:, :], dram["cols2"]).then_inc(ctx_loaded, 16)
                for t in range(KT):
                    sp.dma_start(w.ctx_x[:, t, :], dram["ctxT"][t, :, :]).then_inc(ctx_loaded, 16)
                sp.wait_ge(ctx_loaded, 16 * (KT + 1))
        norm_modulate(c, "b2_norm1", c.x, c.h, col("norm1_g"), mod(1), mod(0), tmp=tmp)
        norm_modulate(c, "b2_norm_ctx", w.ctx_x, w.ctx_h, col("norm1_g"), c.ctxmod[:, KT:2 * KT], c.ctxmod[:, 0:KT],
                      n_tok=CTX, tmp=tmp)
        gla_project(c, w)
    if stop == "gla_in":
        return
    for head in range(4):
        with c.stages():
            gla_prepare(c, f"gla_prep{head}", w, head)
            gla_scan(c, f"gla_scan{head}", w, head)
    if stop == "gla":
        return
    with c.stages():
        gla_out = Linear(c, "gla_out", KT, lambda t: dram["gla_out"][bass.ds(t, 1), :, :].rearrange("a p n -> p (a n)"))
        with nc.Block() as block:
            @block.sync
            def _(sp):
                gla_out.prefetch(sp)
        linear_stage(c, gla_out, lambda kt: c.y[:, kt, :],
                     ("vector", lambda dve: residual_tiles(c, gla_out, dve, mod(2))))
        norm_modulate(c, "b2_norm2", c.x, c.h, col("norm2_g"), mod(4), mod(3), tmp=tmp)
        route(c, "route")
    if stop == "route":
        return
    with c.stages():
        experts(c, "moe", mod(5))
    if stop == "moe":
        return
    with c.stages():
        norm_modulate(c, "final", c.x, c.h, col("final_g"), None, None, tmp=tmp)
        stored = c.sem("out_stored")
        with nc.Block() as block:
            @block.sync
            def _(sp):
                for t in range(KT):
                    sp.dma_start(dram["out"][t, :, :], c.h[:, t, :]).then_inc(stored, 16)
                sp.wait_ge(stored, 16 * KT)


def first_adaln(c, name, which, cond, dst, width):
    nc = c.nc
    cond_load, ready = load_cond(c, name, cond)
    sums = AdaLN(c, name, which, width)
    with nc.Block() as block:
        @block.scalar
        def _(act):
            cond_load(act)
            sums.load(act)

        @block.vector
        def _(dve):
            dve.wait_ge(ready, 1)
            sums.add(dve, 0, sums.pieces)
    adaln_finish(c, name, which, dst, width)


def build(nc, dram):
    with ExitStack() as ctx:
        c = Core(nc, ctx, dram)
        with c.stages():
            load_constants(c)
            first_adaln(c, "ctx_mod", 2, 3, c.ctxmod[:, :], 2 * D)
        with c.stages():
            first_adaln(c, "mod0", 0, 0, c.mod[:, :], 6 * D)
        with nc.Fori(0, L) as layer:
            with c.stages():
                block_one_layer(c, layer)
        block_two(c)


def kernel(**inputs):
    import concourse.bacc as bacc
    from concourse.bass_utils import run_bass_kernel_spmd

    nc = bacc.Bacc("TRN2", target_bir_lowering=False, num_devices=1)
    arrays = {f"in_{n}": a for n, a in host_layout(inputs).items()}
    dram = {n[3:]: nc.dram_tensor(n, a.shape, F32, kind="ExternalInput").ap() for n, a in arrays.items()}
    dram["gates"] = nc.dram_tensor("gates", (E_N, S), F32, kind="Internal").ap()
    dram["out"] = nc.dram_tensor("out", (KT, P, S), F32, kind="ExternalOutput").ap()
    build(nc, dram)
    r = run_bass_kernel_spmd(nc, [arrays], core_ids=[0])
    return np.ascontiguousarray(r.results[0]["out"].reshape(D, S).T).reshape(1, S, D)


def host_layout(i):
    f = np.float32
    A = {k: np.asarray(v) for k, v in i.items()}

    def tiles(w, k_tiles=None):
        K, N = w.shape
        return np.ascontiguousarray(w.reshape(K // P, P, N // P, P).transpose(2, 1, 0, 3).reshape(N // P, P, K))

    def cols(v):
        return v.reshape(-1, P).T

    out = {"xT": np.ascontiguousarray(A["x"][0].T.reshape(KT, P, S))}
    w_in = np.concatenate([A["w_in"], np.zeros((L, D, IN_T * P - A["w_in"].shape[2]), f)], axis=2)
    out["w_in"] = np.concatenate([tiles(w_in[l]) for l in range(L)])
    out["w_out"] = np.concatenate([tiles(A["w_out"][l]) for l in range(L)])
    pairs = lambda w: w.reshape(*w.shape[:-1], 2, FT, P).swapaxes(-3, -2).reshape(*w.shape)
    out["ffn_up"] = np.concatenate([tiles(pairs(A["ffn_up"][l])) for l in range(L)])
    out["ffn_down"] = np.concatenate([tiles(A["ffn_down"][l]) for l in range(L)])
    ada = lambda w: w.reshape(KT, P, 6 * D).transpose(1, 0, 2)
    out["ada"] = np.stack([ada(A["ada_w"][0]), ada(A["ada_w"][1]), ada(A["w_mod_2"][0])])
    out["ada_b"] = np.stack([cols(v) for v in (A["ada_b"][0], A["ada_b"][1], A["b_mod_2"][0])])
    out["cond"] = np.stack([cols(v) for v in (A["c"][0], A["c"][0], A["c_2"][0], A["c_ctx_2"])])

    lam_init = [0.8 - 0.6 * math.exp(-0.3 * l) for l in range(L)]
    packed = []
    for l in range(L):
        taps = np.concatenate([A["ffn_conv"][l], A["ffn_conv_b"][l][None]])
        taps = pairs(taps).reshape(4, 2 * FT, P).transpose(2, 1, 0).reshape(P, 8 * FT)
        f_b = np.zeros((P, 1), f)
        f_b[0:4, 0] = A["fx_f_b"][l]
        lam = np.concatenate([A["df_lam_q1"][l], A["df_lam_q2"][l], A["df_lam_k1"][l], A["df_lam_k2"][l]])
        part = {
            "norm1_g": cols(A["norm1_g"][l]), "norm2_g": cols(A["norm2_g"][l]), "rw_mu": cols(A["rw_mu"][l]),
            "rw_w0": cols(A["rw_w0"][l]), "rw_a0": cols(A["rw_a0"][l]), "rw_k_k": cols(A["rw_k_k"][l]),
            "rw_k_a": cols(A["rw_k_a"][l]), "rw_r_k": cols(A["rw_r_k"][l].reshape(-1)),
            "rw_ln_g": cols(A["rw_ln_g"][l]), "rw_ln_b": cols(A["rw_ln_b"][l]),
            "df_q_g": np.tile(A["df_q_g"][l], 4)[:, None], "df_k_g": np.tile(A["df_k_g"][l], 4)[:, None],
            "df_sub_g": np.tile(A["df_sub_g"][l], 2)[:, None], "sg_ln_g": cols(A["sg_ln_g"][l]),
            "sg_ln_b": cols(A["sg_ln_b"][l]), "fx_q_g": np.tile(A["fx_q_g"][l], 2)[:, None],
            "fx_k_g": np.tile(A["fx_k_g"][l], 2)[:, None], "fx_f_b": f_b,
            "lam_init": np.full((P, 1), lam_init[l], f), "lam_vec": np.tile(lam[None, :], (P, 1)),
            "ffn_tap": taps, "ffn_bias": np.zeros((P, 44), f),
        }
        packed.append(np.concatenate([part[n].astype(f, copy=False) for n, _ in COLS], axis=1))
    out["cols"] = np.stack(packed)
    out["rw_lora"] = np.concatenate([A["rw_w_up"], A["rw_a_up"], A["rw_g_up"]], axis=1)
    out["sg_wT"] = np.ascontiguousarray(A["sg_w"].transpose(0, 3, 1, 2).reshape(L, P, 4 * P))
    out["sg_b"] = A["sg_b"]
    pick = np.zeros((4, 256), f)
    for g in range(4):
        pick[g, g * 64:(g + 1) * 64] = 1.0
    out["sg_pick"] = pick
    out["const"] = constants()

    w = A["gla_w_in_2"][0]
    q, k, v, r = w[:, 0:512], w[:, 512:1024], w[:, 1024:2048], w[:, 2048:3072]
    out["gla_in"] = tiles(np.concatenate([q, r, k, v], axis=1))
    low = np.zeros((D, 64), f)
    low[:, 0:16], low[:, 32:48] = A["gla_w_gate_a_2"][0, 0], A["gla_w_gate_a_2"][0, 1]
    out["gla_low"] = np.ascontiguousarray(low.reshape(KT, P, 64).transpose(1, 0, 2).reshape(P, KT * 64))
    gb = np.zeros((P, 512), f)
    gb[0:16], gb[32:48] = A["gla_w_gate_b_2"][0, 0], A["gla_w_gate_b_2"][0, 1]
    out["gla_gb"] = gb
    out["gla_out"] = tiles(A["gla_w_out_2"][0])
    out["ctxT"] = np.ascontiguousarray(A["ctx_2"][0].T.reshape(KT, P, CTX))
    part = {"norm1_g": cols(A["norm1_g_2"][0]), "norm2_g": cols(A["norm2_g_2"][0]), "final_g": cols(A["final_g_2"]),
            "b_gate": cols(A["gla_b_gate_2"][0].reshape(-1)), "gla_norm_g": cols(A["gla_norm_g_2"][0]),
            "b_router": np.tile(A["b_router_2"][None, :], (P, 1))}
    out["cols2"] = np.concatenate([part[n] for n, _ in COLS2], axis=1)
    out["router"] = np.ascontiguousarray(A["w_router_2"].reshape(KT, P, E_N).transpose(1, 0, 2).reshape(P, KT * E_N))

    def experts(w):
        return np.stack([tiles(w[e]).transpose(1, 0, 2).reshape(P, -1) for e in range(E_N)])

    out["moe_gate"], out["moe_up"], out["moe_down"] = (experts(A[n][0]) for n in ("w_gate_e_2", "w_up_e_2", "w_down_e_2"))
    return out


def constants():
    f = np.float32
    n = np.arange(P)
    k = {"ident": np.eye(P), "ones": np.ones((P, P)), "bo64": np.kron(np.eye(2), np.ones((64, 64))),
         "bo32": np.kron(np.eye(4), np.ones((32, 32)))}
    perm = np.zeros((P, P))
    for m in range(P):
        if m % 32 < 16:
            perm[m + 16, m] = -1.0
        else:
            perm[m - 16, m] = 1.0
    k["perm"] = perm
    inv = (1.0 / (f(10000.0) ** (np.arange(0, 32, 2, dtype=f) / f(32)))).astype(f)
    ang = (np.arange(S, dtype=f)[None, :] * inv[:, None]).astype(f)
    k["cos"], k["sin"] = np.tile(np.cos(ang), (8, 1)), np.tile(np.sin(ang), (8, 1))
    k["mask_causal"] = np.where(n[None, :] <= n[:, None], 0.0, NEG)
    k["mask_chunk"] = np.where(n[None, :] // 64 <= n[:, None] // 64, 0.0, NEG)
    k["scan"] = np.tile((np.arange(S) % CH != 0).astype(f)[None, :], (P, 1))
    r, q = n[:, None], n[None, :]
    head, block16 = r // 64 == q // 64, r // 16 == q // 16
    four = lambda m: np.tile(m.astype(f), (1, 4))
    k["m_ld"], k["m_ldT"] = four(head & block16 & (q < r)), four(head & block16 & (q > r))
    k["m_loT"], k["m_kaT"] = four(head & ~block16 & (q > r)), four(head & (q > r))
    k["m_r"] = four(q % 64 >= r % 64)
    k["ident4"] = four(r == q)
    t = np.arange(64)
    k["gla_f"] = np.tile((t[None, :] >= t[:, None]).astype(f), (2, 4))
    k["gla_b"] = np.tile((t[None, :] <= t[:, None]).astype(f), (2, 4))
    k["eps"], k["gn_eps"] = np.full((P, 1), EPS), np.full((P, 1), GN_EPS)
    k["kk_shift"] = np.full((P, 1), 0.5 * math.log(KK_SCALE))
    return np.concatenate([k[name].astype(f) for name, _ in CONST], axis=1)
```

```python
import math
from contextlib import ExitStack, contextmanager

import numpy as np
import concourse.bass as bass
from concourse import mybir

F32 = mybir.dt.float32
F32R = mybir.dt.float32r
I32 = mybir.dt.int32
ACT = mybir.ActivationFunctionType
ALU = mybir.AluOpType
AXX = mybir.AxisListType.X

P = 128
D = 1024
KT = D // P
S = 512
L = 2
NMOD = 6 * KT
FF = 2816
FT = FF // P
IN_T = 24
RING = 4
CH = 64
NCH = S // CH
E_N = 16
DE = 512
ET = DE // P
CTX = 256
LNC = CTX // CH
EPS = 1e-6
GN_EPS = 64e-5
NEG = -1e30

COLS = [("norm1_g", 8), ("norm2_g", 8), ("rw_mu", 7), ("rw_w0", 2), ("rw_a0", 2), ("rw_k_k", 2), ("rw_k_a", 2),
        ("rw_r_k", 2), ("rw_ln_g", 2), ("rw_ln_b", 2), ("df_q_g", 1), ("df_k_g", 1), ("df_sub_g", 1),
        ("sg_ln_g", 2), ("sg_ln_b", 2), ("fx_q_g", 1), ("fx_k_g", 1), ("fx_f_b", 1), ("lam_init", 1),
        ("lam_vec", 128), ("ffn_tap", 176), ("ffn_bias", 44)]
COLS2 = [("norm1_g", 8), ("norm2_g", 8), ("final_g", 8), ("b_gate", 8), ("gla_norm_g", 2), ("b_router", 16)]
CONST = [("ident", 128), ("ones", 128), ("bo64", 128), ("bo32", 128), ("perm", 128), ("cos", 512), ("sin", 512),
         ("mask_causal", 128), ("mask_chunk", 128), ("scan", 512), ("m_ld", 512), ("m_ldT", 512), ("m_loT", 512),
         ("m_kaT", 512), ("m_r", 512), ("ident4", 512), ("gla_f", 256), ("gla_b", 256), ("eps", 1), ("gn_eps", 1),
         ("kk_shift", 1), ("before", 128), ("iota", 128)]
KK_SCALE = 2.0 ** 40


def offsets(table):
    at, n = {}, 0
    for name, width in table:
        at[name] = n
        n += width
    return at, n


C_AT, C_N = offsets(COLS)
C2_AT, C2_N = offsets(COLS2)
K_AT, K_N = offsets(CONST)


class Core:

    def __init__(self, nc, ctx, dram):
        self.nc, self.ctx, self.dram = nc, ctx, dram
        self.groups = []

        self.address = {}

        def sb(name, *shape):
            t = ctx.enter_context(nc.sbuf_tensor(name, [P, *shape], F32))
            self.address[name] = nc.sbuf_base - 4 * math.prod(shape)
            return t

        self.x = sb("x", KT, S)
        self.h = sb("h", KT, S)
        self.p = sb("p", IN_T, S)
        self.y = sb("y", KT, S)
        self.ring = sb("ring", 4 * FT * P)
        self.vt = sb("vt", 4, 1024)
        self.k = sb("k", K_N)
        self.cols = sb("cols", C_N)
        self.mod = sb("mod", NMOD)
        self.w2b = sb("w2b", 4, 1024)
        self.cols2 = sb("cols2", C2_N)
        self.o_lo = ctx.enter_context(nc.sbuf_tensor("o_lo", [P, D], F32R))
        self.numbers = ctx.enter_context(nc.sbuf_tensor("numbers", [P, 32], I32))
        self.cond = sb("cond", KT)
        self.ctxmod = sb("ctxmod", 2 * KT)
        self.small = sb("small", 128)
        self.small2 = sb("small2", 256)
        self.acc = [self.y[:, 2 * i:2 * i + 2, :].rearrange("p a n -> p (a n)") for i in range(4)]
        self.acc += [self.vt[:, i, :] for i in range(2)]
        self.piece = [self.vt[:, 2 + i, :] for i in range(2)]
        self.w_hi = self.alias("w_hi", "ring", RING * D, [2, D], F32R)
        self.w_lo = self.alias("w_lo", "ring", RING * D + 2 * D, [2, D], F32R)
        self.a_hi = self.alias("a_hi", "w2b", 0, [KT, S], F32R)
        self.h_lo = self.alias("h_lo", "h", 0, [KT, S], F32R)
        self.y_lo = self.alias("y_lo", "y", 0, [KT, S], F32R)
        self.low_hi, self.low_lo = (self.alias(n, "ring", RING * D + (9 + i) * S, [S], F32R)
                                    for i, n in enumerate(("low_hi", "low_lo")))
        self.ctx_hi, self.ctx_lo = (self.alias(n, "y", i * 4 * S, [KT, CTX], F32R)
                                    for i, n in enumerate(("ctx_hi", "ctx_lo")))
        self.ps = ctx.enter_context(nc.psum_tensor("ps", [P, 8, 512], F32))

    def sem(self, name):
        stack, sems = self.groups[-1]
        s = stack.enter_context(self.nc.semaphore(name))
        sems.append(s)
        return s

    def alias(self, name, of, at, shape, dtype):
        return self.nc.alloc_sbuf_tensor_at(name, [P, *shape], dtype, offset=self.address[of] + 4 * at)

    @contextmanager
    def stages(self):
        with ExitStack() as stack:
            self.groups.append((stack, []))
            yield
            _, sems = self.groups.pop()
            self.clear(sems)

    def const(self, name, width=None):
        at = K_AT[name]
        return self.k[:, at:at + (width or dict(CONST)[name])]

    def col(self, name, i=0, n=1):
        at = C_AT[name] + i
        return self.cols[:, at:at + n]

    def slot(self, s, size=D):
        return self.ring[:, s * size:(s + 1) * size]

    def clear(self, sems):
        nc = self.nc
        with nc.Block() as block:
            @block.gpsimd
            def _(pool):
                for s in sems:
                    nc.gpsimd.sem_clear(s)


class Chain:

    def __init__(self, eng, sem):
        self.eng, self.sem, self.n = eng, sem, 0

    def __call__(self, ins):
        self.n += 1
        ins.then_inc(self.sem, 1)
        self.eng.wait_ge(self.sem, self.n)


def load_constants(c):
    nc, dram = c.nc, c.dram
    loaded = c.sem("const_loaded")
    with nc.Block() as block:
        @block.sync
        def _(sp):
            sp.dma_start(c.k[:, :], dram["const"]).then_inc(loaded, 16)
            for t in range(KT):
                sp.dma_start(c.x[:, t, :], dram["xT"][t, :, :]).then_inc(loaded, 16)
            sp.wait_ge(loaded, 16 * (KT + 1))


class AdaLN:

    def __init__(self, c, name, which, width=6 * D):
        self.c, self.which, self.per_row = c, which, width // D
        self.pieces = KT * self.per_row
        self.loaded = [c.sem(f"{name}_piece_loaded{i}") for i in range(2)]
        self.used = c.sem(f"{name}_piece_used")

    def load(self, queue):
        for n in range(self.pieces):
            kt, j = divmod(n, self.per_row)
            if n >= 2:
                queue.wait_ge(self.used, n - 1)
            src = self.c.dram["ada"][bass.ds(self.which, 1), :, kt, j * D:(j + 1) * D]
            queue.dma_start(self.c.piece[n % 2], src.rearrange("a p n -> p (a n)")).then_inc(self.loaded[n % 2], 16)

    def add(self, dve, first, last):
        c, nc = self.c, self.c.nc
        for n in range(first, last):
            kt, j = divmod(n, self.per_row)
            dve.wait_ge(self.loaded[n % 2], 16 * (n // 2 + 1))
            out, cond = c.acc[j], c.cond[:, kt:kt + 1]
            if kt == 0:
                ins = nc.vector.tensor_scalar(out, c.piece[n % 2], cond, None, ALU.mult)
            else:
                dve.wait_ge(self.used, n - self.per_row + 1)
                ins = nc.vector.scalar_tensor_tensor(out, c.piece[n % 2], cond, out, ALU.mult, ALU.add)
            ins.then_inc(self.used, 1)


def load_cond(c, name, which):
    nc, dram = c.nc, c.dram
    loaded, ready = c.sem(f"{name}_cond_loaded"), c.sem(f"{name}_cond_ready")

    def scalar(act):
        act.dma_start(c.small[:, 0:KT], dram["cond"][bass.ds(which, 1), :, :].rearrange("a p n -> p (a n)")
                      ).then_inc(loaded, 16)
        act.wait_ge(loaded, 16)
        nc.scalar.activation(c.cond[:, :], c.small[:, 0:KT], ACT.Silu).then_inc(ready, 1)

    return scalar, ready


def adaln_finish(c, name, which, dst, width=6 * D):
    nc, dram = c.nc, c.dram
    summed, biased, loaded = c.sem(f"{name}_summed"), c.sem(f"{name}_biased"), c.sem(f"{name}_bias_loaded")
    n = width // P
    with nc.Block() as block:
        @block.sync
        def _(sp):
            sp.dma_start(dst, dram["ada_b"][bass.ds(which, 1), :, 0:n].rearrange("a p n -> p (a n)")
                         ).then_inc(loaded, 16)

        @block.tensor
        def _(pe):
            for t in range(n):
                last = nc.tensor.matmul(c.ps[:, 0, t:t + 1], c.acc[t // KT][:, t % KT * P:(t % KT + 1) * P], c.const("ones", 1),
                                        start=True, stop=True)
            last.then_inc(summed, 1)

        @block.vector
        def _(dve):
            dve.wait_ge(loaded, 16)
            dve.wait_ge(summed, 1)
            nc.vector.tensor_tensor(dst, c.ps[:, 0, 0:n], dst, ALU.add).then_inc(biased, 1)
            dve.wait_ge(biased, 1)


def norm_modulate(c, name, x, h, gain, scale, shift, n_tok=S, extra_act=None, tmp=None, split=None):
    nc = c.nc
    squared, summed, rs_ready = c.sem(f"{name}_squared"), c.sem(f"{name}_summed"), c.sem(f"{name}_rs")
    a_ready, scaled, done = c.sem(f"{name}_a"), c.sem(f"{name}_scaled"), c.sem(f"{name}_done")
    rs = tmp[:, 0:n_tok]
    a = c.small[:, 16:24]
    with nc.Block() as block:
        @block.tensor
        def _(pe):
            for t in range(KT):
                pe.wait_ge(squared, t + 1)
                last = nc.tensor.matmul(c.ps[:, 0, 0:n_tok], c.const("ones"), h[:, t, :], start=(t == 0),
                                        stop=(t == KT - 1))
            last.then_inc(summed, 1)

        @block.scalar
        def _(act):
            for t in range(KT):
                nc.scalar.activation(h[:, t, :], x[:, t, :], ACT.Square).then_inc(squared, 1)
            act.wait_ge(summed, 1)
            nc.scalar.activation(rs, c.ps[:, 0, 0:n_tok], ACT.Ln, bias=c.const("eps"), scale=1.0 / D
                                 ).then_inc(rs_ready, 1)
            act.wait_ge(rs_ready, 1)
            nc.scalar.activation(rs, rs, ACT.Exp, scale=-0.5).then_inc(rs_ready, 1)
            for t in range(KT):
                if shift is not None:
                    act.wait_ge(scaled, t + 1)
                    out = h if split is None else split[0]
                    nc.scalar.activation(out[:, t, :], h[:, t, :], ACT.Identity, bias=shift[:, t:t + 1]
                                         ).then_inc(done, 1)
            if extra_act is not None:
                extra_act(act)

        @block.vector
        def _(dve):
            if scale is not None:
                nc.vector.tensor_scalar(a, scale, 1.0, None, ALU.add).then_inc(a_ready, 1)
                dve.wait_ge(a_ready, 1)
                nc.vector.tensor_tensor(a, a, gain, ALU.mult).then_inc(a_ready, 1)
                dve.wait_ge(a_ready, 2)
            g = a if scale is not None else gain

            def low(t):
                hi, lo = split
                dve.wait_ge(done, t + 1)
                nc.vector.scalar_tensor_tensor(lo[:, t, :], h[:, t, :], shift[:, t:t + 1], hi[:, t, :].bitcast(F32),
                                               ALU.add, ALU.subtract)

            dve.wait_ge(rs_ready, 2)
            for t in range(KT):
                nc.vector.scalar_tensor_tensor(h[:, t, :], x[:, t, :], g[:, t:t + 1], rs, ALU.mult, ALU.mult
                                               ).then_inc(scaled, 1)
                if split is not None and t >= 2:
                    low(t - 2)
            if split is not None:
                low(KT - 2)
                low(KT - 1)


class Linear:

    def __init__(self, c, name, n_tiles, weights, k_tiles=KT, size=D):
        self.c, self.n, self.weights, self.kt, self.size = c, n_tiles, weights, k_tiles, size
        assert n_tiles % RING == 0
        self.loaded = [c.sem(f"{name}_w_loaded{s}") for s in range(RING)]
        self.multiplied = c.sem(f"{name}_multiplied")
        self.emptied = c.sem(f"{name}_bank_emptied")

    def prefetch(self, sp):
        for s in range(RING):
            sp.dma_start(self.c.slot(s, self.size), self.weights(s)).then_inc(self.loaded[s], 16)

    def load(self, sp):
        with sp.Fori(1, self.n // RING) as g:
            for s in range(RING):
                sp.wait_ge(self.multiplied, (g - 1) * RING + s + 1)
                sp.dma_start(self.c.slot(s, self.size), self.weights(g * RING + s)).then_inc(self.loaded[s], 16)

    def multiply(self, pe, rhs):
        nc, c = self.c.nc, self.c

        def tile(s, g):
            pe.wait_ge(self.loaded[s], 16 * (g + 1))
            w = c.slot(s, self.size)
            for kt in range(self.kt):
                last = nc.tensor.matmul(c.ps[:, s, :], w[:, kt * P:(kt + 1) * P], rhs(kt), start=(kt == 0),
                                        stop=(kt == self.kt - 1))
            last.then_inc(self.multiplied, 1)

        for s in range(RING):
            tile(s, 0)
        with pe.Fori(1, self.n // RING) as g:
            for s in range(RING):
                pe.wait_ge(self.emptied, (g - 1) * RING + s + 1)
                tile(s, g)


class SplitLinear(Linear):

    def __init__(self, c, name, n_tiles, weights):
        super().__init__(c, name, n_tiles, weights)
        self.high, self.low = c.sem(f"{name}_w_high"), c.sem(f"{name}_w_low")

    def load(self, sp):
        with sp.Fori(1, self.n // RING) as g:
            for s in range(RING):
                sp.wait_ge(self.low, (g - 1) * RING + s + 1)
                sp.dma_start(self.c.slot(s), self.weights(g * RING + s)).then_inc(self.loaded[s], 16)

    def split_high(self, act, s, g, first=False):
        act.wait_ge(self.loaded[s], 16 * (g + 1))
        if not first:
            act.wait_ge(self.multiplied, g * RING + s - 1)
        self.c.nc.scalar.activation(self.c.w_hi[:, s % 2, :], self.c.slot(s), ACT.Copy).then_inc(self.high, 1)

    def split_low(self, dve, s, g, first=False):
        dve.wait_ge(self.high, g * RING + s + 1)
        self.c.nc.vector.tensor_tensor(self.c.w_lo[:, s % 2, :], self.c.slot(s), self.c.w_hi[:, s % 2, :].bitcast(F32),
                                       ALU.subtract).then_inc(self.low, 1)

    def tiles(self, eng, split, work, first=None):
        rounds = self.n // RING

        def one(s, g, work, last=False):
            if not (last and s + 2 >= RING):
                split(eng, (s + 2) % RING, g + (s + 2) // RING)
            work(s, g)

        for s in range(RING):
            one(s, 0, first or work)
        if rounds > 2:
            with eng.Fori(1, rounds - 1) as g:
                for s in range(RING):
                    one(s, g, work)
        for s in range(RING):
            one(s, rounds - 1, work, last=True)

    def products(self, s, bank, rhs, last=True):
        c, nc = self.c, self.c.nc
        hi, lo = rhs
        for kt in range(KT):
            at = slice(kt * P, (kt + 1) * P)
            nc.tensor.matmul(bank, c.w_hi[:, s % 2, at], hi(kt), start=(kt == 0), stop=False)
            nc.tensor.matmul(bank, c.w_hi[:, s % 2, at], lo(kt), start=False, stop=False)
            ins = nc.tensor.matmul(bank, c.w_lo[:, s % 2, at], hi(kt), start=False, stop=(kt == KT - 1))
        return ins

    def multiply(self, pe, rhs, ready=None):
        c = self.c

        def tile(s, g):
            pe.wait_ge(self.low, g * RING + s + 1)
            self.products(s, c.ps[:, s, :], rhs).then_inc(self.multiplied, 1)

        for s in range(RING):
            tile(s, 0)
        with pe.Fori(1, self.n // RING) as g:
            for s in range(RING):
                pe.wait_ge(self.emptied, (g - 1) * RING + s + 1)
                tile(s, g)


def split_stage(c, lin, lo, out, prefetch=None, x=None):
    nc = c.nc
    engine, work = out
    if x is not None:
        x_high, x_low = c.sem("x_high"), c.sem("x_low")
    nothing = lambda s, g: None
    with nc.Block() as block:
        @block.sync
        def _(sp):
            lin.load(sp)
            if prefetch is not None:
                sp.wait_ge(lin.multiplied, lin.n)
                prefetch(sp)

        @block.tensor
        def _(pe):
            if x is not None:
                pe.wait_ge(x_low, KT)
            lin.multiply(pe, (lambda kt: c.a_hi[:, kt, :], lambda kt: lo[:, kt, :]))

        @block.scalar
        def _(act):
            lin.split_high(act, 0, 0, first=True)
            if x is not None:
                for t in range(KT):
                    nc.scalar.activation(c.a_hi[:, t, :], x[:, t, :], ACT.Copy).then_inc(x_high, 1)
            lin.split_high(act, 1, 0, first=True)
            lin.tiles(act, lin.split_high, work(act) if engine == "scalar" else nothing)

        @block.vector
        def _(dve):
            lin.split_low(dve, 0, 0)
            if x is not None:
                for t in range(KT):
                    dve.wait_ge(x_high, t + 1)
                    nc.vector.tensor_tensor(lo[:, t, :], x[:, t, :], c.a_hi[:, t, :].bitcast(F32), ALU.subtract
                                            ).then_inc(x_low, 1)
            lin.split_low(dve, 1, 0)
            lin.tiles(dve, lin.split_low, work(dve) if engine == "vector" else nothing)


def copy_out(c, lin, dst):
    def of(act):
        def work(s, g):
            act.wait_ge(lin.multiplied, g * RING + s + 1)
            out = dst(g * RING + s)
            c.nc.scalar.activation(out, c.ps[:, s, :], ACT.Copy).then_inc(lin.emptied, 1)
        return work
    return "scalar", of


def add_residual(c, lin, gate):
    return "vector", lambda dve: lambda s, g: residual_tiles(c, lin, dve, gate, g * RING + s, g * RING + s + 1)


def copy_out_tiles(c, lin, act, dst):
    nc = c.nc
    with act.Fori(0, lin.n // RING) as g:
        for s in range(RING):
            act.wait_ge(lin.multiplied, g * RING + s + 1)
            out = dst[:, bass.ds(g * RING + s, 1), :].rearrange("p a n -> p (a n)")
            nc.scalar.activation(out, c.ps[:, s, :], ACT.Copy).then_inc(lin.emptied, 1)


def residual_tiles(c, lin, dve, gate, first=0, last=KT):
    nc = c.nc
    for t in range(first, last):
        dve.wait_ge(lin.multiplied, t + 1)
        nc.vector.scalar_tensor_tensor(c.x[:, t, :], c.ps[:, t % RING, :], gate[:, t:t + 1], c.x[:, t, :], ALU.mult,
                                       ALU.add).then_inc(lin.emptied, 1)


def after(steps, n):
    return sum(s <= n for s in steps)


T_A, T_B, T_C, T_D = 0, 7, 13, 17
V_B, V_D, V_C = 0, 256, 512
Y_A, Y_B, Y_C, Y_D = 0, 2, 4, 6


def scratch(c, i, n=1):
    at = RING * D + i * S
    return c.ring[:, at:at + n * S]


def prepare_attentions(c, name, prefetch):
    nc = c.nc
    blocks, blocks_out = c.sem(f"{name}_v_transposed"), c.sem(f"{name}_v_copied")
    squared, summed = c.sem(f"{name}_squared"), c.sem(f"{name}_summed")
    rs_step, rs_ready, normed = c.sem(f"{name}_rs_step"), c.sem(f"{name}_rs_ready"), c.sem(f"{name}_normed")
    gains = c.sem(f"{name}_gains")
    rotated, roped = c.sem(f"{name}_rotated"), c.sem(f"{name}_roped")
    f_in, f_exp, f_dve, f_ready, f_moved = (c.sem(f"{name}_f_{n}") for n in ("in", "exp", "dve", "ready", "moved"))
    f_one = c.sem(f"{name}_f_one")

    qb, qd = c.small[:, 24:25], c.small[:, 25:26]
    jobs = [(T_B + 0, "bo32", 32, qb), (T_B + 1, "bo32", 32, qb), (T_B + 2, "bo32", 32, c.col("df_k_g")),
            (T_B + 3, "bo32", 32, c.col("df_k_g")), (T_D + 0, "bo64", 64, qd), (T_D + 1, "bo64", 64, qd),
            (T_D + 2, "bo64", 64, c.col("fx_k_g")), (T_D + 3, "bo64", 64, c.col("fx_k_g"))]
    values = [(T_B + 4, V_B), (T_B + 5, V_B + P), (T_D + 4, V_D), (T_D + 5, V_D + P)]
    sq = [scratch(c, i) for i in range(2)]
    rs = [scratch(c, 2 + i) for i in range(2)]
    turn = scratch(c, 4)
    f_gate, f_abs = scratch(c, 5)[0:4, :], scratch(c, 6)[0:4, :]
    f_neg = scratch(c, 7)[0:4, :]

    with nc.Block() as block:
        @block.sync
        def _(sp):
            prefetch(sp)
            sp.wait_ge(f_ready, 2)
            sp.wait_ge(f_one, 2)
            for h in range(4):
                sp.dma_start(c.h[1:2, h, :], f_gate[h:h + 1, :]).then_inc(f_moved, 16)
                sp.dma_start(c.h[0:1, 4 + h, :], f_neg[h:h + 1, :]).then_inc(f_moved, 16)
            sp.wait_ge(f_moved, 16 * 8)

        @block.gpsimd
        def _(pool):
            nc.gpsimd.memset(c.h[0:2, 0:4, :], 1.0).then_inc(f_one, 1)
            nc.gpsimd.memset(c.h[0:2, 4:8, :], 1.0).then_inc(f_one, 1)

        @block.tensor
        def _(pe):
            for j, (tile, _) in enumerate(values):
                for b in range(4):
                    last = nc.tensor.transpose(c.ps[:, 4 + j, b * P:(b + 1) * P], c.p[:, tile, b * P:(b + 1) * P],
                                               c.const("ident"))
                last.then_inc(blocks, 1)
            for j, (_, ones, _, _) in enumerate(jobs):
                pe.wait_ge(squared, j + 1)
                if j >= 2:
                    pe.wait_ge(rs_step, j - 1)
                nc.tensor.matmul(c.ps[:, j % 2, :], c.const(ones), sq[j % 2], start=True, stop=True
                                 ).then_inc(summed, 1)
            for j in range(4):
                pe.wait_ge(normed, j + 1)
                if j >= 2:
                    pe.wait_ge(roped, 3 * (j - 2) + 1)
                nc.tensor.matmul(c.ps[:, 2 + j % 2, :], c.const("perm"), c.p[:, T_B + j, :], start=True, stop=True
                                 ).then_inc(rotated, 1)

        @block.scalar
        def _(act):
            nc.scalar.activation(f_gate, c.p[0:4, IN_T - 1, :], ACT.Identity, bias=c.col("fx_f_b")[0:4, :]
                                 ).then_inc(f_in, 1)
            act.wait_ge(f_in, 1)
            nc.scalar.activation(f_abs, f_gate, ACT.Abs).then_inc(f_in, 1)
            act.wait_ge(f_in, 2)
            nc.scalar.activation(f_abs, f_abs, ACT.Exp, scale=-1.0).then_inc(f_in, 1)
            act.wait_ge(f_in, 3)
            nc.scalar.activation(f_abs, f_abs, ACT.Ln, bias=1.0).then_inc(f_exp, 1)
            for j, (_, off) in enumerate(values):
                act.wait_ge(blocks, j + 1)
                nc.scalar.activation(c.vt[:, :, off:off + P], c.ps[:, 4 + j, :].rearrange("p (b n) -> p b n", b=4),
                                     ACT.Copy).then_inc(blocks_out, 1)

            def square(j):
                if j >= 2:
                    act.wait_ge(summed, j - 1)
                nc.scalar.activation(sq[j % 2], c.p[:, jobs[j][0], :], ACT.Square).then_inc(squared, 1)

            square(0)
            for j, (_, _, n, _) in enumerate(jobs):
                if j + 1 < len(jobs):
                    square(j + 1)
                act.wait_ge(summed, j + 1)
                if j >= 2:
                    act.wait_ge(normed, j - 1)
                nc.scalar.activation(rs[j % 2], c.ps[:, j % 2, :], ACT.Ln, bias=c.const("eps"), scale=1.0 / n
                                     ).then_inc(rs_step, 1)
                act.wait_ge(rs_step, j + 1)
                nc.scalar.activation(rs[j % 2], rs[j % 2], ACT.Exp, scale=-0.5).then_inc(rs_ready, 1)
            act.wait_ge(blocks_out, 4)

        @block.vector
        def _(dve):
            nc.vector.tensor_scalar(qb, c.col("df_q_g"), 32 ** -0.5, None, ALU.mult).then_inc(gains, 1)
            nc.vector.tensor_scalar(qd, c.col("fx_q_g"), 64 ** -0.5, None, ALU.mult).then_inc(gains, 1)
            dve.wait_ge(f_exp, 1)
            nc.vector.scalar_tensor_tensor(f_gate, f_gate, 0.0, f_abs, ALU.min, ALU.subtract).then_inc(f_dve, 1)
            dve.wait_ge(f_dve, 1)
            nc.vector.tensor_tensor_scan(f_abs, c.const("ones", 1)[0:4, :].to_broadcast([4, S]), f_gate, 0.0, ALU.mult,
                                         ALU.add).then_inc(f_dve, 1)
            dve.wait_ge(f_dve, 2)
            nc.vector.tensor_copy(f_gate, f_abs).then_inc(f_ready, 1)
            nc.vector.tensor_scalar(f_neg, f_abs, -1.0, None, ALU.mult).then_inc(f_ready, 1)
            dve.wait_ge(gains, 2)
            for j, (tile, _, _, gain) in enumerate(jobs):
                dve.wait_ge(rs_ready, j + 1)
                nc.vector.scalar_tensor_tensor(c.p[:, tile, :], c.p[:, tile, :], gain, rs[j % 2], ALU.mult, ALU.mult
                                               ).then_inc(normed, 1)
            for j in range(4):
                q = c.p[:, T_B + j, :]
                dve.wait_ge(rotated, j + 1)
                if j >= 1:
                    dve.wait_ge(roped, 3 * j)
                nc.vector.tensor_tensor(turn, c.ps[:, 2 + j % 2, :], c.const("sin"), ALU.mult).then_inc(roped, 1)
                nc.vector.tensor_tensor(q, q, c.const("cos"), ALU.mult).then_inc(roped, 1)
                dve.wait_ge(roped, 3 * j + 2)
                nc.vector.tensor_tensor(q, q, turn, ALU.add).then_inc(roped, 1)
            dve.wait_ge(roped, 12)


def attention_forget(c, name):
    nc = c.nc
    scored, masked, maxed = c.sem(f"{name}_scored"), c.sem(f"{name}_masked"), c.sem(f"{name}_maxed")
    exped, inv, scaled = c.sem(f"{name}_exped"), c.sem(f"{name}_inv"), c.sem(f"{name}_scaled")
    turned, copied, summed = c.sem(f"{name}_turned"), c.sem(f"{name}_copied"), c.sem(f"{name}_summed")
    out = c.sem(f"{name}_out")
    units = [(h, i) for h in range(4) for i in range(4)]
    NU = len(units)
    prob = [scratch(c, i) for i in range(3)]
    prob_t = [scratch(c, 3 + i) for i in range(2)]
    nmax, rsum = c.small[:, 32:48], c.small[:, 48:64]

    def rows(h):
        return slice(64 * (h % 2), 64 * (h % 2) + 64)

    with nc.Block() as block:
        @block.tensor
        def _(pe):
            def score(u):
                h, i = units[u]
                nk = (i + 1) * P
                if u >= 2:
                    pe.wait_ge(exped, u - 1)
                bank = c.ps[:, u % 2, 0:nk]
                nc.tensor.matmul(bank, c.p[rows(h), T_D + h // 2, i * P:(i + 1) * P],
                                 c.p[rows(h), T_D + 2 + h // 2, 0:nk], start=True, stop=False)
                nc.tensor.matmul(bank, c.h[0:2, h, i * P:(i + 1) * P], c.h[0:2, 4 + h, 0:nk], start=False, stop=True
                                 ).then_inc(scored, 1)

            def turn(u):
                _, i = units[u]
                pe.wait_ge(scaled, u + 1)
                if u >= 2:
                    pe.wait_ge(copied, u - 1)
                for b in range(i + 1):
                    last = nc.tensor.transpose(c.ps[:, 2 + u % 2, b * P:(b + 1) * P],
                                               prob[u % 3][:, b * P:(b + 1) * P], c.const("ident"))
                last.then_inc(turned, 1)

            def sum_values(u):
                h, i = units[u]
                pe.wait_ge(copied, u + 1)
                for b in range(i + 1):
                    v = c.vt[:, b, V_D + 64 * h:V_D + 64 * h + 64]
                    last = nc.tensor.matmul(c.ps[rows(h), 4 + h // 2, i * P:(i + 1) * P], v,
                                            prob_t[u % 2][:, b * P:(b + 1) * P], start=(b == 0), stop=(b == i))
                last.then_inc(summed, 1)

            score(0)
            score(1)
            for u in range(NU):
                turn(u)
                if u + 2 < NU:
                    score(u + 2)
                if u >= 1:
                    sum_values(u - 1)
            sum_values(NU - 1)

        @block.scalar
        def _(act):
            def exp(u):
                nk = (units[u][1] + 1) * P
                act.wait_ge(maxed, u + 1)
                if u >= 3:
                    act.wait_ge(turned, u - 2)
                nc.scalar.activation(prob[u % 3][:, 0:nk], c.ps[:, u % 2, 0:nk], ACT.Exp, bias=nmax[:, u:u + 1],
                                     accum_out=rsum[:, u:u + 1]).then_inc(exped, 1)

            def copy(u):
                nk = (units[u][1] + 1) * P
                act.wait_ge(turned, u + 1)
                if u >= 2:
                    act.wait_ge(summed, u - 1)
                nc.scalar.activation(prob_t[u % 2][:, 0:nk], c.ps[:, 2 + u % 2, 0:nk], ACT.Copy).then_inc(copied, 1)

            exp(0)
            for u in range(NU):
                if u + 1 < NU:
                    exp(u + 1)
                copy(u)
            for t in range(2):
                act.wait_ge(summed, 8 * (t + 1))
                nc.scalar.activation(c.y[:, Y_D + t, :], c.ps[:, 4 + t, :], ACT.Copy).then_inc(out, 1)

        @block.vector
        def _(dve):
            def maximum(u):
                i = units[u][1]
                dve.wait_ge(scored, u + 1)
                diagonal = c.ps[:, u % 2, i * P:(i + 1) * P]
                nc.vector.tensor_tensor(diagonal, diagonal, c.const("mask_causal"), ALU.add).then_inc(masked, 1)
                dve.wait_ge(masked, u + 1)
                nc.vector.tensor_reduce(nmax[:, u:u + 1], c.ps[:, u % 2, 0:(i + 1) * P], AXX, ALU.max, negate=True
                                        ).then_inc(maxed, 1)

            def normalise(u):
                nk = (units[u][1] + 1) * P
                dve.wait_ge(exped, u + 1)
                nc.vector.reciprocal(rsum[:, u:u + 1], rsum[:, u:u + 1]).then_inc(inv, 1)
                dve.wait_ge(inv, u + 1)
                nc.vector.tensor_scalar(prob[u % 3][:, 0:nk], prob[u % 3][:, 0:nk], rsum[:, u:u + 1], None, ALU.mult
                                        ).then_inc(scaled, 1)

            maximum(0)
            for u in range(NU):
                if u + 1 < NU:
                    maximum(u + 1)
                normalise(u)


def attention_diff(c, name):
    nc = c.nc
    lam_dve, lam_exp, lam_ready = c.sem(f"{name}_lam_dve"), c.sem(f"{name}_lam_exp"), c.sem(f"{name}_lam_ready")
    scored, masked, maxed = c.sem(f"{name}_scored"), c.sem(f"{name}_masked"), c.sem(f"{name}_maxed")
    exped, inv, mixed = c.sem(f"{name}_exped"), c.sem(f"{name}_inv"), c.sem(f"{name}_mixed")
    turned, copied, summed = c.sem(f"{name}_turned"), c.sem(f"{name}_copied"), c.sem(f"{name}_summed")
    squared, ms, rs_ready, out = (c.sem(f"{name}_{n}") for n in ("squared", "ms", "rs_ready", "out"))
    units = [(h, i) for h in range(4) for i in range(4)]
    NU = len(units)
    prob = [[scratch(c, 2 * i + m) for m in range(2)] for i in range(2)]
    prob_t = [scratch(c, 4 + i) for i in range(2)]
    o, sq, rs = [scratch(c, 6), scratch(c, 7)], [scratch(c, 8), scratch(c, 9)], [scratch(c, 0), scratch(c, 1)]
    nmax, rsum = c.small[:, 32:64], c.small[:, 64:96]
    lam_prod = c.cols[:, C_AT["lam_vec"]:C_AT["lam_vec"] + 64].rearrange("p (m n) -> p m n", m=2)
    lam_other = c.cols[:, C_AT["lam_vec"] + 64:C_AT["lam_vec"] + 128].rearrange("p (m n) -> p m n", m=2)
    lam2, nlam, sub_gain = c.small[:, 26:28], c.small[:, 28:29], c.small[:, 29:30]

    with nc.Block() as block:
        @block.tensor
        def _(pe):
            def score(u):
                h, i = units[u]
                nk = (i + 1) * P
                for m in range(2):
                    lane = 32 * ((2 * h + m) % 4)
                    if u >= 2:
                        pe.wait_ge(exped, 2 * (u - 2) + m + 1)
                    nc.tensor.matmul(c.ps[:, 2 * (u % 2) + m, 0:nk], c.p[lane:lane + 32, T_B + h // 2, i * P:(i + 1) * P],
                                     c.p[lane:lane + 32, T_B + 2 + h // 2, 0:nk], start=True, stop=True,
                                     tile_position=(lane, 0)).then_inc(scored, 1)

            def turn(u):
                _, i = units[u]
                pe.wait_ge(mixed, u + 1)
                if u >= 2:
                    pe.wait_ge(copied, u - 1)
                for b in range(i + 1):
                    last = nc.tensor.transpose(c.ps[:, 4 + u % 2, b * P:(b + 1) * P],
                                               prob[u % 2][0][:, b * P:(b + 1) * P], c.const("ident"))
                last.then_inc(turned, 1)

            def sum_values(u):
                h, i = units[u]
                r = slice(64 * (h % 2), 64 * (h % 2) + 64)
                pe.wait_ge(copied, u + 1)
                for b in range(i + 1):
                    v = c.vt[:, b, V_B + 64 * h:V_B + 64 * h + 64]
                    last = nc.tensor.matmul(c.ps[r, 6 + h // 2, i * P:(i + 1) * P], v,
                                            prob_t[u % 2][:, b * P:(b + 1) * P], start=(b == 0), stop=(b == i))
                last.then_inc(summed, 1)

            score(0)
            score(1)
            for u in range(NU):
                turn(u)
                if u + 2 < NU:
                    score(u + 2)
                if u >= 1:
                    sum_values(u - 1)
            sum_values(NU - 1)
            for t in range(2):
                pe.wait_ge(squared, 2 * t + 2)
                nc.tensor.matmul(c.ps[:, t, :], c.const("bo64"), sq[t], start=True, stop=True).then_inc(ms, 1)

        @block.scalar
        def _(act):
            def exp(u):
                nk = (units[u][1] + 1) * P
                for m in range(2):
                    n = 2 * u + m
                    act.wait_ge(maxed, n + 1)
                    if u >= 2:
                        act.wait_ge(turned, u - 1)
                    nc.scalar.activation(prob[u % 2][m][:, 0:nk], c.ps[:, 2 * (u % 2) + m, 0:nk], ACT.Exp,
                                         bias=nmax[:, n:n + 1], accum_out=rsum[:, n:n + 1]).then_inc(exped, 1)

            def copy(u):
                nk = (units[u][1] + 1) * P
                act.wait_ge(turned, u + 1)
                if u >= 2:
                    act.wait_ge(summed, u - 1)
                nc.scalar.activation(prob_t[u % 2][:, 0:nk], c.ps[:, 4 + u % 2, 0:nk], ACT.Copy).then_inc(copied, 1)

            act.wait_ge(lam_dve, 2)
            nc.scalar.activation(lam2, lam2, ACT.Exp).then_inc(lam_exp, 1)
            exp(0)
            for u in range(NU):
                if u + 1 < NU:
                    exp(u + 1)
                copy(u)
            for t in range(2):
                act.wait_ge(summed, 8 * (t + 1))
                nc.scalar.activation(o[t], c.ps[:, 6 + t, :], ACT.Copy).then_inc(squared, 1)
                nc.scalar.activation(sq[t], c.ps[:, 6 + t, :], ACT.Square).then_inc(squared, 1)
            for t in range(2):
                act.wait_ge(ms, t + 1)
                nc.scalar.activation(rs[t], c.ps[:, t, :], ACT.Ln, bias=c.const("eps"), scale=1.0 / 64
                                     ).then_inc(rs_ready, 1)
                act.wait_ge(rs_ready, 2 * t + 1)
                nc.scalar.activation(rs[t], rs[t], ACT.Exp, scale=-0.5).then_inc(rs_ready, 1)

        @block.vector
        def _(dve):
            nc.vector.tensor_tensor(lam_prod, lam_prod, lam_other, ALU.mult).then_inc(lam_dve, 1)
            dve.wait_ge(lam_dve, 1)
            nc.vector.tensor_reduce(lam2, lam_prod, AXX, ALU.add).then_inc(lam_dve, 1)
            dve.wait_ge(lam_exp, 1)
            nc.vector.tensor_tensor(nlam, lam2[:, 1:2], lam2[:, 0:1], ALU.subtract).then_inc(lam_ready, 1)
            dve.wait_ge(lam_ready, 1)
            nc.vector.tensor_tensor(nlam, nlam, c.col("lam_init"), ALU.subtract).then_inc(lam_ready, 1)
            nc.vector.tensor_scalar(sub_gain, c.col("lam_init"), -1.0, 1.0, ALU.mult, ALU.add).then_inc(lam_ready, 1)
            dve.wait_ge(lam_ready, 3)
            nc.vector.tensor_tensor(sub_gain, sub_gain, c.col("df_sub_g"), ALU.mult).then_inc(lam_ready, 1)
            dve.wait_ge(lam_ready, 4)

            def maximum(u):
                i = units[u][1]
                for m in range(2):
                    n = 2 * u + m
                    bank = 2 * (u % 2) + m
                    dve.wait_ge(scored, n + 1)
                    diagonal = c.ps[:, bank, i * P:(i + 1) * P]
                    nc.vector.tensor_tensor(diagonal, diagonal, c.const("mask_chunk"), ALU.add).then_inc(masked, 1)
                    dve.wait_ge(masked, n + 1)
                    nc.vector.tensor_reduce(nmax[:, n:n + 1], c.ps[:, bank, 0:(i + 1) * P], AXX, ALU.max, negate=True
                                            ).then_inc(maxed, 1)

            def mix(u):
                nk = (units[u][1] + 1) * P
                dve.wait_ge(exped, 2 * u + 2)
                r = rsum[:, 2 * u:2 * u + 2]
                nc.vector.reciprocal(r, r).then_inc(inv, 1)
                dve.wait_ge(inv, 3 * u + 1)
                nc.vector.tensor_tensor(r[:, 1:2], r[:, 1:2], nlam, ALU.mult).then_inc(inv, 1)
                dve.wait_ge(inv, 3 * u + 2)
                p1, p2 = prob[u % 2][0][:, 0:nk], prob[u % 2][1][:, 0:nk]
                nc.vector.tensor_scalar(p2, p2, r[:, 1:2], None, ALU.mult).then_inc(inv, 1)
                dve.wait_ge(inv, 3 * u + 3)
                nc.vector.scalar_tensor_tensor(p1, p1, r[:, 0:1], p2, ALU.mult, ALU.add).then_inc(mixed, 1)

            maximum(0)
            for u in range(NU):
                if u + 1 < NU:
                    maximum(u + 1)
                mix(u)
            for t in range(2):
                dve.wait_ge(rs_ready, 2 * t + 2)
                nc.vector.scalar_tensor_tensor(c.y[:, Y_B + t, :], o[t], sub_gain, rs[t], ALU.mult, ALU.mult
                                               ).then_inc(out, 1)
            dve.wait_ge(out, 2)


def spatial_gating(c, name):
    nc = c.nc
    gelu, loaded, mean_of, centred = (c.sem(f"{name}_{n}") for n in ("gelu", "w_loaded", "mean", "centred"))
    squared, var, rs_ready, normed = (c.sem(f"{name}_{n}") for n in ("squared", "var", "rs_ready", "normed"))
    turned, copied, mixed, out = (c.sem(f"{name}_{n}") for n in ("turned", "copied", "mixed", "out"))
    sq, rs = [scratch(c, 0), scratch(c, 1)], scratch(c, 2)
    w = scratch(c, 3)
    bias, pick = c.h[0:4, 0, 0:P], c.h[0:4, 1, 0:2 * P]
    masked = c.sem(f"{name}_w_masked")
    u, v = [c.p[:, T_C + t, :] for t in range(2)], [c.p[:, T_C + 2 + t, :] for t in range(2)]
    layer = c.layer
    with nc.Block() as block:
        @block.sync
        def _(sp):
            sp.dma_start(w, c.dram["sg_wT"][bass.ds(layer, 1), :, :].rearrange("a p n -> p (a n)")).then_inc(loaded, 16)
            sp.dma_start(bias, c.dram["sg_b"][bass.ds(layer, 1), :, :].rearrange("a p n -> p (a n)")
                         ).then_inc(loaded, 16)
            sp.dma_start(pick, c.dram["sg_pick"]).then_inc(loaded, 16)
            sp.wait_ge(loaded, 48)

        @block.gpsimd
        def _(pool):
            pool.wait_ge(loaded, 48)
            w3 = w.rearrange("p (g i) -> p g i", g=4)
            nc.gpsimd.affine_select(out=w3, in_=w3, compare_op=ALU.is_ge, fill=0.0, base=0, pattern=[[0, 4], [1, P]],
                                    channel_multiplier=-1).then_inc(masked, 1)

        @block.tensor
        def _(pe):
            for t in range(2):
                pe.wait_ge(gelu, 3 + t)
                last = nc.tensor.matmul(c.ps[:, 0, :], c.const("ones"), v[t], start=(t == 0), stop=(t == 1))
            last.then_inc(mean_of, 1)
            for t in range(2):
                pe.wait_ge(squared, t + 1)
                last = nc.tensor.matmul(c.ps[:, 1, :], c.const("ones"), sq[t], start=(t == 0), stop=(t == 1))
            last.then_inc(var, 1)
            for t in range(2):
                pe.wait_ge(normed, 2 * t + 2)
                for b in range(4):
                    last = nc.tensor.transpose(c.ps[:, 2 + t, b * P:(b + 1) * P], v[t][:, b * P:(b + 1) * P],
                                               c.const("ident"))
                last.then_inc(turned, 1)
            pe.wait_ge(copied, 2)
            pe.wait_ge(masked, 1)
            for t in range(2):
                for n in range(4):
                    nc.tensor.matmul(c.ps[:, 4 + t, n * P:(n + 1) * P], pick[:, t * P:(t + 1) * P], bias,
                                     start=(n == 0), stop=False, skip_group_check=True)
                for g in (2 * t, 2 * t + 1):
                    r = slice(64 * (g % 2), 64 * (g % 2) + 64)
                    for n in range(4):
                        last = nc.tensor.matmul(c.ps[r, 4 + t, n * P:(n + 1) * P],
                                                c.vt[:, n, V_C + 64 * g:V_C + 64 * g + 64], w[:, g * P:(g + 1) * P],
                                                start=False, stop=(n == 3), skip_group_check=True)
                last.then_inc(mixed, 1)

        @block.scalar
        def _(act):
            for tile in (*u, *v):
                nc.scalar.activation(tile, tile, ACT.Gelu).then_inc(gelu, 1)
            for t in range(2):
                act.wait_ge(centred, t + 1)
                nc.scalar.activation(sq[t], v[t], ACT.Square).then_inc(squared, 1)
            act.wait_ge(var, 1)
            nc.scalar.activation(rs, c.ps[:, 1, :], ACT.Ln, bias=c.const("eps"), scale=1.0 / 256).then_inc(rs_ready, 1)
            act.wait_ge(rs_ready, 1)
            nc.scalar.activation(rs, rs, ACT.Exp, scale=-0.5).then_inc(rs_ready, 1)
            for t in range(2):
                act.wait_ge(turned, t + 1)
                nc.scalar.activation(c.vt[:, :, V_C + t * P:V_C + (t + 1) * P],
                                     c.ps[:, 2 + t, :].rearrange("p (b n) -> p b n", b=4), ACT.Copy
                                     ).then_inc(copied, 1)

        @block.vector
        def _(dve):
            dve.wait_ge(mean_of, 1)
            for t in range(2):
                nc.vector.scalar_tensor_tensor(v[t], c.ps[:, 0, :], -1.0 / 256, v[t], ALU.mult, ALU.add
                                               ).then_inc(centred, 1)
            dve.wait_ge(rs_ready, 2)
            dve.wait_ge(centred, 2)
            dve.wait_ge(squared, 2)
            for t in range(2):
                nc.vector.scalar_tensor_tensor(v[t], v[t], c.col("sg_ln_g", t), rs, ALU.mult, ALU.mult
                                               ).then_inc(normed, 1)
                dve.wait_ge(normed, 2 * t + 1)
                nc.vector.tensor_scalar(v[t], v[t], c.col("sg_ln_b", t), None, ALU.add).then_inc(normed, 1)
            for t in range(2):
                dve.wait_ge(mixed, t + 1)
                nc.vector.tensor_tensor(c.y[:, Y_C + t, :], c.ps[:, 4 + t, :], u[t], ALU.mult).then_inc(out, 1)
            dve.wait_ge(out, 2)


class Rwkv:

    def __init__(self, c):
        self.c, self.used = c, 0
        self.keep = [dict(ax=self.tiles(2), xT=self.tiles(2), kaT=self.tiles(2), rT=self.tiles(2), b_tok=self.tiles(2),
                          k_tok=self.tiles(2), v_tok=self.tiles(1), r=self.tiles(1), gate=self.tiles(1),
                          bonus=self.tiles(1)) for _ in range(2)]
        self.bx, self.kx = self.tiles(2), self.tiles(2)
        at = self.used
        self.temp = [self.tiles(1) for _ in range(9)]
        self.used = at
        self.group = [[self.tiles(1) for _ in range(5)] for _ in range(2)]
        self.lora = self.c.y[:, 0, :]
        self.pt = [self.c.y[:, 1, :], self.c.p[:, IN_T - 1, :]]
        self.last_decay = c.small[:, 96:112]

    def tiles(self, n):
        c, i = self.c, self.used
        if n == 2 and i % 2:
            i += 1
        self.used = i + n
        if i < 8:
            return c.h[:, i:i + n, :].rearrange("p a n -> p (a n)")
        if i < 24:
            return c.p[:, T_B + i - 8:T_B + i - 8 + n, :].rearrange("p a n -> p (a n)")
        if i < 38:
            return scratch(c, i - 24, n)
        flat = c.vt[:, :, :].rearrange("p b n -> p (b n)")
        assert i + n <= 46
        return flat[:, (i - 38) * S:(i - 38 + n) * S]


def by_chunk(ap, width):
    return ap.rearrange("p (c n) -> p c n", n=width)


def rwkv_shift(c, name, w):
    nc = c.nc
    done, act_done = c.sem(f"{name}_dve"), c.sem(f"{name}_act")
    diff = [w.temp[0], w.temp[1]]
    lora = w.lora
    with nc.Block() as block:
        @block.vector
        def _(dve):
            for j in range(7):
                x, d = c.p[:, T_A + j, :], diff[j % 2]
                if j >= 2:
                    dve.wait_ge(done, 3 * (j - 1))
                nc.vector.tensor_tensor(d[:, 1:S], x[:, 0:S - 1], x[:, 1:S], ALU.subtract).then_inc(done, 1)
                nc.vector.tensor_scalar(d[:, 0:1], x[:, 0:1], -1.0, None, ALU.mult).then_inc(done, 1)
                dve.wait_ge(done, 3 * j + 2)
                nc.vector.scalar_tensor_tensor(x, d, c.col("rw_mu", j), x, ALU.mult, ALU.add).then_inc(done, 1)
            dve.wait_ge(done, 21)

        @block.scalar
        def _(act):
            act.wait_ge(done, 21)
            m = c.p[:, T_A + 6, :]
            nc.scalar.activation(lora[0:32, :], m[0:32, :], ACT.Tanh).then_inc(act_done, 1)
            nc.scalar.activation(lora[32:64, :], m[32:64, :], ACT.Copy).then_inc(act_done, 1)
            nc.scalar.activation(lora[64:128, :], m[64:128, :], ACT.Sigmoid).then_inc(act_done, 1)
            act.wait_ge(act_done, 3)


def rwkv_prepare(c, name, w, pair):
    nc = c.nc
    keep = w.keep[pair]
    r, k, v = (c.p[:, T_A + 2 * i + pair, :] for i in range(3))
    logw, a, cum, cum_ex, e_neg, kk, ss, key, e_pos = w.temp
    lora_w = c.small2[:, :]
    loaded, zeroed = c.sem(f"{name}_lora_loaded"), c.sem(f"{name}_zeroed")
    lora, sig, dec, exps = (c.sem(f"{name}_{n}") for n in ("lora", "sig", "decay", "exps"))
    kk_raw, kk_sq, kk_ss, kk_cl, kk_rs = (c.sem(f"{name}_{n}") for n in ("kk_raw", "kk_sq", "kk_ss", "kk_cl", "kk_rs"))
    vx_s, v_turn, v_tok, bon_in, bon = (c.sem(f"{name}_{n}") for n in ("vx", "v_turn", "v_tok", "bon_in", "bon"))
    gate_s, chain_s, act_chain = c.sem(f"{name}_gate"), c.sem(f"{name}_dve"), c.sem(f"{name}_act")
    cs = slice(pair * P, (pair + 1) * P)
    vx = [keep["kaT"][:, 0:S], keep["kaT"][:, S:2 * S]]
    halves = [(slice(0, 64), 0), (slice(64, 128), 1)]

    def half(x, hh, rows):
        return x.rearrange("p (c h n) -> p c h n", h=2, n=64)[rows, :, hh, :]

    def chunks(x, rows):
        return x.rearrange("p (c n) -> p c n", n=64)[rows, :, :]

    def vhalf(i, hh, rows):
        return vx[i].rearrange("p (c h n) -> p c h n", h=2, n=64)[rows, :, hh, :]

    with nc.Block() as block:
        @block.sync
        def _(sp):
            sp.dma_start(lora_w, c.dram["rw_lora"][bass.ds(c.layer, 1), :, :].rearrange("a p n -> p (a n)")
                         ).then_inc(loaded, 16)
            sp.wait_ge(loaded, 16)

        @block.gpsimd
        def _(pool):
            for x in (vx[0], vx[1], keep["ax"], w.bx, w.kx):
                nc.gpsimd.memset(x, 0.0).then_inc(zeroed, 1)

        @block.tensor
        def _(pe):
            pe.wait_ge(loaded, 16)
            nc.tensor.matmul(c.ps[:, 0, :], lora_w[0:32, cs], w.lora[0:32, :], start=True, stop=True).then_inc(lora, 1)
            nc.tensor.matmul(c.ps[:, 1, :], lora_w[32:64, cs], w.lora[32:64, :], start=True, stop=True,
                             tile_position=(32, 0)).then_inc(lora, 1)
            nc.tensor.matmul(c.ps[:, 2, :], lora_w[64:128, cs], w.lora[64:128, :], start=True, stop=True
                             ).then_inc(lora, 1)
            for i in range(2):
                pe.wait_ge(vx_s, 2 * i + 2)
                for n in range(4):
                    last = nc.tensor.transpose(c.ps[:, 5 + i, n * P:(n + 1) * P], vx[i][:, n * P:(n + 1) * P],
                                               c.const("ident"))
                last.then_inc(v_turn, 1)
            pe.wait_ge(kk_sq, 1)
            nc.tensor.matmul(c.ps[:, 3, :], c.const("bo64"), ss, start=True, stop=True).then_inc(kk_ss, 1)
            pe.wait_ge(bon_in, 1)
            nc.tensor.matmul(c.ps[:, 4, :], c.const("bo64"), c.p[:, T_A + pair, :], start=True, stop=True
                             ).then_inc(bon, 1)

        @block.scalar
        def _(act):
            chain = Chain(act, act_chain)
            act.wait_ge(lora, 1)
            nc.scalar.activation(logw, c.ps[:, 0, :], ACT.Sigmoid, bias=c.col("rw_w0", pair)).then_inc(sig, 1)
            act.wait_ge(lora, 2)
            nc.scalar.activation(a, c.ps[:, 1, :], ACT.Sigmoid, bias=c.col("rw_a0", pair)).then_inc(sig, 1)
            act.wait_ge(lora, 3)
            nc.scalar.activation(keep["gate"], c.ps[:, 2, :], ACT.Copy).then_inc(gate_s, 1)
            act.wait_ge(zeroed, 2)
            for i in range(2):
                for rows, hh in halves:
                    nc.scalar.activation(vhalf(i, hh, rows), chunks(v, rows)[:, 4 * i:4 * i + 4, :], ACT.Copy
                                         ).then_inc(vx_s, 1)
            act.wait_ge(kk_raw, 1)
            nc.scalar.activation(ss, kk, ACT.Square).then_inc(kk_sq, 1)
            act.wait_ge(dec, 2)
            nc.scalar.activation(e_pos, cum, ACT.Exp).then_inc(exps, 1)
            nc.scalar.activation(cum_ex, cum_ex, ACT.Exp).then_inc(exps, 1)
            nc.scalar.activation(e_neg, cum, ACT.Exp, scale=-1.0).then_inc(exps, 1)
            act.wait_ge(kk_cl, 1)
            chain(nc.scalar.activation(ss, ss, ACT.Ln, scale=KK_SCALE))
            nc.scalar.activation(ss, ss, ACT.Exp, scale=-0.5, bias=c.const("kk_shift")).then_inc(kk_rs, 1)
            for i in range(2):
                act.wait_ge(v_turn, i + 1)
                for rows, hh in halves:
                    src = c.ps[:, 5 + i, :].rearrange("p (c h n) -> p c h n", h=2, n=64)[rows, :, hh, :]
                    nc.scalar.activation(chunks(keep["v_tok"], rows)[:, 4 * i:4 * i + 4, :], src, ACT.Copy
                                         ).then_inc(v_tok, 1)
            act.wait_ge(v_tok, 4)
            act.wait_ge(gate_s, 1)

        @block.vector
        def _(dve):
            chain = Chain(dve, chain_s)
            nc.vector.tensor_scalar(kk, k, c.col("rw_k_k", pair), None, ALU.mult).then_inc(kk_raw, 1)
            dve.wait_ge(sig, 1)
            chain(nc.vector.tensor_scalar(logw, logw, -math.exp(-0.5), None, ALU.mult))
            nc.vector.tensor_tensor_scan(cum, c.const("scan"), logw, 0.0, ALU.mult, ALU.add).then_inc(dec, 1)
            dve.wait_ge(dec, 1)
            nc.vector.tensor_tensor(cum_ex, cum, logw, ALU.subtract).then_inc(dec, 1)
            dve.wait_ge(sig, 2)
            chain(nc.vector.tensor_scalar(key, a, -1.0, c.col("rw_k_a", pair), ALU.add, ALU.mult))
            chain(nc.vector.scalar_tensor_tensor(key, key, 1.0, k, ALU.add, ALU.mult))
            dve.wait_ge(kk_ss, 1)
            nc.vector.tensor_scalar(ss, c.ps[:, 3, :], 1e-24, None, ALU.max).then_inc(kk_cl, 1)
            dve.wait_ge(exps, 3)
            chain(nc.vector.tensor_tensor(keep["r"], r, e_pos, ALU.mult))
            chain(nc.vector.scalar_tensor_tensor(r, r, c.col("rw_r_k", pair), key, ALU.mult, ALU.mult))
            nc.vector.tensor_copy(w.last_decay[:, 8 * pair:8 * pair + 8], by_chunk(e_pos, 64)[:, :, 63]
                                  ).then_inc(bon_in, 1)
            dve.wait_ge(zeroed, 5)
            for rows, hh in halves:
                chain(nc.vector.tensor_tensor(half(w.kx, hh, rows), chunks(key, rows), chunks(e_neg, rows), ALU.mult))
            dve.wait_ge(kk_rs, 1)
            chain(nc.vector.tensor_tensor(kk, kk, ss, ALU.mult))
            for rows, hh in halves:
                chain(nc.vector.scalar_tensor_tensor(half(keep["ax"], hh, rows), chunks(kk, rows), -1.0,
                                                     chunks(cum_ex, rows), ALU.mult, ALU.mult))
            chain(nc.vector.tensor_tensor(kk, kk, a, ALU.mult))
            for rows, hh in halves:
                chain(nc.vector.tensor_tensor(half(w.bx, hh, rows), chunks(kk, rows), chunks(e_neg, rows), ALU.mult))
            dve.wait_ge(bon, 1)
            chain(nc.vector.tensor_tensor(keep["bonus"], c.ps[:, 4, :], v, ALU.mult))


def rwkv_intra(c, name, w, pair):
    nc = c.nc
    keep = w.keep[pair]
    multiplied, on_dve, on_act, dve_chain = (c.sem(f"{name}_{n}") for n in ("multiplied", "on_dve", "on_act", "chain"))
    STEPS = 10
    DVE_AT, ACT_AT = [0, 1, 2, 3, 4, 6, 8, 9], [0, 1, 2, 3, 5, 6, 7]

    def buffers(g):
        A, B, LO, C2, E2 = w.group[g]
        return A, B, LO, C2, E2, w.pt[g]

    def unit(x, n):
        return x[:, n * P:(n + 1) * P]

    def seen(steps, s, g):
        return 2 * after(steps, s - 1) + (g + 1 if s in steps else 0)

    with nc.Block() as block:
        @block.tensor
        def _(pe):
            for s in range(STEPS):
                for g in range(2):
                    A, B, LO, C2, E2, PT = buffers(g)
                    bank = [c.ps[:, 4 * g + i, :] for i in range(4)]
                    if s >= 1:
                        n = seen(DVE_AT, s - 1, g)
                        pe.wait_ge(on_dve, n)
                        pe.wait_ge(on_act, seen(ACT_AT, s - 1, g))
                    last = None
                    for n in range(4):
                        u = 4 * g + n
                        ax, bx, kx = (x[:, u * P:(u + 1) * P] for x in (keep["ax"], w.bx, w.kx))
                        r = keep["r"][:, u * 64:(u + 1) * 64]

                        def mm(i, lhsT, rhs):
                            return nc.tensor.matmul(unit(bank[i], n), lhsT, rhs, start=True, stop=True)
                        if s == 0:
                            mm(0, ax, bx)
                            mm(1, bx, ax)
                            mm(2, kx, ax)
                            nc.tensor.matmul(bank[3][:, n * P:n * P + 64], bx, r, start=True, stop=True)
                            last = nc.tensor.matmul(bank[3][:, n * P + 64:(n + 1) * P], kx, r, start=True, stop=True)
                        elif s == 1:
                            mm(0, unit(B, n), unit(A, n))
                            last = mm(1, unit(A, n), unit(B, n))
                        elif s == 2:
                            mm(0, unit(E2, n), unit(C2, n))
                            mm(1, unit(C2, n), unit(E2, n))
                            last = mm(2, unit(C2, n), unit(PT, n))
                        elif s == 3:
                            mm(0, unit(B, n), unit(A, n))
                            last = mm(2, unit(A, n), unit(PT, n))
                        elif s == 4:
                            last = mm(1, unit(E2, n), unit(PT, n))
                        elif s == 5:
                            last = nc.tensor.transpose(unit(bank[0], n), unit(PT, n), c.const("ident"))
                        elif s == 6:
                            mm(1, unit(A, n), unit(LO, n))
                            last = mm(2, unit(LO, n), unit(A, n))
                        elif s == 7:
                            last = mm(0, unit(C2, n), unit(E2, n))
                        elif s == 8:
                            last = mm(1, unit(B, n), unit(PT, n))
                        else:
                            last = mm(2, unit(E2, n), unit(PT, n))
                    last.then_inc(multiplied, 1)
            for g in range(2):
                pe.wait_ge(on_dve, 2 * len(DVE_AT))
                pe.wait_ge(on_act, 2 * len(ACT_AT))
                for n in range(4):
                    u = 4 * g + n
                    nc.tensor.transpose(unit(c.ps[:, 4 * g, :], n), w.bx[:, u * P:(u + 1) * P], c.const("ident"))
                    last = nc.tensor.transpose(unit(c.ps[:, 4 * g + 1, :], n), w.kx[:, u * P:(u + 1) * P],
                                               c.const("ident"))
                last.then_inc(multiplied, 1)

        @block.scalar
        def _(act):
            for s in ACT_AT:
                for g in range(2):
                    A, B, LO, C2, E2, PT = buffers(g)
                    bank = [c.ps[:, 4 * g + i, :] for i in range(4)]
                    act.wait_ge(multiplied, 2 * s + g + 1)
                    out, i = {0: (None, None), 1: (C2, 0), 2: (A, 0), 3: (E2, 0), 5: (A, 0), 6: (C2, 1), 7: (B, 0)}[s]
                    if s == 0:
                        out, i = keep["rT"][:, g * S:(g + 1) * S], 3
                    nc.scalar.activation(out, bank[i], ACT.Copy).then_inc(on_act, 1)
            for g in range(2):
                act.wait_ge(multiplied, 2 * STEPS + g + 1)
                nc.scalar.activation(keep["b_tok"][:, g * S:(g + 1) * S], c.ps[:, 4 * g, :], ACT.Copy
                                     ).then_inc(on_act, 1)
            act.wait_ge(on_act, 2 * len(ACT_AT) + 2)

        @block.vector
        def _(dve):
            chain = Chain(dve, dve_chain)
            for s in DVE_AT:
                for g in range(2):
                    A, B, LO, C2, E2, PT = buffers(g)
                    bank = [c.ps[:, 4 * g + i, :] for i in range(4)]
                    cols = slice(g * S, (g + 1) * S)
                    dve.wait_ge(multiplied, 2 * s + g + 1)
                    if s == 0:
                        chain(nc.vector.tensor_tensor(A, bank[0], c.const("m_ld"), ALU.mult))
                        chain(nc.vector.tensor_tensor(B, bank[1], c.const("m_ldT"), ALU.mult))
                        chain(nc.vector.tensor_tensor(keep["kaT"][:, cols], bank[2], c.const("m_kaT"), ALU.mult))
                        chain(nc.vector.tensor_tensor(LO, bank[1], c.const("m_loT"), ALU.mult))
                        chain(nc.vector.tensor_tensor(PT, B, c.const("ident4"), ALU.add))
                        dve.wait_ge(on_act, g + 1)
                        rT = keep["rT"][:, cols]
                        last = nc.vector.tensor_tensor(rT, rT, c.const("m_r"), ALU.mult)
                    elif s == 1:
                        last = nc.vector.tensor_copy(E2, bank[1])
                    elif s == 2:
                        chain(nc.vector.tensor_copy(B, bank[1]))
                        last = nc.vector.tensor_tensor(PT, bank[2], PT, ALU.add)
                    elif s == 3:
                        last = nc.vector.tensor_tensor(PT, bank[2], PT, ALU.add)
                    elif s == 4:
                        last = nc.vector.tensor_tensor(PT, bank[1], PT, ALU.add)
                    elif s == 6:
                        last = nc.vector.tensor_copy(E2, bank[2])
                    elif s == 8:
                        last = nc.vector.tensor_tensor(PT, bank[1], PT, ALU.add)
                    else:
                        last = nc.vector.tensor_tensor(keep["xT"][:, cols], bank[2], PT, ALU.add)
                    last.then_inc(on_dve, 1)
            for g in range(2):
                dve.wait_ge(multiplied, 2 * STEPS + g + 1)
                chain(nc.vector.tensor_copy(keep["k_tok"][:, g * S:(g + 1) * S], c.ps[:, 4 * g + 1, :]))


def rwkv_scan(c, name, w):
    nc = c.nc
    names = ("zeroed", "rhs", "rhs_out", "sa", "sa_out", "state_mm", "state_add", "state", "y_mm", "y_out")
    zeroed, rhs, rhs_out, sa, sa_out, state_mm, state_add, state, y_mm, y_out = (c.sem(f"{name}_{n}") for n in names)
    mean, cent, sq, var, rs_s, chain_s = (c.sem(f"{name}_{n}") for n in ("mean", "cent", "sq", "var", "rs", "chain"))
    st = [[w.bx[:, (2 * q + i) * 64:(2 * q + i + 1) * 64] for i in range(2)] for q in range(2)]
    rh = [w.bx[:, 256 + q * 64:256 + (q + 1) * 64] for q in range(2)]
    sav = [w.bx[:, 384 + q * 64:384 + (q + 1) * 64] for q in range(2)]
    order = [(n, q) for n in range(NCH) for q in range(2)]
    y = [w.temp[0], w.temp[1]]
    sqt, rs = [w.temp[2], w.temp[3]], [w.temp[4], w.temp[5]]
    mmean = [w.temp[6], w.temp[7]]
    ONCE = len(order)

    with nc.Block() as block:
        @block.gpsimd
        def _(pool):
            for q in range(2):
                nc.gpsimd.memset(st[q][0], 0.0).then_inc(zeroed, 1)

        @block.tensor
        def _(pe):
            pe.wait_ge(zeroed, 2)

            def unit(x, n, width=P):
                return x[:, n * width:(n + 1) * width]

            def first(i):
                n, q = order[i]
                keep = w.keep[q]
                if n >= 1:
                    pe.wait_ge(state, i - 2 + 1)
                bank = c.ps[:, q, 0:64]
                nc.tensor.matmul(bank, unit(keep["ax"], n), st[q][n % 2], start=True, stop=False)
                nc.tensor.matmul(bank, unit(keep["kaT"], n), unit(keep["v_tok"], n, 64), start=False, stop=True
                                 ).then_inc(rhs, 1)

            def second(i):
                n, q = order[i]
                pe.wait_ge(rhs_out, i + 1)
                nc.tensor.matmul(c.ps[:, q, 64:128], unit(w.keep[q]["xT"], n), rh[q], start=True, stop=True
                                 ).then_inc(sa, 1)

            def third(i):
                n, q = order[i]
                keep = w.keep[q]
                pe.wait_ge(sa_out, i + 1)
                bank = c.ps[:, 2 + q, 0:64]
                nc.tensor.matmul(bank, unit(keep["b_tok"], n), sav[q], start=True, stop=False)
                nc.tensor.matmul(bank, unit(keep["k_tok"], n), unit(keep["v_tok"], n, 64), start=False, stop=True
                                 ).then_inc(state_mm, 1)
                for hh in range(2):
                    rows = slice(64 * hh, 64 * hh + 64)
                    out = c.ps[rows, 4 + q, n * 64:(n + 1) * 64]
                    rT = unit(keep["rT"], n)
                    nc.tensor.matmul(out, st[q][n % 2][rows, :], keep["r"][rows, n * 64:(n + 1) * 64], start=True,
                                     stop=False)
                    nc.tensor.matmul(out, sav[q][rows, :], rT[rows, 0:64], start=False, stop=False)
                    last = nc.tensor.matmul(out, unit(keep["v_tok"], n, 64)[rows, :], rT[rows, 64:128], start=False,
                                            stop=True)
                last.then_inc(y_mm, 1)

            for i in range(0, ONCE, 2):
                first(i)
                first(i + 1)
                second(i)
                second(i + 1)
                third(i)
                third(i + 1)
            for q in range(2):
                pe.wait_ge(y_out, q + 1)
                nc.tensor.matmul(c.ps[:, 6, :], c.const("bo64"), y[q], start=True, stop=True).then_inc(mean, 1)
                pe.wait_ge(sq, q + 1)
                nc.tensor.matmul(c.ps[:, 7, :], c.const("bo64"), sqt[q], start=True, stop=True).then_inc(var, 1)

        @block.scalar
        def _(act):
            for i, (n, q) in enumerate(order):
                act.wait_ge(rhs, i + 1)
                if i >= 2:
                    act.wait_ge(sa, i - 1)
                nc.scalar.activation(rh[q], c.ps[:, q, 0:64], ACT.Copy).then_inc(rhs_out, 1)
            for q in range(2):
                act.wait_ge(y_mm, ONCE - 1 + q)
                nc.scalar.activation(y[q], c.ps[:, 4 + q, :], ACT.Copy).then_inc(y_out, 1)
            for q in range(2):
                act.wait_ge(cent, q + 1)
                nc.scalar.activation(sqt[q], y[q], ACT.Square).then_inc(sq, 1)
                act.wait_ge(var, q + 1)
                nc.scalar.activation(rs[q], c.ps[:, 7, :], ACT.Ln, bias=c.const("gn_eps"), scale=1.0 / 64
                                     ).then_inc(rs_s, 1)
                act.wait_ge(rs_s, 2 * q + 1)
                nc.scalar.activation(rs[q], rs[q], ACT.Exp, scale=-0.5).then_inc(rs_s, 1)

        @block.vector
        def _(dve):
            for i, (n, q) in enumerate(order):
                if q == 0:
                    for j in (i, i + 1):
                        qq = order[j][1]
                        dve.wait_ge(sa, j + 1)
                        if j >= 2:
                            dve.wait_ge(y_mm, j - 1)
                        nc.vector.tensor_copy(sav[qq], c.ps[:, qq, 64:128]).then_inc(sa_out, 1)
                new = st[q][(n + 1) % 2]
                dve.wait_ge(state_mm, i + 1)
                if i >= 2:
                    dve.wait_ge(y_mm, i - 1)
                nc.vector.tensor_tensor(new, c.ps[:, 2 + q, 0:64], st[q][n % 2], ALU.add).then_inc(state_add, 1)
                dve.wait_ge(state_add, i + 1)
                nc.vector.tensor_scalar(new, new, w.last_decay[:, 8 * q + n:8 * q + n + 1], None, ALU.mult
                                        ).then_inc(state, 1)
            chain = Chain(dve, chain_s)
            for q in range(2):
                dve.wait_ge(mean, q + 1)
                nc.vector.scalar_tensor_tensor(y[q], c.ps[:, 6, :], -1.0 / 64, y[q], ALU.mult, ALU.add
                                               ).then_inc(cent, 1)
                dve.wait_ge(rs_s, 2 * q + 2)
                chain(nc.vector.scalar_tensor_tensor(y[q], y[q], c.col("rw_ln_g", q), rs[q], ALU.mult, ALU.mult))
                chain(nc.vector.scalar_tensor_tensor(y[q], y[q], c.col("rw_ln_b", q), w.keep[q]["bonus"], ALU.add,
                                                     ALU.add))
                chain(nc.vector.tensor_tensor(c.y[:, Y_A + q, :], y[q], w.keep[q]["gate"], ALU.mult))


def feed_forward_up(c, name, up):
    nc = c.nc
    tapped, act_g, conv = c.sem(f"{name}_tapped"), c.sem(f"{name}_silu"), c.sem(f"{name}_conv")
    hidden = c.sem(f"{name}_hidden")
    work_tile = [c.y[:, s, :] for s in range(RING)]
    GATES = (1, 3)

    def tap(i, t):
        at = C_AT["ffn_tap"]
        return c.cols[:, bass.ds(t * 4 + (at + i), 1)]

    @contextmanager_block(nc)
    def _(block):
        @block.sync
        def _(sp):
            up.load(sp)

        @block.tensor
        def _(pe):
            up.multiply(pe, (lambda kt: c.a_hi[:, kt, :], lambda kt: c.h_lo[:, kt, :]))

        @block.scalar
        def _(act):
            def tile(s, g):
                act.wait_ge(up.multiplied, g * RING + s + 1)
                nc.scalar.activation(work_tile[s], c.ps[:, s, :], ACT.Identity, bias=tap(3, g * RING + s),
                                     scale=tap(2, g * RING + s)).then_inc(tapped, 1)

            def silu(i, g):
                s = GATES[i]
                act.wait_ge(conv, g * 2 * RING + 2 * s + 2)
                nc.scalar.activation(work_tile[s], work_tile[s], ACT.Silu).then_inc(act_g, 1)

            def work_on(first):
                def work(s, g):
                    if not first:
                        act.wait_ge(hidden, 2 * (g - 1) + s // 2 + 1)
                    tile(s, g)
                    if s in GATES:
                        silu(s // 2, g)
                return work

            up.split_high(act, 0, 0, first=True)
            up.split_high(act, 1, 0, first=True)
            up.tiles(act, up.split_high, work_on(False), first=work_on(True))

        @block.vector
        def _(dve):
            def work(s, g):
                t = g * RING + s
                dve.wait_ge(tapped, t + 1)
                o, u = work_tile[s], c.ps[:, s, :]
                nc.vector.scalar_tensor_tensor(o[:, 1:S], u[:, 0:S - 1], tap(1, t), o[:, 1:S], ALU.mult,
                                               ALU.add).then_inc(conv, 1)
                dve.wait_ge(conv, t * 2 + 1)
                nc.vector.scalar_tensor_tensor(o[:, 2:S], u[:, 0:S - 2], tap(0, t), o[:, 2:S], ALU.mult,
                                               ALU.add).then_inc(conv, 1)
                dve.wait_ge(conv, t * 2 + 2)
                dve.sem_inc(up.emptied, 1)
                if s in GATES:
                    i = s // 2
                    dve.wait_ge(act_g, g * 2 + i + 1)
                    out = c.p[:, bass.ds(g * 2 + i, 1), :].rearrange("p a n -> p (a n)")
                    nc.vector.tensor_tensor(out, work_tile[2 * i], work_tile[2 * i + 1], ALU.mult).then_inc(hidden, 1)

            up.split_low(dve, 0, 0)
            up.split_low(dve, 1, 0)
            up.tiles(dve, up.split_low, work)
            dve.wait_ge(hidden, up.n // 2)


class contextmanager_block:

    def __init__(self, nc):
        self.nc = nc

    def __call__(self, f):
        with self.nc.Block() as block:
            f(block)


def linear_stage(c, lin, rhs, out, prefetch=None, load=True):
    nc = c.nc
    engine, body = out
    with nc.Block() as block:
        @block.sync
        def _(sp):
            if load:
                lin.load(sp)
            if prefetch is not None:
                sp.wait_ge(lin.multiplied, lin.n)
                prefetch(sp)

        @block.tensor
        def _(pe):
            lin.multiply(pe, rhs)

        if engine == "scalar":
            @block.scalar
            def _(act):
                body(act)
        else:
            @block.vector
            def _(dve):
                body(dve)


def block_one_layer(c, layer, stop=None):
    nc, dram = c.nc, c.dram
    c.layer = layer

    def of_layer(name, tiles):
        return lambda t: dram[name][bass.ds(layer * tiles + t, 1), :, :].rearrange("a p n -> p (a n)")

    w_in = SplitLinear(c, "w_in", IN_T, of_layer("w_in", IN_T))
    w_out = SplitLinear(c, "w_out", KT, of_layer("w_out", KT))
    ffn_up = SplitLinear(c, "ffn_up", 2 * FT, of_layer("ffn_up", 2 * FT))
    ffn_down = Linear(c, "ffn_down", KT, of_layer("ffn_down", KT), k_tiles=FT, size=FT * P)
    cols_loaded = c.sem("cols_loaded")
    mod = lambda i: c.mod[:, i * KT:(i + 1) * KT]
    tmp = c.ring[:, RING * D:]

    def start(sp):
        sp.dma_start(c.cols[:, :], dram["cols"][bass.ds(layer, 1), :, :].rearrange("a p n -> p (a n)")
                     ).then_inc(cols_loaded, 16)
        w_in.prefetch(sp)
        sp.wait_ge(cols_loaded, 16)

    with nc.Block() as block:
        @block.sync
        def _(sp):
            start(sp)
    next_cond, cond_ready = load_cond(c, "next_mod", layer + 1)
    norm_modulate(c, "norm1", c.x, c.h, c.col("norm1_g", 0, 8), mod(1), mod(0), tmp=tmp, extra_act=next_cond,
                  split=(c.a_hi, c.h_lo))
    tile_of_p = lambda t: c.p[:, bass.ds(t, 1), :].rearrange("p a n -> p (a n)")
    split_stage(c, w_in, c.h_lo, copy_out(c, w_in, tile_of_p))
    if stop == "w_in":
        return
    with c.stages():
        prepare_attentions(c, "prep", w_out.prefetch)
        attention_forget(c, "fx")
        attention_diff(c, "df")
        spatial_gating(c, "sg")
    if stop == "attn":
        return
    w = Rwkv(c)
    with c.stages():
        rwkv_shift(c, "rw_shift", w)
        for q in range(2):
            rwkv_prepare(c, f"rw_prep{q}", w, q)
            rwkv_intra(c, f"rw_intra{q}", w, q)
        rwkv_scan(c, "rw_scan", w)
    if stop == "mix":
        return
    split_stage(c, w_out, c.y_lo, add_residual(c, w_out, mod(2)), prefetch=ffn_up.prefetch, x=c.y)
    next_sums = AdaLN(c, "next_mod", layer + 1)
    norm_modulate(c, "norm2", c.x, c.h, c.col("norm2_g", 0, 8), mod(4), mod(3), tmp=tmp, split=(c.a_hi, c.h_lo))
    feed_forward_up(c, "ffn", ffn_up)
    with nc.Block() as block:
        @block.sync
        def _(sp):
            ffn_down.prefetch(sp)
            ffn_down.load(sp)

        @block.scalar
        def _(act):
            next_sums.load(act)

        @block.tensor
        def _(pe):
            ffn_down.multiply(pe, lambda kt: c.p[:, kt, :])

        @block.vector
        def _(dve):
            per_tile = next_sums.pieces // KT
            for t in range(KT):
                next_sums.add(dve, t * per_tile, (t + 1) * per_tile)
                residual_tiles(c, ffn_down, dve, mod(5), t, t + 1)
    adaln_finish(c, "next_mod", layer + 1, c.mod[:, :])


class Gla:

    LAT, SEG = S, S + CTX
    CHUNKS = 2 * (NCH + LNC)

    def __init__(self, c):
        self.c = c
        flat = lambda t: t.rearrange("p a n -> p (a n)")
        h, y, vt = flat(c.h[:, :, :]), flat(c.y[:, :, :]), flat(c.vt[:, :, :])
        self.ctx_x, self.ctx_h = (t.rearrange("p (a n) -> p a n", n=CTX) for t in (y[:, 0:4 * S], y[:, 4 * S:8 * S]))
        self.kc = vt[:, 0:4 * CTX].rearrange("p (a n) -> p a n", n=CTX)
        self.vc = vt[:, 4 * CTX:12 * CTX].rearrange("p (a n) -> p a n", n=CTX)
        self.low = vt[:, 12 * CTX:15 * CTX]
        self.q, self.r, self.k, self.v = 0, 4, 12, 16
        self.g, self.cum = h[:, 0:3 * S], h[:, 3 * S:6 * S]
        self.state = h[:, 6 * S:8 * S].rearrange("p (z i n) -> p z i n", z=2, i=2)
        self.e_pos, self.e_neg = scratch(c, 0, 2), scratch(c, 2, 3)
        self.k_tok = scratch(c, 5, 3)
        self.v_tok = scratch(c, 8, 3).rearrange("p (b n) -> p b n", n=2 * P)
        self.scores = scratch(c, 11, 2)
        self.gb = scratch(c, 13)
        self.tot, self.half, self.em, self.step = (c.small[:, 24 * i:24 * i + 24] for i in range(4))


def gla_project(c, w):
    nc = c.nc
    n1, n2 = 12, 12
    of = lambda first: lambda t: c.dram["gla_in"][bass.ds(first + t, 1), :, :].rearrange("a p n -> p (a n)")
    qr = SplitLinear(c, "gla_qr", n1, of(0))
    kv = SplitLinear(c, "gla_kv", n2, of(n1))
    ctx_multiplied, ctx_emptied = c.sem("gla_ctx_multiplied"), c.sem("gla_ctx_emptied")
    low_loaded, low_done, low_out = c.sem("gla_low_loaded"), c.sem("gla_low"), c.sem("gla_low_out")
    low_w = scratch(c, 8)
    low_hi, low_lo = c.low_hi, c.low_lo
    low_split = c.sem("gla_low_split")
    ctx_kv = c.vt[:, :, :].rearrange("p b n -> p (b n)")
    tile_of_p = lambda t: c.p[:, bass.ds(t, 1), :].rearrange("p a n -> p (a n)")
    latent = (lambda kt: c.a_hi[:, kt, :], lambda kt: c.h_lo[:, kt, :])
    context = (lambda kt: c.ctx_hi[:, kt, :], lambda kt: c.ctx_lo[:, kt, :])

    with nc.Block() as block:
        @block.sync
        def _(sp):
            qr.prefetch(sp)
            sp.dma_start(low_w, c.dram["gla_low"]).then_inc(low_loaded, 16)
            sp.dma_start(w.gb, c.dram["gla_gb"]).then_inc(low_loaded, 16)
            qr.load(sp)
            for s in range(RING):
                sp.wait_ge(qr.low, n1 - RING + s + 1)
                sp.dma_start(c.slot(s), kv.weights(s)).then_inc(kv.loaded[s], 16)

        @block.tensor
        def _(pe):
            qr.multiply(pe, latent)
            pe.wait_ge(low_split, 2)
            for half, (x, n) in enumerate(((latent, S), (context, CTX))):
                hi, lo = x
                for kt in range(KT):
                    at = slice(kt * 64, (kt + 1) * 64)
                    bank = c.ps[0:64, 4 + half, 0:n]
                    nc.tensor.matmul(bank, low_hi[:, at], hi(kt), start=(kt == 0), stop=False)
                    nc.tensor.matmul(bank, low_hi[:, at], lo(kt), start=False, stop=False)
                    last = nc.tensor.matmul(bank, low_lo[:, at], hi(kt), start=False, stop=(kt == KT - 1))
                last.then_inc(low_done, 1)

        @block.scalar
        def _(act):
            qr.split_high(act, 0, 0, first=True)
            qr.split_high(act, 1, 0, first=True)
            qr.tiles(act, qr.split_high, copy_out(c, qr, lambda t: tile_of_p(t))[1](act))
            act.wait_ge(low_loaded, 32)
            nc.scalar.activation(low_hi[:, :], low_w, ACT.Copy).then_inc(low_split, 1)
            act.wait_ge(low_done, 2)
            nc.scalar.activation(w.low[0:64, 0:S], c.ps[0:64, 4, :], ACT.Copy).then_inc(low_out, 1)
            nc.scalar.activation(w.low[0:64, S:S + CTX], c.ps[0:64, 5, 0:CTX], ACT.Copy).then_inc(low_out, 1)

        @block.vector
        def _(dve):
            qr.split_low(dve, 0, 0)
            qr.split_low(dve, 1, 0)
            qr.tiles(dve, qr.split_low, lambda s, g: None)
            dve.wait_ge(low_split, 1)
            nc.vector.tensor_tensor(low_lo[:, :], low_w, low_hi[:, :].bitcast(F32), ALU.subtract).then_inc(low_split, 1)

    with nc.Block() as block:
        @block.sync
        def _(sp):
            kv.load(sp)

        @block.tensor
        def _(pe):
            def tile(s, g):
                pe.wait_ge(kv.low, g * RING + s + 1)
                kv.products(s, c.ps[:, s, :], latent)
                kv.products(s, c.ps[:, RING + s, 0:CTX], context).then_inc(kv.multiplied, 1)

            for s in range(RING):
                tile(s, 0)
            with pe.Fori(1, n2 // RING) as g:
                for s in range(RING):
                    pe.wait_ge(kv.emptied, (g - 1) * RING + s + 1)
                    pe.wait_ge(ctx_emptied, (g - 1) * RING + s + 1)
                    tile(s, g)

        @block.scalar
        def _(act):
            kv.split_high(act, 0, 0, first=True)
            kv.split_high(act, 1, 0, first=True)
            kv.tiles(act, kv.split_high, copy_out(c, kv, lambda t: tile_of_p(t + n1))[1](act))

        @block.vector
        def _(dve):
            def copy_ctx(s, g):
                dve.wait_ge(kv.multiplied, g * RING + s + 1)
                out = ctx_kv[:, bass.ds(g * (RING * CTX) + s * CTX, CTX)]
                nc.vector.tensor_copy(out, c.ps[:, RING + s, 0:CTX]).then_inc(ctx_emptied, 1)

            kv.split_low(dve, 0, 0)
            kv.split_low(dve, 1, 0)
            kv.tiles(dve, kv.split_low, copy_ctx)


def gla_prepare(c, name, w, head):
    nc = c.nc
    z, z_in, ln_in, soft, gate, scanned = (c.sem(f"{name}_{n}") for n in ("z", "z_in", "ln_in", "soft", "gate", "scan"))
    exps, q_done, k_done, chain_s = (c.sem(f"{name}_{n}") for n in ("exps", "q", "k", "chain"))
    v_turn, v_out, k_turn, k_out, act_chain = (c.sem(f"{name}_{n}") for n in ("v_turn", "v_out", "k_turn", "k_out", "act"))
    zeroed = c.sem(f"{name}_zeroed")
    cs = slice(head * P, (head + 1) * P)
    b = [c.cols2[:, C2_AT["b_gate"] + 4 * z_ + head:C2_AT["b_gate"] + 4 * z_ + head + 1] for z_ in range(2)]
    SEG = w.SEG
    parts = [(0, S, 0, 0, 0), (S, CTX, 2, 0, 0), (SEG, S, 1, 0, 1), (SEG + S, CTX, 6, 0, 1)]
    chunks = lambda t: t.rearrange("p (c n) -> p c n", n=CH)
    bc = lambda t, n: t.unsqueeze(2).to_broadcast([P, n, CH])
    with nc.Block() as block:
        @block.gpsimd
        def _(pool):
            nc.gpsimd.memset(w.scores, 0.0).then_inc(zeroed, 1)
            pool.wait_ge(zeroed, 1)

        @block.tensor
        def _(pe):
            for to, n, bank, frm, z_ in parts:
                lo = w.low[32 * z_:32 * z_ + 16, 0 if n == S else S:S if n == S else SEG]
                last = nc.tensor.matmul(c.ps[:, bank, frm:frm + n], w.gb[32 * z_:32 * z_ + 16, cs], lo, start=True,
                                        stop=True, tile_position=(32 * z_, 0))
            last.then_inc(z, 1)
            for j in range(2):
                for n in range(4):
                    nc.tensor.transpose(c.ps[:, 3 + j, n * P:(n + 1) * P],
                                        c.p[:, w.v + 2 * head + j, n * P:(n + 1) * P], c.const("ident"))
            for j in range(2):
                for n in range(2):
                    last = nc.tensor.transpose(c.ps[:, 5, (2 * j + n) * P:(2 * j + n + 1) * P],
                                               w.vc[:, 2 * head + j, n * P:(n + 1) * P], c.const("ident"))
            last.then_inc(v_turn, 1)
            pe.wait_ge(k_done, 4)
            pe.wait_ge(z_in, 8)
            for n in range(12):
                last = nc.tensor.transpose(c.ps[:, n // 4, n % 4 * P:(n % 4 + 1) * P], w.e_neg[:, n * P:(n + 1) * P],
                                           c.const("ident"))
                if n % 4 == 3:
                    last.then_inc(k_turn, 1)

        @block.scalar
        def _(act):
            chain = Chain(act, act_chain)
            act.wait_ge(z, 1)
            for to, n, bank, frm, z_ in parts:
                src = c.ps[:, bank, frm:frm + n]
                nc.scalar.activation(w.g[:, to:to + n], src, ACT.Identity, bias=b[z_]).then_inc(z_in, 1)
                nc.scalar.activation(w.cum[:, to:to + n], src, ACT.Abs, bias=b[z_]).then_inc(z_in, 1)
            act.wait_ge(z_in, 8)
            chain(nc.scalar.activation(w.cum, w.cum, ACT.Exp, scale=-1.0))
            nc.scalar.activation(w.cum, w.cum, ACT.Ln, bias=1.0).then_inc(soft, 1)
            act.wait_ge(v_turn, 1)
            for j in range(2):
                nc.scalar.activation(w.v_tok[:, 0:4, j * P:(j + 1) * P],
                                     c.ps[:, 3 + j, :].rearrange("p (b n) -> p b n", n=P), ACT.Copy).then_inc(v_out, 1)
                nc.scalar.activation(w.v_tok[:, 4:6, j * P:(j + 1) * P],
                                     c.ps[:, 5, 2 * j * P:2 * (j + 1) * P].rearrange("p (b n) -> p b n", n=P), ACT.Copy
                                     ).then_inc(v_out, 1)
            act.wait_ge(gate, 1)
            nc.scalar.activation(w.e_neg, w.cum, ACT.Exp, scale=-1.0 / 16).then_inc(exps, 1)
            nc.scalar.activation(w.e_pos[:, 0:S], w.cum[:, 0:S], ACT.Exp, scale=1.0 / 16).then_inc(exps, 1)
            nc.scalar.activation(w.e_pos[:, S:2 * S], w.cum[:, SEG:SEG + S], ACT.Exp, scale=1.0 / 16).then_inc(exps, 1)
            nc.scalar.activation(w.em, w.half, ACT.Exp, scale=1.0 / 16).then_inc(exps, 1)
            for i in range(3):
                act.wait_ge(k_turn, i + 1)
                nc.scalar.activation(w.k_tok[:, i * S:(i + 1) * S], c.ps[:, i, :], ACT.Copy).then_inc(k_out, 1)

        @block.vector
        def _(dve):
            chain = Chain(dve, chain_s)
            dve.wait_ge(soft, 1)
            chain(nc.vector.scalar_tensor_tensor(w.g, w.g, 0.0, w.cum, ALU.min, ALU.subtract))
            for i in range(3):
                chain(nc.vector.tensor_tensor_scan(w.cum[:, i * S:(i + 1) * S], c.const("scan"),
                                                   w.g[:, i * S:(i + 1) * S], 0.0, ALU.mult, ALU.add))
            chain(nc.vector.tensor_copy(w.tot, chunks(w.cum)[:, :, CH - 1]))
            chain(nc.vector.tensor_scalar(w.half, w.tot, 0.5, None, ALU.mult))
            f, r = w.cum[:, 0:SEG], w.cum[:, SEG:2 * SEG]
            chain(nc.vector.tensor_tensor(chunks(f), chunks(f), bc(w.half[:, 0:12], 12), ALU.subtract))
            chain(nc.vector.tensor_tensor(r, w.g[:, SEG:2 * SEG], r, ALU.subtract))
            chain(nc.vector.tensor_tensor(chunks(r), chunks(r), bc(w.half[:, 12:24], 12), ALU.add))
            nc.vector.tensor_scalar(w.cum, w.cum, 80.0 * 16, -80.0 * 16, ALU.min, ALU.max).then_inc(gate, 1)
            dve.wait_ge(exps, 1)
            k, kc = c.p[:, w.k + head, :], w.kc[:, head, :]
            for to, n, _, _, _ in parts:
                x = w.e_neg[:, to:to + n]
                nc.vector.tensor_tensor(x, x, k if n == S else kc, ALU.mult).then_inc(k_done, 1)
            dve.wait_ge(exps, 4)
            q = c.p[:, w.q + head, :]
            for z_ in range(2):
                x = w.e_pos[:, z_ * S:(z_ + 1) * S]
                nc.vector.scalar_tensor_tensor(x, q, P ** -0.5, x, ALU.mult, ALU.mult).then_inc(q_done, 1)
            em = w.em
            for lo, n in ((0, 7), (8, 3), (12, 7), (20, 3)):
                chain(nc.vector.tensor_tensor(w.step[:, lo:lo + n], em[:, lo:lo + n], em[:, lo + 1:lo + n + 1], ALU.mult))
            chain(nc.vector.tensor_tensor(w.step[:, 11:12], em[:, 11:12], em[:, 0:1], ALU.mult))
            chain(nc.vector.tensor_tensor(w.step[:, 23:24], em[:, 20:21], em[:, 19:20], ALU.mult))


def gla_scan(c, name, w, head):
    nc = c.nc
    scored, masked, update, added, state, summed = (c.sem(f"{name}_{n}") for n in
                                                    ("scored", "masked", "update", "added", "state", "summed"))
    squared, ms, rs_s, silu, chain_s = (c.sem(f"{name}_{n}") for n in ("squared", "ms", "rs", "silu", "chain"))
    STEPS = NCH + LNC
    seg = w.SEG

    def chunk(z, s):
        if s < LNC:
            return 12 * z + 8 + (s if z == 0 else LNC - 1 - s), None
        n = s - LNC if z == 0 else NCH - 1 - (s - LNC)
        return 12 * z + n, n

    def step_col(z, s):
        a, b = chunk(z, s)[0], chunk(z, s + 1)[0]
        return min(a, b) if abs(a - b) == 1 and s != LNC - 1 else 12 * z + 11

    sq = [w.g[:, 0:S], w.g[:, S:2 * S]]
    rs = w.g[:, 2 * S:3 * S]
    t1 = [w.cum[:, 0:S], w.cum[:, S:2 * S]]
    with nc.Block() as block:
        @block.tensor
        def _(pe):
            for z in range(2):
                for n in range(NCH):
                    rows = slice(64 * (n % 2), 64 * (n % 2) + 64)
                    last = nc.tensor.matmul(c.ps[rows, z, n * CH:(n + 1) * CH], w.e_neg[:, z * seg + n * CH:z * seg + (n + 1) * CH],
                                            w.e_pos[:, z * S + n * CH:z * S + (n + 1) * CH], start=True, stop=True)
            last.then_inc(scored, 1)

            def update_of(z, s):
                g, _ = chunk(z, s)
                rows = slice(64 * (g % 2), 64 * (g % 2) + 64)
                block_of = g % 12 // 2
                if s >= 2:
                    pe.wait_ge(added, 2 * (s - 2) + z + 1)
                nc.tensor.matmul(c.ps[:, 4 + 2 * z + s % 2, 0:2 * P], w.k_tok[rows, (g // 2) * P:(g // 2 + 1) * P],
                                 w.v_tok[rows, block_of, :], start=True, stop=True).then_inc(update, 1)

            for z in range(2):
                update_of(z, 0)
            pe.wait_ge(masked, 4)
            for z in range(2):
                for n in range(NCH // 2):
                    for j in range(2):
                        nc.tensor.matmul(c.ps[:, 2 + j, n * P:(n + 1) * P], w.v_tok[:, n, j * P:(j + 1) * P],
                                         w.scores[:, z * S + n * P:z * S + (n + 1) * P], start=(z == 0 and n == 0),
                                         stop=False, skip_group_check=True)
            for s in range(STEPS):
                for z in range(2):
                    if 1 <= s < STEPS - 1:
                        update_of(z, s)
                if s < LNC:
                    continue
                for z in range(2):
                    _, n = chunk(z, s)
                    pe.wait_ge(state, 2 * (s - 1) + z + 1)
                    for j in range(2):
                        last = nc.tensor.matmul(c.ps[:, 2 + j, n * CH:(n + 1) * CH],
                                                w.state[:, z, s % 2, j * P:(j + 1) * P],
                                                w.e_pos[:, z * S + n * CH:z * S + (n + 1) * CH], start=False,
                                                stop=(s == STEPS - 1 and z == 1), skip_group_check=True)
                    last.then_inc(summed, 1)
            for j in range(2):
                pe.wait_ge(squared, j + 1)
                last = nc.tensor.matmul(c.ps[:, 1, :], c.const("ones"), sq[j], start=(j == 0), stop=(j == 1))
            last.then_inc(ms, 1)

        @block.scalar
        def _(act):
            for j in range(2):
                r = c.p[:, w.r + 2 * head + j, :]
                nc.scalar.activation(r, r, ACT.Silu).then_inc(silu, 1)
            act.wait_ge(summed, 2 * NCH)
            for j in range(2):
                nc.scalar.activation(sq[j], c.ps[:, 2 + j, :], ACT.Square).then_inc(squared, 1)
            act.wait_ge(ms, 1)
            nc.scalar.activation(rs, c.ps[:, 1, :], ACT.Ln, bias=c.const("eps"), scale=1.0 / (2 * P)).then_inc(rs_s, 1)
            act.wait_ge(rs_s, 1)
            nc.scalar.activation(rs, rs, ACT.Exp, scale=-0.5).then_inc(rs_s, 1)

        @block.vector
        def _(dve):
            dve.wait_ge(scored, 1)
            pairs = lambda t, par: t.rearrange("p (n h i) -> p n h i", h=2, i=CH)[64 * par:64 * par + 64, :, par, :]
            for z, mask in enumerate(("gla_f", "gla_b")):
                for par in range(2):
                    m = c.const(mask).rearrange("p (n i) -> p n i", i=CH)[64 * par:64 * par + 64]
                    nc.vector.tensor_tensor(pairs(w.scores[:, z * S:(z + 1) * S], par), pairs(c.ps[:, z, :], par), m,
                                            ALU.mult).then_inc(masked, 1)
            for s in range(STEPS - 1):
                for z in range(2):
                    n = 2 * s + z
                    dve.wait_ge(update, n + 1)
                    new, old = w.state[:, z, (s + 1) % 2, :], w.state[:, z, s % 2, :]
                    u = c.ps[:, 4 + 2 * z + s % 2, 0:2 * P]
                    if s > LNC:
                        dve.wait_ge(summed, 2 * (s - 1 - LNC) + z + 1)
                    at = step_col(z, s)
                    decay = w.step[:, at:at + 1]
                    if s == 0:
                        nc.vector.tensor_copy(new, u).then_inc(added, 1)
                    else:
                        dve.wait_ge(state, n - 1)
                        nc.vector.tensor_tensor(new, u, old, ALU.add).then_inc(added, 1)
                    dve.wait_ge(added, n + 1)
                    nc.vector.tensor_scalar(new, new, decay, None, ALU.mult).then_inc(state, 1)
            chain = Chain(dve, chain_s)
            dve.wait_ge(rs_s, 2)
            dve.wait_ge(silu, 2)
            for j in range(2):
                gain = c.cols2[:, C2_AT["gla_norm_g"] + j:C2_AT["gla_norm_g"] + j + 1]
                chain(nc.vector.scalar_tensor_tensor(t1[j], c.ps[:, 2 + j, :], gain, rs, ALU.mult, ALU.mult))
                chain(nc.vector.tensor_tensor(c.y[:, 2 * head + j, :], t1[j], c.p[:, w.r + 2 * head + j, :], ALU.mult))


def route(c, name, m):
    nc = c.nc
    B = m.B
    names = ("loaded", "logits", "sig", "chosen", "placed", "chain", "turned", "high", "low")
    loaded, logits, sig, chosen_s, placed, chain_s, turned, high, low = (c.sem(f"{name}_{n}") for n in names)
    router_w = c.p[:, 0, 0:KT * E_N]
    cell = [c.p[:, 1 + i, :] for i in range(13)]
    score, sel, rank, best_in, top, t0, t1, gs, chosen, slot, cnt, big, num = (x[:, 0:B * E_N] for x in cell)
    wide = c.p[:, 14, :]
    four = lambda t: t.rearrange("p (g e) -> p g e", e=4)
    with nc.Block() as block:
        @block.sync
        def _(sp):
            sp.dma_start(router_w, c.dram["router"]).then_inc(loaded, 16)
            sp.wait_ge(loaded, 16)

        @block.tensor
        def _(pe):
            pe.wait_ge(loaded, 16)
            for b in range(B):
                for kt in range(KT):
                    last = nc.tensor.matmul(c.ps[:, 0, b * E_N:(b + 1) * E_N], c.h[:, kt, b * P:(b + 1) * P],
                                            router_w[:, kt * E_N:(kt + 1) * E_N], start=(kt == 0), stop=(kt == KT - 1))
            last.then_inc(logits, 1)
            for n in range(2 * B):
                b, half = divmod(n, 2)
                if n >= 6:
                    pe.wait_ge(low, n - 5)
                for i in range(4):
                    last = nc.tensor.transpose(c.ps[:, 2 + n % 6, i * P:(i + 1) * P],
                                               c.h[:, 4 * half + i, b * P:(b + 1) * P], c.const("ident"))
                last.then_inc(turned, 1)
            pe.wait_ge(chosen_s, 1)
            for b in range(B):
                at = c.ps[:, 1, b * E_N:(b + 1) * E_N]
                for b2 in range(b + 1):
                    lhsT = c.const("before") if b2 == b else c.const("ones")
                    nc.tensor.matmul(at, lhsT, top[:, b2 * E_N:(b2 + 1) * E_N], start=(b2 == 0), stop=(b2 == b))
            for b in range(B):
                last = nc.tensor.matmul(c.ps[:, 1, B * E_N:(B + 1) * E_N], c.const("ones"),
                                        top[:, b * E_N:(b + 1) * E_N], start=(b == 0), stop=(b == B - 1))
            last.then_inc(placed, 1)

        @block.scalar
        def _(act):
            act.wait_ge(logits, 1)
            nc.scalar.activation(score, c.ps[:, 0, 0:B * E_N], ACT.Sigmoid).then_inc(sig, 1)
            for n in range(2 * B):
                b, half = divmod(n, 2)
                act.wait_ge(turned, n + 1)
                nc.scalar.activation(m.h_hi[:, b, half * S:(half + 1) * S], c.ps[:, 2 + n % 6, :], ACT.Copy
                                     ).then_inc(high, 1)

        @block.vector
        def _(dve):
            chain = Chain(dve, chain_s)
            for n in range(2 * B):
                b, half = divmod(n, 2)
                dve.wait_ge(high, n + 1)
                cols = slice(half * S, (half + 1) * S)
                nc.vector.tensor_tensor(m.h_lo[:, b, cols], c.ps[:, 2 + n % 6, :], m.h_hi[:, b, cols].bitcast(F32),
                                        ALU.subtract).then_inc(low, 1)
            dve.wait_ge(sig, 1)
            bias = c.cols2[:, C2_AT["b_router"]:C2_AT["b_router"] + E_N]
            for b in range(B):
                chain(nc.vector.tensor_tensor(sel[:, b * E_N:(b + 1) * E_N], score[:, b * E_N:(b + 1) * E_N], bias,
                                              ALU.add))
            chain(nc.vector.memset(rank, 0.0))
            for i in range(4):
                for j in range(i + 1, 4):
                    si, sj = four(sel)[:, :, i], four(sel)[:, :, j]
                    ri, rj = four(rank)[:, :, i], four(rank)[:, :, j]
                    ge = t0[:, 0:16]
                    chain(nc.vector.tensor_tensor(ge, si, sj, ALU.is_ge))
                    chain(nc.vector.tensor_tensor(rj, rj, ge, ALU.add))
                    chain(nc.vector.tensor_tensor(ri, ri, ge, ALU.subtract))
                    chain(nc.vector.tensor_scalar(ri, ri, 1.0, None, ALU.add))
            chain(nc.vector.tensor_scalar(top, rank, 1.5, None, ALU.is_lt))
            chain(nc.vector.tensor_tensor(t0, top, sel, ALU.mult))
            chain(nc.vector.tensor_reduce(gs[:, 0:16], four(t0), AXX, ALU.add))
            groups = gs[:, 0:16].rearrange("p (b g) -> p b g", g=4)
            win = t1[:, 0:16]
            wins = win.rearrange("p (b g) -> p b g", g=4)
            ge = best_in[:, 0:4]
            chain(nc.vector.memset(win, 0.0))
            for i in range(4):
                for j in range(i + 1, 4):
                    chain(nc.vector.tensor_tensor(ge, groups[:, :, i], groups[:, :, j], ALU.is_ge))
                    chain(nc.vector.tensor_tensor(wins[:, :, i], wins[:, :, i], ge, ALU.add))
                    chain(nc.vector.tensor_tensor(wins[:, :, j], wins[:, :, j], ge, ALU.subtract))
                    chain(nc.vector.tensor_scalar(wins[:, :, j], wins[:, :, j], 1.0, None, ALU.add))
            chain(nc.vector.tensor_scalar(win, win, 2.5, None, ALU.is_gt))
            for e in range(4):
                chain(nc.vector.tensor_tensor(four(top)[:, :, e], four(top)[:, :, e], win, ALU.mult))
            nc.vector.tensor_tensor(chosen, top, score, ALU.mult).then_inc(chosen_s, 1)
            dve.wait_ge(chosen_s, 1)
            by_token = lambda t: t.rearrange("p (b e) -> p b e", e=E_N)
            total = t1[:, 16:16 + B]
            chain(nc.vector.tensor_reduce(total, by_token(chosen), AXX, ALU.add))
            chain(nc.vector.reciprocal(total, total))
            for b in range(B):
                chain(nc.vector.tensor_scalar(chosen[:, b * E_N:(b + 1) * E_N], chosen[:, b * E_N:(b + 1) * E_N],
                                              total[:, b:b + 1], None, ALU.mult))
            dve.wait_ge(placed, 1)
            count, blocks, ends, base = (cnt[:, i * E_N:(i + 1) * E_N] for i in range(4))
            chain(nc.vector.tensor_copy(count, c.ps[:, 1, B * E_N:(B + 1) * E_N]))
            chain(nc.vector.tensor_scalar(blocks, count, 0.5, None, ALU.is_gt))
            for j in range(1, B):
                chain(nc.vector.tensor_scalar(t0[:, 0:E_N], count, j * P + 0.5, None, ALU.is_gt))
                chain(nc.vector.tensor_tensor(blocks, blocks, t0[:, 0:E_N], ALU.add))
            chain(nc.vector.tensor_tensor_scan(ends, c.const("ones", E_N), blocks, 0.0, ALU.mult, ALU.add))
            chain(nc.vector.tensor_tensor(base, ends, blocks, ALU.subtract))
            chain(nc.vector.tensor_scalar(base, base, float(P), None, ALU.mult))
            for b in range(B):
                at = slice(b * E_N, (b + 1) * E_N)
                chain(nc.vector.tensor_tensor(slot[:, at], c.ps[:, 1, at], base, ALU.add))
            chain(nc.vector.tensor_tensor(big, slot, top, ALU.mult))
            chain(nc.vector.tensor_reduce(m.slots[:, B:2 * B], by_token(big), AXX, ALU.max))
            chain(nc.vector.tensor_scalar(t0, top, -65536.0, 65536.0, ALU.mult, ALU.add))
            chain(nc.vector.tensor_tensor(big, big, t0, ALU.add))
            chain(nc.vector.tensor_reduce(m.slots[:, 0:B], by_token(big), AXX, ALU.min))
            for z in range(2):
                for b in range(B):
                    at = slice(b * E_N, (b + 1) * E_N)
                    chain(nc.vector.tensor_scalar(t0[:, at], slot[:, at], m.slots[:, z * B + b:z * B + b + 1], None,
                                                  ALU.is_equal))
                chain(nc.vector.tensor_tensor(t0, t0, chosen, ALU.mult))
                chain(nc.vector.tensor_reduce(m.weights[:, z * B:(z + 1) * B], by_token(t0), AXX, ALU.add))
            NB = m.MAX_BLOCKS
            cmp = wide[:, 0:NB * E_N].rearrange("p (j e) -> p j e", e=E_N)
            j_of = c.const("iota")[:, 0:NB].unsqueeze(2).to_broadcast([P, NB, E_N])
            chain(nc.vector.tensor_tensor(cmp, ends.unsqueeze(1).to_broadcast([P, NB, E_N]), j_of, ALU.is_le))
            chain(nc.vector.tensor_reduce(num[:, 0:NB], cmp, AXX, ALU.add))
            chain(nc.vector.tensor_scalar(num[:, 0:NB], num[:, 0:NB], E_N - 1.0, None, ALU.min))
            chain(nc.vector.tensor_scalar(t0[:, 0:NB // 2], c.const("iota")[:, 0:NB // 2], 2.0, ends[:, E_N - 1:E_N],
                                          ALU.mult, ALU.is_lt))
            chain(nc.vector.tensor_reduce(num[:, NB:NB + 1], t0[:, 1:NB // 2], AXX, ALU.add))
            chain(nc.vector.tensor_copy(m.numbers[:, 0:NB + 1], num[:, 0:NB + 1]))


class Experts:

    B = S // P
    MAX_BLOCKS = 24

    def __init__(self, c):
        flat = lambda t: t.rearrange("p a n -> p (a n)")
        p, h = flat(c.p[:, :, :]), flat(c.h[:, :, :])
        big = KT * DE
        self.w1 = [p[:, 0:big], c.ring[:, 0:big]]
        self.w3 = [p[:, big:2 * big], c.ring[:, big:2 * big]]
        self.w2 = [p[:, 2 * big:3 * big], flat(c.w2b[:, :, :])]
        self.h_hi = c.alias("tok_hi", "y", 0, [4, D], F32R)
        self.h_lo = c.alias("tok_lo", "vt", 0, [4, D], F32R)
        self.xg, self.xgT, self.he, self.heT, self.sil = h[:, 0:D], h[:, D:2 * D], h[:, 4 * S:5 * S], h[:, 5 * S:6 * S], h[:, 6 * S:7 * S]
        self.g1 = h[:, 7 * S:8 * S]
        tail = 2 * big
        self.g2 = c.ring[:, tail:tail + S]
        self.g = c.alias("g", "ring", tail + S, [S], F32R)
        self.gT = [c.alias(f"gT{i}", "ring", tail + (2 + i) * S, [S], F32R) for i in range(2)]
        self.o_hi = c.alias("o_hi", "ring", tail + 4 * S, [D], F32R)
        self.o_lo = c.o_lo
        self.numbers = c.numbers
        self.slots, self.weights, self.slot_w = c.small[:, 32:40], c.small[:, 40:48], c.small[:, 48:50]


def experts(c, name, gain, m):
    nc = c.nc
    B = m.B
    loaded = [[c.sem(f"{name}_{n}_loaded{i}") for n in ("w1", "w3", "w2")] for i in range(2)]
    names = ("g_part", "g_ready", "slot_w", "gathered", "g_turned", "slot_w_out", "xg_out", "gT_out", "x_turned", "xT_out",
             "up", "silu", "prod", "he_turned", "heT_out", "down", "o_hi", "o_lo", "spread", "added", "moved")
    (g_part, g_ready, slot_w, gathered, g_turned, slot_w_out, xg_out, gT_out, x_turned, xT_out, up, silu, prod, he_turned,
     heT_out, down, o_hi, o_lo, spread, added, moved) = (c.sem(f"{name}_{n}") for n in names)
    SPREAD = (2, 3, 0, 1)
    NBM = m.MAX_BLOCKS
    cols = lambda t, n: t[:, n * P:(n + 1) * P]

    def more_rounds(eng):
        return eng.value_load(m.numbers[0:1, NBM:NBM + 1], min_val=3, max_val=NBM // 2 - 1)

    def loop(eng, body):
        body(0, 0, True)
        body(1, 1, False)
        with eng.Fori(1, more_rounds(eng) + 1) as r:
            body(0, 2 * r, False)
            body(1, 2 * r + 1, False)

    with nc.Block() as block:
        @block.sync
        def _(sp):
            def load(i, j, first):
                e = sp.value_load(m.numbers[0:1, bass.ds(j, 1)] if not first else m.numbers[0:1, j:j + 1], min_val=0,
                                  max_val=E_N - 1)
                row = lambda t: c.dram[t][bass.ds(e, 1), :, :].rearrange("a p n -> p (a n)")
                if not first:
                    sp.wait_ge(up, j - 1)
                sp.dma_start(m.w1[i], row("moe_gate")).then_inc(loaded[i][0], 16)
                sp.dma_start(m.w3[i], row("moe_up")).then_inc(loaded[i][1], 16)
                if not first:
                    sp.wait_ge(down, 2 * j - 2)
                sp.dma_start(m.w2[i], row("moe_down")).then_inc(loaded[i][2], 16)

            load(0, 0, True)
            load(1, 1, True)
            with sp.Fori(1, more_rounds(sp) + 1) as r:
                load(0, 2 * r, False)
                load(1, 2 * r + 1, False)

        @block.tensor
        def _(pe):
            def gather(j, first=False, second=False):
                pe.wait_ge(g_ready, j + 1)
                if not first:
                    pe.wait_ge(slot_w_out, j)
                if not (first or second):
                    pe.wait_ge(heT_out, j - 1)
                for z, g in enumerate((m.g1, m.g2)):
                    for b in range(B):
                        last = nc.tensor.matmul(c.ps[:, 7, 0:1], cols(g, b), m.weights[:, z * B + b:z * B + b + 1],
                                                start=(z == 0 and b == 0), stop=(z == 1 and b == B - 1))
                last.then_inc(slot_w, 1)
                for half in range(2):
                    for b in range(B):
                        for n, part in enumerate((m.h_hi, m.h_lo)):
                            last = nc.tensor.matmul(c.ps[:, half, :], cols(m.g, b), part[:, b, half * S:(half + 1) * S],
                                                    start=(b == 0 and n == 0), stop=(b == B - 1 and n == 1))
                last.then_inc(gathered, 1)
                if not first:
                    pe.wait_ge(gT_out, j)
                for b in range(B):
                    last = nc.tensor.transpose(cols(c.ps[:, 6, :], b), cols(m.g, b).bitcast(F32), c.const("ident"))
                last.then_inc(g_turned, 1)

            def ups(i, j, rnd, first):
                for w in range(2):
                    pe.wait_ge(loaded[i][w], 16 * (rnd + 1))
                pe.wait_ge(xT_out, 2 * (j + 1))
                if not first:
                    pe.wait_ge(o_hi, 2 * j)
                    pe.wait_ge(o_lo, 2 * j)
                for w, weights in enumerate((m.w1[i], m.w3[i])):
                    for kt in range(KT):
                        last = nc.tensor.matmul(c.ps[:, 4 + w, :], cols(m.xgT, kt), weights[:, kt * DE:(kt + 1) * DE],
                                                start=(kt == 0), stop=(kt == KT - 1))
                last.then_inc(up, 1)

            def turn_x(j):
                pe.wait_ge(xg_out, 2 * (j + 1))
                for kt in range(KT):
                    last = nc.tensor.transpose(cols(c.ps[:, 2 + kt // 4, :], kt % 4), cols(m.xg, kt), c.const("ident"))
                last.then_inc(x_turned, 1)

            def spread_out(i, j, final=False):
                pe.wait_ge(o_hi, 2 * (j + 1))
                pe.wait_ge(o_lo, 2 * (j + 1))
                pe.wait_ge(gT_out, j + 1)
                pe.wait_ge(xT_out, 2 * (j + 2))
                if not final:
                    pe.wait_ge(xg_out, 2 * (j + 3))
                for t in range(KT):
                    if t >= len(SPREAD):
                        pe.wait_ge(added, j * KT + t - len(SPREAD) + 1)
                    bank = c.ps[:, SPREAD[t % len(SPREAD)], :]
                    nc.tensor.matmul(bank, cols(m.o_hi, t), m.gT[i][:, :], start=True, stop=False)
                    nc.tensor.matmul(bank, cols(m.o_lo, t), m.gT[i][:, :], start=False, stop=True).then_inc(spread, 1)

            def body(i, j, first, rnd):
                gather(j + 1, second=first)
                ups(i, j, rnd, first)
                if not first:
                    spread_out(1 - i, j - 1)
                pe.wait_ge(prod, j + 1)
                pe.wait_ge(slot_w_out, j + 2)
                for f in range(ET):
                    last = nc.tensor.transpose(cols(c.ps[:, 7, :], f), cols(m.he, f), c.const("ident"))
                last.then_inc(he_turned, 1)
                if not first:
                    pe.wait_ge(added, j * KT)
                turn_x(j + 1)
                pe.wait_ge(loaded[i][2], 16 * (rnd + 1))
                pe.wait_ge(heT_out, j + 1)
                for half in range(2):
                    for f in range(ET):
                        last = nc.tensor.matmul(c.ps[:, 4 + half, :], cols(m.heT, f),
                                                m.w2[i][:, f * D + half * S:f * D + (half + 1) * S], start=(f == 0),
                                                stop=(f == ET - 1))
                    last.then_inc(down, 1)

            more = more_rounds(pe)
            gather(0, True)
            turn_x(0)
            body(0, 0, True, 0)
            body(1, 1, False, 0)
            with pe.Fori(1, more + 1) as r:
                body(0, 2 * r, False, r)
                body(1, 2 * r + 1, False, r)
            spread_out(1, 2 * more + 1, final=True)

        @block.scalar
        def _(act):
            def copies(i, j, first, very_first=False):
                act.wait_ge(slot_w, j + 1)
                if not first:
                    act.wait_ge(o_lo, 2 * (j - 1))
                nc.scalar.activation(m.slot_w[:, i:i + 1], c.ps[:, 7, 0:1], ACT.Copy).then_inc(slot_w_out, 1)
                act.wait_ge(gathered, j + 1)
                if not very_first:
                    act.wait_ge(x_turned, j)
                for half in range(2):
                    nc.scalar.activation(m.xg[:, half * S:(half + 1) * S], c.ps[:, half, :], ACT.Copy
                                         ).then_inc(xg_out, 1)

            def copy_gT(i, j, first):
                act.wait_ge(g_turned, j + 1)
                if not first:
                    act.wait_ge(spread, (j - 1) * KT)
                nc.scalar.activation(m.gT[i][:, :], c.ps[:, 6, :], ACT.Copy).then_inc(gT_out, 1)

            def copy_xT(j):
                act.wait_ge(x_turned, j + 1)
                for half in range(2):
                    nc.scalar.activation(m.xgT[:, half * S:(half + 1) * S], c.ps[:, 2 + half, :], ACT.Copy
                                         ).then_inc(xT_out, 1)

            def body(i, j, first):
                copies(1 - i, j + 1, first)
                act.wait_ge(up, j + 1)
                nc.scalar.activation(m.sil, c.ps[:, 4, :], ACT.Silu).then_inc(silu, 1)
                copy_gT(1 - i, j + 1, first)
                act.wait_ge(he_turned, j + 1)
                nc.scalar.activation(m.heT, c.ps[:, 7, :], ACT.Copy).then_inc(heT_out, 1)
                copy_xT(j + 1)
                if not first:
                    act.wait_ge(spread, j * KT)
                for half in range(2):
                    act.wait_ge(down, 2 * j + half + 1)
                    nc.scalar.activation(m.o_hi[:, half * S:(half + 1) * S], c.ps[:, 4 + half, :], ACT.Copy,
                                         scale=m.slot_w[:, i:i + 1]).then_inc(o_hi, 1)

            copies(0, 0, True, True)
            copy_gT(0, 0, True)
            copy_xT(0)
            loop(act, body)

        @block.vector
        def _(dve):
            def build(j, first=False):
                if not first:
                    dve.wait_ge(g_turned, j)
                for z, g in enumerate((m.g1, m.g2)):
                    for b in range(B):
                        nc.vector.tensor_scalar(cols(g, b), c.const("iota"), m.slots[:, z * B + b:z * B + b + 1], None,
                                                ALU.is_equal).then_inc(g_part, 1)
                dve.wait_ge(g_part, 2 * B * (j + 1))
                nc.vector.tensor_scalar(m.slots, m.slots, -float(P), None, ALU.add).then_inc(moved, 1)
                nc.vector.tensor_tensor(m.g[:, :], m.g1, m.g2, ALU.add).then_inc(g_ready, 1)
                dve.wait_ge(moved, j + 1)

            def add(j):
                for t in range(KT):
                    dve.wait_ge(spread, j * KT + t + 1)
                    nc.vector.scalar_tensor_tensor(c.x[:, t, :], c.ps[:, SPREAD[t % len(SPREAD)], :], gain[:, t:t + 1],
                                                   c.x[:, t, :], ALU.mult, ALU.add).then_inc(added, 1)

            def body(i, j, first):
                build(j + 2)
                dve.wait_ge(silu, j + 1)
                if not first:
                    dve.wait_ge(he_turned, j)
                nc.vector.tensor_tensor(m.he, c.ps[:, 5, :], m.sil, ALU.mult).then_inc(prod, 1)
                if not first:
                    add(j - 1)
                for half in range(2):
                    dve.wait_ge(o_hi, 2 * j + half + 1)
                    at = slice(half * S, (half + 1) * S)
                    nc.vector.scalar_tensor_tensor(m.o_lo[:, at], c.ps[:, 4 + half, :], m.slot_w[:, i:i + 1],
                                                   m.o_hi[:, at].bitcast(F32), ALU.mult, ALU.subtract
                                                   ).then_inc(o_lo, 1)

            more = more_rounds(dve)
            build(0, True)
            build(1)
            body(0, 0, True)
            body(1, 1, False)
            with dve.Fori(1, more + 1) as r:
                body(0, 2 * r, False)
                body(1, 2 * r + 1, False)
            add(2 * more + 1)


def block_two(c, stop=None):
    nc, dram = c.nc, c.dram
    mod = lambda i: c.mod[:, i * KT:(i + 1) * KT]
    col = lambda n, k=8: c.cols2[:, C2_AT[n]:C2_AT[n] + k]
    tmp = c.ring[:, RING * D:]
    w = Gla(c)
    with c.stages():
        ctx_loaded = c.sem("ctx_loaded")
        with nc.Block() as block:
            @block.sync
            def _(sp):
                sp.dma_start(c.cols2[:, :], dram["cols2"]).then_inc(ctx_loaded, 16)
                for t in range(KT):
                    sp.dma_start(w.ctx_x[:, t, :], dram["ctxT"][t, :, :]).then_inc(ctx_loaded, 16)
                sp.wait_ge(ctx_loaded, 16 * (KT + 1))
        norm_modulate(c, "b2_norm1", c.x, c.h, col("norm1_g"), mod(1), mod(0), tmp=tmp, split=(c.a_hi, c.h_lo))
        norm_modulate(c, "b2_norm_ctx", w.ctx_x, w.ctx_h, col("norm1_g"), c.ctxmod[:, KT:2 * KT], c.ctxmod[:, 0:KT],
                      n_tok=CTX, tmp=tmp, split=(c.ctx_hi, c.ctx_lo))
        gla_project(c, w)
    if stop == "gla_in":
        return
    for head in range(4):
        with c.stages():
            gla_prepare(c, f"gla_prep{head}", w, head)
            gla_scan(c, f"gla_scan{head}", w, head)
    if stop == "gla":
        return
    moe = Experts(c)
    with c.stages():
        gla_out = SplitLinear(c, "gla_out", KT, lambda t: dram["gla_out"][bass.ds(t, 1), :, :].rearrange("a p n -> p (a n)"))
        with nc.Block() as block:
            @block.sync
            def _(sp):
                gla_out.prefetch(sp)
        split_stage(c, gla_out, c.y_lo, add_residual(c, gla_out, mod(2)), x=c.y)
        norm_modulate(c, "b2_norm2", c.x, c.h, col("norm2_g"), mod(4), mod(3), tmp=tmp)
        route(c, "route", moe)
    if stop == "route":
        return
    with c.stages():
        experts(c, "moe", mod(5), moe)
    if stop == "moe":
        return
    with c.stages():
        norm_modulate(c, "final", c.x, c.h, col("final_g"), None, None, tmp=tmp)
        stored = c.sem("out_stored")
        with nc.Block() as block:
            @block.sync
            def _(sp):
                for t in range(KT):
                    sp.dma_start(dram["out"][t, :, :], c.h[:, t, :]).then_inc(stored, 16)
                sp.wait_ge(stored, 16 * KT)


def first_adaln(c, name, which, cond, dst, width):
    nc = c.nc
    cond_load, ready = load_cond(c, name, cond)
    sums = AdaLN(c, name, which, width)
    with nc.Block() as block:
        @block.scalar
        def _(act):
            cond_load(act)
            sums.load(act)

        @block.vector
        def _(dve):
            dve.wait_ge(ready, 1)
            sums.add(dve, 0, sums.pieces)
    adaln_finish(c, name, which, dst, width)


def build(nc, dram):
    with ExitStack() as ctx:
        c = Core(nc, ctx, dram)
        with c.stages():
            load_constants(c)
            first_adaln(c, "ctx_mod", 2, 3, c.ctxmod[:, :], 2 * D)
        with c.stages():
            first_adaln(c, "mod0", 0, 0, c.mod[:, :], 6 * D)
        with nc.Fori(0, L) as layer:
            with c.stages():
                block_one_layer(c, layer)
        block_two(c)


def kernel(**inputs):
    import concourse.bacc as bacc
    from concourse.bass_utils import run_bass_kernel_spmd

    nc = bacc.Bacc("TRN2", target_bir_lowering=False, num_devices=1)
    arrays = {f"in_{n}": a for n, a in host_layout(inputs).items()}
    dram = {n[3:]: nc.dram_tensor(n, a.shape, F32, kind="ExternalInput").ap() for n, a in arrays.items()}
    dram["out"] = nc.dram_tensor("out", (KT, P, S), F32, kind="ExternalOutput").ap()
    build(nc, dram)
    r = run_bass_kernel_spmd(nc, [arrays], core_ids=[0])
    return np.ascontiguousarray(r.results[0]["out"].reshape(D, S).T).reshape(1, S, D)


def host_layout(i):
    f = np.float32
    A = {k: np.asarray(v) for k, v in i.items()}

    def tiles(w, k_tiles=None):
        K, N = w.shape
        return np.ascontiguousarray(w.reshape(K // P, P, N // P, P).transpose(2, 1, 0, 3).reshape(N // P, P, K))

    def cols(v):
        return v.reshape(-1, P).T

    out = {"xT": np.ascontiguousarray(A["x"][0].T.reshape(KT, P, S))}
    w_in = np.concatenate([A["w_in"], np.zeros((L, D, IN_T * P - A["w_in"].shape[2]), f)], axis=2)
    out["w_in"] = np.concatenate([tiles(w_in[l]) for l in range(L)])
    out["w_out"] = np.concatenate([tiles(A["w_out"][l]) for l in range(L)])
    pairs = lambda w: w.reshape(*w.shape[:-1], 2, FT, P).swapaxes(-3, -2).reshape(*w.shape)
    out["ffn_up"] = np.concatenate([tiles(pairs(A["ffn_up"][l])) for l in range(L)])
    out["ffn_down"] = np.concatenate([tiles(A["ffn_down"][l]) for l in range(L)])
    ada = lambda w: w.reshape(KT, P, 6 * D).transpose(1, 0, 2)
    out["ada"] = np.stack([ada(A["ada_w"][0]), ada(A["ada_w"][1]), ada(A["w_mod_2"][0])])
    out["ada_b"] = np.stack([cols(v) for v in (A["ada_b"][0], A["ada_b"][1], A["b_mod_2"][0])])
    out["cond"] = np.stack([cols(v) for v in (A["c"][0], A["c"][0], A["c_2"][0], A["c_ctx_2"])])

    lam_init = [0.8 - 0.6 * math.exp(-0.3 * l) for l in range(L)]
    packed = []
    for l in range(L):
        taps = np.concatenate([A["ffn_conv"][l], A["ffn_conv_b"][l][None]])
        taps = pairs(taps).reshape(4, 2 * FT, P).transpose(2, 1, 0).reshape(P, 8 * FT)
        f_b = np.zeros((P, 1), f)
        f_b[0:4, 0] = A["fx_f_b"][l]
        lam = np.concatenate([A["df_lam_q1"][l], A["df_lam_q2"][l], A["df_lam_k1"][l], A["df_lam_k2"][l]])
        part = {
            "norm1_g": cols(A["norm1_g"][l]), "norm2_g": cols(A["norm2_g"][l]), "rw_mu": cols(A["rw_mu"][l]),
            "rw_w0": cols(A["rw_w0"][l]), "rw_a0": cols(A["rw_a0"][l]), "rw_k_k": cols(A["rw_k_k"][l]),
            "rw_k_a": cols(A["rw_k_a"][l]), "rw_r_k": cols(A["rw_r_k"][l].reshape(-1)),
            "rw_ln_g": cols(A["rw_ln_g"][l]), "rw_ln_b": cols(A["rw_ln_b"][l]),
            "df_q_g": np.tile(A["df_q_g"][l], 4)[:, None], "df_k_g": np.tile(A["df_k_g"][l], 4)[:, None],
            "df_sub_g": np.tile(A["df_sub_g"][l], 2)[:, None], "sg_ln_g": cols(A["sg_ln_g"][l]),
            "sg_ln_b": cols(A["sg_ln_b"][l]), "fx_q_g": np.tile(A["fx_q_g"][l], 2)[:, None],
            "fx_k_g": np.tile(A["fx_k_g"][l], 2)[:, None], "fx_f_b": f_b,
            "lam_init": np.full((P, 1), lam_init[l], f), "lam_vec": np.tile(lam[None, :], (P, 1)),
            "ffn_tap": taps, "ffn_bias": np.zeros((P, 44), f),
        }
        packed.append(np.concatenate([part[n].astype(f, copy=False) for n, _ in COLS], axis=1))
    out["cols"] = np.stack(packed)
    out["rw_lora"] = np.concatenate([A["rw_w_up"], A["rw_a_up"], A["rw_g_up"]], axis=1)
    out["sg_wT"] = np.ascontiguousarray(A["sg_w"].transpose(0, 3, 1, 2).reshape(L, P, 4 * P))
    out["sg_b"] = A["sg_b"]
    pick = np.zeros((4, 256), f)
    for g in range(4):
        pick[g, g * 64:(g + 1) * 64] = 1.0
    out["sg_pick"] = pick
    out["const"] = constants()

    w = A["gla_w_in_2"][0]
    q, k, v, r = w[:, 0:512], w[:, 512:1024], w[:, 1024:2048], w[:, 2048:3072]
    out["gla_in"] = tiles(np.concatenate([q, r, k, v], axis=1))
    low = np.zeros((D, 64), f)
    low[:, 0:16], low[:, 32:48] = A["gla_w_gate_a_2"][0, 0], A["gla_w_gate_a_2"][0, 1]
    out["gla_low"] = np.ascontiguousarray(low.reshape(KT, P, 64).transpose(1, 0, 2).reshape(P, KT * 64))
    gb = np.zeros((P, 512), f)
    gb[0:16], gb[32:48] = A["gla_w_gate_b_2"][0, 0], A["gla_w_gate_b_2"][0, 1]
    out["gla_gb"] = gb
    out["gla_out"] = tiles(A["gla_w_out_2"][0])
    out["ctxT"] = np.ascontiguousarray(A["ctx_2"][0].T.reshape(KT, P, CTX))
    part = {"norm1_g": cols(A["norm1_g_2"][0]), "norm2_g": cols(A["norm2_g_2"][0]), "final_g": cols(A["final_g_2"]),
            "b_gate": cols(A["gla_b_gate_2"][0].reshape(-1)), "gla_norm_g": cols(A["gla_norm_g_2"][0]),
            "b_router": np.tile(A["b_router_2"][None, :], (P, 1))}
    out["cols2"] = np.concatenate([part[n] for n, _ in COLS2], axis=1)
    out["router"] = np.ascontiguousarray(A["w_router_2"].reshape(KT, P, E_N).transpose(1, 0, 2).reshape(P, KT * E_N))

    def experts(w):
        return np.ascontiguousarray(w.reshape(E_N, -1, P, w.shape[2]).transpose(0, 2, 1, 3).reshape(E_N, P, -1))

    out["moe_gate"], out["moe_up"], out["moe_down"] = (experts(A[n][0]) for n in ("w_gate_e_2", "w_up_e_2", "w_down_e_2"))
    return out


def constants():
    f = np.float32
    n = np.arange(P)
    k = {"ident": np.eye(P), "ones": np.ones((P, P)), "bo64": np.kron(np.eye(2), np.ones((64, 64))),
         "bo32": np.kron(np.eye(4), np.ones((32, 32)))}
    perm = np.zeros((P, P))
    for m in range(P):
        if m % 32 < 16:
            perm[m + 16, m] = -1.0
        else:
            perm[m - 16, m] = 1.0
    k["perm"] = perm
    inv = (1.0 / (f(10000.0) ** (np.arange(0, 32, 2, dtype=f) / f(32)))).astype(f)
    ang = (np.arange(S, dtype=f)[None, :] * inv[:, None]).astype(f)
    k["cos"], k["sin"] = np.tile(np.cos(ang), (8, 1)), np.tile(np.sin(ang), (8, 1))
    k["mask_causal"] = np.where(n[None, :] <= n[:, None], 0.0, NEG)
    k["mask_chunk"] = np.where(n[None, :] // 64 <= n[:, None] // 64, 0.0, NEG)
    k["scan"] = np.tile((np.arange(S) % CH != 0).astype(f)[None, :], (P, 1))
    r, q = n[:, None], n[None, :]
    head, block16 = r // 64 == q // 64, r // 16 == q // 16
    four = lambda m: np.tile(m.astype(f), (1, 4))
    k["m_ld"], k["m_ldT"] = four(head & block16 & (q < r)), four(head & block16 & (q > r))
    k["m_loT"], k["m_kaT"] = four(head & ~block16 & (q > r)), four(head & (q > r))
    k["m_r"] = four(q % 64 >= r % 64)
    k["ident4"] = four(r == q)
    t = np.arange(64)
    k["gla_f"] = np.tile((t[None, :] >= t[:, None]).astype(f), (2, 4))
    k["gla_b"] = np.tile((t[None, :] <= t[:, None]).astype(f), (2, 4))
    k["eps"], k["gn_eps"] = np.full((P, 1), EPS), np.full((P, 1), GN_EPS)
    k["kk_shift"] = np.full((P, 1), 0.5 * math.log(KK_SCALE))
    k["before"] = (r < q).astype(f)
    k["iota"] = np.tile(n[None, :], (P, 1))
    return np.concatenate([k[name].astype(f) for name, _ in CONST], axis=1)
```

```python
import math
from contextlib import ExitStack, contextmanager

import numpy as np
import concourse.bass as bass
from concourse import mybir

F32 = mybir.dt.float32
F32R = mybir.dt.float32r
I32 = mybir.dt.int32
ACT = mybir.ActivationFunctionType
ALU = mybir.AluOpType
AXX = mybir.AxisListType.X

P = 128
D = 1024
KT = D // P
S = 512
L = 2
NMOD = 6 * KT
FF = 2816
FT = FF // P
IN_T = 24
RING = 4
CH = 64
NCH = S // CH
E_N = 16
DE = 512
ET = DE // P
CTX = 256
LNC = CTX // CH
EPS = 1e-6
GN_EPS = 64e-5
NEG = -1e30

COLS = [("norm1_g", 8), ("norm2_g", 8), ("rw_mu", 7), ("rw_w0", 2), ("rw_a0", 2), ("rw_k_k", 2), ("rw_k_a", 2),
        ("rw_r_k", 2), ("rw_ln_g", 2), ("rw_ln_b", 2), ("df_q_g", 1), ("df_k_g", 1), ("df_sub_g", 1),
        ("sg_ln_g", 2), ("sg_ln_b", 2), ("fx_q_g", 1), ("fx_k_g", 1), ("fx_f_b", 1), ("lam_init", 1),
        ("lam_vec", 128), ("ffn_tap", 176), ("ffn_bias", 44)]
COLS2 = [("norm1_g", 8), ("norm2_g", 8), ("final_g", 8), ("b_gate", 8), ("gla_norm_g", 2), ("b_router", 16)]
CONST = [("ident", 128), ("ones", 128), ("bo64", 128), ("bo32", 128), ("perm", 128), ("cos", 512), ("sin", 512),
         ("mask_causal", 128), ("mask_chunk", 128), ("scan", 512), ("m_ld", 512), ("m_ldT", 512), ("m_loT", 512),
         ("m_kaT", 512), ("m_r", 512), ("ident4", 512), ("gla_f", 256), ("gla_b", 256), ("eps", 1), ("gn_eps", 1),
         ("kk_shift", 1), ("before", 128), ("iota", 128)]
KK_SCALE = 2.0 ** 40


def offsets(table):
    at, n = {}, 0
    for name, width in table:
        at[name] = n
        n += width
    return at, n


C_AT, C_N = offsets(COLS)
C2_AT, C2_N = offsets(COLS2)
K_AT, K_N = offsets(CONST)


class Core:

    def __init__(self, nc, ctx, dram):
        self.nc, self.ctx, self.dram = nc, ctx, dram
        self.groups = []

        self.address = {}

        def sb(name, *shape):
            t = ctx.enter_context(nc.sbuf_tensor(name, [P, *shape], F32))
            self.address[name] = nc.sbuf_base - 4 * math.prod(shape)
            return t

        self.x = sb("x", KT, S)
        self.h = sb("h", KT, S)
        self.p = sb("p", IN_T, S)
        self.y = sb("y", KT, S)
        self.ring = sb("ring", 4 * FT * P)
        self.vt = sb("vt", 4, 1024)
        self.k = sb("k", K_N)
        self.cols = sb("cols", C_N)
        self.mod = sb("mod", NMOD)
        self.w2b = sb("w2b", 4, 1024)
        self.cols2 = sb("cols2", C2_N)
        self.o_lo = ctx.enter_context(nc.sbuf_tensor("o_lo", [P, D], F32R))
        self.numbers = ctx.enter_context(nc.sbuf_tensor("numbers", [P, 32], I32))
        self.cond = sb("cond", KT)
        self.cond_ctx = sb("cond_ctx", KT)
        self.ctxmod = sb("ctxmod", 2 * KT)
        self.small = sb("small", 128)
        self.small2 = sb("small2", 256)
        self.w_hi = self.alias("w_hi", "ring", RING * D, [2, D], F32R)
        self.w_lo = self.alias("w_lo", "ring", RING * D + 2 * D, [2, D], F32R)
        self.a_hi = self.alias("a_hi", "w2b", 0, [KT, S], F32R)
        self.h_lo = self.alias("h_lo", "h", 0, [KT, S], F32R)
        self.y_lo = self.alias("y_lo", "y", 0, [KT, S], F32R)
        self.p_lo = self.alias("p_lo", "p", 0, [FT, S], F32R)
        half = FT * P // 2
        self.half_hi = self.alias("half_hi", "ring", 4 * half, [2, half], F32R)
        self.half_lo = self.alias("half_lo", "ring", 6 * half, [2, half], F32R)
        self.low_hi, self.low_lo = (self.alias(n, "ring", RING * D + (9 + i) * S, [S], F32R)
                                    for i, n in enumerate(("low_hi", "low_lo")))
        self.ctx_hi, self.ctx_lo = (self.alias(n, "y", i * 4 * S, [KT, CTX], F32R)
                                    for i, n in enumerate(("ctx_hi", "ctx_lo")))
        self.ps = ctx.enter_context(nc.psum_tensor("ps", [P, 8, 512], F32))

    def sem(self, name):
        stack, sems = self.groups[-1]
        s = stack.enter_context(self.nc.semaphore(name))
        sems.append(s)
        return s

    def alias(self, name, of, at, shape, dtype):
        return self.nc.alloc_sbuf_tensor_at(name, [P, *shape], dtype, offset=self.address[of] + 4 * at)

    @contextmanager
    def stages(self):
        with ExitStack() as stack:
            self.groups.append((stack, []))
            yield
            _, sems = self.groups.pop()
            self.clear(sems)

    def const(self, name, width=None):
        at = K_AT[name]
        return self.k[:, at:at + (width or dict(CONST)[name])]

    def col(self, name, i=0, n=1):
        at = C_AT[name] + i
        return self.cols[:, at:at + n]

    def slot(self, s, size=D):
        return self.ring[:, s * size:(s + 1) * size]

    def clear(self, sems):
        nc = self.nc
        with nc.Block() as block:
            @block.gpsimd
            def _(pool):
                for s in sems:
                    nc.gpsimd.sem_clear(s)


class Chain:

    def __init__(self, eng, sem):
        self.eng, self.sem, self.n = eng, sem, 0

    def __call__(self, ins):
        self.n += 1
        ins.then_inc(self.sem, 1)
        self.eng.wait_ge(self.sem, self.n)


def quarters(t):
    flat = t.rearrange("p a n -> p (a n)")
    return [flat[:, i * D:(i + 1) * D] for i in range(4)]


class AdaLN:

    def __init__(self, c, name, which, first, count, piece, sums):
        self.c, self.which, self.first, self.count = c, which, first, count
        self.piece, self.sums = piece, sums
        self.pieces = KT * count
        self.loaded = [c.sem(f"{name}_piece_loaded{i}") for i in range(len(piece))]
        self.used, self.bias = c.sem(f"{name}_piece_used"), c.sem(f"{name}_bias_loaded")

    def load(self, queue, n, kt=None):
        B, M = len(self.piece), len(self.sums)
        if kt is None:
            kt, j, b = n // self.count, n % self.count, n % B
        else:
            j = b = n
            n = kt * self.count + j
        if not isinstance(n, int) or n >= B:
            queue.wait_ge(self.used, (n - B + 1) * M)
        src = self.c.dram["ada"][bass.ds(self.which, 1), :, bass.ds(kt, 1),
                                 (self.first + j) * D:(self.first + j + 1) * D]
        queue.dma_start(self.piece[b], src.rearrange("a p k n -> p (a k n)")).then_inc(self.loaded[b], 16)

    def load_bias(self, queue, dsts):
        src = self.c.dram["ada_b"][bass.ds(self.which, 1), :, self.first * KT:(self.first + self.count) * KT]
        for dst in dsts:
            queue.dma_start(dst, src.rearrange("a p n -> p (a n)")).then_inc(self.bias, 16)
        self.dsts = dsts

    def add(self, dve, n, kt=None):
        nc = self.c.nc
        B, M = len(self.piece), len(self.sums)
        if kt is None:
            kt, j, b, turn = n // self.count, n % self.count, n % B, n // B
        else:
            j = b = n
            n, turn = kt * self.count + j, kt
        dve.wait_ge(self.loaded[b], (turn + 1) * 16)
        for m, (cond, acc) in enumerate(self.sums):
            out, factor = acc[j], cond[:, bass.ds(kt, 1)]
            if isinstance(kt, int) and kt == 0:
                ins = nc.vector.tensor_scalar(out, self.piece[b], factor, None, ALU.mult)
            else:
                dve.wait_ge(self.used, (n - self.count) * M + m + 1)
                ins = nc.vector.scalar_tensor_tensor(out, self.piece[b], factor, out, ALU.mult, ALU.add)
            ins.then_inc(self.used, 1)


class AdaLNPool(AdaLN):

    def __init__(self, *args, product):
        super().__init__(*args)
        self.product, self.multiplied = product, self.c.sem("ada_pool_multiplied")

    def add_pool(self, pool, n):
        nc = self.c.nc
        B = len(self.piece)
        (cond, acc), = self.sums
        kt, j = divmod(n, self.count)
        pool.wait_ge(self.loaded[n % B], 16 * (n // B + 1))
        if kt == 0:
            nc.gpsimd.tensor_scalar(acc[j], self.piece[n % B], cond[:, kt:kt + 1], None, ALU.mult
                                    ).then_inc(self.used, 1)
            return
        at = n - self.count + 1
        pool.wait_ge(self.used, n)
        nc.gpsimd.tensor_scalar(self.product, self.piece[n % B], cond[:, kt:kt + 1], None, ALU.mult
                                ).then_inc(self.multiplied, 1)
        pool.wait_ge(self.multiplied, at)
        nc.gpsimd.tensor_tensor(acc[j], self.product, acc[j], ALU.add).then_inc(self.used, 1)


def load_cond(c, name, which, dst=None):
    nc, dram = c.nc, c.dram
    loaded, ready = c.sem(f"{name}_cond_loaded"), c.sem(f"{name}_cond_ready")
    dst = c.cond[:, :] if dst is None else dst

    def scalar(act):
        act.dma_start(c.small[:, 0:KT], dram["cond"][bass.ds(which, 1), :, :].rearrange("a p n -> p (a n)")
                      ).then_inc(loaded, 16)
        act.wait_ge(loaded, 16)
        nc.scalar.activation(dst, c.small[:, 0:KT], ACT.Silu).then_inc(ready, 1)

    return scalar, ready


def adaln_finish_parts(c, name, ada, bank=0):
    nc = c.nc
    summed = c.sem(f"{name}_summed")
    ada.biased = c.sem(f"{name}_biased")
    n = ada.count * KT

    def sums(pe):
        for m, (_, acc) in enumerate(ada.sums):
            for t in range(n):
                last = nc.tensor.matmul(c.ps[:, bank + m, t:t + 1], acc[t // KT][:, t % KT * P:(t % KT + 1) * P],
                                        c.const("ones", 1), start=True, stop=True)
        last.then_inc(summed, 1)

    def bias(dve):
        dve.wait_ge(ada.bias, 16 * len(ada.dsts))
        dve.wait_ge(summed, 1)
        for m, dst in enumerate(ada.dsts):
            nc.vector.tensor_tensor(dst, c.ps[:, bank + m, 0:n], dst, ALU.add).then_inc(ada.biased, 1)
        dve.wait_ge(ada.biased, len(ada.dsts))

    return sums, bias


def adaln_finish(c, name, ada):
    sums, bias = adaln_finish_parts(c, name, ada)
    with c.nc.Block() as block:
        @block.tensor
        def _(pe):
            sums(pe)

        @block.vector
        def _(dve):
            bias(dve)


def norm_modulate(c, name, x, h, gain, scale, shift, n_tok=S, extra_act=None, tmp=None, split=None,
                  loads=None, gain_loaded=None):
    nc = c.nc
    squared, summed, rs_ready = c.sem(f"{name}_squared"), c.sem(f"{name}_summed"), c.sem(f"{name}_rs")
    a_ready, scaled, done = c.sem(f"{name}_a"), c.sem(f"{name}_scaled"), c.sem(f"{name}_done")
    rs = tmp[:, 0:n_tok]
    a = c.small[:, 16:24]
    with nc.Block() as block:
        if loads is not None:
            @block.sync
            def _(sp):
                loads(sp)

        @block.tensor
        def _(pe):
            for t in range(KT):
                pe.wait_ge(squared, t + 1)
                last = nc.tensor.matmul(c.ps[:, 0, 0:n_tok], c.const("ones"), h[:, t, :], start=(t == 0),
                                        stop=(t == KT - 1))
            last.then_inc(summed, 1)

        @block.scalar
        def _(act):
            for t in range(KT):
                nc.scalar.activation(h[:, t, :], x[:, t, :], ACT.Square).then_inc(squared, 1)
            act.wait_ge(summed, 1)
            nc.scalar.activation(rs, c.ps[:, 0, 0:n_tok], ACT.Ln, bias=c.const("eps"), scale=1.0 / D
                                 ).then_inc(rs_ready, 1)
            act.wait_ge(rs_ready, 1)
            nc.scalar.activation(rs, rs, ACT.Exp, scale=-0.5).then_inc(rs_ready, 1)
            for t in range(KT):
                if shift is not None:
                    act.wait_ge(scaled, t + 1)
                    out = h if split is None else split[0]
                    nc.scalar.activation(out[:, t, :], h[:, t, :], ACT.Identity, bias=shift[:, t:t + 1]
                                         ).then_inc(done, 1)
            if extra_act is not None:
                extra_act(act)

        @block.vector
        def _(dve):
            if gain_loaded is not None:
                dve.wait_ge(gain_loaded, 16)
            if scale is not None:
                nc.vector.tensor_scalar(a, scale, 1.0, None, ALU.add).then_inc(a_ready, 1)
                dve.wait_ge(a_ready, 1)
                nc.vector.tensor_tensor(a, a, gain, ALU.mult).then_inc(a_ready, 1)
                dve.wait_ge(a_ready, 2)
            g = a if scale is not None else gain

            def low(t):
                hi, lo = split
                dve.wait_ge(done, t + 1)
                nc.vector.scalar_tensor_tensor(lo[:, t, :], h[:, t, :], shift[:, t:t + 1], hi[:, t, :].bitcast(F32),
                                               ALU.add, ALU.subtract)

            dve.wait_ge(rs_ready, 2)
            for t in range(KT):
                nc.vector.scalar_tensor_tensor(h[:, t, :], x[:, t, :], g[:, t:t + 1], rs, ALU.mult, ALU.mult
                                               ).then_inc(scaled, 1)
                if split is not None and t >= 2:
                    low(t - 2)
            if split is not None:
                low(KT - 2)
                low(KT - 1)


class Linear:

    def __init__(self, c, name, n_tiles, weights, k_tiles=KT, size=D):
        self.c, self.n, self.weights, self.kt, self.size = c, n_tiles, weights, k_tiles, size
        assert n_tiles % RING == 0
        self.loaded = [c.sem(f"{name}_w_loaded{s}") for s in range(RING)]
        self.multiplied = c.sem(f"{name}_multiplied")
        self.emptied = c.sem(f"{name}_bank_emptied")

    def prefetch(self, sp):
        for s in range(RING):
            sp.dma_start(self.c.slot(s, self.size), self.weights(s)).then_inc(self.loaded[s], 16)

    def load(self, sp):
        with sp.Fori(1, self.n // RING) as g:
            for s in range(RING):
                sp.wait_ge(self.multiplied, (g - 1) * RING + s + 1)
                sp.dma_start(self.c.slot(s, self.size), self.weights(g * RING + s)).then_inc(self.loaded[s], 16)

    def multiply(self, pe, rhs):
        nc, c = self.c.nc, self.c

        def tile(s, g):
            pe.wait_ge(self.loaded[s], 16 * (g + 1))
            w = c.slot(s, self.size)
            for kt in range(self.kt):
                last = nc.tensor.matmul(c.ps[:, s, :], w[:, kt * P:(kt + 1) * P], rhs(kt), start=(kt == 0),
                                        stop=(kt == self.kt - 1))
            last.then_inc(self.multiplied, 1)

        for s in range(RING):
            tile(s, 0)
        with pe.Fori(1, self.n // RING) as g:
            for s in range(RING):
                pe.wait_ge(self.emptied, (g - 1) * RING + s + 1)
                tile(s, g)


class SplitLinear(Linear):

    def __init__(self, c, name, n_tiles, weights):
        super().__init__(c, name, n_tiles, weights)
        self.high, self.low = c.sem(f"{name}_w_high"), c.sem(f"{name}_w_low")

    def load(self, sp):
        with sp.Fori(1, self.n // RING) as g:
            for s in range(RING):
                self.load_one(sp, s, g)

    def load_one(self, sp, s, g):
        sp.wait_ge(self.low, (g - 1) * RING + s + 1)
        sp.dma_start(self.c.slot(s), self.weights(g * RING + s)).then_inc(self.loaded[s], 16)

    def split_high(self, act, s, g, first=False):
        act.wait_ge(self.loaded[s], 16 * (g + 1))
        if not first:
            act.wait_ge(self.multiplied, g * RING + s - 1)
        self.c.nc.scalar.activation(self.c.w_hi[:, s % 2, :], self.c.slot(s), ACT.Copy).then_inc(self.high, 1)

    def split_low(self, dve, s, g, first=False):
        dve.wait_ge(self.high, g * RING + s + 1)
        self.c.nc.vector.tensor_tensor(self.c.w_lo[:, s % 2, :], self.c.slot(s), self.c.w_hi[:, s % 2, :].bitcast(F32),
                                       ALU.subtract).then_inc(self.low, 1)

    def tiles(self, eng, split, work, first=None):
        rounds = self.n // RING

        def one(s, g, work, last=False):
            if not (last and s + 2 >= RING):
                split(eng, (s + 2) % RING, g + (s + 2) // RING)
            work(s, g)

        for s in range(RING):
            one(s, 0, first or work)
        if rounds > 2:
            with eng.Fori(1, rounds - 1) as g:
                for s in range(RING):
                    one(s, g, work)
        for s in range(RING):
            one(s, rounds - 1, work, last=True)

    def products(self, s, bank, rhs, last=True):
        c, nc = self.c, self.c.nc
        hi, lo = rhs
        for kt in range(KT):
            at = slice(kt * P, (kt + 1) * P)
            nc.tensor.matmul(bank, c.w_hi[:, s % 2, at], hi(kt), start=(kt == 0), stop=False)
            nc.tensor.matmul(bank, c.w_hi[:, s % 2, at], lo(kt), start=False, stop=False)
            ins = nc.tensor.matmul(bank, c.w_lo[:, s % 2, at], hi(kt), start=False, stop=(kt == KT - 1))
        return ins

    def multiply(self, pe, rhs, ready=None):
        c = self.c

        def tile(s, g):
            pe.wait_ge(self.low, g * RING + s + 1)
            self.products(s, c.ps[:, s, :], rhs).then_inc(self.multiplied, 1)

        for s in range(RING):
            tile(s, 0)
        with pe.Fori(1, self.n // RING) as g:
            for s in range(RING):
                pe.wait_ge(self.emptied, (g - 1) * RING + s + 1)
                tile(s, g)


def split_stage(c, lin, lo, out, prefetch=None, x=None, load=None, dve_work=None):
    nc = c.nc
    engine, work = out
    if x is not None:
        x_high, x_low = c.sem("x_high"), c.sem("x_low")
    nothing = lambda s, g: None
    with nc.Block() as block:
        @block.sync
        def _(sp):
            (load or lin.load)(sp)
            if prefetch is not None:
                sp.wait_ge(lin.multiplied, lin.n)
                prefetch(sp)

        @block.tensor
        def _(pe):
            if x is not None:
                pe.wait_ge(x_low, KT)
            lin.multiply(pe, (lambda kt: c.a_hi[:, kt, :], lambda kt: lo[:, kt, :]))

        @block.scalar
        def _(act):
            lin.split_high(act, 0, 0, first=True)
            if x is not None:
                for t in range(KT):
                    nc.scalar.activation(c.a_hi[:, t, :], x[:, t, :], ACT.Copy).then_inc(x_high, 1)
            lin.split_high(act, 1, 0, first=True)
            lin.tiles(act, lin.split_high, work(act) if engine == "scalar" else nothing)

        @block.vector
        def _(dve):
            lin.split_low(dve, 0, 0)
            if x is not None:
                for t in range(KT):
                    dve.wait_ge(x_high, t + 1)
                    nc.vector.tensor_tensor(lo[:, t, :], x[:, t, :], c.a_hi[:, t, :].bitcast(F32), ALU.subtract
                                            ).then_inc(x_low, 1)
            lin.split_low(dve, 1, 0)
            lin.tiles(dve, lin.split_low, work(dve) if engine == "vector" else dve_work(dve) if dve_work else nothing)


def copy_out(c, lin, dst):
    def of(act):
        def work(s, g):
            act.wait_ge(lin.multiplied, g * RING + s + 1)
            out = dst(g * RING + s)
            c.nc.scalar.activation(out, c.ps[:, s, :], ACT.Copy).then_inc(lin.emptied, 1)
        return work
    return "scalar", of


def add_residual(c, lin, gate):
    return "vector", lambda dve: lambda s, g: residual_tiles(c, lin, dve, gate, g * RING + s, g * RING + s + 1)


def copy_out_tiles(c, lin, act, dst):
    nc = c.nc
    with act.Fori(0, lin.n // RING) as g:
        for s in range(RING):
            act.wait_ge(lin.multiplied, g * RING + s + 1)
            out = dst[:, bass.ds(g * RING + s, 1), :].rearrange("p a n -> p (a n)")
            nc.scalar.activation(out, c.ps[:, s, :], ACT.Copy).then_inc(lin.emptied, 1)


def residual_tiles(c, lin, dve, gate, first=0, last=KT):
    nc = c.nc
    for t in range(first, last):
        dve.wait_ge(lin.multiplied, t + 1)
        nc.vector.scalar_tensor_tensor(c.x[:, t, :], c.ps[:, t % RING, :], gate[:, t:t + 1], c.x[:, t, :], ALU.mult,
                                       ALU.add).then_inc(lin.emptied, 1)


def after(steps, n):
    return sum(s <= n for s in steps)


T_A, T_B, T_C, T_D = 0, 7, 13, 17
V_B, V_D, V_C = 0, 256, 512
Y_A, Y_B, Y_C, Y_D = 0, 2, 4, 6


def scratch(c, i, n=1):
    at = RING * D + i * S
    return c.ring[:, at:at + n * S]


def prepare_attentions(c, name, prefetch, sums):
    nc = c.nc
    blocks, blocks_out = c.sem(f"{name}_v_transposed"), c.sem(f"{name}_v_copied")
    squared, summed = c.sem(f"{name}_squared"), c.sem(f"{name}_summed")
    rs_step, rs_ready, normed = c.sem(f"{name}_rs_step"), c.sem(f"{name}_rs_ready"), c.sem(f"{name}_normed")
    gains = c.sem(f"{name}_gains")
    rotated, roped = c.sem(f"{name}_rotated"), c.sem(f"{name}_roped")
    f_in, f_exp, f_dve, f_ready, f_moved = (c.sem(f"{name}_f_{n}") for n in ("in", "exp", "dve", "ready", "moved"))
    f_one = c.sem(f"{name}_f_one")

    qb, qd = c.small[:, 24:25], c.small[:, 25:26]
    jobs = [(T_B + 0, "bo32", 32, qb), (T_B + 1, "bo32", 32, qb), (T_B + 2, "bo32", 32, c.col("df_k_g")),
            (T_B + 3, "bo32", 32, c.col("df_k_g")), (T_D + 0, "bo64", 64, qd), (T_D + 1, "bo64", 64, qd),
            (T_D + 2, "bo64", 64, c.col("fx_k_g")), (T_D + 3, "bo64", 64, c.col("fx_k_g"))]
    values = [(T_B + 4, V_B), (T_B + 5, V_B + P), (T_D + 4, V_D), (T_D + 5, V_D + P)]
    sq = [scratch(c, i) for i in range(2)]
    rs = [scratch(c, 6 + i) for i in range(8)]
    turn = scratch(c, 2)
    f_gate, f_abs, f_neg = (scratch(c, 3 + i)[0:4, :] for i in range(3))
    finish_sums, finish_bias = adaln_finish_parts(c, "mod", sums, bank=2)

    with nc.Block() as block:
        @block.sync
        def _(sp):
            prefetch(sp)
            sp.wait_ge(f_ready, 2)
            sp.wait_ge(f_one, 2)
            for h in range(4):
                sp.dma_start(c.h[1:2, h, :], f_gate[h:h + 1, :]).then_inc(f_moved, 16)
                sp.dma_start(c.h[0:1, 4 + h, :], f_neg[h:h + 1, :]).then_inc(f_moved, 16)
            sp.wait_ge(f_moved, 16 * 8)

        @block.gpsimd
        def _(pool):
            nc.gpsimd.memset(c.h[0:2, 0:4, :], 1.0).then_inc(f_one, 1)
            nc.gpsimd.memset(c.h[0:2, 4:8, :], 1.0).then_inc(f_one, 1)

        @block.tensor
        def _(pe):
            for j, (tile, _) in enumerate(values):
                for b in range(4):
                    last = nc.tensor.transpose(c.ps[:, 4 + j, b * P:(b + 1) * P], c.p[:, tile, b * P:(b + 1) * P],
                                               c.const("ident"))
                last.then_inc(blocks, 1)
            for j, (_, ones, _, _) in enumerate(jobs):
                pe.wait_ge(squared, j + 1)
                if j >= 2:
                    pe.wait_ge(rs_step, j - 1)
                nc.tensor.matmul(c.ps[:, j % 2, :], c.const(ones), sq[j % 2], start=True, stop=True
                                 ).then_inc(summed, 1)
            finish_sums(pe)
            for j in range(4):
                if j == 0:
                    pe.wait_ge(sums.biased, 1)
                pe.wait_ge(normed, j + 1)
                if j >= 2:
                    pe.wait_ge(roped, 3 * (j - 2) + 1)
                nc.tensor.matmul(c.ps[:, 2 + j % 2, :], c.const("perm"), c.p[:, T_B + j, :], start=True, stop=True
                                 ).then_inc(rotated, 1)

        @block.scalar
        def _(act):
            nc.scalar.activation(f_gate, c.p[0:4, IN_T - 1, :], ACT.Identity, bias=c.col("fx_f_b")[0:4, :]
                                 ).then_inc(f_in, 1)
            act.wait_ge(f_in, 1)
            nc.scalar.activation(f_abs, f_gate, ACT.Abs).then_inc(f_in, 1)
            act.wait_ge(f_in, 2)
            nc.scalar.activation(f_abs, f_abs, ACT.Exp, scale=-1.0).then_inc(f_in, 1)
            act.wait_ge(f_in, 3)
            nc.scalar.activation(f_abs, f_abs, ACT.Ln, bias=1.0).then_inc(f_exp, 1)
            for j, (_, off) in enumerate(values):
                act.wait_ge(blocks, j + 1)
                nc.scalar.activation(c.vt[:, :, off:off + P], c.ps[:, 4 + j, :].rearrange("p (b n) -> p b n", b=4),
                                     ACT.Copy).then_inc(blocks_out, 1)

            def square(j):
                if j >= 2:
                    act.wait_ge(summed, j - 1)
                nc.scalar.activation(sq[j % 2], c.p[:, jobs[j][0], :], ACT.Square).then_inc(squared, 1)

            square(0)
            for j, (_, _, n, _) in enumerate(jobs):
                if j + 1 < len(jobs):
                    square(j + 1)
                act.wait_ge(summed, j + 1)
                nc.scalar.activation(rs[j], c.ps[:, j % 2, :], ACT.Ln, bias=c.const("eps"), scale=1.0 / n
                                     ).then_inc(rs_step, 1)
            for j in range(len(jobs)):
                act.wait_ge(rs_step, j + 1)
                nc.scalar.activation(rs[j], rs[j], ACT.Exp, scale=-0.5).then_inc(rs_ready, 1)
            act.wait_ge(blocks_out, 4)

        @block.vector
        def _(dve):
            nc.vector.tensor_scalar(qb, c.col("df_q_g"), 32 ** -0.5, None, ALU.mult).then_inc(gains, 1)
            nc.vector.tensor_scalar(qd, c.col("fx_q_g"), 64 ** -0.5, None, ALU.mult).then_inc(gains, 1)
            dve.wait_ge(f_exp, 1)
            nc.vector.scalar_tensor_tensor(f_gate, f_gate, 0.0, f_abs, ALU.min, ALU.subtract).then_inc(f_dve, 1)
            dve.wait_ge(f_dve, 1)
            nc.vector.tensor_tensor_scan(f_abs, c.const("ones", 1)[0:4, :].to_broadcast([4, S]), f_gate, 0.0, ALU.mult,
                                         ALU.add).then_inc(f_dve, 1)
            dve.wait_ge(f_dve, 2)
            nc.vector.tensor_copy(f_gate, f_abs).then_inc(f_ready, 1)
            nc.vector.tensor_scalar(f_neg, f_abs, -1.0, None, ALU.mult).then_inc(f_ready, 1)
            dve.wait_ge(gains, 2)
            for j, (tile, _, _, gain) in enumerate(jobs):
                dve.wait_ge(rs_ready, j + 1)
                nc.vector.scalar_tensor_tensor(c.p[:, tile, :], c.p[:, tile, :], gain, rs[j], ALU.mult, ALU.mult
                                               ).then_inc(normed, 1)
                if j == 0:
                    finish_bias(dve)
            for j in range(4):
                q = c.p[:, T_B + j, :]
                dve.wait_ge(rotated, j + 1)
                if j >= 1:
                    dve.wait_ge(roped, 3 * j)
                nc.vector.tensor_tensor(turn, c.ps[:, 2 + j % 2, :], c.const("sin"), ALU.mult).then_inc(roped, 1)
                nc.vector.tensor_tensor(q, q, c.const("cos"), ALU.mult).then_inc(roped, 1)
                dve.wait_ge(roped, 3 * j + 2)
                nc.vector.tensor_tensor(q, q, turn, ALU.add).then_inc(roped, 1)
            dve.wait_ge(roped, 12)


def attention_forget(c, name):
    nc = c.nc
    scored, masked, maxed = c.sem(f"{name}_scored"), c.sem(f"{name}_masked"), c.sem(f"{name}_maxed")
    exped, inv, scaled = c.sem(f"{name}_exped"), c.sem(f"{name}_inv"), c.sem(f"{name}_scaled")
    turned, copied, summed = c.sem(f"{name}_turned"), c.sem(f"{name}_copied"), c.sem(f"{name}_summed")
    out = c.sem(f"{name}_out")
    units = [(h, i) for h in range(4) for i in range(4)]
    NU = len(units)
    prob = [scratch(c, i) for i in range(3)]
    prob_t = [scratch(c, 3 + i) for i in range(2)]
    nmax, rsum = c.small[:, 32:48], c.small[:, 48:64]

    def rows(h):
        return slice(64 * (h % 2), 64 * (h % 2) + 64)

    with nc.Block() as block:
        @block.tensor
        def _(pe):
            def score(u):
                h, i = units[u]
                nk = (i + 1) * P
                if u >= 2:
                    pe.wait_ge(exped, u - 1)
                bank = c.ps[:, u % 2, 0:nk]
                nc.tensor.matmul(bank, c.p[rows(h), T_D + h // 2, i * P:(i + 1) * P],
                                 c.p[rows(h), T_D + 2 + h // 2, 0:nk], start=True, stop=False)
                nc.tensor.matmul(bank, c.h[0:2, h, i * P:(i + 1) * P], c.h[0:2, 4 + h, 0:nk], start=False, stop=True
                                 ).then_inc(scored, 1)

            def turn(u):
                _, i = units[u]
                pe.wait_ge(scaled, u + 1)
                if u >= 2:
                    pe.wait_ge(copied, u - 1)
                for b in range(i + 1):
                    last = nc.tensor.transpose(c.ps[:, 2 + u % 2, b * P:(b + 1) * P],
                                               prob[u % 3][:, b * P:(b + 1) * P], c.const("ident"))
                last.then_inc(turned, 1)

            def sum_values(u):
                h, i = units[u]
                pe.wait_ge(copied, u + 1)
                for b in range(i + 1):
                    v = c.vt[:, b, V_D + 64 * h:V_D + 64 * h + 64]
                    last = nc.tensor.matmul(c.ps[rows(h), 4 + h // 2, i * P:(i + 1) * P], v,
                                            prob_t[u % 2][:, b * P:(b + 1) * P], start=(b == 0), stop=(b == i))
                last.then_inc(summed, 1)

            score(0)
            score(1)
            for u in range(NU):
                turn(u)
                if u + 2 < NU:
                    score(u + 2)
                if u >= 1:
                    sum_values(u - 1)
            sum_values(NU - 1)

        @block.scalar
        def _(act):
            def exp(u):
                nk = (units[u][1] + 1) * P
                act.wait_ge(maxed, u + 1)
                if u >= 3:
                    act.wait_ge(turned, u - 2)
                nc.scalar.activation(prob[u % 3][:, 0:nk], c.ps[:, u % 2, 0:nk], ACT.Exp, bias=nmax[:, u:u + 1],
                                     accum_out=rsum[:, u:u + 1]).then_inc(exped, 1)

            def copy(u):
                nk = (units[u][1] + 1) * P
                act.wait_ge(turned, u + 1)
                if u >= 2:
                    act.wait_ge(summed, u - 1)
                nc.scalar.activation(prob_t[u % 2][:, 0:nk], c.ps[:, 2 + u % 2, 0:nk], ACT.Copy).then_inc(copied, 1)

            exp(0)
            for u in range(NU):
                if u + 1 < NU:
                    exp(u + 1)
                copy(u)
            for t in range(2):
                act.wait_ge(summed, 8 * (t + 1))
                nc.scalar.activation(c.y[:, Y_D + t, :], c.ps[:, 4 + t, :], ACT.Copy).then_inc(out, 1)

        @block.vector
        def _(dve):
            def maximum(u):
                i = units[u][1]
                dve.wait_ge(scored, u + 1)
                diagonal = c.ps[:, u % 2, i * P:(i + 1) * P]
                nc.vector.tensor_tensor(diagonal, diagonal, c.const("mask_causal"), ALU.add).then_inc(masked, 1)
                dve.wait_ge(masked, u + 1)
                nc.vector.tensor_reduce(nmax[:, u:u + 1], c.ps[:, u % 2, 0:(i + 1) * P], AXX, ALU.max, negate=True
                                        ).then_inc(maxed, 1)

            def normalise(u):
                nk = (units[u][1] + 1) * P
                dve.wait_ge(exped, u + 1)
                nc.vector.reciprocal(rsum[:, u:u + 1], rsum[:, u:u + 1]).then_inc(inv, 1)
                dve.wait_ge(inv, u + 1)
                nc.vector.tensor_scalar(prob[u % 3][:, 0:nk], prob[u % 3][:, 0:nk], rsum[:, u:u + 1], None, ALU.mult
                                        ).then_inc(scaled, 1)

            maximum(0)
            for u in range(NU):
                if u + 1 < NU:
                    maximum(u + 1)
                normalise(u)


def attention_diff(c, name):
    nc = c.nc
    lam_dve, lam_exp, lam_ready = c.sem(f"{name}_lam_dve"), c.sem(f"{name}_lam_exp"), c.sem(f"{name}_lam_ready")
    scored, masked, maxed = c.sem(f"{name}_scored"), c.sem(f"{name}_masked"), c.sem(f"{name}_maxed")
    exped, inv, mixed = c.sem(f"{name}_exped"), c.sem(f"{name}_inv"), c.sem(f"{name}_mixed")
    turned, copied, summed = c.sem(f"{name}_turned"), c.sem(f"{name}_copied"), c.sem(f"{name}_summed")
    squared, ms, rs_ready, out = (c.sem(f"{name}_{n}") for n in ("squared", "ms", "rs_ready", "out"))
    units = [(h, i) for h in range(4) for i in range(4)]
    NU = len(units)
    prob = [[scratch(c, 2 * i + m) for m in range(2)] for i in range(2)]
    prob_t = [scratch(c, 4 + i) for i in range(2)]
    o, sq, rs = [scratch(c, 6), scratch(c, 7)], [scratch(c, 8), scratch(c, 9)], [scratch(c, 0), scratch(c, 1)]
    nmax, rsum = c.small[:, 32:64], c.small[:, 64:96]
    lam_prod = c.cols[:, C_AT["lam_vec"]:C_AT["lam_vec"] + 64].rearrange("p (m n) -> p m n", m=2)
    lam_other = c.cols[:, C_AT["lam_vec"] + 64:C_AT["lam_vec"] + 128].rearrange("p (m n) -> p m n", m=2)
    lam2, nlam, sub_gain = c.small[:, 26:28], c.small[:, 28:29], c.small[:, 29:30]

    with nc.Block() as block:
        @block.tensor
        def _(pe):
            def score(u):
                h, i = units[u]
                nk = (i + 1) * P
                for m in range(2):
                    lane = 32 * ((2 * h + m) % 4)
                    if u >= 2:
                        pe.wait_ge(exped, 2 * (u - 2) + m + 1)
                    nc.tensor.matmul(c.ps[:, 2 * (u % 2) + m, 0:nk], c.p[lane:lane + 32, T_B + h // 2, i * P:(i + 1) * P],
                                     c.p[lane:lane + 32, T_B + 2 + h // 2, 0:nk], start=True, stop=True,
                                     tile_position=(lane, 0)).then_inc(scored, 1)

            def turn(u):
                _, i = units[u]
                pe.wait_ge(mixed, u + 1)
                if u >= 2:
                    pe.wait_ge(copied, u - 1)
                for b in range(i + 1):
                    last = nc.tensor.transpose(c.ps[:, 4 + u % 2, b * P:(b + 1) * P],
                                               prob[u % 2][0][:, b * P:(b + 1) * P], c.const("ident"))
                last.then_inc(turned, 1)

            def sum_values(u):
                h, i = units[u]
                r = slice(64 * (h % 2), 64 * (h % 2) + 64)
                pe.wait_ge(copied, u + 1)
                for b in range(i + 1):
                    v = c.vt[:, b, V_B + 64 * h:V_B + 64 * h + 64]
                    last = nc.tensor.matmul(c.ps[r, 6 + h // 2, i * P:(i + 1) * P], v,
                                            prob_t[u % 2][:, b * P:(b + 1) * P], start=(b == 0), stop=(b == i))
                last.then_inc(summed, 1)

            score(0)
            score(1)
            for u in range(NU):
                turn(u)
                if u + 2 < NU:
                    score(u + 2)
                if u >= 1:
                    sum_values(u - 1)
            sum_values(NU - 1)
            for t in range(2):
                pe.wait_ge(squared, 2 * t + 2)
                nc.tensor.matmul(c.ps[:, t, :], c.const("bo64"), sq[t], start=True, stop=True).then_inc(ms, 1)

        @block.scalar
        def _(act):
            def exp(u):
                nk = (units[u][1] + 1) * P
                for m in range(2):
                    n = 2 * u + m
                    act.wait_ge(maxed, n + 1)
                    if u >= 2:
                        act.wait_ge(turned, u - 1)
                    nc.scalar.activation(prob[u % 2][m][:, 0:nk], c.ps[:, 2 * (u % 2) + m, 0:nk], ACT.Exp,
                                         bias=nmax[:, n:n + 1], accum_out=rsum[:, n:n + 1]).then_inc(exped, 1)

            def copy(u):
                nk = (units[u][1] + 1) * P
                act.wait_ge(turned, u + 1)
                if u >= 2:
                    act.wait_ge(summed, u - 1)
                nc.scalar.activation(prob_t[u % 2][:, 0:nk], c.ps[:, 4 + u % 2, 0:nk], ACT.Copy).then_inc(copied, 1)

            act.wait_ge(lam_dve, 2)
            nc.scalar.activation(lam2, lam2, ACT.Exp).then_inc(lam_exp, 1)
            exp(0)
            for u in range(NU):
                if u + 1 < NU:
                    exp(u + 1)
                copy(u)
            for t in range(2):
                act.wait_ge(summed, 8 * (t + 1))
                nc.scalar.activation(o[t], c.ps[:, 6 + t, :], ACT.Copy).then_inc(squared, 1)
                nc.scalar.activation(sq[t], c.ps[:, 6 + t, :], ACT.Square).then_inc(squared, 1)
            for t in range(2):
                act.wait_ge(ms, t + 1)
                nc.scalar.activation(rs[t], c.ps[:, t, :], ACT.Ln, bias=c.const("eps"), scale=1.0 / 64
                                     ).then_inc(rs_ready, 1)
                act.wait_ge(rs_ready, 2 * t + 1)
                nc.scalar.activation(rs[t], rs[t], ACT.Exp, scale=-0.5).then_inc(rs_ready, 1)

        @block.vector
        def _(dve):
            nc.vector.tensor_tensor(lam_prod, lam_prod, lam_other, ALU.mult).then_inc(lam_dve, 1)
            dve.wait_ge(lam_dve, 1)
            nc.vector.tensor_reduce(lam2, lam_prod, AXX, ALU.add).then_inc(lam_dve, 1)
            dve.wait_ge(lam_exp, 1)
            nc.vector.tensor_tensor(nlam, lam2[:, 1:2], lam2[:, 0:1], ALU.subtract).then_inc(lam_ready, 1)
            dve.wait_ge(lam_ready, 1)
            nc.vector.tensor_tensor(nlam, nlam, c.col("lam_init"), ALU.subtract).then_inc(lam_ready, 1)
            nc.vector.tensor_scalar(sub_gain, c.col("lam_init"), -1.0, 1.0, ALU.mult, ALU.add).then_inc(lam_ready, 1)
            dve.wait_ge(lam_ready, 3)
            nc.vector.tensor_tensor(sub_gain, sub_gain, c.col("df_sub_g"), ALU.mult).then_inc(lam_ready, 1)
            dve.wait_ge(lam_ready, 4)

            def maximum(u):
                i = units[u][1]
                for m in range(2):
                    n = 2 * u + m
                    bank = 2 * (u % 2) + m
                    dve.wait_ge(scored, n + 1)
                    diagonal = c.ps[:, bank, i * P:(i + 1) * P]
                    nc.vector.tensor_tensor(diagonal, diagonal, c.const("mask_chunk"), ALU.add).then_inc(masked, 1)
                    dve.wait_ge(masked, n + 1)
                    nc.vector.tensor_reduce(nmax[:, n:n + 1], c.ps[:, bank, 0:(i + 1) * P], AXX, ALU.max, negate=True
                                            ).then_inc(maxed, 1)

            def mix(u):
                nk = (units[u][1] + 1) * P
                dve.wait_ge(exped, 2 * u + 2)
                r = rsum[:, 2 * u:2 * u + 2]
                nc.vector.reciprocal(r, r).then_inc(inv, 1)
                dve.wait_ge(inv, 3 * u + 1)
                nc.vector.tensor_tensor(r[:, 1:2], r[:, 1:2], nlam, ALU.mult).then_inc(inv, 1)
                dve.wait_ge(inv, 3 * u + 2)
                p1, p2 = prob[u % 2][0][:, 0:nk], prob[u % 2][1][:, 0:nk]
                nc.vector.tensor_scalar(p2, p2, r[:, 1:2], None, ALU.mult).then_inc(inv, 1)
                dve.wait_ge(inv, 3 * u + 3)
                nc.vector.scalar_tensor_tensor(p1, p1, r[:, 0:1], p2, ALU.mult, ALU.add).then_inc(mixed, 1)

            maximum(0)
            for u in range(NU):
                if u + 1 < NU:
                    maximum(u + 1)
                mix(u)
            for t in range(2):
                dve.wait_ge(rs_ready, 2 * t + 2)
                nc.vector.scalar_tensor_tensor(c.y[:, Y_B + t, :], o[t], sub_gain, rs[t], ALU.mult, ALU.mult
                                               ).then_inc(out, 1)
            dve.wait_ge(out, 2)


def spatial_gating(c, name):
    nc = c.nc
    gelu, loaded, mean_of, centred = (c.sem(f"{name}_{n}") for n in ("gelu", "w_loaded", "mean", "centred"))
    squared, var, rs_ready, normed = (c.sem(f"{name}_{n}") for n in ("squared", "var", "rs_ready", "normed"))
    turned, copied, mixed, out = (c.sem(f"{name}_{n}") for n in ("turned", "copied", "mixed", "out"))
    sq, rs = [scratch(c, 0), scratch(c, 1)], scratch(c, 2)
    w = scratch(c, 3)
    bias, pick = c.h[0:4, 0, 0:P], c.h[0:4, 1, 0:2 * P]
    masked = c.sem(f"{name}_w_masked")
    u, v = [c.p[:, T_C + t, :] for t in range(2)], [c.p[:, T_C + 2 + t, :] for t in range(2)]
    layer = c.layer
    with nc.Block() as block:
        @block.sync
        def _(sp):
            sp.dma_start(w, c.dram["sg_wT"][bass.ds(layer, 1), :, :].rearrange("a p n -> p (a n)")).then_inc(loaded, 16)
            sp.dma_start(bias, c.dram["sg_b"][bass.ds(layer, 1), :, :].rearrange("a p n -> p (a n)")
                         ).then_inc(loaded, 16)
            sp.dma_start(pick, c.dram["sg_pick"]).then_inc(loaded, 16)
            sp.wait_ge(loaded, 48)

        @block.gpsimd
        def _(pool):
            pool.wait_ge(loaded, 48)
            w3 = w.rearrange("p (g i) -> p g i", g=4)
            nc.gpsimd.affine_select(out=w3, in_=w3, compare_op=ALU.is_ge, fill=0.0, base=0, pattern=[[0, 4], [1, P]],
                                    channel_multiplier=-1).then_inc(masked, 1)

        @block.tensor
        def _(pe):
            for t in range(2):
                pe.wait_ge(gelu, 3 + t)
                last = nc.tensor.matmul(c.ps[:, 0, :], c.const("ones"), v[t], start=(t == 0), stop=(t == 1))
            last.then_inc(mean_of, 1)
            for t in range(2):
                pe.wait_ge(squared, t + 1)
                last = nc.tensor.matmul(c.ps[:, 1, :], c.const("ones"), sq[t], start=(t == 0), stop=(t == 1))
            last.then_inc(var, 1)
            for t in range(2):
                pe.wait_ge(normed, 2 * t + 2)
                for b in range(4):
                    last = nc.tensor.transpose(c.ps[:, 2 + t, b * P:(b + 1) * P], v[t][:, b * P:(b + 1) * P],
                                               c.const("ident"))
                last.then_inc(turned, 1)
            pe.wait_ge(copied, 2)
            pe.wait_ge(masked, 1)
            for t in range(2):
                for n in range(4):
                    nc.tensor.matmul(c.ps[:, 4 + t, n * P:(n + 1) * P], pick[:, t * P:(t + 1) * P], bias,
                                     start=(n == 0), stop=False, skip_group_check=True)
                for g in (2 * t, 2 * t + 1):
                    r = slice(64 * (g % 2), 64 * (g % 2) + 64)
                    for n in range(4):
                        last = nc.tensor.matmul(c.ps[r, 4 + t, n * P:(n + 1) * P],
                                                c.vt[:, n, V_C + 64 * g:V_C + 64 * g + 64], w[:, g * P:(g + 1) * P],
                                                start=False, stop=(n == 3), skip_group_check=True)
                last.then_inc(mixed, 1)

        @block.scalar
        def _(act):
            for tile in (*u, *v):
                nc.scalar.activation(tile, tile, ACT.Gelu).then_inc(gelu, 1)
            for t in range(2):
                act.wait_ge(centred, t + 1)
                nc.scalar.activation(sq[t], v[t], ACT.Square).then_inc(squared, 1)
            act.wait_ge(var, 1)
            nc.scalar.activation(rs, c.ps[:, 1, :], ACT.Ln, bias=c.const("eps"), scale=1.0 / 256).then_inc(rs_ready, 1)
            act.wait_ge(rs_ready, 1)
            nc.scalar.activation(rs, rs, ACT.Exp, scale=-0.5).then_inc(rs_ready, 1)
            for t in range(2):
                act.wait_ge(turned, t + 1)
                nc.scalar.activation(c.vt[:, :, V_C + t * P:V_C + (t + 1) * P],
                                     c.ps[:, 2 + t, :].rearrange("p (b n) -> p b n", b=4), ACT.Copy
                                     ).then_inc(copied, 1)

        @block.vector
        def _(dve):
            dve.wait_ge(mean_of, 1)
            for t in range(2):
                nc.vector.scalar_tensor_tensor(v[t], c.ps[:, 0, :], -1.0 / 256, v[t], ALU.mult, ALU.add
                                               ).then_inc(centred, 1)
            dve.wait_ge(rs_ready, 2)
            dve.wait_ge(centred, 2)
            dve.wait_ge(squared, 2)
            for t in range(2):
                nc.vector.scalar_tensor_tensor(v[t], v[t], c.col("sg_ln_g", t), rs, ALU.mult, ALU.mult
                                               ).then_inc(normed, 1)
                dve.wait_ge(normed, 2 * t + 1)
                nc.vector.tensor_scalar(v[t], v[t], c.col("sg_ln_b", t), None, ALU.add).then_inc(normed, 1)
            for t in range(2):
                dve.wait_ge(mixed, t + 1)
                nc.vector.tensor_tensor(c.y[:, Y_C + t, :], c.ps[:, 4 + t, :], u[t], ALU.mult).then_inc(out, 1)
            dve.wait_ge(out, 2)


class Rwkv:

    def __init__(self, c):
        self.c, self.used = c, 0
        self.keep = [dict(ax=self.tiles(2), xT=self.tiles(2), kaT=self.tiles(2), rT=self.tiles(2), b_tok=self.tiles(2),
                          k_tok=self.tiles(2), v_tok=self.tiles(1), r=self.tiles(1), gate=self.tiles(1),
                          bonus=self.tiles(1)) for _ in range(2)]
        self.bx, self.kx = self.tiles(2), self.tiles(2)
        at = self.used
        self.temp = [self.tiles(1) for _ in range(9)]
        self.used = at
        self.group = [[self.tiles(1) for _ in range(5)] for _ in range(2)]
        self.lora = self.c.y[:, 0, :]
        self.pt = [self.c.y[:, 1, :], self.c.p[:, IN_T - 1, :]]
        self.last_decay = c.small[:, 96:112]

    def tiles(self, n):
        c, i = self.c, self.used
        if n == 2 and i % 2:
            i += 1
        self.used = i + n
        if i < 8:
            return c.h[:, i:i + n, :].rearrange("p a n -> p (a n)")
        if i < 24:
            return c.p[:, T_B + i - 8:T_B + i - 8 + n, :].rearrange("p a n -> p (a n)")
        if i < 38:
            return scratch(c, i - 24, n)
        flat = c.vt[:, :, :].rearrange("p b n -> p (b n)")
        assert i + n <= 46
        return flat[:, (i - 38) * S:(i - 38 + n) * S]


def by_chunk(ap, width):
    return ap.rearrange("p (c n) -> p c n", n=width)


def rwkv_shift(c, name, w):
    nc = c.nc
    done, act_done = c.sem(f"{name}_dve"), c.sem(f"{name}_act")
    diff = [w.temp[0], w.temp[1]]
    lora = w.lora
    with nc.Block() as block:
        @block.vector
        def _(dve):
            for j in range(7):
                x, d = c.p[:, T_A + j, :], diff[j % 2]
                if j >= 2:
                    dve.wait_ge(done, 3 * (j - 1))
                nc.vector.tensor_tensor(d[:, 1:S], x[:, 0:S - 1], x[:, 1:S], ALU.subtract).then_inc(done, 1)
                nc.vector.tensor_scalar(d[:, 0:1], x[:, 0:1], -1.0, None, ALU.mult).then_inc(done, 1)
                dve.wait_ge(done, 3 * j + 2)
                nc.vector.scalar_tensor_tensor(x, d, c.col("rw_mu", j), x, ALU.mult, ALU.add).then_inc(done, 1)
            dve.wait_ge(done, 21)

        @block.scalar
        def _(act):
            act.wait_ge(done, 21)
            m = c.p[:, T_A + 6, :]
            nc.scalar.activation(lora[0:32, :], m[0:32, :], ACT.Tanh).then_inc(act_done, 1)
            nc.scalar.activation(lora[32:64, :], m[32:64, :], ACT.Copy).then_inc(act_done, 1)
            nc.scalar.activation(lora[64:128, :], m[64:128, :], ACT.Sigmoid).then_inc(act_done, 1)
            act.wait_ge(act_done, 3)


def rwkv_prepare(c, name, w, pair):
    nc = c.nc
    keep = w.keep[pair]
    r, k, v = (c.p[:, T_A + 2 * i + pair, :] for i in range(3))
    logw, a, cum, cum_ex, e_neg, kk, ss, key, e_pos = w.temp
    lora_w = c.small2[:, :]
    loaded, zeroed = c.sem(f"{name}_lora_loaded"), c.sem(f"{name}_zeroed")
    lora, sig, dec, exps = (c.sem(f"{name}_{n}") for n in ("lora", "sig", "decay", "exps"))
    kk_raw, kk_sq, kk_ss, kk_cl, kk_rs = (c.sem(f"{name}_{n}") for n in ("kk_raw", "kk_sq", "kk_ss", "kk_cl", "kk_rs"))
    vx_s, v_turn, v_tok, bon_in, bon = (c.sem(f"{name}_{n}") for n in ("vx", "v_turn", "v_tok", "bon_in", "bon"))
    gate_s, chain_s, act_chain = c.sem(f"{name}_gate"), c.sem(f"{name}_dve"), c.sem(f"{name}_act")
    cs = slice(pair * P, (pair + 1) * P)
    vx = [keep["kaT"][:, 0:S], keep["kaT"][:, S:2 * S]]
    halves = [(slice(0, 64), 0), (slice(64, 128), 1)]

    def half(x, hh, rows):
        return x.rearrange("p (c h n) -> p c h n", h=2, n=64)[rows, :, hh, :]

    def chunks(x, rows):
        return x.rearrange("p (c n) -> p c n", n=64)[rows, :, :]

    def vhalf(i, hh, rows):
        return vx[i].rearrange("p (c h n) -> p c h n", h=2, n=64)[rows, :, hh, :]

    with nc.Block() as block:
        @block.sync
        def _(sp):
            sp.dma_start(lora_w, c.dram["rw_lora"][bass.ds(c.layer, 1), :, :].rearrange("a p n -> p (a n)")
                         ).then_inc(loaded, 16)
            sp.wait_ge(loaded, 16)

        @block.gpsimd
        def _(pool):
            for x in (vx[0], vx[1], keep["ax"], w.bx, w.kx):
                nc.gpsimd.memset(x, 0.0).then_inc(zeroed, 1)

        @block.tensor
        def _(pe):
            pe.wait_ge(loaded, 16)
            nc.tensor.matmul(c.ps[:, 0, :], lora_w[0:32, cs], w.lora[0:32, :], start=True, stop=True).then_inc(lora, 1)
            nc.tensor.matmul(c.ps[:, 1, :], lora_w[32:64, cs], w.lora[32:64, :], start=True, stop=True,
                             tile_position=(32, 0)).then_inc(lora, 1)
            nc.tensor.matmul(c.ps[:, 2, :], lora_w[64:128, cs], w.lora[64:128, :], start=True, stop=True
                             ).then_inc(lora, 1)
            for i in range(2):
                pe.wait_ge(vx_s, 2 * i + 2)
                for n in range(4):
                    last = nc.tensor.transpose(c.ps[:, 5 + i, n * P:(n + 1) * P], vx[i][:, n * P:(n + 1) * P],
                                               c.const("ident"))
                last.then_inc(v_turn, 1)
            pe.wait_ge(kk_sq, 1)
            nc.tensor.matmul(c.ps[:, 3, :], c.const("bo64"), ss, start=True, stop=True).then_inc(kk_ss, 1)
            pe.wait_ge(bon_in, 1)
            nc.tensor.matmul(c.ps[:, 4, :], c.const("bo64"), c.p[:, T_A + pair, :], start=True, stop=True
                             ).then_inc(bon, 1)

        @block.scalar
        def _(act):
            chain = Chain(act, act_chain)
            act.wait_ge(lora, 1)
            nc.scalar.activation(logw, c.ps[:, 0, :], ACT.Sigmoid, bias=c.col("rw_w0", pair)).then_inc(sig, 1)
            act.wait_ge(lora, 2)
            nc.scalar.activation(a, c.ps[:, 1, :], ACT.Sigmoid, bias=c.col("rw_a0", pair)).then_inc(sig, 1)
            act.wait_ge(lora, 3)
            nc.scalar.activation(keep["gate"], c.ps[:, 2, :], ACT.Copy).then_inc(gate_s, 1)
            act.wait_ge(zeroed, 2)
            for i in range(2):
                for rows, hh in halves:
                    nc.scalar.activation(vhalf(i, hh, rows), chunks(v, rows)[:, 4 * i:4 * i + 4, :], ACT.Copy
                                         ).then_inc(vx_s, 1)
            act.wait_ge(kk_raw, 1)
            nc.scalar.activation(ss, kk, ACT.Square).then_inc(kk_sq, 1)
            act.wait_ge(dec, 2)
            nc.scalar.activation(e_pos, cum, ACT.Exp).then_inc(exps, 1)
            nc.scalar.activation(cum_ex, cum_ex, ACT.Exp).then_inc(exps, 1)
            nc.scalar.activation(e_neg, cum, ACT.Exp, scale=-1.0).then_inc(exps, 1)
            act.wait_ge(kk_cl, 1)
            chain(nc.scalar.activation(ss, ss, ACT.Ln, scale=KK_SCALE))
            nc.scalar.activation(ss, ss, ACT.Exp, scale=-0.5, bias=c.const("kk_shift")).then_inc(kk_rs, 1)
            for i in range(2):
                act.wait_ge(v_turn, i + 1)
                for rows, hh in halves:
                    src = c.ps[:, 5 + i, :].rearrange("p (c h n) -> p c h n", h=2, n=64)[rows, :, hh, :]
                    nc.scalar.activation(chunks(keep["v_tok"], rows)[:, 4 * i:4 * i + 4, :], src, ACT.Copy
                                         ).then_inc(v_tok, 1)
            act.wait_ge(v_tok, 4)
            act.wait_ge(gate_s, 1)

        @block.vector
        def _(dve):
            chain = Chain(dve, chain_s)
            nc.vector.tensor_scalar(kk, k, c.col("rw_k_k", pair), None, ALU.mult).then_inc(kk_raw, 1)
            dve.wait_ge(sig, 1)
            chain(nc.vector.tensor_scalar(logw, logw, -math.exp(-0.5), None, ALU.mult))
            nc.vector.tensor_tensor_scan(cum, c.const("scan"), logw, 0.0, ALU.mult, ALU.add).then_inc(dec, 1)
            dve.wait_ge(dec, 1)
            nc.vector.tensor_tensor(cum_ex, cum, logw, ALU.subtract).then_inc(dec, 1)
            dve.wait_ge(sig, 2)
            chain(nc.vector.tensor_scalar(key, a, -1.0, c.col("rw_k_a", pair), ALU.add, ALU.mult))
            chain(nc.vector.scalar_tensor_tensor(key, key, 1.0, k, ALU.add, ALU.mult))
            dve.wait_ge(kk_ss, 1)
            nc.vector.tensor_scalar(ss, c.ps[:, 3, :], 1e-24, None, ALU.max).then_inc(kk_cl, 1)
            dve.wait_ge(exps, 3)
            chain(nc.vector.tensor_tensor(keep["r"], r, e_pos, ALU.mult))
            chain(nc.vector.scalar_tensor_tensor(r, r, c.col("rw_r_k", pair), key, ALU.mult, ALU.mult))
            nc.vector.tensor_copy(w.last_decay[:, 8 * pair:8 * pair + 8], by_chunk(e_pos, 64)[:, :, 63]
                                  ).then_inc(bon_in, 1)
            dve.wait_ge(zeroed, 5)
            for rows, hh in halves:
                chain(nc.vector.tensor_tensor(half(w.kx, hh, rows), chunks(key, rows), chunks(e_neg, rows), ALU.mult))
            dve.wait_ge(kk_rs, 1)
            chain(nc.vector.tensor_tensor(kk, kk, ss, ALU.mult))
            for rows, hh in halves:
                chain(nc.vector.scalar_tensor_tensor(half(keep["ax"], hh, rows), chunks(kk, rows), -1.0,
                                                     chunks(cum_ex, rows), ALU.mult, ALU.mult))
            chain(nc.vector.tensor_tensor(kk, kk, a, ALU.mult))
            for rows, hh in halves:
                chain(nc.vector.tensor_tensor(half(w.bx, hh, rows), chunks(kk, rows), chunks(e_neg, rows), ALU.mult))
            dve.wait_ge(bon, 1)
            chain(nc.vector.tensor_tensor(keep["bonus"], c.ps[:, 4, :], v, ALU.mult))


def rwkv_intra(c, name, w, pair):
    nc = c.nc
    keep = w.keep[pair]
    multiplied, on_dve, on_act, dve_chain = (c.sem(f"{name}_{n}") for n in ("multiplied", "on_dve", "on_act", "chain"))
    STEPS = 10
    DVE_AT, ACT_AT = [0, 1, 2, 3, 4, 6, 8, 9], [0, 1, 2, 3, 5, 6, 7]

    def buffers(g):
        A, B, LO, C2, E2 = w.group[g]
        return A, B, LO, C2, E2, w.pt[g]

    def unit(x, n):
        return x[:, n * P:(n + 1) * P]

    def seen(steps, s, g):
        return 2 * after(steps, s - 1) + (g + 1 if s in steps else 0)

    with nc.Block() as block:
        @block.tensor
        def _(pe):
            for s in range(STEPS):
                for g in range(2):
                    A, B, LO, C2, E2, PT = buffers(g)
                    bank = [c.ps[:, 4 * g + i, :] for i in range(4)]
                    if s >= 1:
                        n = seen(DVE_AT, s - 1, g)
                        pe.wait_ge(on_dve, n)
                        pe.wait_ge(on_act, seen(ACT_AT, s - 1, g))
                    last = None
                    for n in range(4):
                        u = 4 * g + n
                        ax, bx, kx = (x[:, u * P:(u + 1) * P] for x in (keep["ax"], w.bx, w.kx))
                        r = keep["r"][:, u * 64:(u + 1) * 64]

                        def mm(i, lhsT, rhs):
                            return nc.tensor.matmul(unit(bank[i], n), lhsT, rhs, start=True, stop=True)
                        if s == 0:
                            mm(0, ax, bx)
                            mm(1, bx, ax)
                            mm(2, kx, ax)
                            nc.tensor.matmul(bank[3][:, n * P:n * P + 64], bx, r, start=True, stop=True)
                            last = nc.tensor.matmul(bank[3][:, n * P + 64:(n + 1) * P], kx, r, start=True, stop=True)
                        elif s == 1:
                            mm(0, unit(B, n), unit(A, n))
                            last = mm(1, unit(A, n), unit(B, n))
                        elif s == 2:
                            mm(0, unit(E2, n), unit(C2, n))
                            mm(1, unit(C2, n), unit(E2, n))
                            last = mm(2, unit(C2, n), unit(PT, n))
                        elif s == 3:
                            mm(0, unit(B, n), unit(A, n))
                            last = mm(2, unit(A, n), unit(PT, n))
                        elif s == 4:
                            last = mm(1, unit(E2, n), unit(PT, n))
                        elif s == 5:
                            last = nc.tensor.transpose(unit(bank[0], n), unit(PT, n), c.const("ident"))
                        elif s == 6:
                            mm(1, unit(A, n), unit(LO, n))
                            last = mm(2, unit(LO, n), unit(A, n))
                        elif s == 7:
                            last = mm(0, unit(C2, n), unit(E2, n))
                        elif s == 8:
                            last = mm(1, unit(B, n), unit(PT, n))
                        else:
                            last = mm(2, unit(E2, n), unit(PT, n))
                    last.then_inc(multiplied, 1)
            for g in range(2):
                pe.wait_ge(on_dve, 2 * len(DVE_AT))
                pe.wait_ge(on_act, 2 * len(ACT_AT))
                for n in range(4):
                    u = 4 * g + n
                    nc.tensor.transpose(unit(c.ps[:, 4 * g, :], n), w.bx[:, u * P:(u + 1) * P], c.const("ident"))
                    last = nc.tensor.transpose(unit(c.ps[:, 4 * g + 1, :], n), w.kx[:, u * P:(u + 1) * P],
                                               c.const("ident"))
                last.then_inc(multiplied, 1)

        @block.scalar
        def _(act):
            for s in ACT_AT:
                for g in range(2):
                    A, B, LO, C2, E2, PT = buffers(g)
                    bank = [c.ps[:, 4 * g + i, :] for i in range(4)]
                    act.wait_ge(multiplied, 2 * s + g + 1)
                    out, i = {0: (None, None), 1: (C2, 0), 2: (A, 0), 3: (E2, 0), 5: (A, 0), 6: (C2, 1), 7: (B, 0)}[s]
                    if s == 0:
                        out, i = keep["rT"][:, g * S:(g + 1) * S], 3
                    nc.scalar.activation(out, bank[i], ACT.Copy).then_inc(on_act, 1)
            for g in range(2):
                act.wait_ge(multiplied, 2 * STEPS + g + 1)
                nc.scalar.activation(keep["b_tok"][:, g * S:(g + 1) * S], c.ps[:, 4 * g, :], ACT.Copy
                                     ).then_inc(on_act, 1)
            act.wait_ge(on_act, 2 * len(ACT_AT) + 2)

        @block.vector
        def _(dve):
            chain = Chain(dve, dve_chain)
            for s in DVE_AT:
                for g in range(2):
                    A, B, LO, C2, E2, PT = buffers(g)
                    bank = [c.ps[:, 4 * g + i, :] for i in range(4)]
                    cols = slice(g * S, (g + 1) * S)
                    dve.wait_ge(multiplied, 2 * s + g + 1)
                    if s == 0:
                        chain(nc.vector.tensor_tensor(A, bank[0], c.const("m_ld"), ALU.mult))
                        chain(nc.vector.tensor_tensor(B, bank[1], c.const("m_ldT"), ALU.mult))
                        chain(nc.vector.tensor_tensor(keep["kaT"][:, cols], bank[2], c.const("m_kaT"), ALU.mult))
                        chain(nc.vector.tensor_tensor(LO, bank[1], c.const("m_loT"), ALU.mult))
                        chain(nc.vector.tensor_tensor(PT, B, c.const("ident4"), ALU.add))
                        dve.wait_ge(on_act, g + 1)
                        rT = keep["rT"][:, cols]
                        last = nc.vector.tensor_tensor(rT, rT, c.const("m_r"), ALU.mult)
                    elif s == 1:
                        last = nc.vector.tensor_copy(E2, bank[1])
                    elif s == 2:
                        chain(nc.vector.tensor_copy(B, bank[1]))
                        last = nc.vector.tensor_tensor(PT, bank[2], PT, ALU.add)
                    elif s == 3:
                        last = nc.vector.tensor_tensor(PT, bank[2], PT, ALU.add)
                    elif s == 4:
                        last = nc.vector.tensor_tensor(PT, bank[1], PT, ALU.add)
                    elif s == 6:
                        last = nc.vector.tensor_copy(E2, bank[2])
                    elif s == 8:
                        last = nc.vector.tensor_tensor(PT, bank[1], PT, ALU.add)
                    else:
                        last = nc.vector.tensor_tensor(keep["xT"][:, cols], bank[2], PT, ALU.add)
                    last.then_inc(on_dve, 1)
            for g in range(2):
                dve.wait_ge(multiplied, 2 * STEPS + g + 1)
                chain(nc.vector.tensor_copy(keep["k_tok"][:, g * S:(g + 1) * S], c.ps[:, 4 * g + 1, :]))


def rwkv_scan(c, name, w):
    nc = c.nc
    names = ("zeroed", "rhs", "rhs_out", "sa", "sa_out", "state_mm", "state_add", "state", "y_mm", "y_out")
    zeroed, rhs, rhs_out, sa, sa_out, state_mm, state_add, state, y_mm, y_out = (c.sem(f"{name}_{n}") for n in names)
    mean, cent, sq, var, rs_s, chain_s = (c.sem(f"{name}_{n}") for n in ("mean", "cent", "sq", "var", "rs", "chain"))
    st = [[w.bx[:, (2 * q + i) * 64:(2 * q + i + 1) * 64] for i in range(2)] for q in range(2)]
    rh = [w.bx[:, 256 + q * 64:256 + (q + 1) * 64] for q in range(2)]
    sav = [w.bx[:, 384 + q * 64:384 + (q + 1) * 64] for q in range(2)]
    order = [(n, q) for n in range(NCH) for q in range(2)]
    y = [w.temp[0], w.temp[1]]
    sqt, rs = [w.temp[2], w.temp[3]], [w.temp[4], w.temp[5]]
    mmean = [w.temp[6], w.temp[7]]
    ONCE = len(order)

    with nc.Block() as block:
        @block.gpsimd
        def _(pool):
            for q in range(2):
                nc.gpsimd.memset(st[q][0], 0.0).then_inc(zeroed, 1)

        @block.tensor
        def _(pe):
            pe.wait_ge(zeroed, 2)

            def unit(x, n, width=P):
                return x[:, n * width:(n + 1) * width]

            def first(i):
                n, q = order[i]
                keep = w.keep[q]
                if n >= 1:
                    pe.wait_ge(state, i - 2 + 1)
                bank = c.ps[:, q, 0:64]
                nc.tensor.matmul(bank, unit(keep["ax"], n), st[q][n % 2], start=True, stop=False)
                nc.tensor.matmul(bank, unit(keep["kaT"], n), unit(keep["v_tok"], n, 64), start=False, stop=True
                                 ).then_inc(rhs, 1)

            def second(i):
                n, q = order[i]
                pe.wait_ge(rhs_out, i + 1)
                nc.tensor.matmul(c.ps[:, q, 64:128], unit(w.keep[q]["xT"], n), rh[q], start=True, stop=True
                                 ).then_inc(sa, 1)

            def third(i):
                n, q = order[i]
                keep = w.keep[q]
                pe.wait_ge(sa_out, i + 1)
                bank = c.ps[:, 2 + q, 0:64]
                nc.tensor.matmul(bank, unit(keep["b_tok"], n), sav[q], start=True, stop=False)
                nc.tensor.matmul(bank, unit(keep["k_tok"], n), unit(keep["v_tok"], n, 64), start=False, stop=True
                                 ).then_inc(state_mm, 1)
                for hh in range(2):
                    rows = slice(64 * hh, 64 * hh + 64)
                    out = c.ps[rows, 4 + q, n * 64:(n + 1) * 64]
                    rT = unit(keep["rT"], n)
                    nc.tensor.matmul(out, st[q][n % 2][rows, :], keep["r"][rows, n * 64:(n + 1) * 64], start=True,
                                     stop=False)
                    nc.tensor.matmul(out, sav[q][rows, :], rT[rows, 0:64], start=False, stop=False)
                    last = nc.tensor.matmul(out, unit(keep["v_tok"], n, 64)[rows, :], rT[rows, 64:128], start=False,
                                            stop=True)
                last.then_inc(y_mm, 1)

            for i in range(0, ONCE, 2):
                first(i)
                first(i + 1)
                second(i)
                second(i + 1)
                third(i)
                third(i + 1)
            for q in range(2):
                pe.wait_ge(y_out, q + 1)
                nc.tensor.matmul(c.ps[:, 6, :], c.const("bo64"), y[q], start=True, stop=True).then_inc(mean, 1)
                pe.wait_ge(sq, q + 1)
                nc.tensor.matmul(c.ps[:, 7, :], c.const("bo64"), sqt[q], start=True, stop=True).then_inc(var, 1)

        @block.scalar
        def _(act):
            for i, (n, q) in enumerate(order):
                act.wait_ge(rhs, i + 1)
                if i >= 2:
                    act.wait_ge(sa, i - 1)
                nc.scalar.activation(rh[q], c.ps[:, q, 0:64], ACT.Copy).then_inc(rhs_out, 1)
            for q in range(2):
                act.wait_ge(y_mm, ONCE - 1 + q)
                nc.scalar.activation(y[q], c.ps[:, 4 + q, :], ACT.Copy).then_inc(y_out, 1)
            for q in range(2):
                act.wait_ge(cent, q + 1)
                nc.scalar.activation(sqt[q], y[q], ACT.Square).then_inc(sq, 1)
                act.wait_ge(var, q + 1)
                nc.scalar.activation(rs[q], c.ps[:, 7, :], ACT.Ln, bias=c.const("gn_eps"), scale=1.0 / 64
                                     ).then_inc(rs_s, 1)
                act.wait_ge(rs_s, 2 * q + 1)
                nc.scalar.activation(rs[q], rs[q], ACT.Exp, scale=-0.5).then_inc(rs_s, 1)

        @block.vector
        def _(dve):
            for i, (n, q) in enumerate(order):
                if q == 0:
                    for j in (i, i + 1):
                        qq = order[j][1]
                        dve.wait_ge(sa, j + 1)
                        if j >= 2:
                            dve.wait_ge(y_mm, j - 1)
                        nc.vector.tensor_copy(sav[qq], c.ps[:, qq, 64:128]).then_inc(sa_out, 1)
                new = st[q][(n + 1) % 2]
                dve.wait_ge(state_mm, i + 1)
                if i >= 2:
                    dve.wait_ge(y_mm, i - 1)
                nc.vector.tensor_tensor(new, c.ps[:, 2 + q, 0:64], st[q][n % 2], ALU.add).then_inc(state_add, 1)
                dve.wait_ge(state_add, i + 1)
                nc.vector.tensor_scalar(new, new, w.last_decay[:, 8 * q + n:8 * q + n + 1], None, ALU.mult
                                        ).then_inc(state, 1)
            chain = Chain(dve, chain_s)
            for q in range(2):
                dve.wait_ge(mean, q + 1)
                nc.vector.scalar_tensor_tensor(y[q], c.ps[:, 6, :], -1.0 / 64, y[q], ALU.mult, ALU.add
                                               ).then_inc(cent, 1)
                dve.wait_ge(rs_s, 2 * q + 2)
                chain(nc.vector.scalar_tensor_tensor(y[q], y[q], c.col("rw_ln_g", q), rs[q], ALU.mult, ALU.mult))
                chain(nc.vector.scalar_tensor_tensor(y[q], y[q], c.col("rw_ln_b", q), w.keep[q]["bonus"], ALU.add,
                                                     ALU.add))
                chain(nc.vector.tensor_tensor(c.y[:, Y_A + q, :], y[q], w.keep[q]["gate"], ALU.mult))


def feed_forward_up(c, name, up):
    nc = c.nc
    tapped, act_g, conv = c.sem(f"{name}_tapped"), c.sem(f"{name}_silu"), c.sem(f"{name}_conv")
    hidden = c.sem(f"{name}_hidden")
    work_tile = [c.y[:, s, :] for s in range(RING)]
    GATES = (1, 3)

    def tap(i, t):
        at = C_AT["ffn_tap"]
        return c.cols[:, bass.ds(t * 4 + (at + i), 1)]

    @contextmanager_block(nc)
    def _(block):
        @block.sync
        def _(sp):
            up.load(sp)

        @block.tensor
        def _(pe):
            up.multiply(pe, (lambda kt: c.a_hi[:, kt, :], lambda kt: c.h_lo[:, kt, :]))

        @block.scalar
        def _(act):
            def tile(s, g):
                act.wait_ge(up.multiplied, g * RING + s + 1)
                nc.scalar.activation(work_tile[s], c.ps[:, s, :], ACT.Identity, bias=tap(3, g * RING + s),
                                     scale=tap(2, g * RING + s)).then_inc(tapped, 1)

            def silu(i, g):
                s = GATES[i]
                act.wait_ge(conv, g * 2 * RING + 2 * s + 2)
                nc.scalar.activation(work_tile[s], work_tile[s], ACT.Silu).then_inc(act_g, 1)

            def work_on(first):
                def work(s, g):
                    if not first:
                        act.wait_ge(hidden, 2 * (g - 1) + s // 2 + 1)
                    tile(s, g)
                    if s in GATES:
                        silu(s // 2, g)
                return work

            up.split_high(act, 0, 0, first=True)
            up.split_high(act, 1, 0, first=True)
            up.tiles(act, up.split_high, work_on(False), first=work_on(True))

        @block.vector
        def _(dve):
            def work(s, g):
                t = g * RING + s
                dve.wait_ge(tapped, t + 1)
                o, u = work_tile[s], c.ps[:, s, :]
                nc.vector.scalar_tensor_tensor(o[:, 1:S], u[:, 0:S - 1], tap(1, t), o[:, 1:S], ALU.mult,
                                               ALU.add).then_inc(conv, 1)
                dve.wait_ge(conv, t * 2 + 1)
                nc.vector.scalar_tensor_tensor(o[:, 2:S], u[:, 0:S - 2], tap(0, t), o[:, 2:S], ALU.mult,
                                               ALU.add).then_inc(conv, 1)
                dve.wait_ge(conv, t * 2 + 2)
                dve.sem_inc(up.emptied, 1)
                if s in GATES:
                    i = s // 2
                    dve.wait_ge(act_g, g * 2 + i + 1)
                    out = c.p[:, bass.ds(g * 2 + i, 1), :].rearrange("p a n -> p (a n)")
                    nc.vector.tensor_tensor(out, work_tile[2 * i], work_tile[2 * i + 1], ALU.mult).then_inc(hidden, 1)

            up.split_low(dve, 0, 0)
            up.split_low(dve, 1, 0)
            up.tiles(dve, up.split_low, work)
            dve.wait_ge(hidden, up.n // 2)


class contextmanager_block:

    def __init__(self, nc):
        self.nc = nc

    def __call__(self, f):
        with self.nc.Block() as block:
            f(block)


def linear_stage(c, lin, rhs, out, prefetch=None, load=True):
    nc = c.nc
    engine, body = out
    with nc.Block() as block:
        @block.sync
        def _(sp):
            if load:
                lin.load(sp)
            if prefetch is not None:
                sp.wait_ge(lin.multiplied, lin.n)
                prefetch(sp)

        @block.tensor
        def _(pe):
            lin.multiply(pe, rhs)

        if engine == "scalar":
            @block.scalar
            def _(act):
                body(act)
        else:
            @block.vector
            def _(dve):
                body(dve)


def block_one_layer(c, layer, stop=None):
    nc, dram = c.nc, c.dram
    c.layer = layer

    def of_layer(name, tiles):
        return lambda t: dram[name][bass.ds(layer * tiles + t, 1), :, :].rearrange("a p n -> p (a n)")

    w_in = SplitLinear(c, "w_in", IN_T, of_layer("w_in", IN_T))
    w_out = SplitLinear(c, "w_out", KT, of_layer("w_out", KT))
    ffn_up = SplitLinear(c, "ffn_up", 2 * FT, of_layer("ffn_up", 2 * FT))
    cols_loaded = c.sem("cols_loaded")
    mod = lambda i: c.mod[:, i * KT:(i + 1) * KT]
    tmp = c.ring[:, RING * D:]

    def first_loads(sp):
        sp.dma_start(c.cols[:, :], dram["cols"][bass.ds(layer, 1), :, :].rearrange("a p n -> p (a n)")
                     ).then_inc(cols_loaded, 16)
        w_in.prefetch(sp)
        for n in range(RING):
            mod_sums.load(sp, n)

    mod_sums = AdaLN(c, "mod", layer, 2, 4, quarters(c.vt[:, :, :]), [(c.cond[:, :], quarters(c.y[:, :, :]))])
    norm_modulate(c, "norm1", c.x, c.h, c.col("norm1_g", 0, 8), mod(1), mod(0), tmp=tmp, loads=first_loads,
                  gain_loaded=cols_loaded,
                  split=(c.a_hi, c.h_lo))
    tile_of_p = lambda t: c.p[:, bass.ds(t, 1), :].rearrange("p a n -> p (a n)")
    rounds = IN_T // RING

    def pieces_of(s, g):
        if isinstance(g, int) and g in (0, rounds - 1):
            at = 0 if g == 0 else mod_sums.pieces - 2 * RING
            return [(at + 2 * s, None), (at + 2 * s + 1, None)]
        return [(s, g + 1)]

    def load_w_in(sp):
        mod_sums.load_bias(sp, [c.mod[:, 2 * KT:]])
        for s in range(RING):
            if s >= 2:
                for n in (2 * s, 2 * s + 1):
                    mod_sums.load(sp, n)
            w_in.load_one(sp, s, 1)
        with sp.Fori(1, rounds - 1) as g:
            for s in range(RING):
                for n, kt in pieces_of(s, g):
                    mod_sums.load(sp, n, kt)
                w_in.load_one(sp, s, g + 1)
        for s in range(RING):
            for n, kt in pieces_of(s, rounds - 1):
                mod_sums.load(sp, n, kt)

    split_stage(c, w_in, c.h_lo, copy_out(c, w_in, tile_of_p), load=load_w_in,
                dve_work=lambda dve: lambda s, g: [mod_sums.add(dve, n, kt) for n, kt in pieces_of(s, g)])
    if stop == "w_in":
        return
    with c.stages():
        prepare_attentions(c, "prep", w_out.prefetch, mod_sums)
        attention_forget(c, "fx")
        attention_diff(c, "df")
        spatial_gating(c, "sg")
    if stop == "attn":
        return
    w = Rwkv(c)
    with c.stages():
        rwkv_shift(c, "rw_shift", w)
        for q in range(2):
            rwkv_prepare(c, f"rw_prep{q}", w, q)
            rwkv_intra(c, f"rw_intra{q}", w, q)
        rwkv_scan(c, "rw_scan", w)
    if stop == "mix":
        return
    split_stage(c, w_out, c.y_lo, add_residual(c, w_out, mod(2)), prefetch=ffn_up.prefetch, x=c.y)
    next_cond, _ = load_cond(c, "next_mod", layer + 1)
    norm_modulate(c, "norm2", c.x, c.h, c.col("norm2_g", 0, 8), mod(4), mod(3), tmp=tmp, split=(c.a_hi, c.h_lo),
                  extra_act=next_cond)
    feed_forward_up(c, "ffn", ffn_up)
    flat = lambda t: t.rearrange("p a n -> p (a n)")
    acc = quarters(c.vt[:, :, :])
    next_sums = AdaLN(c, "next_mod", layer + 1, 0, 2, [flat(c.y[:, KT - 2:KT, :]), flat(c.p[:, FT:FT + 2, :])],
                      [(c.cond[:, :], acc[0:2]), (c.cond_ctx[:, :], acc[2:4])])
    feed_forward_down(c, "down", of_layer("ffn_down", KT), mod(5), next_sums)
    adaln_finish(c, "next_mod", next_sums)


def feed_forward_down(c, name, weights, gate, sums):
    nc = c.nc
    HALF = FT // 2
    N = 2 * KT
    raw = [c.ring[:, i * FT * P:(i + 1) * FT * P] for i in range(2)]
    hi_of = lambda kt: (c.h_lo, c.a_hi, c.y_lo)[kt // KT][:, kt % KT, :]
    loaded = [c.sem(f"{name}_w_loaded{i}") for i in range(2)]
    x_high, x_low, high, low, multiplied, added = (c.sem(f"{name}_{n}") for n in
                                                   ("x_high", "x_low", "w_high", "w_low", "multiplied", "added"))

    def load_tile(sp, t):
        if t >= 2:
            sp.wait_ge(low, 2 * (t - 1))
        sp.dma_start(raw[t % 2], weights(t)).then_inc(loaded[t % 2], 16)

    half_of = lambda n: raw[n // 2 % 2][:, n % 2 * HALF * P:(n % 2 + 1) * HALF * P]

    with nc.Block() as block:
        @block.sync
        def _(sp):
            for t in range(2):
                load_tile(sp, t)
            for n in range(2):
                sums.load(sp, n)
            sums.load_bias(sp, [c.mod[:, 0:2 * KT], c.ctxmod[:, :]])
            for t in range(2, KT):
                load_tile(sp, t)
                for n in (2 * t - 2, 2 * t - 1):
                    sums.load(sp, n)
            for n in range(N - 2, N):
                sums.load(sp, n)

        @block.tensor
        def _(pe):
            for n in range(N):
                t = n // 2
                if n < 2:
                    pe.wait_ge(x_low, (n + 1) * HALF)
                if n % 2 == 0 and t >= RING:
                    pe.wait_ge(added, t - RING + 1)
                pe.wait_ge(low, n + 1)
                bank = c.ps[:, t % RING, :]
                for k in range(HALF):
                    kt, at = n % 2 * HALF + k, slice(k * P, (k + 1) * P)
                    nc.tensor.matmul(bank, c.half_hi[:, n % 2, at], hi_of(kt), start=(kt == 0), stop=False)
                    nc.tensor.matmul(bank, c.half_hi[:, n % 2, at], c.p_lo[:, kt, :], start=False, stop=False)
                    last = nc.tensor.matmul(bank, c.half_lo[:, n % 2, at], hi_of(kt), start=False,
                                            stop=(kt == FT - 1))
                last.then_inc(multiplied, 1)

        @block.scalar
        def _(act):
            def split(n):
                act.wait_ge(loaded[n // 2 % 2], 16 * (n // 4 + 1))
                if n >= 2:
                    act.wait_ge(multiplied, n - 1)
                nc.scalar.activation(c.half_hi[:, n % 2, :], half_of(n), ACT.Copy).then_inc(high, 1)

            for n in range(2):
                for kt in range(n * HALF, (n + 1) * HALF):
                    nc.scalar.activation(hi_of(kt), c.p[:, kt, :], ACT.Copy).then_inc(x_high, 1)
                split(n)
            for n in range(2, N):
                split(n)

        @block.vector
        def _(dve):
            def split(n):
                dve.wait_ge(high, n + 1)
                nc.vector.tensor_tensor(c.half_lo[:, n % 2, :], half_of(n), c.half_hi[:, n % 2, :].bitcast(F32),
                                        ALU.subtract).then_inc(low, 1)

            for n in range(2):
                for kt in range(n * HALF, (n + 1) * HALF):
                    dve.wait_ge(x_high, kt + 1)
                    nc.vector.tensor_tensor(c.p_lo[:, kt, :], c.p[:, kt, :], hi_of(kt).bitcast(F32), ALU.subtract
                                            ).then_inc(x_low, 1)
                split(n)
            for n in range(N):
                if n + 2 < N:
                    split(n + 2)
                sums.add(dve, n)
                if n % 2:
                    t = n // 2
                    dve.wait_ge(multiplied, n + 1)
                    nc.vector.scalar_tensor_tensor(c.x[:, t, :], c.ps[:, t % RING, :], gate[:, t:t + 1], c.x[:, t, :],
                                                   ALU.mult, ALU.add).then_inc(added, 1)


class Gla:

    LAT, SEG = S, S + CTX
    CHUNKS = 2 * (NCH + LNC)

    def __init__(self, c):
        self.c = c
        flat = lambda t: t.rearrange("p a n -> p (a n)")
        h, y, vt = flat(c.h[:, :, :]), flat(c.y[:, :, :]), flat(c.vt[:, :, :])
        self.ctx_x, self.ctx_h = (t.rearrange("p (a n) -> p a n", n=CTX) for t in (y[:, 0:4 * S], y[:, 4 * S:8 * S]))
        self.kc = vt[:, 0:4 * CTX].rearrange("p (a n) -> p a n", n=CTX)
        self.vc = vt[:, 4 * CTX:12 * CTX].rearrange("p (a n) -> p a n", n=CTX)
        self.low = vt[:, 12 * CTX:15 * CTX]
        self.q, self.r, self.k, self.v = 0, 4, 12, 16
        self.g, self.cum = h[:, 0:3 * S], h[:, 3 * S:6 * S]
        self.state = h[:, 6 * S:8 * S].rearrange("p (z i n) -> p z i n", z=2, i=2)
        self.e_pos, self.e_neg = scratch(c, 0, 2), scratch(c, 2, 3)
        self.k_tok = scratch(c, 5, 3)
        self.v_tok = scratch(c, 8, 3).rearrange("p (b n) -> p b n", n=2 * P)
        self.scores = scratch(c, 11, 2)
        self.gb = scratch(c, 13)
        self.tot, self.half, self.em, self.step = (c.small[:, 24 * i:24 * i + 24] for i in range(4))


def gla_project(c, w):
    nc = c.nc
    n1, n2 = 12, 12
    of = lambda first: lambda t: c.dram["gla_in"][bass.ds(first + t, 1), :, :].rearrange("a p n -> p (a n)")
    qr = SplitLinear(c, "gla_qr", n1, of(0))
    kv = SplitLinear(c, "gla_kv", n2, of(n1))
    ctx_multiplied, ctx_emptied = c.sem("gla_ctx_multiplied"), c.sem("gla_ctx_emptied")
    low_loaded, low_done, low_out = c.sem("gla_low_loaded"), c.sem("gla_low"), c.sem("gla_low_out")
    low_w = scratch(c, 8)
    low_hi, low_lo = c.low_hi, c.low_lo
    low_split = c.sem("gla_low_split")
    ctx_kv = c.vt[:, :, :].rearrange("p b n -> p (b n)")
    tile_of_p = lambda t: c.p[:, bass.ds(t, 1), :].rearrange("p a n -> p (a n)")
    latent = (lambda kt: c.a_hi[:, kt, :], lambda kt: c.h_lo[:, kt, :])
    context = (lambda kt: c.ctx_hi[:, kt, :], lambda kt: c.ctx_lo[:, kt, :])

    with nc.Block() as block:
        @block.sync
        def _(sp):
            qr.prefetch(sp)
            sp.dma_start(low_w, c.dram["gla_low"]).then_inc(low_loaded, 16)
            sp.dma_start(w.gb, c.dram["gla_gb"]).then_inc(low_loaded, 16)
            qr.load(sp)
            for s in range(RING):
                sp.wait_ge(qr.low, n1 - RING + s + 1)
                sp.dma_start(c.slot(s), kv.weights(s)).then_inc(kv.loaded[s], 16)

        @block.tensor
        def _(pe):
            qr.multiply(pe, latent)
            pe.wait_ge(low_split, 2)
            for half, (x, n) in enumerate(((latent, S), (context, CTX))):
                hi, lo = x
                for kt in range(KT):
                    at = slice(kt * 64, (kt + 1) * 64)
                    bank = c.ps[0:64, 4 + half, 0:n]
                    nc.tensor.matmul(bank, low_hi[:, at], hi(kt), start=(kt == 0), stop=False)
                    nc.tensor.matmul(bank, low_hi[:, at], lo(kt), start=False, stop=False)
                    last = nc.tensor.matmul(bank, low_lo[:, at], hi(kt), start=False, stop=(kt == KT - 1))
                last.then_inc(low_done, 1)

        @block.scalar
        def _(act):
            qr.split_high(act, 0, 0, first=True)
            qr.split_high(act, 1, 0, first=True)
            qr.tiles(act, qr.split_high, copy_out(c, qr, lambda t: tile_of_p(t))[1](act))
            act.wait_ge(low_loaded, 32)
            nc.scalar.activation(low_hi[:, :], low_w, ACT.Copy).then_inc(low_split, 1)
            act.wait_ge(low_done, 2)
            nc.scalar.activation(w.low[0:64, 0:S], c.ps[0:64, 4, :], ACT.Copy).then_inc(low_out, 1)
            nc.scalar.activation(w.low[0:64, S:S + CTX], c.ps[0:64, 5, 0:CTX], ACT.Copy).then_inc(low_out, 1)

        @block.vector
        def _(dve):
            qr.split_low(dve, 0, 0)
            qr.split_low(dve, 1, 0)
            qr.tiles(dve, qr.split_low, lambda s, g: None)
            dve.wait_ge(low_split, 1)
            nc.vector.tensor_tensor(low_lo[:, :], low_w, low_hi[:, :].bitcast(F32), ALU.subtract).then_inc(low_split, 1)

    with nc.Block() as block:
        @block.sync
        def _(sp):
            kv.load(sp)

        @block.tensor
        def _(pe):
            def tile(s, g):
                pe.wait_ge(kv.low, g * RING + s + 1)
                kv.products(s, c.ps[:, s, :], latent)
                kv.products(s, c.ps[:, RING + s, 0:CTX], context).then_inc(kv.multiplied, 1)

            for s in range(RING):
                tile(s, 0)
            with pe.Fori(1, n2 // RING) as g:
                for s in range(RING):
                    pe.wait_ge(kv.emptied, (g - 1) * RING + s + 1)
                    pe.wait_ge(ctx_emptied, (g - 1) * RING + s + 1)
                    tile(s, g)

        @block.scalar
        def _(act):
            kv.split_high(act, 0, 0, first=True)
            kv.split_high(act, 1, 0, first=True)
            kv.tiles(act, kv.split_high, copy_out(c, kv, lambda t: tile_of_p(t + n1))[1](act))

        @block.vector
        def _(dve):
            def copy_ctx(s, g):
                dve.wait_ge(kv.multiplied, g * RING + s + 1)
                out = ctx_kv[:, bass.ds(g * (RING * CTX) + s * CTX, CTX)]
                nc.vector.tensor_copy(out, c.ps[:, RING + s, 0:CTX]).then_inc(ctx_emptied, 1)

            kv.split_low(dve, 0, 0)
            kv.split_low(dve, 1, 0)
            kv.tiles(dve, kv.split_low, copy_ctx)


def gla_prepare(c, name, w, head):
    nc = c.nc
    z, z_in, ln_in, soft, gate, scanned = (c.sem(f"{name}_{n}") for n in ("z", "z_in", "ln_in", "soft", "gate", "scan"))
    exps, q_done, k_done, chain_s = (c.sem(f"{name}_{n}") for n in ("exps", "q", "k", "chain"))
    v_turn, v_out, k_turn, k_out, act_chain = (c.sem(f"{name}_{n}") for n in ("v_turn", "v_out", "k_turn", "k_out", "act"))
    zeroed = c.sem(f"{name}_zeroed")
    cs = slice(head * P, (head + 1) * P)
    b = [c.cols2[:, C2_AT["b_gate"] + 4 * z_ + head:C2_AT["b_gate"] + 4 * z_ + head + 1] for z_ in range(2)]
    SEG = w.SEG
    parts = [(0, S, 0, 0, 0), (S, CTX, 2, 0, 0), (SEG, S, 1, 0, 1), (SEG + S, CTX, 6, 0, 1)]
    chunks = lambda t: t.rearrange("p (c n) -> p c n", n=CH)
    bc = lambda t, n: t.unsqueeze(2).to_broadcast([P, n, CH])
    with nc.Block() as block:
        @block.gpsimd
        def _(pool):
            nc.gpsimd.memset(w.scores, 0.0).then_inc(zeroed, 1)
            pool.wait_ge(zeroed, 1)

        @block.tensor
        def _(pe):
            for to, n, bank, frm, z_ in parts:
                lo = w.low[32 * z_:32 * z_ + 16, 0 if n == S else S:S if n == S else SEG]
                last = nc.tensor.matmul(c.ps[:, bank, frm:frm + n], w.gb[32 * z_:32 * z_ + 16, cs], lo, start=True,
                                        stop=True, tile_position=(32 * z_, 0))
            last.then_inc(z, 1)
            for j in range(2):
                for n in range(4):
                    nc.tensor.transpose(c.ps[:, 3 + j, n * P:(n + 1) * P],
                                        c.p[:, w.v + 2 * head + j, n * P:(n + 1) * P], c.const("ident"))
            for j in range(2):
                for n in range(2):
                    last = nc.tensor.transpose(c.ps[:, 5, (2 * j + n) * P:(2 * j + n + 1) * P],
                                               w.vc[:, 2 * head + j, n * P:(n + 1) * P], c.const("ident"))
            last.then_inc(v_turn, 1)
            pe.wait_ge(k_done, 4)
            pe.wait_ge(z_in, 8)
            for n in range(12):
                last = nc.tensor.transpose(c.ps[:, n // 4, n % 4 * P:(n % 4 + 1) * P], w.e_neg[:, n * P:(n + 1) * P],
                                           c.const("ident"))
                if n % 4 == 3:
                    last.then_inc(k_turn, 1)

        @block.scalar
        def _(act):
            chain = Chain(act, act_chain)
            act.wait_ge(z, 1)
            for to, n, bank, frm, z_ in parts:
                src = c.ps[:, bank, frm:frm + n]
                nc.scalar.activation(w.g[:, to:to + n], src, ACT.Identity, bias=b[z_]).then_inc(z_in, 1)
                nc.scalar.activation(w.cum[:, to:to + n], src, ACT.Abs, bias=b[z_]).then_inc(z_in, 1)
            act.wait_ge(z_in, 8)
            chain(nc.scalar.activation(w.cum, w.cum, ACT.Exp, scale=-1.0))
            nc.scalar.activation(w.cum, w.cum, ACT.Ln, bias=1.0).then_inc(soft, 1)
            act.wait_ge(v_turn, 1)
            for j in range(2):
                nc.scalar.activation(w.v_tok[:, 0:4, j * P:(j + 1) * P],
                                     c.ps[:, 3 + j, :].rearrange("p (b n) -> p b n", n=P), ACT.Copy).then_inc(v_out, 1)
                nc.scalar.activation(w.v_tok[:, 4:6, j * P:(j + 1) * P],
                                     c.ps[:, 5, 2 * j * P:2 * (j + 1) * P].rearrange("p (b n) -> p b n", n=P), ACT.Copy
                                     ).then_inc(v_out, 1)
            act.wait_ge(gate, 1)
            nc.scalar.activation(w.e_neg, w.cum, ACT.Exp, scale=-1.0 / 16).then_inc(exps, 1)
            nc.scalar.activation(w.e_pos[:, 0:S], w.cum[:, 0:S], ACT.Exp, scale=1.0 / 16).then_inc(exps, 1)
            nc.scalar.activation(w.e_pos[:, S:2 * S], w.cum[:, SEG:SEG + S], ACT.Exp, scale=1.0 / 16).then_inc(exps, 1)
            nc.scalar.activation(w.em, w.half, ACT.Exp, scale=1.0 / 16).then_inc(exps, 1)
            for i in range(3):
                act.wait_ge(k_turn, i + 1)
                nc.scalar.activation(w.k_tok[:, i * S:(i + 1) * S], c.ps[:, i, :], ACT.Copy).then_inc(k_out, 1)

        @block.vector
        def _(dve):
            chain = Chain(dve, chain_s)
            dve.wait_ge(soft, 1)
            chain(nc.vector.scalar_tensor_tensor(w.g, w.g, 0.0, w.cum, ALU.min, ALU.subtract))
            for i in range(3):
                chain(nc.vector.tensor_tensor_scan(w.cum[:, i * S:(i + 1) * S], c.const("scan"),
                                                   w.g[:, i * S:(i + 1) * S], 0.0, ALU.mult, ALU.add))
            chain(nc.vector.tensor_copy(w.tot, chunks(w.cum)[:, :, CH - 1]))
            chain(nc.vector.tensor_scalar(w.half, w.tot, 0.5, None, ALU.mult))
            f, r = w.cum[:, 0:SEG], w.cum[:, SEG:2 * SEG]
            chain(nc.vector.tensor_tensor(chunks(f), chunks(f), bc(w.half[:, 0:12], 12), ALU.subtract))
            chain(nc.vector.tensor_tensor(r, w.g[:, SEG:2 * SEG], r, ALU.subtract))
            chain(nc.vector.tensor_tensor(chunks(r), chunks(r), bc(w.half[:, 12:24], 12), ALU.add))
            nc.vector.tensor_scalar(w.cum, w.cum, 80.0 * 16, -80.0 * 16, ALU.min, ALU.max).then_inc(gate, 1)
            dve.wait_ge(exps, 1)
            k, kc = c.p[:, w.k + head, :], w.kc[:, head, :]
            for to, n, _, _, _ in parts:
                x = w.e_neg[:, to:to + n]
                nc.vector.tensor_tensor(x, x, k if n == S else kc, ALU.mult).then_inc(k_done, 1)
            dve.wait_ge(exps, 4)
            q = c.p[:, w.q + head, :]
            for z_ in range(2):
                x = w.e_pos[:, z_ * S:(z_ + 1) * S]
                nc.vector.scalar_tensor_tensor(x, q, P ** -0.5, x, ALU.mult, ALU.mult).then_inc(q_done, 1)
            em = w.em
            for lo, n in ((0, 7), (8, 3), (12, 7), (20, 3)):
                chain(nc.vector.tensor_tensor(w.step[:, lo:lo + n], em[:, lo:lo + n], em[:, lo + 1:lo + n + 1], ALU.mult))
            chain(nc.vector.tensor_tensor(w.step[:, 11:12], em[:, 11:12], em[:, 0:1], ALU.mult))
            chain(nc.vector.tensor_tensor(w.step[:, 23:24], em[:, 20:21], em[:, 19:20], ALU.mult))


def gla_scan(c, name, w, head, sums):
    nc = c.nc
    scored, masked, update, added, state, summed = (c.sem(f"{name}_{n}") for n in
                                                    ("scored", "masked", "update", "added", "state", "summed"))
    squared, ms, rs_s, silu, chain_s = (c.sem(f"{name}_{n}") for n in ("squared", "ms", "rs", "silu", "chain"))
    STEPS = NCH + LNC
    seg = w.SEG

    def chunk(z, s):
        if s < LNC:
            return 12 * z + 8 + (s if z == 0 else LNC - 1 - s), None
        n = s - LNC if z == 0 else NCH - 1 - (s - LNC)
        return 12 * z + n, n

    def step_col(z, s):
        a, b = chunk(z, s)[0], chunk(z, s + 1)[0]
        return min(a, b) if abs(a - b) == 1 and s != LNC - 1 else 12 * z + 11

    quarter = range(8 * head, 8 * head + 8)
    sq = [w.g[:, 0:S], w.g[:, S:2 * S]]
    rs = w.g[:, 2 * S:3 * S]
    t1 = [w.cum[:, 0:S], w.cum[:, S:2 * S]]
    with nc.Block() as block:
        @block.sync
        def _(sp):
            if head == 0:
                sums.load_bias(sp, [c.mod[:, 2 * KT:]])
            for n in quarter:
                sums.load(sp, n)

        @block.gpsimd
        def _(pool):
            for n in quarter:
                sums.add_pool(pool, n)

        @block.tensor
        def _(pe):
            for z in range(2):
                for n in range(NCH):
                    rows = slice(64 * (n % 2), 64 * (n % 2) + 64)
                    last = nc.tensor.matmul(c.ps[rows, z, n * CH:(n + 1) * CH], w.e_neg[:, z * seg + n * CH:z * seg + (n + 1) * CH],
                                            w.e_pos[:, z * S + n * CH:z * S + (n + 1) * CH], start=True, stop=True)
            last.then_inc(scored, 1)

            def update_of(z, s):
                g, _ = chunk(z, s)
                rows = slice(64 * (g % 2), 64 * (g % 2) + 64)
                block_of = g % 12 // 2
                if s >= 2:
                    pe.wait_ge(added, 2 * (s - 2) + z + 1)
                nc.tensor.matmul(c.ps[:, 4 + 2 * z + s % 2, 0:2 * P], w.k_tok[rows, (g // 2) * P:(g // 2 + 1) * P],
                                 w.v_tok[rows, block_of, :], start=True, stop=True).then_inc(update, 1)

            for z in range(2):
                update_of(z, 0)
            pe.wait_ge(masked, 4)
            for z in range(2):
                for n in range(NCH // 2):
                    for j in range(2):
                        nc.tensor.matmul(c.ps[:, 2 + j, n * P:(n + 1) * P], w.v_tok[:, n, j * P:(j + 1) * P],
                                         w.scores[:, z * S + n * P:z * S + (n + 1) * P], start=(z == 0 and n == 0),
                                         stop=False, skip_group_check=True)
            for s in range(STEPS):
                for z in range(2):
                    if 1 <= s < STEPS - 1:
                        update_of(z, s)
                if s < LNC:
                    continue
                for z in range(2):
                    _, n = chunk(z, s)
                    pe.wait_ge(state, 2 * (s - 1) + z + 1)
                    for j in range(2):
                        last = nc.tensor.matmul(c.ps[:, 2 + j, n * CH:(n + 1) * CH],
                                                w.state[:, z, s % 2, j * P:(j + 1) * P],
                                                w.e_pos[:, z * S + n * CH:z * S + (n + 1) * CH], start=False,
                                                stop=(s == STEPS - 1 and z == 1), skip_group_check=True)
                    last.then_inc(summed, 1)
            for j in range(2):
                pe.wait_ge(squared, j + 1)
                last = nc.tensor.matmul(c.ps[:, 1, :], c.const("ones"), sq[j], start=(j == 0), stop=(j == 1))
            last.then_inc(ms, 1)

        @block.scalar
        def _(act):
            for j in range(2):
                r = c.p[:, w.r + 2 * head + j, :]
                nc.scalar.activation(r, r, ACT.Silu).then_inc(silu, 1)
            act.wait_ge(summed, 2 * NCH)
            for j in range(2):
                nc.scalar.activation(sq[j], c.ps[:, 2 + j, :], ACT.Square).then_inc(squared, 1)
            act.wait_ge(ms, 1)
            nc.scalar.activation(rs, c.ps[:, 1, :], ACT.Ln, bias=c.const("eps"), scale=1.0 / (2 * P)).then_inc(rs_s, 1)
            act.wait_ge(rs_s, 1)
            nc.scalar.activation(rs, rs, ACT.Exp, scale=-0.5).then_inc(rs_s, 1)

        @block.vector
        def _(dve):
            dve.wait_ge(scored, 1)
            pairs = lambda t, par: t.rearrange("p (n h i) -> p n h i", h=2, i=CH)[64 * par:64 * par + 64, :, par, :]
            for z, mask in enumerate(("gla_f", "gla_b")):
                for par in range(2):
                    m = c.const(mask).rearrange("p (n i) -> p n i", i=CH)[64 * par:64 * par + 64]
                    nc.vector.tensor_tensor(pairs(w.scores[:, z * S:(z + 1) * S], par), pairs(c.ps[:, z, :], par), m,
                                            ALU.mult).then_inc(masked, 1)
            for s in range(STEPS - 1):
                for z in range(2):
                    n = 2 * s + z
                    dve.wait_ge(update, n + 1)
                    new, old = w.state[:, z, (s + 1) % 2, :], w.state[:, z, s % 2, :]
                    u = c.ps[:, 4 + 2 * z + s % 2, 0:2 * P]
                    if s > LNC:
                        dve.wait_ge(summed, 2 * (s - 1 - LNC) + z + 1)
                    at = step_col(z, s)
                    decay = w.step[:, at:at + 1]
                    if s == 0:
                        nc.vector.tensor_copy(new, u).then_inc(added, 1)
                    else:
                        dve.wait_ge(state, n - 1)
                        nc.vector.tensor_tensor(new, u, old, ALU.add).then_inc(added, 1)
                    dve.wait_ge(added, n + 1)
                    nc.vector.tensor_scalar(new, new, decay, None, ALU.mult).then_inc(state, 1)
            chain = Chain(dve, chain_s)
            dve.wait_ge(rs_s, 2)
            dve.wait_ge(silu, 2)
            for j in range(2):
                gain = c.cols2[:, C2_AT["gla_norm_g"] + j:C2_AT["gla_norm_g"] + j + 1]
                chain(nc.vector.scalar_tensor_tensor(t1[j], c.ps[:, 2 + j, :], gain, rs, ALU.mult, ALU.mult))
                chain(nc.vector.tensor_tensor(c.y[:, 2 * head + j, :], t1[j], c.p[:, w.r + 2 * head + j, :], ALU.mult))


def route(c, name, m):
    nc = c.nc
    B = m.B
    names = ("loaded", "logits", "sig", "chosen", "placed", "chain", "turned", "high", "low")
    loaded, logits, sig, chosen_s, placed, chain_s, turned, high, low = (c.sem(f"{name}_{n}") for n in names)
    router_w = c.p[:, 0, 0:KT * E_N]
    cell = [c.p[:, 1 + i, :] for i in range(13)]
    score, sel, rank, best_in, top, t0, t1, gs, chosen, slot, cnt, big, num = (x[:, 0:B * E_N] for x in cell)
    wide = c.p[:, 14, :]
    four = lambda t: t.rearrange("p (g e) -> p g e", e=4)
    with nc.Block() as block:
        @block.sync
        def _(sp):
            sp.dma_start(router_w, c.dram["router"]).then_inc(loaded, 16)
            sp.wait_ge(loaded, 16)

        @block.tensor
        def _(pe):
            pe.wait_ge(loaded, 16)
            for b in range(B):
                for kt in range(KT):
                    last = nc.tensor.matmul(c.ps[:, 0, b * E_N:(b + 1) * E_N], c.h[:, kt, b * P:(b + 1) * P],
                                            router_w[:, kt * E_N:(kt + 1) * E_N], start=(kt == 0), stop=(kt == KT - 1))
            last.then_inc(logits, 1)
            for n in range(2 * B):
                b, half = divmod(n, 2)
                if n >= 6:
                    pe.wait_ge(low, n - 5)
                for i in range(4):
                    last = nc.tensor.transpose(c.ps[:, 2 + n % 6, i * P:(i + 1) * P],
                                               c.h[:, 4 * half + i, b * P:(b + 1) * P], c.const("ident"))
                last.then_inc(turned, 1)
            pe.wait_ge(chosen_s, 1)
            for b in range(B):
                at = c.ps[:, 1, b * E_N:(b + 1) * E_N]
                for b2 in range(b + 1):
                    lhsT = c.const("before") if b2 == b else c.const("ones")
                    nc.tensor.matmul(at, lhsT, top[:, b2 * E_N:(b2 + 1) * E_N], start=(b2 == 0), stop=(b2 == b))
            for b in range(B):
                last = nc.tensor.matmul(c.ps[:, 1, B * E_N:(B + 1) * E_N], c.const("ones"),
                                        top[:, b * E_N:(b + 1) * E_N], start=(b == 0), stop=(b == B - 1))
            last.then_inc(placed, 1)

        @block.scalar
        def _(act):
            act.wait_ge(logits, 1)
            nc.scalar.activation(score, c.ps[:, 0, 0:B * E_N], ACT.Sigmoid).then_inc(sig, 1)
            for n in range(2 * B):
                b, half = divmod(n, 2)
                act.wait_ge(turned, n + 1)
                nc.scalar.activation(m.h_hi[:, b, half * S:(half + 1) * S], c.ps[:, 2 + n % 6, :], ACT.Copy
                                     ).then_inc(high, 1)

        @block.vector
        def _(dve):
            chain = Chain(dve, chain_s)
            for n in range(2 * B):
                b, half = divmod(n, 2)
                dve.wait_ge(high, n + 1)
                cols = slice(half * S, (half + 1) * S)
                nc.vector.tensor_tensor(m.h_lo[:, b, cols], c.ps[:, 2 + n % 6, :], m.h_hi[:, b, cols].bitcast(F32),
                                        ALU.subtract).then_inc(low, 1)
            dve.wait_ge(sig, 1)
            bias = c.cols2[:, C2_AT["b_router"]:C2_AT["b_router"] + E_N]
            for b in range(B):
                chain(nc.vector.tensor_tensor(sel[:, b * E_N:(b + 1) * E_N], score[:, b * E_N:(b + 1) * E_N], bias,
                                              ALU.add))
            chain(nc.vector.memset(rank, 0.0))
            for i in range(4):
                for j in range(i + 1, 4):
                    si, sj = four(sel)[:, :, i], four(sel)[:, :, j]
                    ri, rj = four(rank)[:, :, i], four(rank)[:, :, j]
                    ge = t0[:, 0:16]
                    chain(nc.vector.tensor_tensor(ge, si, sj, ALU.is_ge))
                    chain(nc.vector.tensor_tensor(rj, rj, ge, ALU.add))
                    chain(nc.vector.tensor_tensor(ri, ri, ge, ALU.subtract))
                    chain(nc.vector.tensor_scalar(ri, ri, 1.0, None, ALU.add))
            chain(nc.vector.tensor_scalar(top, rank, 1.5, None, ALU.is_lt))
            chain(nc.vector.tensor_tensor(t0, top, sel, ALU.mult))
            chain(nc.vector.tensor_reduce(gs[:, 0:16], four(t0), AXX, ALU.add))
            groups = gs[:, 0:16].rearrange("p (b g) -> p b g", g=4)
            win = t1[:, 0:16]
            wins = win.rearrange("p (b g) -> p b g", g=4)
            ge = best_in[:, 0:4]
            chain(nc.vector.memset(win, 0.0))
            for i in range(4):
                for j in range(i + 1, 4):
                    chain(nc.vector.tensor_tensor(ge, groups[:, :, i], groups[:, :, j], ALU.is_ge))
                    chain(nc.vector.tensor_tensor(wins[:, :, i], wins[:, :, i], ge, ALU.add))
                    chain(nc.vector.tensor_tensor(wins[:, :, j], wins[:, :, j], ge, ALU.subtract))
                    chain(nc.vector.tensor_scalar(wins[:, :, j], wins[:, :, j], 1.0, None, ALU.add))
            chain(nc.vector.tensor_scalar(win, win, 2.5, None, ALU.is_gt))
            for e in range(4):
                chain(nc.vector.tensor_tensor(four(top)[:, :, e], four(top)[:, :, e], win, ALU.mult))
            nc.vector.tensor_tensor(chosen, top, score, ALU.mult).then_inc(chosen_s, 1)
            dve.wait_ge(chosen_s, 1)
            by_token = lambda t: t.rearrange("p (b e) -> p b e", e=E_N)
            total = t1[:, 16:16 + B]
            chain(nc.vector.tensor_reduce(total, by_token(chosen), AXX, ALU.add))
            chain(nc.vector.reciprocal(total, total))
            for b in range(B):
                chain(nc.vector.tensor_scalar(chosen[:, b * E_N:(b + 1) * E_N], chosen[:, b * E_N:(b + 1) * E_N],
                                              total[:, b:b + 1], None, ALU.mult))
            dve.wait_ge(placed, 1)
            count, blocks, ends, base = (cnt[:, i * E_N:(i + 1) * E_N] for i in range(4))
            chain(nc.vector.tensor_copy(count, c.ps[:, 1, B * E_N:(B + 1) * E_N]))
            chain(nc.vector.tensor_scalar(blocks, count, 0.5, None, ALU.is_gt))
            for j in range(1, B):
                chain(nc.vector.tensor_scalar(t0[:, 0:E_N], count, j * P + 0.5, None, ALU.is_gt))
                chain(nc.vector.tensor_tensor(blocks, blocks, t0[:, 0:E_N], ALU.add))
            chain(nc.vector.tensor_tensor_scan(ends, c.const("ones", E_N), blocks, 0.0, ALU.mult, ALU.add))
            chain(nc.vector.tensor_tensor(base, ends, blocks, ALU.subtract))
            chain(nc.vector.tensor_scalar(base, base, float(P), None, ALU.mult))
            for b in range(B):
                at = slice(b * E_N, (b + 1) * E_N)
                chain(nc.vector.tensor_tensor(slot[:, at], c.ps[:, 1, at], base, ALU.add))
            chain(nc.vector.tensor_tensor(big, slot, top, ALU.mult))
            chain(nc.vector.tensor_reduce(m.slots[:, B:2 * B], by_token(big), AXX, ALU.max))
            chain(nc.vector.tensor_scalar(t0, top, -65536.0, 65536.0, ALU.mult, ALU.add))
            chain(nc.vector.tensor_tensor(big, big, t0, ALU.add))
            chain(nc.vector.tensor_reduce(m.slots[:, 0:B], by_token(big), AXX, ALU.min))
            for z in range(2):
                for b in range(B):
                    at = slice(b * E_N, (b + 1) * E_N)
                    chain(nc.vector.tensor_scalar(t0[:, at], slot[:, at], m.slots[:, z * B + b:z * B + b + 1], None,
                                                  ALU.is_equal))
                chain(nc.vector.tensor_tensor(t0, t0, chosen, ALU.mult))
                chain(nc.vector.tensor_reduce(m.weights[:, z * B:(z + 1) * B], by_token(t0), AXX, ALU.add))
            NB = m.MAX_BLOCKS
            cmp = wide[:, 0:NB * E_N].rearrange("p (j e) -> p j e", e=E_N)
            j_of = c.const("iota")[:, 0:NB].unsqueeze(2).to_broadcast([P, NB, E_N])
            chain(nc.vector.tensor_tensor(cmp, ends.unsqueeze(1).to_broadcast([P, NB, E_N]), j_of, ALU.is_le))
            chain(nc.vector.tensor_reduce(num[:, 0:NB], cmp, AXX, ALU.add))
            chain(nc.vector.tensor_scalar(num[:, 0:NB], num[:, 0:NB], E_N - 1.0, None, ALU.min))
            chain(nc.vector.tensor_scalar(t0[:, 0:NB // 2], c.const("iota")[:, 0:NB // 2], 2.0, ends[:, E_N - 1:E_N],
                                          ALU.mult, ALU.is_lt))
            chain(nc.vector.tensor_reduce(num[:, NB:NB + 1], t0[:, 1:NB // 2], AXX, ALU.add))
            chain(nc.vector.tensor_copy(m.numbers[:, 0:NB + 1], num[:, 0:NB + 1]))


class Experts:

    B = S // P
    MAX_BLOCKS = 24

    def __init__(self, c):
        flat = lambda t: t.rearrange("p a n -> p (a n)")
        p, h = flat(c.p[:, :, :]), flat(c.h[:, :, :])
        big = KT * DE
        self.raw = [p[:, i * big:(i + 1) * big] for i in range(3)]
        self.w_hi = c.alias("moe_w_hi", "ring", 0, [4, D], F32R)
        self.w_lo = c.alias("moe_w_lo", "ring", 4 * D, [4, D], F32R)
        self.h_hi = c.alias("tok_hi", "y", 0, [4, D], F32R)
        self.h_lo = c.alias("tok_lo", "vt", 0, [4, D], F32R)
        self.xg, self.he, self.sil, self.g1 = h[:, 0:D], h[:, 4 * S:5 * S], h[:, 5 * S:6 * S], h[:, 6 * S:7 * S]
        tail = 8 * D
        self.g2 = c.ring[:, tail:tail + S]
        self.g = c.alias("g", "ring", tail + S, [S], F32R)
        self.gT = [c.alias(f"gT{i}", "ring", tail + (2 + i) * S, [S], F32R) for i in range(2)]
        self.o_hi = c.alias("o_hi", "ring", tail + 4 * S, [D], F32R)
        self.o_lo = c.o_lo
        self.x_hi, self.x_lo = (c.alias(n, "w2b", i * D, [D], F32R) for i, n in enumerate(("moe_x_hi", "moe_x_lo")))
        self.he_hi, self.he_lo = (c.alias(n, "w2b", 2 * D + i * DE, [DE], F32R)
                                  for i, n in enumerate(("moe_he_hi", "moe_he_lo")))
        self.numbers = c.numbers
        self.slots, self.weights, self.slot_w = c.small[:, 32:40], c.small[:, 40:48], c.small[:, 48:50]


def experts(c, name, gain, m):
    nc = c.nc
    B = m.B
    loaded = [c.sem(f"{name}_{n}_loaded") for n in ("w1", "w3", "w2")]
    names = ("g_part", "g_ready", "slot_w", "gathered", "g_turned", "slot_w_out", "xg_out", "gT_out", "x_turned", "x_high",
             "x_low", "high", "low", "low_pool", "used", "silu", "prod", "he_turned", "he_high", "he_low", "o_hi", "o_lo",
             "spread", "added", "moved")
    (g_part, g_ready, slot_w, gathered, g_turned, slot_w_out, xg_out, gT_out, x_turned, x_high, x_low, high, low, low_pool,
     used, silu, prod, he_turned, he_high, he_low, o_hi, o_lo, spread, added, moved) = (c.sem(f"{name}_{n}") for n in names)
    SPREAD = (2, 3, 0, 1)
    NBM = m.MAX_BLOCKS
    CHUNKS, UPS = 12, 8
    by_pool = lambda n: n % 3 == 2
    pool_count = lambda n: (n + 1) // 3
    dve_count = lambda n: n + 1 - pool_count(n)
    raw = lambda n: m.raw[n // 4][:, n % 4 * D:(n % 4 + 1) * D]
    cols = lambda t, n: t[:, n * P:(n + 1) * P]
    halves = [slice(0, S), slice(S, 2 * S)]

    def more_rounds(eng):
        return eng.value_load(m.numbers[0:1, NBM:NBM + 1], min_val=3, max_val=NBM // 2 - 1)

    def loop(eng, body):
        more = more_rounds(eng)
        body(0, 0, True)
        body(1, 1, False)
        with eng.Fori(1, more + 1) as r:
            body(0, 2 * r, False)
            body(1, 2 * r + 1, False)
        return 2 * more + 1

    def subtract_chunk(eng, ops, n, j, done):
        eng.wait_ge(high, j * CHUNKS + n + 1)
        ops.tensor_tensor(m.w_lo[:, n % 4, :], raw(n), m.w_hi[:, n % 4, :].bitcast(F32), ALU.subtract).then_inc(done, 1)

    with nc.Block() as block:
        @block.sync
        def _(sp):
            def load(i, j, first):
                e = sp.value_load(m.numbers[0:1, bass.ds(j, 1)], min_val=0, max_val=E_N - 1)
                for w, t in enumerate(("moe_gate", "moe_up", "moe_down")):
                    if not first:
                        sp.wait_ge(used, (j - 1) * CHUNKS + 4 * w + 4)
                    sp.dma_start(m.raw[w], c.dram[t][bass.ds(e, 1), :, :].rearrange("a p n -> p (a n)")
                                 ).then_inc(loaded[w], 16)

            loop(sp, load)

        @block.tensor
        def _(pe):
            def gather(j, first=False, second=False, third=False):
                pe.wait_ge(g_ready, j + 1)
                if not first:
                    pe.wait_ge(slot_w_out, j)
                if not (first or second):
                    pe.wait_ge(he_low, j - 1)
                    if not third:
                        pe.wait_ge(added, (j - 2) * KT)
                for z, g in enumerate((m.g1, m.g2)):
                    for b in range(B):
                        last = nc.tensor.matmul(c.ps[:, 7, 0:1], cols(g, b), m.weights[:, z * B + b:z * B + b + 1],
                                                start=(z == 0 and b == 0), stop=(z == 1 and b == B - 1))
                last.then_inc(slot_w, 1)
                for half in range(2):
                    for b in range(B):
                        for n, part in enumerate((m.h_hi, m.h_lo)):
                            last = nc.tensor.matmul(c.ps[:, half, :], cols(m.g, b), part[:, b, half * S:(half + 1) * S],
                                                    start=(b == 0 and n == 0), stop=(b == B - 1 and n == 1))
                last.then_inc(gathered, 1)
                if not first:
                    pe.wait_ge(gT_out, j)
                for b in range(B):
                    last = nc.tensor.transpose(cols(c.ps[:, 6, :], b), cols(m.g, b).bitcast(F32), c.const("ident"))
                last.then_inc(g_turned, 1)

            def wait_chunk(n, j):
                if by_pool(n):
                    pe.wait_ge(low_pool, j * pool_count(CHUNKS - 1) + pool_count(n))
                else:
                    pe.wait_ge(low, j * dve_count(CHUNKS - 1) + dve_count(n))

            def three(bank, x, n, at, start, stop):
                w_hi, w_lo = m.w_hi[:, n % 4, at], m.w_lo[:, n % 4, at]
                nc.tensor.matmul(bank, x[0], w_hi, start=start, stop=False)
                nc.tensor.matmul(bank, x[1], w_hi, start=False, stop=False)
                return nc.tensor.matmul(bank, x[0], w_lo, start=False, stop=stop)

            def ups(i, j, first):
                pe.wait_ge(x_low, 2 * (j + 1))
                if not first:
                    pe.wait_ge(o_hi, 2 * j)
                    pe.wait_ge(o_lo, 2 * j)
                for n in range(UPS):
                    wait_chunk(n, j)
                    for k in range(2):
                        kt = n % 4 * 2 + k
                        last = three(c.ps[:, 4 + n // 4, :], (cols(m.x_hi, kt), cols(m.x_lo, kt)), n,
                                     slice(k * DE, (k + 1) * DE), kt == 0, kt == KT - 1)
                    last.then_inc(used, 1)
                    if n >= 4 and not first:
                        spread_tile(1 - i, j - 1, n - 4)

            def turn_x(j):
                pe.wait_ge(xg_out, 2 * (j + 1))
                for kt in range(KT):
                    last = nc.tensor.transpose(cols(c.ps[:, 2 + kt // 4, :], kt % 4), cols(m.xg, kt), c.const("ident"))
                last.then_inc(x_turned, 1)

            def spread_tile(i, j, t, final=False):
                if t == 0:
                    pe.wait_ge(o_hi, 2 * (j + 1))
                    pe.wait_ge(o_lo, 2 * (j + 1))
                    pe.wait_ge(gT_out, j + 1)
                    pe.wait_ge(x_low, 2 * (j + 2))
                    if not final:
                        pe.wait_ge(xg_out, 2 * (j + 3))
                if t >= len(SPREAD):
                    pe.wait_ge(added, j * KT + t - len(SPREAD) + 1)
                bank = c.ps[:, SPREAD[t % len(SPREAD)], :]
                nc.tensor.matmul(bank, cols(m.o_hi, t), m.gT[i][:, :], start=True, stop=False)
                nc.tensor.matmul(bank, cols(m.o_lo, t), m.gT[i][:, :], start=False, stop=True).then_inc(spread, 1)

            def body(i, j, first):
                gather(j + 1, second=first, third=isinstance(j, int))
                ups(i, j, first)
                if not first:
                    for t in range(KT // 2, KT):
                        spread_tile(1 - i, j - 1, t)
                pe.wait_ge(prod, j + 1)
                pe.wait_ge(slot_w_out, j + 2)
                for f in range(ET):
                    last = nc.tensor.transpose(cols(c.ps[:, 7, :], f), cols(m.he, f), c.const("ident"))
                last.then_inc(he_turned, 1)
                if not first:
                    pe.wait_ge(added, j * KT - 2)
                turn_x(j + 1)
                pe.wait_ge(he_low, j + 1)
                for f in range(ET):
                    wait_chunk(UPS + f, j)
                    for half in range(2):
                        last = three(c.ps[:, 4 + half, :], (cols(m.he_hi, f), cols(m.he_lo, f)), UPS + f, halves[half],
                                     f == 0, f == ET - 1)
                    last.then_inc(used, 1)

            gather(0, True)
            turn_x(0)
            end = loop(pe, body)
            for t in range(KT):
                spread_tile(1, end, t, final=True)

        @block.scalar
        def _(act):
            def round_chunk(n, j, first):
                act.wait_ge(loaded[n // 4], 16 * (j + 1))
                if not (first and n < 4):
                    act.wait_ge(used, j * CHUNKS + n - 3)
                nc.scalar.activation(m.w_hi[:, n % 4, :], raw(n), ACT.Copy).then_inc(high, 1)

            def copy_slot_w(i, j, first):
                act.wait_ge(slot_w, j + 1)
                if not first:
                    act.wait_ge(o_lo, 2 * (j - 1))
                nc.scalar.activation(m.slot_w[:, i:i + 1], c.ps[:, 7, 0:1], ACT.Copy).then_inc(slot_w_out, 1)

            def copy_xg(j, very_first=False):
                act.wait_ge(gathered, j + 1)
                if not very_first:
                    act.wait_ge(x_turned, j)
                for half in range(2):
                    nc.scalar.activation(m.xg[:, halves[half]], c.ps[:, half, :], ACT.Copy).then_inc(xg_out, 1)

            def copy_gT(i, j, first):
                act.wait_ge(g_turned, j + 1)
                if not first:
                    act.wait_ge(spread, (j - 1) * KT)
                nc.scalar.activation(m.gT[i][:, :], c.ps[:, 6, :], ACT.Copy).then_inc(gT_out, 1)

            def round_x(j):
                act.wait_ge(x_turned, j + 1)
                for half in range(2):
                    nc.scalar.activation(m.x_hi[:, halves[half]], c.ps[:, 2 + half, :], ACT.Copy).then_inc(x_high, 1)

            def round_o(i, j, first=False):
                act.wait_ge(used, (j + 1) * CHUNKS)
                if not first:
                    act.wait_ge(spread, j * KT)
                for half in range(2):
                    nc.scalar.activation(m.o_hi[:, halves[half]], c.ps[:, 4 + half, :], ACT.Copy,
                                         scale=m.slot_w[:, i:i + 1]).then_inc(o_hi, 1)

            def body(i, j, first):
                for n in range(3):
                    round_chunk(n, j, first)
                if not first:
                    round_o(1 - i, j - 1, first=(isinstance(j, int) and j == 1))
                round_chunk(3, j, first)
                copy_slot_w(1 - i, j + 1, first)
                copy_xg(j + 1)
                for n in range(4, CHUNKS - 1):
                    round_chunk(n, j, first)
                act.wait_ge(used, j * CHUNKS + UPS)
                nc.scalar.activation(m.sil, c.ps[:, 4, :], ACT.Silu).then_inc(silu, 1)
                round_chunk(CHUNKS - 1, j, first)
                copy_gT(1 - i, j + 1, first)
                act.wait_ge(he_turned, j + 1)
                nc.scalar.activation(m.he_hi[:, :], c.ps[:, 7, :], ACT.Copy).then_inc(he_high, 1)
                round_x(j + 1)

            copy_slot_w(0, 0, True)
            copy_xg(0, True)
            copy_gT(0, 0, True)
            round_x(0)
            end = loop(act, body)
            round_o(1, end)

        @block.gpsimd
        def _(pool):
            def body(i, j, first):
                for n in filter(by_pool, range(CHUNKS)):
                    subtract_chunk(pool, nc.gpsimd, n, j, low_pool)

            loop(pool, body)

        @block.vector
        def _(dve):
            def build(j, first=False):
                if not first:
                    dve.wait_ge(g_turned, j)
                for z, g in enumerate((m.g1, m.g2)):
                    for b in range(B):
                        nc.vector.tensor_scalar(cols(g, b), c.const("iota"), m.slots[:, z * B + b:z * B + b + 1], None,
                                                ALU.is_equal).then_inc(g_part, 1)
                dve.wait_ge(g_part, 2 * B * (j + 1))
                nc.vector.tensor_scalar(m.slots, m.slots, -float(P), None, ALU.add).then_inc(moved, 1)
                nc.vector.tensor_tensor(m.g[:, :], m.g1, m.g2, ALU.add).then_inc(g_ready, 1)
                dve.wait_ge(moved, j + 1)

            def add(j, tiles):
                for t in tiles:
                    dve.wait_ge(spread, j * KT + t + 1)
                    nc.vector.scalar_tensor_tensor(c.x[:, t, :], c.ps[:, SPREAD[t % len(SPREAD)], :], gain[:, t:t + 1],
                                                   c.x[:, t, :], ALU.mult, ALU.add).then_inc(added, 1)

            def lower(j, chunks):
                for n in chunks:
                    subtract_chunk(dve, nc.vector, n, j, low)

            def lower_x(j):
                for half in range(2):
                    dve.wait_ge(x_high, 2 * j + half + 1)
                    nc.vector.tensor_tensor(m.x_lo[:, halves[half]], c.ps[:, 2 + half, :],
                                            m.x_hi[:, halves[half]].bitcast(F32), ALU.subtract).then_inc(x_low, 1)

            def lower_o(i, j):
                for half in range(2):
                    dve.wait_ge(o_hi, 2 * j + half + 1)
                    nc.vector.scalar_tensor_tensor(m.o_lo[:, halves[half]], c.ps[:, 4 + half, :], m.slot_w[:, i:i + 1],
                                                   m.o_hi[:, halves[half]].bitcast(F32), ALU.mult, ALU.subtract
                                                   ).then_inc(o_lo, 1)

            def body(i, j, first):
                lower(j, (0, 1))
                if not first:
                    lower_o(1 - i, j - 1)
                lower(j, (3,))
                build(j + 2)
                lower(j, (4, 6, 7))
                if not first:
                    add(j - 1, range(0, 2))
                lower(j, (9,))
                if not first:
                    add(j - 1, range(2, 3))
                lower(j, (10,))
                dve.wait_ge(silu, j + 1)
                if not first:
                    dve.wait_ge(he_turned, j)
                nc.vector.tensor_tensor(m.he, c.ps[:, 5, :], m.sil, ALU.mult).then_inc(prod, 1)
                if not first:
                    add(j - 1, range(3, KT))
                dve.wait_ge(he_high, j + 1)
                nc.vector.tensor_tensor(m.he_lo[:, :], c.ps[:, 7, :], m.he_hi[:, :].bitcast(F32), ALU.subtract
                                        ).then_inc(he_low, 1)
                lower_x(j + 1)

            build(0, True)
            build(1)
            lower_x(0)
            end = loop(dve, body)
            lower_o(1, end)
            add(end, range(KT))


def block_two(c, stop=None):
    nc, dram = c.nc, c.dram
    mod = lambda i: c.mod[:, i * KT:(i + 1) * KT]
    col = lambda n, k=8: c.cols2[:, C2_AT[n]:C2_AT[n] + k]
    tmp = c.ring[:, RING * D:]
    w = Gla(c)
    with c.stages():
        ctx_loaded = c.sem("ctx_loaded")
        with nc.Block() as block:
            @block.sync
            def _(sp):
                sp.dma_start(c.cols2[:, :], dram["cols2"]).then_inc(ctx_loaded, 16)
                for t in range(KT):
                    sp.dma_start(w.ctx_x[:, t, :], dram["ctxT"][t, :, :]).then_inc(ctx_loaded, 16)
                sp.wait_ge(ctx_loaded, 16 * (KT + 1))
        norm_modulate(c, "b2_norm1", c.x, c.h, col("norm1_g"), mod(1), mod(0), tmp=tmp, split=(c.a_hi, c.h_lo))
        norm_modulate(c, "b2_norm_ctx", w.ctx_x, w.ctx_h, col("norm1_g"), c.ctxmod[:, KT:2 * KT], c.ctxmod[:, 0:KT],
                      n_tok=CTX, tmp=tmp, split=(c.ctx_hi, c.ctx_lo))
        gla_project(c, w)
    if stop == "gla_in":
        return
    with c.stages():
        slots = quarters(c.ring[:, 0:4 * D].rearrange("p (a n) -> p a n", n=D))
        rest = AdaLNPool(c, "b2_mod", L, 2, 4, slots[0:3], [(c.cond[:, :], quarters(c.w2b[:, :, :]))],
                         product=slots[3])
        for head in range(4):
            with c.stages():
                gla_prepare(c, f"gla_prep{head}", w, head)
                gla_scan(c, f"gla_scan{head}", w, head, rest)
        adaln_finish(c, "b2_mod", rest)
    if stop == "gla":
        return
    moe = Experts(c)
    with c.stages():
        gla_out = SplitLinear(c, "gla_out", KT, lambda t: dram["gla_out"][bass.ds(t, 1), :, :].rearrange("a p n -> p (a n)"))
        with nc.Block() as block:
            @block.sync
            def _(sp):
                gla_out.prefetch(sp)
        split_stage(c, gla_out, c.y_lo, add_residual(c, gla_out, mod(2)), x=c.y)
        norm_modulate(c, "b2_norm2", c.x, c.h, col("norm2_g"), mod(4), mod(3), tmp=tmp)
        route(c, "route", moe)
    if stop == "route":
        return
    with c.stages():
        experts(c, "moe", mod(5), moe)
    if stop == "moe":
        return
    with c.stages():
        norm_modulate(c, "final", c.x, c.h, col("final_g"), None, None, tmp=tmp)
        stored = c.sem("out_stored")
        with nc.Block() as block:
            @block.sync
            def _(sp):
                for t in range(KT):
                    sp.dma_start(dram["out"][t, :, :], c.h[:, t, :]).then_inc(stored, 16)
                sp.wait_ge(stored, 16 * KT)


def first_adaln(c):
    nc = c.nc
    own_cond, ready = load_cond(c, "own", 0)
    ctx_cond, _ = load_cond(c, "ctx", L + 1, dst=c.cond_ctx[:, :])
    p = c.p[:, :, :].rearrange("p a n -> p (a n)")
    sums = AdaLN(c, "mod0", 0, 0, 2, [p[:, i * D:(i + 1) * D] for i in range(8)],
                 [(c.cond[:, :], quarters(c.y[:, :, :])[0:2])])
    const_loaded, x_loaded = c.sem("const_loaded"), c.sem("x_loaded")
    with nc.Block() as block:
        @block.sync
        def _(sp):
            for n in range(sums.pieces):
                sums.load(sp, n)
            sums.load_bias(sp, [c.mod[:, 0:2 * KT]])
            sp.dma_start(c.k[:, :], c.dram["const"]).then_inc(const_loaded, 16)
            for t in range(KT):
                sp.dma_start(c.x[:, t, :], c.dram["xT"][t, :, :]).then_inc(x_loaded, 16)
            sp.wait_ge(const_loaded, 16)
            sp.wait_ge(x_loaded, 16 * KT)

        @block.scalar
        def _(act):
            own_cond(act)
            act.wait_ge(ready, 1)
            ctx_cond(act)

        @block.vector
        def _(dve):
            dve.wait_ge(ready, 1)
            for n in range(sums.pieces):
                sums.add(dve, n)
    adaln_finish(c, "mod0", sums)


def build(nc, dram):
    with ExitStack() as ctx:
        c = Core(nc, ctx, dram)
        with c.stages():
            first_adaln(c)
        with nc.Fori(0, L) as layer:
            with c.stages():
                block_one_layer(c, layer)
        block_two(c)


def kernel(**inputs):
    import concourse.bacc as bacc
    from concourse.bass_utils import run_bass_kernel_spmd

    nc = bacc.Bacc("TRN2", target_bir_lowering=False, num_devices=1)
    arrays = {f"in_{n}": a for n, a in host_layout(inputs).items()}
    dram = {n[3:]: nc.dram_tensor(n, a.shape, F32, kind="ExternalInput").ap() for n, a in arrays.items()}
    dram["out"] = nc.dram_tensor("out", (KT, P, S), F32, kind="ExternalOutput").ap()
    build(nc, dram)
    r = run_bass_kernel_spmd(nc, [arrays], core_ids=[0])
    return np.ascontiguousarray(r.results[0]["out"].reshape(D, S).T).reshape(1, S, D)


def host_layout(i):
    f = np.float32
    A = {k: np.asarray(v) for k, v in i.items()}

    def tiles(w, k_tiles=None):
        K, N = w.shape
        return np.ascontiguousarray(w.reshape(K // P, P, N // P, P).transpose(2, 1, 0, 3).reshape(N // P, P, K))

    def cols(v):
        return v.reshape(-1, P).T

    out = {"xT": np.ascontiguousarray(A["x"][0].T.reshape(KT, P, S))}
    w_in = np.concatenate([A["w_in"], np.zeros((L, D, IN_T * P - A["w_in"].shape[2]), f)], axis=2)
    out["w_in"] = np.concatenate([tiles(w_in[l]) for l in range(L)])
    out["w_out"] = np.concatenate([tiles(A["w_out"][l]) for l in range(L)])
    pairs = lambda w: w.reshape(*w.shape[:-1], 2, FT, P).swapaxes(-3, -2).reshape(*w.shape)
    out["ffn_up"] = np.concatenate([tiles(pairs(A["ffn_up"][l])) for l in range(L)])
    out["ffn_down"] = np.concatenate([tiles(A["ffn_down"][l]) for l in range(L)])
    ada = lambda w: w.reshape(KT, P, 6 * D).transpose(1, 0, 2)
    out["ada"] = np.stack([ada(A["ada_w"][0]), ada(A["ada_w"][1]), ada(A["w_mod_2"][0])])
    out["ada_b"] = np.stack([cols(v) for v in (A["ada_b"][0], A["ada_b"][1], A["b_mod_2"][0])])
    out["cond"] = np.stack([cols(v) for v in (A["c"][0], A["c"][0], A["c_2"][0], A["c_ctx_2"])])

    lam_init = [0.8 - 0.6 * math.exp(-0.3 * l) for l in range(L)]
    packed = []
    for l in range(L):
        taps = np.concatenate([A["ffn_conv"][l], A["ffn_conv_b"][l][None]])
        taps = pairs(taps).reshape(4, 2 * FT, P).transpose(2, 1, 0).reshape(P, 8 * FT)
        f_b = np.zeros((P, 1), f)
        f_b[0:4, 0] = A["fx_f_b"][l]
        lam = np.concatenate([A["df_lam_q1"][l], A["df_lam_q2"][l], A["df_lam_k1"][l], A["df_lam_k2"][l]])
        part = {
            "norm1_g": cols(A["norm1_g"][l]), "norm2_g": cols(A["norm2_g"][l]), "rw_mu": cols(A["rw_mu"][l]),
            "rw_w0": cols(A["rw_w0"][l]), "rw_a0": cols(A["rw_a0"][l]), "rw_k_k": cols(A["rw_k_k"][l]),
            "rw_k_a": cols(A["rw_k_a"][l]), "rw_r_k": cols(A["rw_r_k"][l].reshape(-1)),
            "rw_ln_g": cols(A["rw_ln_g"][l]), "rw_ln_b": cols(A["rw_ln_b"][l]),
            "df_q_g": np.tile(A["df_q_g"][l], 4)[:, None], "df_k_g": np.tile(A["df_k_g"][l], 4)[:, None],
            "df_sub_g": np.tile(A["df_sub_g"][l], 2)[:, None], "sg_ln_g": cols(A["sg_ln_g"][l]),
            "sg_ln_b": cols(A["sg_ln_b"][l]), "fx_q_g": np.tile(A["fx_q_g"][l], 2)[:, None],
            "fx_k_g": np.tile(A["fx_k_g"][l], 2)[:, None], "fx_f_b": f_b,
            "lam_init": np.full((P, 1), lam_init[l], f), "lam_vec": np.tile(lam[None, :], (P, 1)),
            "ffn_tap": taps, "ffn_bias": np.zeros((P, 44), f),
        }
        packed.append(np.concatenate([part[n].astype(f, copy=False) for n, _ in COLS], axis=1))
    out["cols"] = np.stack(packed)
    out["rw_lora"] = np.concatenate([A["rw_w_up"], A["rw_a_up"], A["rw_g_up"]], axis=1)
    out["sg_wT"] = np.ascontiguousarray(A["sg_w"].transpose(0, 3, 1, 2).reshape(L, P, 4 * P))
    out["sg_b"] = A["sg_b"]
    pick = np.zeros((4, 256), f)
    for g in range(4):
        pick[g, g * 64:(g + 1) * 64] = 1.0
    out["sg_pick"] = pick
    out["const"] = constants()

    w = A["gla_w_in_2"][0]
    q, k, v, r = w[:, 0:512], w[:, 512:1024], w[:, 1024:2048], w[:, 2048:3072]
    out["gla_in"] = tiles(np.concatenate([q, r, k, v], axis=1))
    low = np.zeros((D, 64), f)
    low[:, 0:16], low[:, 32:48] = A["gla_w_gate_a_2"][0, 0], A["gla_w_gate_a_2"][0, 1]
    out["gla_low"] = np.ascontiguousarray(low.reshape(KT, P, 64).transpose(1, 0, 2).reshape(P, KT * 64))
    gb = np.zeros((P, 512), f)
    gb[0:16], gb[32:48] = A["gla_w_gate_b_2"][0, 0], A["gla_w_gate_b_2"][0, 1]
    out["gla_gb"] = gb
    out["gla_out"] = tiles(A["gla_w_out_2"][0])
    out["ctxT"] = np.ascontiguousarray(A["ctx_2"][0].T.reshape(KT, P, CTX))
    part = {"norm1_g": cols(A["norm1_g_2"][0]), "norm2_g": cols(A["norm2_g_2"][0]), "final_g": cols(A["final_g_2"]),
            "b_gate": cols(A["gla_b_gate_2"][0].reshape(-1)), "gla_norm_g": cols(A["gla_norm_g_2"][0]),
            "b_router": np.tile(A["b_router_2"][None, :], (P, 1))}
    out["cols2"] = np.concatenate([part[n] for n, _ in COLS2], axis=1)
    out["router"] = np.ascontiguousarray(A["w_router_2"].reshape(KT, P, E_N).transpose(1, 0, 2).reshape(P, KT * E_N))

    def experts(w):
        return np.ascontiguousarray(w.reshape(E_N, -1, P, w.shape[2]).transpose(0, 2, 1, 3).reshape(E_N, P, -1))

    out["moe_gate"], out["moe_up"], out["moe_down"] = (experts(A[n][0]) for n in ("w_gate_e_2", "w_up_e_2", "w_down_e_2"))
    return out


def constants():
    f = np.float32
    n = np.arange(P)
    k = {"ident": np.eye(P), "ones": np.ones((P, P)), "bo64": np.kron(np.eye(2), np.ones((64, 64))),
         "bo32": np.kron(np.eye(4), np.ones((32, 32)))}
    perm = np.zeros((P, P))
    for m in range(P):
        if m % 32 < 16:
            perm[m + 16, m] = -1.0
        else:
            perm[m - 16, m] = 1.0
    k["perm"] = perm
    inv = (1.0 / (f(10000.0) ** (np.arange(0, 32, 2, dtype=f) / f(32)))).astype(f)
    ang = (np.arange(S, dtype=f)[None, :] * inv[:, None]).astype(f)
    k["cos"], k["sin"] = np.tile(np.cos(ang), (8, 1)), np.tile(np.sin(ang), (8, 1))
    k["mask_causal"] = np.where(n[None, :] <= n[:, None], 0.0, NEG)
    k["mask_chunk"] = np.where(n[None, :] // 64 <= n[:, None] // 64, 0.0, NEG)
    k["scan"] = np.tile((np.arange(S) % CH != 0).astype(f)[None, :], (P, 1))
    r, q = n[:, None], n[None, :]
    head, block16 = r // 64 == q // 64, r // 16 == q // 16
    four = lambda m: np.tile(m.astype(f), (1, 4))
    k["m_ld"], k["m_ldT"] = four(head & block16 & (q < r)), four(head & block16 & (q > r))
    k["m_loT"], k["m_kaT"] = four(head & ~block16 & (q > r)), four(head & (q > r))
    k["m_r"] = four(q % 64 >= r % 64)
    k["ident4"] = four(r == q)
    t = np.arange(64)
    k["gla_f"] = np.tile((t[None, :] >= t[:, None]).astype(f), (2, 4))
    k["gla_b"] = np.tile((t[None, :] <= t[:, None]).astype(f), (2, 4))
    k["eps"], k["gn_eps"] = np.full((P, 1), EPS), np.full((P, 1), GN_EPS)
    k["kk_shift"] = np.full((P, 1), 0.5 * math.log(KK_SCALE))
    k["before"] = (r < q).astype(f)
    k["iota"] = np.tile(n[None, :], (P, 1))
    return np.concatenate([k[name].astype(f) for name, _ in CONST], axis=1)
```
